# Optimizing a Trainium2 kernel written in Bass

```python
import math
import jax, jax.numpy as jnp
from jax import lax
import numpy as np

D_MODEL = 1024
BATCH = 1
SEQ = 256
DEPTH = 2

GRID_W = 64
CTX_LEN = 256
ROPE_THETA = 10000.0
NORM_EPS = 1e-6
SUBLN_EPS = 1e-5
LN_EPS = 1e-5
Q_BLOCK = 128

A_GROUPS = 8
A_WIDTH = D_MODEL // 2
A_GROUP_DIM = A_WIDTH // A_GROUPS
A_CHUNK = 128

B_HEADS = 4
B_HEAD_DIM = 64
B_V_DIM = 2 * B_HEAD_DIM
B_WIDTH = B_HEADS * B_V_DIM
B_QK = B_HEADS * 2 * B_HEAD_DIM

EVEN_IN = 3 * A_WIDTH + 2 * B_QK + 2 * B_WIDTH
EVEN_MIX = A_WIDTH + B_WIDTH
EVEN_SPLITS = (A_WIDTH, 2 * A_WIDTH, 3 * A_WIDTH, 3 * A_WIDTH + B_QK,
               3 * A_WIDTH + 2 * B_QK, 3 * A_WIDTH + 2 * B_QK + B_WIDTH)

C_HEADS = 8
C_NOPE = 128
C_ROPE = 64
C_V = 128
C_Q_RANK = 256
C_KV_RANK = 128
C_WIDTH = C_HEADS * C_V
ODD_IN = C_Q_RANK + C_KV_RANK + C_ROPE + C_WIDTH
ODD_SPLITS = (C_Q_RANK, C_Q_RANK + C_KV_RANK, C_Q_RANK + C_KV_RANK + C_ROPE)

N_EVEN = (DEPTH + 1) // 2
N_ODD = DEPTH // 2


F32 = jnp.float32

def rms_norm(x, w, eps=NORM_EPS):
    xf = x.astype(F32)
    y = xf * lax.rsqrt(jnp.mean(xf * xf, axis=-1, keepdims=True) + eps)
    return (y * w.astype(F32)).astype(x.dtype)

def layer_norm(x, w, b, eps=LN_EPS):
    xf = x.astype(F32)
    mu = jnp.mean(xf, axis=-1, keepdims=True)
    xc = xf - mu
    y = xc * lax.rsqrt(jnp.mean(xc * xc, axis=-1, keepdims=True) + eps)
    return (y * w.astype(F32) + b.astype(F32)).astype(x.dtype)

def adaln_terms(cond, w_ada, b_ada):
    m = jax.nn.silu(cond) @ w_ada + b_ada
    return jnp.split(m, 3, axis=-1)

def axial_rope_tables(seq, dim):
    rows = seq // GRID_W
    row = jnp.repeat(jnp.arange(rows), GRID_W).astype(F32)
    col = jnp.tile(jnp.arange(GRID_W), rows).astype(F32)
    half = dim // 2
    inv = ROPE_THETA ** (-jnp.arange(0, half, 2, dtype=F32) / half)
    ang_r = row[:, None] * inv[None, :]
    ang_c = col[:, None] * inv[None, :]
    ang = jnp.concatenate([ang_r, ang_r, ang_c, ang_c], axis=-1)
    return jnp.cos(ang), jnp.sin(ang)

def apply_rope(x, cos, sin):
    extra = x.ndim - 3
    shp = (1, cos.shape[0]) + (1,) * extra + (cos.shape[1],)
    c = cos.reshape(shp)
    s = sin.reshape(shp)
    seg = x.reshape(x.shape[:-1] + (2, 2, x.shape[-1] // 4))
    rot = jnp.concatenate([-seg[..., 1:, :], seg[..., :1, :]], axis=-2).reshape(x.shape)
    return (x.astype(F32) * c + rot.astype(F32) * s).astype(x.dtype)

def sweep_query_blocks(fn, q):
    b, s = q.shape[0], q.shape[1]
    nb = s // Q_BLOCK
    qb = jnp.moveaxis(q.reshape((b, nb, Q_BLOCK) + q.shape[2:]), 1, 0)
    ob = lax.map(fn, qb)
    return jnp.moveaxis(ob, 0, 1).reshape((b, s) + ob.shape[3:])

def spatial_gating(u, v, w_s, b_s, ln_w, ln_b):
    bsz, length, _ = v.shape
    vn = layer_norm(v, ln_w, ln_b)
    vc = vn.reshape(bsz, length // A_CHUNK, A_CHUNK, A_GROUPS, A_GROUP_DIM)
    mixed = jnp.einsum('gpq,bnqgd->bnpgd', w_s, vc) + b_s.T[None, None, :, :, None]
    return u * mixed.reshape(bsz, length, A_WIDTH)

def diff_attn_core(q, k, v, lam):
    s = jnp.einsum('bqhmd,bkhmd->bhmqk', q, k).astype(F32) * (B_HEAD_DIM ** -0.5)
    p = jax.nn.softmax(s, axis=-1)
    a = p[:, :, 0] - lam * p[:, :, 1]
    return jnp.einsum('bhqk,bkhd->bqhd', a.astype(v.dtype), v)

def mla_core(q, k, v):
    s = jnp.einsum('bqhd,bkhd->bhqk', q, k).astype(F32) * ((C_NOPE + C_ROPE) ** -0.5)
    p = jax.nn.softmax(s, axis=-1)
    return jnp.einsum('bhqk,bkhd->bqhd', p.astype(v.dtype), v)

def even_mixer(xl, xc, need_ctx, li, w_in, w_s, b_s, ln_w, ln_b, lq1, lk1, lq2, lk2, subln_w, w_out):
    bsz, seq, _ = xl.shape
    clen = xc.shape[1]
    cos, sin = axial_rope_tables(seq, B_HEAD_DIM)
    lam_init = 0.8 - 0.6 * math.exp(-0.3 * li)
    lam = (jnp.exp(jnp.sum(lq1.astype(F32) * lk1.astype(F32)))
           - jnp.exp(jnp.sum(lq2.astype(F32) * lk2.astype(F32))) + lam_init)

    au_l, av_l, az_l, bq_l, bk_l, bv_l, bz_l = jnp.split(xl @ w_in, EVEN_SPLITS, axis=-1)
    au_c, av_c, az_c, bq_c, bk_c, bv_c, bz_c = jnp.split(xc @ w_in, EVEN_SPLITS, axis=-1)

    def a_branch(u, v, z):
        return spatial_gating(jax.nn.gelu(u, approximate=False), jax.nn.gelu(v, approximate=False),
                              w_s, b_s, ln_w, ln_b) * jax.nn.silu(z)

    def b_post(o, z, length):
        o = rms_norm(o, subln_w, SUBLN_EPS) * (1.0 - lam_init)
        return o.reshape(bsz, length, B_WIDTH) * jax.nn.silu(z)

    qk_shape_l = (bsz, seq, B_HEADS, 2, B_HEAD_DIM)
    qk_shape_c = (bsz, clen, B_HEADS, 2, B_HEAD_DIM)
    q_l = apply_rope(bq_l.reshape(qk_shape_l), cos, sin)
    k_l = apply_rope(bk_l.reshape(qk_shape_l), cos, sin)
    v_l = bv_l.reshape(bsz, seq, B_HEADS, B_V_DIM)
    k_c = bk_c.reshape(qk_shape_c)
    v_c = bv_c.reshape(bsz, clen, B_HEADS, B_V_DIM)
    k_all = jnp.concatenate([k_c, k_l], axis=1)
    v_all = jnp.concatenate([v_c, v_l], axis=1)

    ob_l = sweep_query_blocks(lambda qb: diff_attn_core(qb, k_all, v_all, lam), q_l)
    out_l = jnp.concatenate([a_branch(au_l, av_l, az_l), b_post(ob_l, bz_l, seq)], axis=-1) @ w_out

    out_c = None
    if need_ctx:
        q_c = bq_c.reshape(qk_shape_c)
        ob_c = diff_attn_core(q_c, k_c, v_c, lam)
        out_c = jnp.concatenate([a_branch(au_c, av_c, az_c), b_post(ob_c, bz_c, clen)], axis=-1) @ w_out
    return out_l, out_c

def odd_mixer(xl, xc, need_ctx, w_in, q_norm_w, wq_b, kv_norm_w, wkv_b, w_out):
    bsz, seq, _ = xl.shape
    clen = xc.shape[1]
    cos, sin = axial_rope_tables(seq, C_ROPE)

    cq_l, ckv_l, kr_l, z_l = jnp.split(xl @ w_in, ODD_SPLITS, axis=-1)
    cq_c, ckv_c, kr_c, z_c = jnp.split(xc @ w_in, ODD_SPLITS, axis=-1)

    def queries(cq, length):
        q = (rms_norm(cq, q_norm_w) @ wq_b).reshape(bsz, length, C_HEADS, C_NOPE + C_ROPE)
        return q[..., :C_NOPE], q[..., C_NOPE:]

    def keys_values(ckv, k_rope, length):
        kv = (rms_norm(ckv, kv_norm_w) @ wkv_b).reshape(bsz, length, C_HEADS, C_NOPE + C_V)
        k_rope_h = jnp.broadcast_to(k_rope[:, :, None, :], (bsz, length, C_HEADS, C_ROPE))
        return jnp.concatenate([kv[..., :C_NOPE], k_rope_h], axis=-1), kv[..., C_NOPE:]

    qn_l, qr_l = queries(cq_l, seq)
    q_l = jnp.concatenate([qn_l, apply_rope(qr_l, cos, sin)], axis=-1)
    kr_l_rot = apply_rope(kr_l[:, :, None, :], cos, sin)[:, :, 0, :]
    k_l, v_l = keys_values(ckv_l, kr_l_rot, seq)
    k_c, v_c = keys_values(ckv_c, kr_c, clen)
    k_all = jnp.concatenate([k_c, k_l], axis=1)
    v_all = jnp.concatenate([v_c, v_l], axis=1)

    o_l = sweep_query_blocks(lambda qb: mla_core(qb, k_all, v_all), q_l)
    out_l = (o_l.reshape(bsz, seq, C_WIDTH) * jax.nn.silu(z_l)) @ w_out

    out_c = None
    if need_ctx:
        qn_c, qr_c = queries(cq_c, clen)
        q_c = jnp.concatenate([qn_c, qr_c], axis=-1)
        o_c = mla_core(q_c, k_c, v_c)
        out_c = (o_c.reshape(bsz, clen, C_WIDTH) * jax.nn.silu(z_c)) @ w_out
    return out_l, out_c

def first_inputs(seed: int = 0) -> dict:
    key = jax.random.key(seed)
    ks = jax.random.split(key, 32)
    nrm = jax.random.normal
    D = D_MODEL
    return {
        'x': nrm(ks[0], (BATCH, SEQ, D), F32),
        'c': nrm(ks[1], (BATCH, D), F32),
        'ctx': nrm(ks[2], (BATCH, CTX_LEN, D), F32),
        'c_ctx': nrm(ks[3], (D,), F32),
        'norm_w': 1.0 + 0.02 * nrm(ks[4], (DEPTH, D), F32),
        'ada_w': 0.5 * D ** -0.5 * nrm(ks[5], (DEPTH, D, 3 * D), F32),
        'ada_b': 0.01 * nrm(ks[6], (DEPTH, 3 * D), F32),
        'even_w_in': D ** -0.5 * nrm(ks[7], (N_EVEN, D, EVEN_IN), F32),
        'a_ws': A_CHUNK ** -0.5 * nrm(ks[8], (N_EVEN, A_GROUPS, A_CHUNK, A_CHUNK), F32),
        'a_bs': 1.0 + 0.02 * nrm(ks[9], (N_EVEN, A_GROUPS, A_CHUNK), F32),
        'a_ln_w': 1.0 + 0.02 * nrm(ks[10], (N_EVEN, A_WIDTH), F32),
        'a_ln_b': 0.01 * nrm(ks[11], (N_EVEN, A_WIDTH), F32),
        'b_lq1': 0.1 * nrm(ks[12], (N_EVEN, B_HEAD_DIM), F32),
        'b_lk1': 0.1 * nrm(ks[13], (N_EVEN, B_HEAD_DIM), F32),
        'b_lq2': 0.1 * nrm(ks[14], (N_EVEN, B_HEAD_DIM), F32),
        'b_lk2': 0.1 * nrm(ks[15], (N_EVEN, B_HEAD_DIM), F32),
        'b_subln_w': 1.0 + 0.02 * nrm(ks[16], (N_EVEN, B_V_DIM), F32),
        'even_w_out': EVEN_MIX ** -0.5 * nrm(ks[17], (N_EVEN, EVEN_MIX, D), F32),
        'odd_w_in': D ** -0.5 * nrm(ks[18], (N_ODD, D, ODD_IN), F32),
        'c_q_norm_w': 1.0 + 0.02 * nrm(ks[19], (N_ODD, C_Q_RANK), F32),
        'c_wq_b': C_Q_RANK ** -0.5 * nrm(ks[20], (N_ODD, C_Q_RANK, C_HEADS * (C_NOPE + C_ROPE)), F32),
        'c_kv_norm_w': 1.0 + 0.02 * nrm(ks[21], (N_ODD, C_KV_RANK), F32),
        'c_wkv_b': C_KV_RANK ** -0.5 * nrm(ks[22], (N_ODD, C_KV_RANK, C_HEADS * (C_NOPE + C_V)), F32),
        'odd_w_out': C_WIDTH ** -0.5 * nrm(ks[23], (N_ODD, C_WIDTH, D), F32),
        'final_w': 1.0 + 0.02 * nrm(ks[24], (D,), F32),
    }

def first_block(x, c, ctx, c_ctx, norm_w, ada_w, ada_b, even_w_in, a_ws, a_bs, a_ln_w, a_ln_b,
              b_lq1, b_lk1, b_lq2, b_lk2, b_subln_w, even_w_out, odd_w_in, c_q_norm_w, c_wq_b,
              c_kv_norm_w, c_wkv_b, odd_w_out, final_w):
    h_lat, h_ctx = x, ctx
    for li in range(DEPTH):
        need_ctx = li < DEPTH - 1
        shift_l, scale_l, gate_l = adaln_terms(c, ada_w[li], ada_b[li])
        shift_c, scale_c, gate_c = adaln_terms(c_ctx, ada_w[li], ada_b[li])
        xl = rms_norm(h_lat, norm_w[li]) * (1.0 + scale_l[:, None, :]) + shift_l[:, None, :]
        xc = rms_norm(h_ctx, norm_w[li]) * (1.0 + scale_c) + shift_c
        if li % 2 == 0:
            e = li // 2
            out_l, out_c = even_mixer(xl, xc, need_ctx, li, even_w_in[e], a_ws[e], a_bs[e],
                                      a_ln_w[e], a_ln_b[e], b_lq1[e], b_lk1[e], b_lq2[e], b_lk2[e],
                                      b_subln_w[e], even_w_out[e])
        else:
            o = li // 2
            out_l, out_c = odd_mixer(xl, xc, need_ctx, odd_w_in[o], c_q_norm_w[o], c_wq_b[o],
                                     c_kv_norm_w[o], c_wkv_b[o], odd_w_out[o])
        h_lat = h_lat + gate_l[:, None, :] * out_l
        if need_ctx:
            h_ctx = h_ctx + gate_c * out_c
    return rms_norm(h_lat, final_w)


GLA_HEADS = 4
GLA_VW = D_MODEL // 2
GLA_DV = GLA_VW // GLA_HEADS
GLA_KW = GLA_VW // 2
GLA_DK = GLA_KW // GLA_HEADS
GLA_LORA = 16
GLA_TAU = 16.0
GLA_CHUNK = 64
RWKV_W = D_MODEL - GLA_VW
RWKV_HEAD = 64
RWKV_HEADS = RWKV_W // RWKV_HEAD
RWKV_W_LORA = 32
RWKV_A_LORA = 32
RWKV_G_LORA = 96
RWKV_LNX_EPS = 64e-5
ATT_HEADS = 8
ATT_HEAD = D_MODEL // ATT_HEADS
IDX_HEADS = 8
IDX_DIM = 64
TOPK_MAX = 256
NEG = -1e30
PEER_HEADS = 8
PEER_DKEY = 128
PEER_NKEYS = 128
PEER_N_EXPERTS = PEER_NKEYS * PEER_NKEYS
PEER_TOPK = 16
PEER_TOKEN_BLOCK = 128
DN_ALPHA = (2 * DEPTH) ** 0.25
DN_BETA = (8 * DEPTH) ** -0.25
N_EVEN_2 = (DEPTH + 1) // 2
N_ODD_2 = DEPTH // 2

GLA_SPLITS = (GLA_KW, GLA_KW, GLA_VW, GLA_VW, GLA_LORA)
RWKV_SPLITS = (RWKV_W, RWKV_W, RWKV_W, RWKV_W_LORA, RWKV_A_LORA, RWKV_G_LORA)
GLA_IN = sum(GLA_SPLITS)
RWKV_IN = sum(RWKV_SPLITS)
EVEN_IN_2 = GLA_IN + RWKV_IN
ODD_SPLITS_2 = (ATT_HEADS * ATT_HEAD, ATT_HEAD, ATT_HEAD, IDX_HEADS * IDX_DIM, IDX_DIM, IDX_HEADS)
ODD_IN_2 = sum(ODD_SPLITS_2)


F32_2 = jnp.float32

def _split(t, sizes):
    cuts = [int(c) for c in np.cumsum(sizes)[:-1]]
    return jnp.split(t, cuts, axis=-1)

def layer_norm_2(x, g, b):
    xf = x.astype(F32_2)
    mu = xf.mean(-1, keepdims=True)
    var = jnp.square(xf - mu).mean(-1, keepdims=True)
    return ((xf - mu) * lax.rsqrt(var + LN_EPS) * g + b).astype(x.dtype)

def rope_tables(T, dim):
    inv = ROPE_THETA ** (-jnp.arange(0, dim, 2, dtype=F32_2) / dim)
    ang = jnp.arange(T, dtype=F32_2)[:, None] * inv[None, :]
    return jnp.cos(ang), jnp.sin(ang)

def apply_rope_2(x, cos, sin):
    x1, x2 = jnp.split(x, 2, axis=-1)
    return jnp.concatenate([x1 * cos - x2 * sin, x2 * cos + x1 * sin], -1).astype(x.dtype)

def gla_chunked(q, k, v, log_a):
    B, T, H, dk = q.shape
    dv = v.shape[-1]
    C = GLA_CHUNK
    n = T // C

    def chunks(t):
        return t.astype(F32_2).reshape(B, n, C, H, -1).transpose(0, 3, 1, 2, 4)

    q, k, v, la = chunks(q) * dk ** -0.5, chunks(k), chunks(v), chunks(log_a)
    b = jnp.cumsum(la, axis=3)
    b_last = b[:, :, :, -1:, :]
    q_in = q * jnp.exp(b)
    k_in = k * jnp.exp(-b)
    k_out = k * jnp.exp(b_last - b)
    causal = jnp.tril(jnp.ones((C, C), dtype=bool))
    A = jnp.where(causal, jnp.einsum('bhnid,bhnjd->bhnij', q_in, k_in), 0.0)
    o = jnp.einsum('bhnij,bhnje->bhnie', A, v)
    kv = jnp.einsum('bhnjd,bhnje->bhnde', k_out, v)
    dec = jnp.exp(b_last[:, :, :, 0, :])

    def step(S, inp):
        dec_n, kv_n = inp
        return dec_n[..., None] * S + kv_n, S

    S0 = jnp.zeros((B, H, dk, dv), F32_2)
    _, S_prev = lax.scan(step, S0, (jnp.moveaxis(dec, 2, 0), jnp.moveaxis(kv, 2, 0)))
    S_prev = jnp.moveaxis(S_prev, 0, 2)
    o = o + jnp.einsum('bhnid,bhnde->bhnie', q_in, S_prev)
    return o.transpose(0, 2, 3, 1, 4).reshape(B, T, H, dv)

def rwkv7_scan(r, w, k, v, a, b):
    B, T, H, N = r.shape

    def step(S, inp):
        r_t, w_t, k_t, v_t, a_t, b_t = inp
        sa = jnp.einsum('bhij,bhj->bhi', S, a_t)
        S = S * w_t[:, :, None, :] + sa[..., None] * b_t[:, :, None, :] + v_t[..., None] * k_t[:, :, None, :]
        return S, jnp.einsum('bhij,bhj->bhi', S, r_t)

    xs = tuple(jnp.moveaxis(t.astype(F32_2), 1, 0) for t in (r, w, k, v, a, b))
    _, y = lax.scan(step, jnp.zeros((B, H, N, N), F32_2), xs)
    return jnp.moveaxis(y, 0, 1)

def even_mixer_2(x, w_in, gla_a_w2, gla_a_b, gla_norm_g, rwkv_mu, rwkv_w0, rwkv_w2, rwkv_a0, rwkv_a2,
               rwkv_g2, rwkv_k_k, rwkv_k_a, rwkv_r_k, rwkv_lnx_g, rwkv_lnx_b, w_out):
    B, T, _ = x.shape

    def heads(t, h):
        return t.reshape(B, T, h, -1)

    p = x @ w_in
    gla_p, rw_p = p[..., :GLA_IN], p[..., GLA_IN:]
    gq, gk, gv, gg, gal = _split(gla_p, GLA_SPLITS)
    log_a = jax.nn.log_sigmoid((gal @ gla_a_w2 + gla_a_b).astype(F32_2)) / GLA_TAU
    o = gla_chunked(heads(gq, GLA_HEADS), heads(gk, GLA_HEADS), heads(gv, GLA_HEADS), heads(log_a, GLA_HEADS))
    o = o * lax.rsqrt(jnp.mean(jnp.square(o), -1, keepdims=True) + LN_EPS) * gla_norm_g
    gla_out = (o.reshape(B, T, GLA_VW) * jax.nn.silu(gg.astype(F32_2))).astype(x.dtype)
    prev = jnp.pad(rw_p, ((0, 0), (1, 0), (0, 0)))[:, :-1]
    rw_p = rw_p + (prev - rw_p) * rwkv_mu
    r, k, v, wl, al, gl = _split(rw_p, RWKV_SPLITS)
    w_log = -jax.nn.softplus(-(rwkv_w0 + jnp.tanh(wl) @ rwkv_w2).astype(F32_2)) - 0.5
    decay = jnp.exp(-jnp.exp(w_log))
    a = jax.nn.sigmoid((rwkv_a0 + al @ rwkv_a2).astype(F32_2))
    g = jax.nn.sigmoid(gl) @ rwkv_g2
    kk = heads((k * rwkv_k_k).astype(F32_2), RWKV_HEADS)
    kk = kk / jnp.maximum(jnp.sqrt(jnp.sum(jnp.square(kk), -1, keepdims=True)), 1e-12)
    k = k * (1.0 + (a - 1.0) * rwkv_k_a)
    a_h = heads(a, RWKV_HEADS)
    r_h, k_h, v_h = heads(r, RWKV_HEADS), heads(k, RWKV_HEADS), heads(v, RWKV_HEADS)
    y = rwkv7_scan(r_h, heads(decay, RWKV_HEADS), k_h, v_h, -kk, kk * a_h)
    mu = y.mean(-1, keepdims=True)
    var = jnp.square(y - mu).mean(-1, keepdims=True)
    y = (y - mu) * lax.rsqrt(var + RWKV_LNX_EPS) * rwkv_lnx_g.reshape(RWKV_HEADS, RWKV_HEAD) \
        + rwkv_lnx_b.reshape(RWKV_HEADS, RWKV_HEAD)
    bonus = jnp.sum((r_h * k_h * rwkv_r_k).astype(F32_2), -1, keepdims=True) * v_h.astype(F32_2)
    rwkv_out = ((y + bonus).reshape(B, T, RWKV_W) * g.astype(F32_2)).astype(x.dtype)
    return jnp.concatenate([gla_out, rwkv_out], -1) @ w_out

def dsa_mixer(x, w_in, w_out):
    B, T, _ = x.shape
    q, k, v, qi, ki, wi = _split(x @ w_in, ODD_SPLITS_2)
    q = q.reshape(B, T, ATT_HEADS, ATT_HEAD)
    qi = qi.reshape(B, T, IDX_HEADS, IDX_DIM)
    cos_a, sin_a = rope_tables(T, ATT_HEAD)
    cos_i, sin_i = rope_tables(T, IDX_DIM)
    q = apply_rope_2(q, cos_a[:, None], sin_a[:, None])
    k = apply_rope_2(k, cos_a, sin_a)
    qi = apply_rope_2(qi, cos_i[:, None], sin_i[:, None])
    ki = apply_rope_2(ki, cos_i, sin_i)
    wi = wi.astype(F32_2) * (IDX_HEADS ** -0.5 * IDX_DIM ** -0.5)
    n_sel = min(TOPK_MAX, T // 4)
    key_pos = jnp.arange(T)
    gather = jax.vmap(lambda tab, ids: tab[ids])

    def block(start):
        qb = lax.dynamic_slice_in_dim(q, start, Q_BLOCK, axis=1)
        qib = lax.dynamic_slice_in_dim(qi, start, Q_BLOCK, axis=1)
        wib = lax.dynamic_slice_in_dim(wi, start, Q_BLOCK, axis=1)
        q_pos = start + jnp.arange(Q_BLOCK)
        s = jax.nn.relu(jnp.einsum('bqhd,bsd->bqhs', qib, ki).astype(F32_2))
        score = jnp.einsum('bqh,bqhs->bqs', wib, s)
        score = jnp.where(key_pos[None, None, :] <= q_pos[None, :, None], score, NEG)
        _, sel = lax.top_k(score, n_sel)
        valid = sel <= q_pos[None, :, None]
        ks, vs = gather(k, sel), gather(v, sel)
        logit = jnp.einsum('bqhd,bqkd->bqhk', qb, ks).astype(F32_2) * ATT_HEAD ** -0.5
        logit = jnp.where(valid[:, :, None, :], logit, NEG)
        pr = jax.nn.softmax(logit, axis=-1).astype(vs.dtype)
        return jnp.einsum('bqhk,bqkd->bqhd', pr, vs)

    starts = jnp.arange(T // Q_BLOCK, dtype=jnp.int32) * Q_BLOCK
    o = lax.map(block, starts)
    o = jnp.moveaxis(o, 0, 1).reshape(B, T, ATT_HEADS * ATT_HEAD)
    return o @ w_out

def peer_ffn(x, w_q, sub_keys, exp_u, exp_v):
    B, T, D = x.shape
    q = (x @ w_q).reshape(B, T, PEER_HEADS, 2, PEER_DKEY // 2)
    s = jnp.einsum('bthcd,hcnd->bthcn', q, sub_keys).astype(F32_2)
    top_s, top_i = lax.top_k(s, PEER_TOPK)
    cand_s = (top_s[..., 0, :, None] + top_s[..., 1, None, :]).reshape(B, T, PEER_HEADS, -1)
    cand_i = (top_i[..., 0, :, None] * PEER_NKEYS + top_i[..., 1, None, :]).reshape(B, T, PEER_HEADS, -1)
    best_s, pos = lax.top_k(cand_s, PEER_TOPK)
    idx = jnp.take_along_axis(cand_i, pos, axis=-1)
    gate = jax.nn.softmax(best_s, axis=-1)
    nb = (B * T) // PEER_TOKEN_BLOCK
    hk = PEER_HEADS * PEER_TOPK
    xs = (x.reshape(nb, PEER_TOKEN_BLOCK, D), idx.reshape(nb, PEER_TOKEN_BLOCK, hk),
          gate.reshape(nb, PEER_TOKEN_BLOCK, hk))

    def block(args):
        xb, ib, gb = args
        h = jax.nn.gelu(jnp.einsum('md,mkd->mk', xb, exp_u[ib]).astype(F32_2), approximate=False)
        coef = (gb * h).astype(xb.dtype)
        return jnp.einsum('mk,mkd->md', coef, exp_v[ib])

    return lax.map(block, xs).reshape(B, T, D)

def second_inputs(seed: int = 0) -> dict:
    key = jax.random.key(seed)
    ks = iter(jax.random.split(key, 32))

    def nrm(shape, scale):
        return jax.random.normal(next(ks), shape, F32_2) * scale

    E, O, L, D = N_EVEN_2, N_ODD_2, DEPTH, D_MODEL
    return {
        'x': nrm((BATCH, SEQ, D), 1.0),
        'even_w_in': nrm((E, D, EVEN_IN_2), D ** -0.5),
        'gla_a_w2': nrm((E, GLA_LORA, GLA_KW), GLA_LORA ** -0.5),
        'gla_a_b': nrm((E, GLA_KW), 0.1),
        'gla_norm_g': 1.0 + nrm((E, GLA_DV), 0.05),
        'rwkv_mu': jax.random.uniform(next(ks), (E, RWKV_IN), F32_2, 0.0, 1.0),
        'rwkv_w0': jax.random.uniform(next(ks), (E, RWKV_W), F32_2, -6.5, -1.5),
        'rwkv_w2': nrm((E, RWKV_W_LORA, RWKV_W), 0.1 * RWKV_W_LORA ** -0.5),
        'rwkv_a0': nrm((E, RWKV_W), 0.1),
        'rwkv_a2': nrm((E, RWKV_A_LORA, RWKV_W), 0.5 * RWKV_A_LORA ** -0.5),
        'rwkv_g2': nrm((E, RWKV_G_LORA, RWKV_W), 2.0 * RWKV_G_LORA ** -0.5),
        'rwkv_k_k': 0.85 + nrm((E, RWKV_W), 0.05),
        'rwkv_k_a': 1.0 + nrm((E, RWKV_W), 0.05),
        'rwkv_r_k': nrm((E, RWKV_HEADS, RWKV_HEAD), 0.1),
        'rwkv_lnx_g': 1.0 + nrm((E, RWKV_W), 0.05),
        'rwkv_lnx_b': nrm((E, RWKV_W), 0.02),
        'even_w_out': nrm((E, D, D), DN_BETA * D ** -0.5),
        'odd_w_in': nrm((O, D, ODD_IN_2), D ** -0.5),
        'odd_w_out': nrm((O, D, D), DN_BETA * D ** -0.5),
        'mix_ln_g': 1.0 + nrm((L, D), 0.05),
        'mix_ln_b': nrm((L, D), 0.02),
        'peer_w_q': nrm((L, D, PEER_HEADS * PEER_DKEY), D ** -0.5),
        'peer_sub_keys': nrm((L, PEER_HEADS, 2, PEER_NKEYS, PEER_DKEY // 2), (PEER_DKEY // 2) ** -0.5),
        'peer_u': nrm((L, PEER_N_EXPERTS, D), D ** -0.5),
        'peer_v': nrm((L, PEER_N_EXPERTS, D), DN_BETA * PEER_HEADS ** -0.5),
        'ffn_ln_g': 1.0 + nrm((L, D), 0.05),
        'ffn_ln_b': nrm((L, D), 0.02),
    }

def second_block(x, even_w_in, gla_a_w2, gla_a_b, gla_norm_g, rwkv_mu, rwkv_w0, rwkv_w2, rwkv_a0, rwkv_a2,
              rwkv_g2, rwkv_k_k, rwkv_k_a, rwkv_r_k, rwkv_lnx_g, rwkv_lnx_b, even_w_out, odd_w_in,
              odd_w_out, mix_ln_g, mix_ln_b, peer_w_q, peer_sub_keys, peer_u, peer_v, ffn_ln_g, ffn_ln_b):
    for layer in range(DEPTH):
        i = layer // 2
        if layer % 2 == 0:
            mix = even_mixer_2(x, even_w_in[i], gla_a_w2[i], gla_a_b[i], gla_norm_g[i], rwkv_mu[i], rwkv_w0[i],
                             rwkv_w2[i], rwkv_a0[i], rwkv_a2[i], rwkv_g2[i], rwkv_k_k[i], rwkv_k_a[i],
                             rwkv_r_k[i], rwkv_lnx_g[i], rwkv_lnx_b[i], even_w_out[i])
        else:
            mix = dsa_mixer(x, odd_w_in[i], odd_w_out[i])
        x = layer_norm_2(DN_ALPHA * x + mix, mix_ln_g[layer], mix_ln_b[layer])
        ffn = peer_ffn(x, peer_w_q[layer], peer_sub_keys[layer], peer_u[layer], peer_v[layer])
        x = layer_norm_2(DN_ALPHA * x + ffn, ffn_ln_g[layer], ffn_ln_b[layer])
    return x


def setup_inputs(seed=0):
    out = dict(first_inputs(seed))
    for name, value in second_inputs(seed + 1).items():
        if name != "x":
            out[name + "_2"] = value
    return out


def reference(
    x, c, ctx, c_ctx, norm_w, ada_w, ada_b, even_w_in, a_ws, a_bs, a_ln_w, a_ln_b, b_lq1, b_lk1,
    b_lq2, b_lk2, b_subln_w, even_w_out, odd_w_in, c_q_norm_w, c_wq_b, c_kv_norm_w, c_wkv_b,
    odd_w_out, final_w, even_w_in_2, gla_a_w2_2, gla_a_b_2, gla_norm_g_2, rwkv_mu_2, rwkv_w0_2,
    rwkv_w2_2, rwkv_a0_2, rwkv_a2_2, rwkv_g2_2, rwkv_k_k_2, rwkv_k_a_2, rwkv_r_k_2,
    rwkv_lnx_g_2, rwkv_lnx_b_2, even_w_out_2, odd_w_in_2, odd_w_out_2, mix_ln_g_2, mix_ln_b_2,
    peer_w_q_2, peer_sub_keys_2, peer_u_2, peer_v_2, ffn_ln_g_2, ffn_ln_b_2,
):
    x = first_block(
        x, c, ctx, c_ctx, norm_w, ada_w, ada_b, even_w_in, a_ws, a_bs, a_ln_w, a_ln_b, b_lq1,
        b_lk1, b_lq2, b_lk2, b_subln_w, even_w_out, odd_w_in, c_q_norm_w, c_wq_b, c_kv_norm_w,
        c_wkv_b, odd_w_out, final_w,
    )
    return second_block(
        x, even_w_in_2, gla_a_w2_2, gla_a_b_2, gla_norm_g_2, rwkv_mu_2, rwkv_w0_2, rwkv_w2_2,
        rwkv_a0_2, rwkv_a2_2, rwkv_g2_2, rwkv_k_k_2, rwkv_k_a_2, rwkv_r_k_2, rwkv_lnx_g_2,
        rwkv_lnx_b_2, even_w_out_2, odd_w_in_2, odd_w_out_2, mix_ln_g_2, mix_ln_b_2, peer_w_q_2,
        peer_sub_keys_2, peer_u_2, peer_v_2, ffn_ln_g_2, ffn_ln_b_2,
    )


_drawn_inputs = setup_inputs


def setup_inputs(seed=0):
    import zlib

    import numpy as np

    out = dict(_drawn_inputs(seed))
    spreads = {}
    factors = {'norm_w': 4.775,
     'ada_b': 3.534,
     'a_bs': 7.172,
     'a_ln_w': 7.886,
     'a_ln_b': 8.0,
     'b_lq1': 4.838,
     'b_lk1': 2.781,
     'b_lq2': 200.0,
     'b_lk2': 4.395,
     'b_subln_w': 6.906,
     'c_q_norm_w': 8.0,
     'c_kv_norm_w': 8.0,
     'gla_a_b_2': 4.827,
     'gla_norm_g_2': 4.761,
     'rwkv_w2_2': 8.0,
     'rwkv_a0_2': 3.099,
     'rwkv_k_k_2': 3.323,
     'rwkv_lnx_g_2': 2.803,
     'rwkv_lnx_b_2': 4.949}
    for name, (base, spread) in spreads.items():
        noise = np.random.default_rng([zlib.crc32(name.encode()), seed]).standard_normal(out[name].shape)
        drawn = base * np.exp(spread * noise) if base else spread * noise
        out[name] = __import__('jax').numpy.asarray(drawn.astype(out[name].dtype))
    for name, factor in factors.items():
        out[name] = (out[name] * factor).astype(out[name].dtype)
    return out
```

```python
import math
from contextlib import ExitStack, contextmanager

import numpy as np

import concourse.bass as bass
from concourse import mybir

F32 = mybir.dt.float32
U32 = mybir.dt.uint32
ALU = mybir.AluOpType
ACT = mybir.ActivationFunctionType
AX_X = mybir.AxisListType.X

P = 128
D = 1024
KC = D // P
T = 256
TC = 512
SLOT = 2048
SLOTS = 4
WB = SLOT // KC
BANK = 512
BANKS = 8

A_W, A_G = 512, 8
B_H, B_D, B_V = 4, 64, 128
C_H, C_N, C_R, C_V, C_Q, C_KV = 8, 128, 64, 128, 256, 128
G_H, G_K, G_V, G_LORA, G_TAU = 4, 64, 128, 16, 16.0
R_H, R_N = 8, 64
CH = 64
S_H, S_D, I_H, I_D, TOPK = 8, 128, 8, 64, 64
NEG = -1e30
GONE = -3e38
P_H, P_K, P_N = 8, 16, 128
DN_ALPHA = 4 ** 0.25
DOWN = math.exp(-0.5)


def axial_tables():
    t = np.arange(T)
    half = B_D // 2
    inv = (np.float32(10000.0) ** (-np.arange(0, half, 2, dtype=np.float32) / np.float32(half))).astype(np.float32)
    r = (t // 64)[:, None].astype(np.float32) * inv
    c = (t % 64)[:, None].astype(np.float32) * inv
    ang = np.concatenate([r, r, c, c], -1).astype(np.float32)
    sign = np.tile(np.repeat([-1.0, 1.0], 16), 2)
    return np.cos(ang), np.sin(ang) * sign


def rope_tables(dim):
    inv = (np.float32(10000.0) ** (-np.arange(0, dim, 2, dtype=np.float32) / np.float32(dim))).astype(np.float32)
    ang = np.arange(T, dtype=np.float32)[:, None] * inv
    return np.cos(ang), np.sin(ang)


def constants():
    i = np.arange(P)
    tiles = lambda a: np.concatenate([a[:P], a[P:]], -1)
    parts = {
        "ident": np.eye(P),
        "ones": np.ones((P, P)),
        "headones": (i[:, None] // 64 == i[None, :] // 64) * 1.0,
        "iota": np.tile(i, (P, 1)) * 1.0,
        "iota16": np.tile(np.arange(16), (P, 1)) * 1.0,
        "headsel": (i[:, None] // 64 == np.arange(2)[None, :]) * 1.0,
        "within": np.tile((np.arange(T) % CH != 0) * 1.0, (P, 1)),
    }
    ca, sa = axial_tables()
    parts["axcos"], parts["axsin"] = tiles(ca), tiles(sa)
    c, s = rope_tables(S_D)
    parts["cosA"], parts["sinA"] = tiles(c), tiles(s)
    c, s = rope_tables(I_D)
    parts["cosI"], parts["sinI"] = tiles(c), tiles(s)
    q = np.arange(T)
    causal = (q[None, :] <= q[:, None]) * 1.0
    parts["causal"] = tiles(causal)
    parts["notcausal"] = tiles((1 - causal) * NEG)
    at, off = {}, 0
    for name, a in parts.items():
        at[name] = (off, a.shape[1])
        off += a.shape[1]
    return np.concatenate(list(parts.values()), 1).astype(np.float32), at


def masks():
    i = np.arange(P)
    a, b = i[:, None], i[None, :]
    chunk = a // CH == b // CH
    parts = {"before": chunk & (a < b), "upto": chunk & (a <= b)}
    m = 1
    while m < CH:
        lower = (a // (2 * m) == b // (2 * m)) & ((a // m) % 2 == 1) & ((b // m) % 2 == 0)
        parts[f"join{m}"] = lower
        parts[f"joinT{m}"] = lower.T
        m *= 2
    at, off = {}, 0
    for name, x in parts.items():
        at[name] = (off, x.shape[1])
        off += x.shape[1]
    return np.concatenate(list(parts.values()), 1).astype(np.uint32), at


CONST, CONST_AT = constants()
MASK, MASK_AT = masks()

COLS = [("norm_w", 16), ("ada_b", 48), ("final_w", 8), ("mix_g", 16), ("mix_b", 16), ("ffn_g", 16),
        ("ffn_b", 16), ("mu_rkv", 12), ("w0", 4), ("a0", 4), ("k_k", 4), ("k_a", 4), ("r_k", 4),
        ("gla_a_b", 2), ("a_bs", 8), ("cond", 16)]
COL_AT, _o = {}, 0
for _n, _w in COLS:
    COL_AT[_n] = (_o, _w)
    _o += _w
NCOLS = _o
ROWS = [("a_ln_w", 512), ("a_ln_b", 512), ("subln_w", 128), ("lq1", 64), ("lq2", 64), ("lk1", 64), ("lk2", 64),
        ("q_norm", 256), ("kv_norm", 128), ("gla_g", 128), ("lnx_g", 512), ("lnx_b", 512)]
ROW_AT, _o = {}, 0
for _n, _w in ROWS:
    ROW_AT[_n] = (_o, _w)
    _o += _w
NROWS = _o


class Steps:

    def __init__(self, sem):
        self.sem, self.n = sem, 0

    def step(self, ins):
        ins.then_inc(self.sem, 1)
        self.n += 1
        return self.n

    def settle(self, eng, n=None):
        eng.wait_ge(self.sem, self.n if n is None else n)


def spread(ap, axis, n):
    a = ap.unsqueeze(axis)
    shape = list(a.shape)
    shape[axis] = n
    return a.broadcast_to(shape)


class Core:

    def __init__(self, nc, ctx, dram):
        self.made = {}
        self.nc, self.ctx, self.whole, self.d = nc, ctx, ctx, dram
        self.ident = self.sb("ident", [P, P])
        self.ones = self.sb("ones", [P, P])
        self.cols = self.sb("cols", [P, NCOLS])
        self.ring = [self.sb(f"ring{s}", [P, SLOT]) for s in range(SLOTS)]
        self.bank = [ctx.enter_context(nc.psum_tensor(f"bank{b}", [P, BANK], F32)) for b in range(BANKS)]
        self.landed = [self.sem(f"weights_landed{s}") for s in range(SLOTS)]
        self.filled = self.sem("bank_filled")
        self.drained = {"act": self.sem("act_drained"), "dve": self.sem("dve_drained")}
        self.nfilled = 0
        self.ndrained = {"act": 0, "dve": 0}
        self.dve = Steps(self.sem("dve_step"))
        self.act = Steps(self.sem("act_step"))
        self.pool = Steps(self.sem("pool_step"))
        self.radicand, self.rooted = self.sem("radicand_ready"), self.sem("rooted")
        self.asked = self.answered = 0
        self.plan = []
        self.free_at = []
        self.fed = 0
        self.taken = 0

    def sb(self, name, shape, dt=F32):
        self.made[name] = self.made.get(name, 0) + 1
        if self.made[name] > 1:
            name = f"{name}_{self.made[name]}"
        return self.ctx.enter_context(self.nc.sbuf_tensor(name, shape, dt))

    @contextmanager
    def room(self):
        outer = self.ctx
        with ExitStack() as self.ctx:
            yield
        self.ctx = outer

    def sem(self, name):
        return self.whole.enter_context(self.nc.semaphore(name))

    def col(self, name, i=0, n=1):
        o = COL_AT[name][0] + i
        return self.cols[:, o:o + n]

    def feed(self, sync, count):
        end = min(len(self.plan), self.taken_before + count + SLOTS)
        while self.fed < end:
            b = self.fed
            if b >= SLOTS:
                sync.wait_ge(self.filled, self.free_at[b - SLOTS])
            src, n = self.plan[b]
            dst = self.ring[b % SLOTS][:, 0:n]
            if len(src.shape) == 3:
                dst = dst.rearrange("p (k n) -> p k n", k=src.shape[1])
            sync.dma_start(dst, src).then_inc(self.landed[b % SLOTS], 16)
            self.fed += 1

    def ask_root(self, dve, x, scale, eps):
        dve.tensor_scalar(x, x, scale, eps, ALU.mult, ALU.add).then_inc(self.radicand, 1)
        self.asked += 1
        dve.wait_ge(self.rooted, self.asked)
        self.dve.step(dve.reciprocal(x, x))
        self.dve.settle(dve)

    def root(self, act, x):
        self.answered += 1
        act.wait_ge(self.radicand, self.answered)
        act.activation(x, x, ACT.Sqrt).then_inc(self.rooted, 1)

    def begin(self):
        self.taken_before = self.taken

    def take(self, pe):
        b = self.taken
        pe.wait_ge(self.landed[b % SLOTS], 16 * (b // SLOTS + 1))
        self.taken += 1
        return self.ring[b % SLOTS]

    def release(self):
        self.free_at.append(self.nfilled)


class Fills:

    def __init__(self, k, owners):
        self.k, self.owners = k, owners
        self.base = k.nfilled
        self.dbase = dict(k.ndrained)
        seen = dict(self.dbase)
        self.count = []
        for o in owners:
            seen[o] += 1
            self.count.append((o, seen[o]))
        k.ndrained.update(seen)

    def bank(self, n):
        return self.k.bank[n % BANKS]

    def wait_free(self, pe, n):
        if n >= BANKS:
            owner, count = self.count[n - BANKS]
            pe.wait_ge(self.k.drained[owner], count)

    def wait_drained(self, eng, n):
        owner, count = self.count[n]
        eng.wait_ge(self.k.drained[owner], count)

    def fill(self, ins):
        ins.then_inc(self.k.filled, 1)
        self.k.nfilled += 1

    def wait_full(self, eng, n):
        eng.wait_ge(self.k.filled, self.base + n + 1)

    def drain(self, n, ins):
        ins.then_inc(self.k.drained[self.owners[n]], 1)


def plan_columns(k, w, c0, c1):
    for c in range(c0, c1, WB):
        n = min(WB, c1 - c)
        k.plan.append((w.rearrange("(k p) n -> p k n", p=P)[:, :, c:c + n], KC * n))


def setup(k):
    nc, d = k.nc, k.d
    k.h = k.sb("residual", [P, KC, TC])
    loaded = k.sem("setup_loaded")
    with nc.Block() as block:
        k.begin()

        @block.sync
        def _(sync):
            sync.dma_start(k.cols[:, :], d["cols"]).then_inc(loaded, 16)
            k.feed(sync, 0)

        @block.scalar
        def _(act):
            o = CONST_AT["ident"][0]
            act.dma_start(k.ident[:, :], d["const"][:, o:o + P]).then_inc(loaded, 16)
            o = CONST_AT["ones"][0]
            act.dma_start(k.ones[:, :], d["const"][:, o:o + P]).then_inc(loaded, 16)
            act.dma_start(k.h[:, :, 0:T], d["xT"].rearrange("(k p) t -> p k t", p=P)).then_inc(loaded, 16)
            act.dma_start(k.h[:, :, T:TC], d["ctxT"].rearrange("(k p) t -> p k t", p=P)).then_inc(loaded, 16)
            act.wait_ge(loaded, 80)


def modulation(k):
    nc = k.nc
    k.mod = k.sb("mod", [P, 2, 24, 2])
    cond = k.sb("silu_cond", [P, KC, 2])
    ready = k.sem("cond_ready")
    with nc.Block() as block:
        k.begin()
        fills = Fills(k, ["dve"] * 24)

        @block.scalar
        def _(act):
            act.activation(cond[:, :, :].rearrange("p k c -> p (k c)"), k.col("cond", 0, 16), ACT.Silu).then_inc(ready, 1)

        @block.tensor
        def _(pe):
            pe.wait_ge(ready, 1)
            for n in range(24):
                layer, b = divmod(n, 12)
                w = k.take(pe)
                for f in range(2):
                    out = k.bank[layer][:, (2 * b + f) * 2:(2 * b + f) * 2 + 2]
                    for c in range(KC):
                        mm = pe.matmul(out, w[:, c * WB + f * P:c * WB + f * P + P], cond[:, c, :],
                                       start=(c == 0), stop=(c == KC - 1))
                fills.fill(mm)
                k.release()

        @block.vector
        def _(dve):
            for layer in range(2):
                fills.wait_full(dve, 12 * layer + 11)
                k.dve.step(dve.tensor_tensor(k.mod[:, layer, :, :], k.bank[layer][:, 0:48].rearrange("p (f c) -> p f c", c=2),
                                  spread(k.col("ada_b", 24 * layer, 24), 2, 2), ALU.add))
                k.dve.settle(dve)
                scale = k.mod[:, layer, 8:16, :]
                k.dve.step(dve.scalar_tensor_tensor(out=scale, in0=scale, scalar=1.0,
                                                    in1=spread(k.col("norm_w", 8 * layer, 8), 2, 2),
                                                    op0=ALU.add, op1=ALU.mult))
            k.ndrained["dve"] -= 24

        @block.sync
        def _(sync):
            k.feed(sync, 24)


def rms_modulate(k, layer, tokens, out, square):
    nc = k.nc
    h = k.h
    squared = k.sem(f"squared_{layer}")
    summed = k.sem(f"summed_{layer}")
    scaled = k.sem(f"scaled_{layer}")
    rstd = square[:, 0, 0:tokens]
    with nc.Block() as block:
        k.begin()

        @block.scalar
        def _(act):
            for c in range(KC):
                act.activation(square[:, c, 0:tokens], h[:, c, 0:tokens], ACT.Square).then_inc(squared, 1)
            k.root(act, rstd)
            for c in range(1, KC, 2):
                act.wait_ge(scaled, c + 1)
                if layer is None:
                    k.act.step(act.activation(out[:, c, 0:tokens], out[:, c, 0:tokens], ACT.Copy, scale=k.col("final_w", c)))
                    continue
                for s in range(tokens // T):
                    o = out[:, c, s * T:s * T + T]
                    k.act.step(act.activation(o, o, ACT.Identity, bias=k.mod[:, layer, c, s:s + 1],
                                              scale=k.mod[:, layer, 8 + c, s:s + 1]))

        @block.tensor
        def _(pe):
            for c in range(KC):
                pe.wait_ge(squared, c + 1)
                mm = pe.matmul(k.bank[0][:, 0:tokens], k.ones[:, :], square[:, c, 0:tokens], start=(c == 0), stop=(c == KC - 1))
            mm.then_inc(summed, 1)

        @block.vector
        def _(dve):
            dve.wait_ge(summed, 1)
            k.dve.step(dve.tensor_copy(rstd, k.bank[0][:, 0:tokens]))
            k.dve.settle(dve)
            k.ask_root(dve, rstd, 1.0 / D, 1e-6)
            for c in range(KC):
                dve.tensor_tensor(out[:, c, 0:tokens], h[:, c, 0:tokens], rstd, ALU.mult).then_inc(scaled, 1)
            for c in range(0, KC, 2):
                dve.wait_ge(scaled, c + 1)
                if layer is None:
                    k.dve.step(dve.tensor_scalar(out[:, c, 0:tokens], out[:, c, 0:tokens], k.col("final_w", c), None, ALU.mult))
                    continue
                for s in range(tokens // T):
                    o = out[:, c, s * T:s * T + T]
                    k.dve.step(dve.tensor_scalar(o, o, k.mod[:, layer, 8 + c, s:s + 1], k.mod[:, layer, c, s:s + 1],
                                                 ALU.mult, ALU.add))

        @block.sync
        def _(sync):
            k.feed(sync, 0)


def project_out(k, src, tokens, update, name):
    nc = k.nc
    with nc.Block() as block:
        k.begin()
        fills = Fills(k, ["dve"] * KC)

        @block.tensor
        def _(pe):
            for b in range(D // WB):
                w = k.take(pe)
                for f in range(2):
                    n = 2 * b + f
                    fills.wait_free(pe, n)
                    for c in range(KC):
                        mm = pe.matmul(fills.bank(n)[:, 0:tokens], w[:, c * WB + f * P:c * WB + f * P + P],
                                       src[:, c, 0:tokens], start=(c == 0), stop=(c == KC - 1))
                    fills.fill(mm)
                k.release()

        @block.vector
        def _(dve):
            for n in range(KC):
                fills.wait_full(dve, n)
                fills.drain(n, update(dve, n, fills.bank(n)))

        @block.sync
        def _(sync):
            k.feed(sync, D // WB)


def to_feature_major(k, jobs, name):
    nc = k.nc
    with nc.Block() as block:
        k.begin()
        fills = Fills(k, [("act", "dve")[n % 2] for n in range(len(jobs))])

        @block.tensor
        def _(pe):
            for n, (sources, _) in enumerate(jobs):
                fills.wait_free(pe, n)
                for j, s in enumerate(sources):
                    w = s.shape[1]
                    mm = pe.transpose(fills.bank(n)[0:w, j * P:j * P + P], s, k.ident[:, :])
                fills.fill(mm)

        @block.scalar
        def _(act):
            for n in range(0, len(jobs), 2):
                fills.wait_full(act, n)
                src = fills.bank(n)[0:jobs[n][1].shape[0], 0:len(jobs[n][0]) * P]
                dst = jobs[n][1]
                if len(dst.shape) == 3:
                    src = src.rearrange("p (a b) -> p a b", a=dst.shape[1])
                fills.drain(n, act.activation(dst, src, ACT.Copy))

        @block.vector
        def _(dve):
            for n in range(1, len(jobs), 2):
                fills.wait_full(dve, n)
                src = fills.bank(n)[0:jobs[n][1].shape[0], 0:len(jobs[n][0]) * P]
                dst = jobs[n][1]
                if len(dst.shape) == 3:
                    src = src.rearrange("p (a b) -> p a b", a=dst.shape[1])
                fills.drain(n, dve.tensor_copy(dst, src))

        @block.sync
        def _(sync):
            k.feed(sync, 0)


def rope_axial(pool, k, x, cos, sin, heads, tmp):
    xv = x.rearrange("p (h s e d) -> p (h s) e d", h=heads, s=2, e=2)
    tv = tmp.rearrange("p (h s e d) -> p (h s) e d", h=heads, s=2, e=2)
    x4 = x.rearrange("p (h s e d) -> p h s e d", h=heads, s=2, e=2)
    t4 = tmp.rearrange("p (h s e d) -> p h s e d", h=heads, s=2, e=2)
    s4 = sin.rearrange("p (s e d) -> p s e d", s=2, e=2)
    for s in range(2):
        for e in range(2):
            k.pool.step(pool.tensor_tensor(t4[:, :, s, e, :], x4[:, :, s, 1 - e, :], spread(s4[:, s, e, :], 1, heads), ALU.mult))
    k.pool.settle(pool)
    x3, t3 = x.rearrange("p (h d) -> p h d", h=heads), tmp.rearrange("p (h d) -> p h d", h=heads)
    k.pool.step(pool.tensor_tensor(x3, x3, spread(cos, 1, heads), ALU.mult))
    k.pool.settle(pool)
    k.pool.step(pool.tensor_tensor(x3, x3, t3, ALU.add))


def even_project(k, xn, proj):
    nc = k.nc
    kinds = ["gelu"] * 4 + ["silu"] * 2 + ["copy"] * 6 + ["silu"] * 2
    tiles = TC // P
    with nc.Block() as block:
        k.begin()
        fills = Fills(k, ["dve" if kinds[b] == "copy" else "act" for b in range(14) for _ in range(tiles)])

        @block.tensor
        def _(pe):
            for b in range(14):
                w = k.take(pe)
                for m in range(tiles):
                    n = tiles * b + m
                    fills.wait_free(pe, n)
                    for c in range(KC):
                        mm = pe.matmul(fills.bank(n)[:, 0:WB], xn[:, c, m * P:m * P + P], w[:, c * WB:c * WB + WB],
                                       start=(c == 0), stop=(c == KC - 1))
                    fills.fill(mm)
                k.release()

        @block.scalar
        def _(act):
            for n in range(14 * tiles):
                b, m = divmod(n, tiles)
                if kinds[b] != "copy":
                    fills.wait_full(act, n)
                    f = ACT.Gelu if kinds[b] == "gelu" else ACT.Silu
                    fills.drain(n, act.activation(proj[:, m, b * WB:b * WB + WB], fills.bank(n)[:, 0:WB], f))

        @block.vector
        def _(dve):
            for n in range(14 * tiles):
                b, m = divmod(n, tiles)
                if kinds[b] == "copy":
                    fills.wait_full(dve, n)
                    fills.drain(n, dve.tensor_copy(proj[:, m, b * WB:b * WB + WB], fills.bank(n)[:, 0:WB]))

        @block.sync
        def _(sync):
            k.feed(sync, 14)


def spatial_gating(k, proj, wsT, row, const, mix, lam):
    nc = k.nc
    tmp = k.sb("rope_tmp", [P, B_H * 2 * B_D])
    vn = k.sb("vn", [P, 2, A_W])
    stats = k.sb("stats", [P, 4, 6])
    mean = k.sb("mean", [P, 4, 2])
    rstd = k.sb("rstd", [P, 4])
    lsum = k.sb("lsum", [P, 2])
    lprod = k.sb("lprod", [P, 2 * B_D])
    normed = k.sem("v_normed")
    mixed = k.sem("v_mixed")
    gated = k.sem("gated")
    lams = k.sem("lambda_sums")
    tiles = TC // P
    with nc.Block() as block:
        k.begin()

        @block.gpsimd
        def _(pool):
            for m in range(T // P):
                cos, sin = const("axcos")[:, m * B_D:m * B_D + B_D], const("axsin")[:, m * B_D:m * B_D + B_D]
                for c0 in (3 * A_W, 4 * A_W):
                    rope_axial(pool, k, proj[:, m, c0:c0 + 512], cos, sin, 2 * B_H, tmp[:, :])
                    k.pool.settle(pool)

        @block.tensor
        def _(pe):
            for m in range(tiles):
                pe.wait_ge(normed, m + 1)
                if m >= 2:
                    pe.wait_ge(gated, m - 1)
                for g in range(A_G):
                    mm = pe.matmul(k.bank[m % 2][:, g * 64:g * 64 + 64], wsT[:, g, :], vn[:, m % 2, g * 64:g * 64 + 64],
                                   start=True, stop=True)
                mm.then_inc(mixed, 1)

        @block.vector
        def _(dve):
            S = k.dve

            def norm(m):
                v = proj[:, m, A_W:2 * A_W]
                x = vn[:, m % 2, :]
                if m >= 2:
                    dve.wait_ge(mixed, m - 1)
                S.step(dve.tensor_scalar(x, v, mean[:, m, 0:1], rstd[:, m:m + 1], ALU.subtract, ALU.mult))
                S.settle(dve)
                S.step(dve.tensor_tensor(x, x, row("a_ln_w"), ALU.mult))
                S.settle(dve)
                dve.tensor_tensor(x, x, row("a_ln_b"), ALU.add).then_inc(normed, 1)

            def gate(m):
                dve.wait_ge(mixed, m + 1)
                out = mix[:, m, 0:A_W]
                o3 = out.rearrange("p (g d) -> p g d", g=A_G)
                dve.tensor_tensor(o3, k.bank[m % 2][:, :].rearrange("p (g d) -> p g d", g=A_G),
                                  spread(k.col("a_bs", 0, 8), 2, 64), ALU.add).then_inc(gated, 1)
                dve.wait_ge(gated, m + 1)
                S.step(dve.tensor_tensor(out, out, proj[:, m, 0:A_W], ALU.mult))
                S.settle(dve)
                S.step(dve.tensor_tensor(out, out, proj[:, m, 2 * A_W:3 * A_W], ALU.mult))

            S.step(dve.tensor_tensor(lprod[:, :], row("lq1", 128), row("lk1", 128), ALU.mult))
            S.settle(dve)
            dve.tensor_reduce(lsum[:, :], lprod[:, :].rearrange("p (a b) -> p a b", a=2), AX_X, ALU.add).then_inc(lams, 1)
            for m in range(tiles):
                S.step(dve.bn_stats(stats[:, m, :], proj[:, m, A_W:2 * A_W]))
            S.settle(dve)
            for m in range(tiles):
                S.step(dve.bn_aggr(mean[:, m, :], stats[:, m, :]))
            S.settle(dve)
            S.step(dve.tensor_copy(rstd[:, :], mean[:, :, 1]))
            S.settle(dve)
            k.ask_root(dve, rstd[:, :], 1.0, 1e-5)
            norm(0)
            for m in range(tiles):
                if m + 1 < tiles:
                    norm(m + 1)
                gate(m)
            dve.wait_ge(lams, 2)
            S.step(dve.tensor_tensor(lam, lsum[:, 1:2], lsum[:, 0:1], ALU.subtract))
            S.settle(dve)
            S.step(dve.tensor_scalar(lam, lam, -(0.8 - 0.6 * math.exp(0.0)), None, ALU.add))

        @block.scalar
        def _(act):
            act.wait_ge(lams, 1)
            act.activation(lsum[:, :], lsum[:, :], ACT.Exp).then_inc(lams, 1)
            k.root(act, rstd[:, :])

        @block.sync
        def _(sync):
            k.feed(sync, 0)


def diff_attention(k, proj, qT, kT, row, nlam, mix):
    nc = k.nc
    units = [(m, h) for m in range(TC // P) for h in range(B_H)]
    n_units = len(units)
    prob = k.sb("prob", [P, 2, 2, TC])
    pT = k.sb("pT", [P, 2, TC])
    mx = k.sb("mx", [P, 2, 2])
    sums = k.sb("sums", [P, 2, 2])
    ss = k.sb("ss", [P, len(units)])
    junk = k.sb("junk", [P, B_V])
    scored, maxed, exped = k.sem("scored"), k.sem("maxed"), k.sem("exped")
    combined, turned, turned_out = k.sem("combined"), k.sem("turned"), k.sem("turned_out")
    mixed, squared, finished = k.sem("attended"), k.sem("out_squared"), k.sem("finished")
    keys = lambda m: (0, TC) if m < 2 else (T, TC)
    with nc.Block() as block:
        k.begin()

        @block.tensor
        def _(pe):
            def scores(u):
                m, h = units[u]
                a, b = keys(m)
                if u >= 2:
                    pe.wait_ge(exped, 2 * (u - 1))
                for j in range(2):
                    r = slice(64 * j, 64 * j + 64)
                    pe.matmul(k.bank[4 * (u % 2) + j][:, 0:b - a], qT[r, h, m * P:m * P + P], kT[r, h, a:b],
                              start=True, stop=True).then_inc(scored, 1)

            def turn(u):
                m, h = units[u]
                a, b = keys(m)
                pe.wait_ge(combined, u + 1)
                if u >= 2:
                    pe.wait_ge(turned_out, u - 1)
                for c in range((b - a) // P):
                    mm = pe.transpose(k.bank[4 * (u % 2) + 2][:, c * P:c * P + P], prob[:, u % 2, 0, c * P:c * P + P], k.ident[:, :])
                mm.then_inc(turned, 1)

            def attend(u):
                m, h = units[u]
                a, b = keys(m)
                pe.wait_ge(turned_out, u + 1)
                if u >= 2:
                    pe.wait_ge(finished, u - 1)
                for c in range((b - a) // P):
                    v = proj[:, a // P + c, 5 * A_W + h * B_V:5 * A_W + h * B_V + B_V]
                    mm = pe.matmul(k.bank[4 * (u % 2) + 3][:, 0:B_V], pT[:, u % 2, c * P:c * P + P], v,
                                   start=(c == 0), stop=(c == (b - a) // P - 1))
                mm.then_inc(mixed, 1)

            for u in range(n_units + 1):
                if u < n_units:
                    scores(u)
                if u >= 1:
                    turn(u - 1)
                    attend(u - 1)

        @block.scalar
        def _(act):
            for u in range(n_units + 1):
                if u < n_units:
                    a, b = keys(units[u][0])
                    act.wait_ge(maxed, u + 1)
                    if u >= 2:
                        act.wait_ge(turned, u - 1)
                    for j in range(2):
                        act.activation(prob[:, u % 2, j, 0:b - a], k.bank[4 * (u % 2) + j][:, 0:b - a], ACT.Exp,
                                       bias=mx[:, u % 2, j:j + 1], scale=B_D ** -0.5,
                                       accum_out=sums[:, u % 2, j:j + 1]).then_inc(exped, 1)
                if u >= 1:
                    w = u - 1
                    a, b = keys(units[w][0])
                    act.wait_ge(turned, w + 1)
                    if w >= 2:
                        act.wait_ge(mixed, w - 1)
                    act.activation(pT[:, w % 2, 0:b - a], k.bank[4 * (w % 2) + 2][:, 0:b - a], ACT.Copy).then_inc(turned_out, 1)
                    act.wait_ge(mixed, w + 1)
                    if w >= 2:
                        act.wait_ge(finished, w - 1)
                    if w >= 1:
                        act.wait_ge(squared, w)
                    act.activation(junk[:, :], k.bank[4 * (w % 2) + 3][:, 0:B_V], ACT.Square,
                                   accum_out=ss[:, w:w + 1]).then_inc(squared, 1)
            k.root(act, ss[:, :])

        @block.vector
        def _(dve):
            S = k.dve

            def maxes(u):
                a, b = keys(units[u][0])
                if u >= 2:
                    dve.wait_ge(exped, 2 * (u - 1))
                for j in range(2):
                    dve.wait_ge(scored, 2 * u + j + 1)
                    S.step(dve.reduce_max(mx[:, u % 2, j:j + 1], k.bank[4 * (u % 2) + j][:, 0:b - a], AX_X))
                S.settle(dve)
                dve.tensor_scalar(mx[:, u % 2, :], mx[:, u % 2, :], -(B_D ** -0.5), None, ALU.mult).then_inc(maxed, 1)

            def combine(u):
                a, b = keys(units[u][0])
                s, p0, p1 = sums[:, u % 2, :], prob[:, u % 2, 0, 0:b - a], prob[:, u % 2, 1, 0:b - a]
                dve.wait_ge(exped, 2 * u + 2)
                S.step(dve.reciprocal(s, s))
                S.settle(dve)
                S.step(dve.tensor_scalar(s[:, 1:2], s[:, 1:2], nlam, None, ALU.mult))
                S.step(dve.tensor_scalar(p0, p0, s[:, 0:1], None, ALU.mult))
                S.settle(dve)
                dve.scalar_tensor_tensor(out=p0, in0=p1, scalar=s[:, 1:2], in1=p0, op0=ALU.mult, op1=ALU.add).then_inc(combined, 1)

            def finish(u):
                m, h = units[u]
                out = mix[:, m, A_W + h * B_V:A_W + h * B_V + B_V]
                dve.wait_ge(squared, u + 1)
                dve.tensor_tensor(out, k.bank[4 * (u % 2) + 3][:, 0:B_V], row("subln_w"), ALU.mult).then_inc(finished, 1)
                dve.wait_ge(finished, u + 1)
                z = proj[:, m, 6 * A_W + h * B_V:6 * A_W + h * B_V + B_V]
                S.step(dve.scalar_tensor_tensor(out=out, in0=out, scalar=1.0 - (0.8 - 0.6 * math.exp(0.0)), in1=z,
                                                op0=ALU.mult, op1=ALU.mult))

            for u in range(n_units + 2):
                if u < n_units:
                    maxes(u)
                if 1 <= u <= n_units:
                    combine(u - 1)
                if u >= 2:
                    finish(u - 2)
            k.ask_root(dve, ss[:, :], 1.0 / B_V, 1e-5)
            for m in range(TC // P):
                out = mix[:, m, A_W:D].rearrange("p (h v) -> p h v", h=B_H)
                S.step(dve.tensor_tensor(out, out, spread(ss[:, B_H * m:B_H * m + B_H], 2, B_V), ALU.mult))

        @block.sync
        def _(sync):
            k.feed(sync, 0)


def attention(k, units, n_keys, scores_of, value_of, scale, bias_of, store, name):
    nc = k.nc
    N = len(units)
    nchunk = n_keys // P
    prob = k.sb(f"prob_{name}", [P, 2, n_keys])
    pT = k.sb(f"pT_{name}", [P, 2, n_keys])
    mx = k.sb(f"mx_{name}", [P, 2])
    sums = k.sb(f"sums_{name}", [P, 2])
    scored, maxed, exped = k.sem(f"scored_{name}"), k.sem(f"maxed_{name}"), k.sem(f"exped_{name}")
    normed, turned, turned_out = k.sem(f"normed_{name}"), k.sem(f"turned_{name}"), k.sem(f"turned_out_{name}")
    mixed, stored = k.sem(f"attended_{name}"), k.sem(f"stored_{name}")
    with nc.Block() as block:
        k.begin()

        @block.tensor
        def _(pe):
            for u in range(N + 1):
                if u < N:
                    if u >= 2:
                        pe.wait_ge(exped, u - 1)
                    scores_of(pe, units[u], k.bank[u % 2][:, 0:n_keys]).then_inc(scored, 1)
                if u >= 1:
                    w = u - 1
                    pe.wait_ge(normed, w + 1)
                    if w >= 2:
                        pe.wait_ge(turned_out, w - 1)
                    for c in range(nchunk):
                        mm = pe.transpose(k.bank[2 + w % 2][:, c * P:c * P + P], prob[:, w % 2, c * P:c * P + P], k.ident[:, :])
                    mm.then_inc(turned, 1)
                    pe.wait_ge(turned_out, w + 1)
                    if w >= 2:
                        pe.wait_ge(stored, w - 1)
                    for c in range(nchunk):
                        mm = pe.matmul(k.bank[4 + w % 2][:, 0:P], value_of(units[w], c), pT[:, w % 2, c * P:c * P + P],
                                       start=(c == 0), stop=(c == nchunk - 1))
                    mm.then_inc(mixed, 1)

        @block.scalar
        def _(act):
            for u in range(N + 1):
                if u < N:
                    act.wait_ge(maxed, u + 1)
                    if u >= 2:
                        act.wait_ge(turned, u - 1)
                    src = k.bank[u % 2][:, 0:n_keys] if bias_of is None else prob[:, u % 2, :]
                    act.activation(prob[:, u % 2, :], src, ACT.Exp, bias=mx[:, u % 2:u % 2 + 1],
                                   scale=scale if bias_of is None else 1.0,
                                   accum_out=sums[:, u % 2:u % 2 + 1]).then_inc(exped, 1)
                if u >= 1:
                    w = u - 1
                    act.wait_ge(turned, w + 1)
                    if w >= 2:
                        act.wait_ge(mixed, w - 1)
                    act.activation(pT[:, w % 2, :], k.bank[2 + w % 2][:, 0:n_keys], ACT.Copy).then_inc(turned_out, 1)

        @block.vector
        def _(dve):
            S = k.dve
            for u in range(N + 2):
                if u < N:
                    dve.wait_ge(scored, u + 1)
                    src, m = k.bank[u % 2][:, 0:n_keys], mx[:, u % 2:u % 2 + 1]
                    if u >= 2:
                        dve.wait_ge(exped, u - 1)
                    if bias_of is not None:
                        if u >= 2:
                            dve.wait_ge(turned, u - 1)
                        S.step(dve.scalar_tensor_tensor(out=prob[:, u % 2, :], in0=src, scalar=scale, in1=bias_of(units[u]),
                                                        op0=ALU.mult, op1=ALU.add))
                        S.settle(dve)
                        src = prob[:, u % 2, :]
                    S.step(dve.reduce_max(m, src, AX_X))
                    S.settle(dve)
                    dve.tensor_scalar(m, m, -scale if bias_of is None else -1.0, None, ALU.mult).then_inc(maxed, 1)
                if 1 <= u <= N:
                    w = u - 1
                    s = sums[:, w % 2:w % 2 + 1]
                    dve.wait_ge(exped, w + 1)
                    S.step(dve.reciprocal(s, s))
                    S.settle(dve)
                    dve.tensor_scalar(prob[:, w % 2, :], prob[:, w % 2, :], s, None, ALU.mult).then_inc(normed, 1)
                if u >= 2:
                    w = u - 2
                    dve.wait_ge(mixed, w + 1)
                    store(dve, units[w], k.bank[4 + w % 2][:, 0:P]).then_inc(stored, 1)

        @block.sync
        def _(sync):
            k.feed(sync, 0)


def odd_project(k, xn, cq, ckv, zT):
    nc = k.nc
    jobs = [("cq", m) for m in range(2)] + [("ckv", m) for m in range(4)] + [("z", f) for f in range(8)]
    with nc.Block() as block:
        k.begin()
        fills = Fills(k, ["dve"] * 6 + ["act"] * 8)

        @block.tensor
        def _(pe):
            w = k.take(pe)
            for n, (kind, m) in enumerate(jobs):
                if n in (2, 6, 8, 10, 12):
                    k.release()
                    w = k.take(pe)
                fills.wait_free(pe, n)
                out = fills.bank(n)
                for c in range(KC):
                    if kind == "z":
                        lhs, rhs, o = w[:, c * WB + (m % 2) * P:c * WB + (m % 2) * P + P], xn[:, c, 0:T], out[:, 0:T]
                    else:
                        width = C_Q if kind == "cq" else C_KV + C_R
                        lhs, rhs, o = xn[:, c, m * P:m * P + P], w[:, c * width:c * width + width], out[:, 0:width]
                    mm = pe.matmul(o, lhs, rhs, start=(c == 0), stop=(c == KC - 1))
                fills.fill(mm)
            k.release()

        @block.vector
        def _(dve):
            for n, (kind, m) in enumerate(jobs):
                if kind != "z":
                    fills.wait_full(dve, n)
                    dst = cq[:, m, :] if kind == "cq" else ckv[:, m, 0:C_KV + C_R]
                    fills.drain(n, dve.tensor_copy(dst, fills.bank(n)[:, 0:dst.shape[1]]))

        @block.scalar
        def _(act):
            for n, (kind, m) in enumerate(jobs):
                if kind == "z":
                    fills.wait_full(act, n)
                    fills.drain(n, act.activation(zT[:, m, :], fills.bank(n)[:, 0:T], ACT.Silu))

        @block.sync
        def _(sync):
            k.feed(sync, 6)


def latent_norms(k, cq, ckv, row, const):
    nc = k.nc
    tmp = k.sb("odd_tmp", [P, C_Q])
    ss = k.sb("odd_ss", [P, 6])
    pooltmp = k.sb("krope_tmp", [P, C_R])
    with nc.Block() as block:
        k.begin()

        @block.gpsimd
        def _(pool):
            for m in range(4):
                kr = ckv[:, m, C_KV:C_KV + C_R]
                if m < 2:
                    rope_axial(pool, k, kr, const("axcos")[:, m * 64:m * 64 + 64], const("axsin")[:, m * 64:m * 64 + 64],
                               1, pooltmp[:, :])
                    k.pool.settle(pool)
                k.pool.step(pool.tensor_copy(ckv[:, m, C_KV + C_R:C_KV + 2 * C_R], kr))

        @block.vector
        def _(dve):
            S = k.dve
            jobs = [(cq[:, m, :], "q_norm") for m in range(2)] + [(ckv[:, m, 0:C_KV], "kv_norm") for m in range(4)]
            for n, (x, w) in enumerate(jobs):
                width = x.shape[1]
                s = ss[:, n:n + 1]
                S.step(dve.tensor_tensor(tmp[:, 0:width], x, x, ALU.mult))
                S.settle(dve)
                S.step(dve.tensor_reduce(s, tmp[:, 0:width], AX_X, ALU.add))
                S.settle(dve)
            k.ask_root(dve, ss[:, 0:2], 1.0 / C_Q, 1e-6)
            k.ask_root(dve, ss[:, 2:6], 1.0 / C_KV, 1e-6)
            for n, (x, w) in enumerate(jobs):
                S.step(dve.scalar_tensor_tensor(out=x, in0=x, scalar=ss[:, n:n + 1], in1=row(w), op0=ALU.mult, op1=ALU.mult))

        @block.scalar
        def _(act):
            k.root(act, ss[:, 0:2])
            k.root(act, ss[:, 2:6])

        @block.sync
        def _(sync):
            k.feed(sync, 0)


def odd_queries(k, cqT, ckvT, qnT, qr, knT, v):
    nc = k.nc
    with nc.Block() as block:
        k.begin()
        jobs = []
        for g in range(2):
            jobs += [("qn", g, i) for i in range(2)] + [("qr", g, i) for i in range(2)]
        jobs += [("kn", 0, h) for h in range(C_H)] + [("v", 0, i) for i in range(8)]
        fills = Fills(k, [("act", "dve")[n % 2] for n in range(len(jobs))])

        def piece(n):
            kind, g, i = jobs[n]
            bank = fills.bank(n)
            if kind == "qn":
                h = 4 * g + 2 * i
                return qnT[:, h:h + 2, :], bank[:, :].rearrange("p (h t) -> p h t", h=2)
            if kind == "qr":
                return (qr[:, i, 256 * g:256 * g + 256], bank[:, 0:256])
            if kind == "kn":
                return knT[:, i, :], bank[:, :]
            m, half = divmod(i, 2)
            return v[:, m, 512 * half:512 * half + 512], bank[:, :]

        @block.tensor
        def _(pe):
            for n, (kind, g, i) in enumerate(jobs):
                bank = fills.bank(n)
                if n in (0, 4, 8):
                    if n:
                        k.release()
                    w = k.take(pe)
                    wq = w[:, 0:2 * 768].rearrange("p (k h d) -> p k h d", k=2, h=4)
                    wkv = w[:, :].rearrange("p (h e) -> p h e", h=C_H)
                fills.wait_free(pe, n)
                if kind == "qn":
                    for j in range(2):
                        for c in range(2):
                            mm = pe.matmul(bank[:, j * T:j * T + T], wq[:, c, 2 * i + j, 0:C_N], cqT[:, c, :],
                                           start=(c == 0), stop=(c == 1))
                elif kind == "qr":
                    for c in range(2):
                        mm = pe.matmul(bank[:, 0:256].rearrange("p (h d) -> p h d", h=4), cqT[:, c, i * P:i * P + P], wq[:, c, :, C_N:C_N + C_R],
                                       start=(c == 0), stop=(c == 1))
                elif kind == "kn":
                    mm = pe.matmul(bank[:, :], wkv[:, i, 0:C_N], ckvT[:, :], start=True, stop=True)
                else:
                    m, half = divmod(i, 2)
                    mm = pe.matmul(bank[:, :].rearrange("p (h d) -> p h d", h=4), ckvT[:, m * P:m * P + P], wkv[:, 4 * half:4 * half + 4, C_N:C_N + C_V],
                                   start=True, stop=True)
                fills.fill(mm)
            k.release()

        @block.scalar
        def _(act):
            for n in range(0, len(jobs), 2):
                dst, src = piece(n)
                fills.wait_full(act, n)
                fills.drain(n, act.activation(dst, src, ACT.Copy))

        @block.vector
        def _(dve):
            for n in range(1, len(jobs), 2):
                dst, src = piece(n)
                fills.wait_full(dve, n)
                fills.drain(n, dve.tensor_copy(dst, src))

        @block.sync
        def _(sync):
            k.feed(sync, 3)


def rotate_queries(k, qr, const):
    nc = k.nc
    tmp = k.sb("qrope_tmp", [P, C_H * C_R])
    with nc.Block() as block:
        k.begin()

        @block.gpsimd
        def _(pool):
            for m in range(2):
                rope_axial(pool, k, qr[:, m, :], const("axcos")[:, m * 64:m * 64 + 64], const("axsin")[:, m * 64:m * 64 + 64],
                           C_H, tmp[:, :])
                k.pool.settle(pool)

        @block.sync
        def _(sync):
            k.feed(sync, 0)


def load(k, name, pairs):
    nc = k.nc
    loaded = k.sem(f"loaded_{name}")
    with nc.Block() as block:
        k.begin()

        @block.sync
        def _(sync):
            k.feed(sync, 0)

        @block.scalar
        def _(act):
            for dst, src in pairs:
                act.dma_start(dst, src).then_inc(loaded, 16)
            act.wait_ge(loaded, 16 * len(pairs))


def first_block(k):
    nc, d = k.nc, k.d
    h = k.h

    def residual(layer):
        def update(dve, n, bank):
            tokens = TC if layer == 0 else T
            for s in range(tokens // T):
                o = h[:, n, s * T:s * T + T]
                last = dve.scalar_tensor_tensor(out=o, in0=bank[:, s * T:s * T + T], scalar=k.mod[:, layer, 16 + n, s:s + 1],
                                                in1=o, op0=ALU.mult, op1=ALU.add)
            return last
        return update

    with k.room():
        rows = k.sb("rows", [P, NROWS])
        consts = k.sb("consts", [P, 2 * 128])
        wsT = k.sb("wsT", [P, A_G, P])
        row = lambda name, n=None: rows[:, ROW_AT[name][0]:ROW_AT[name][0] + (n or ROW_AT[name][1])]
        const = lambda name: consts[:, 0:128] if name == "axcos" else consts[:, 128:256]
        o = CONST_AT["axcos"][0]
        load(k, "rows1", [(rows[:, :], d["rows"].partition_broadcast(P)), (consts[:, :], d["const"][:, o:o + 256]),
                          (wsT[:, :, :], d["a_wsT"])])
        modulation(k)
        nlam = k.sb("nlam", [P, 1])
        with k.room():
            proj = k.sb("proj", [P, 4, 7 * A_W])
            with k.room():
                xn = k.sb("xn", [P, KC, TC])
                with k.room():
                    rms_modulate(k, 0, TC, xn, k.sb("square0", [P, KC, TC]))
                even_project(k, xn, proj)
            mix = k.sb("mix", [P, 4, D])
            with k.room():
                spatial_gating(k, proj, wsT, row, const, mix, nlam[:, :])
            qT = k.sb("qT", [P, B_H, TC])
            kT = k.sb("kT", [P, B_H, TC])
            jobs = []
            for c0, dst in ((3 * A_W, qT), (4 * A_W, kT)):
                for m in range(4):
                    jobs.append(([proj[:, m, c0 + P * f:c0 + P * f + P] for f in range(4)], dst[:, :, m * P:m * P + P]))
            to_feature_major(k, jobs, "even_qk")
            with k.room():
                diff_attention(k, proj, qT, kT, row, nlam[:, :], mix)
            mixT = proj[:, :, :].rearrange("p a b -> p (a b)")[:, 0:KC * TC].rearrange("p (k t) -> p k t", k=KC)
            jobs = [([mix[:, m, 512 * g + P * f:512 * g + P * f + P] for f in range(4)], mixT[:, 4 * g:4 * g + 4, m * P:m * P + P])
                    for g in range(2) for m in range(4)]
            to_feature_major(k, jobs, "even_mix")
            project_out(k, mixT, TC, residual(0), "even")
        with k.room():
            cq = k.sb("cq", [P, 2, C_Q])
            ckv = k.sb("ckv", [P, 4, C_KV + 2 * C_R])
            zT = k.sb("zT", [P, C_H, T])
            with k.room():
                xn = k.sb("xn1", [P, KC, TC])
                with k.room():
                    rms_modulate(k, 1, TC, xn, k.sb("square1", [P, KC, TC]))
                odd_project(k, xn, cq, ckv, zT)
            with k.room():
                latent_norms(k, cq, ckv, row, const)
            cqT = k.sb("cqT", [P, 2, T])
            ckvT = k.sb("ckvT", [P, 2, TC])
            jobs = [([cq[:, m, P * f:P * f + P] for f in range(2)], cqT[:, :, m * P:m * P + P]) for m in range(2)]
            jobs += [([ckv[:, m, P * f:P * f + P] for f in range(2)], ckvT[:, :, m * P:m * P + P]) for m in range(4)]
            to_feature_major(k, jobs, "odd_latent")
            qnT = k.sb("qnT", [P, C_H, T])
            qr = k.sb("qr", [P, 2, C_H * C_R])
            qrT = k.sb("qrT", [P, 4, T])
            knT = k.sb("knT", [P, C_H, TC])
            v = k.sb("v_odd", [P, 4, C_H * C_V])
            odd_queries(k, cqT, ckvT[:, 0, :], qnT, qr, knT, v)
            with k.room():
                rotate_queries(k, qr, const)
            to_feature_major(k, [([qr[:, m, P * f:P * f + P] for f in range(4)], qrT[:, :, m * P:m * P + P]) for m in range(2)],
                             "odd_qr")
            mixT = k.sb("mixT1", [P, C_H, T])

            def scores_of(pe, unit, out):
                m, hd = unit
                r = slice(64 * (hd % 2), 64 * (hd % 2) + 64)
                pe.matmul(out, qnT[:, hd, m * P:m * P + P], knT[:, hd, :], start=True, stop=False)
                return pe.matmul(out, qrT[r, hd // 2, m * P:m * P + P], ckvT[r, 1, :], start=False, stop=True)

            def store(dve, unit, bank):
                m, hd = unit
                return dve.tensor_tensor(mixT[:, hd, m * P:m * P + P], bank, zT[:, hd, m * P:m * P + P], ALU.mult)

            with k.room():
                attention(k, [(m, hd) for m in range(2) for hd in range(C_H)], TC, scores_of,
                          lambda unit, c: v[:, c, unit[1] * C_V:unit[1] * C_V + C_V],
                          (C_N + C_R) ** -0.5, None, store, "odd")
            project_out(k, mixT, T, residual(1), "odd")
        with k.room():
            rms_modulate(k, None, T, k.x, k.sb("square2", [P, KC, TC]))


def layer_norm(k, y, g, b, name):
    nc = k.nc
    x = k.x
    square = k.sb("ln_square", [P, KC, T])
    mean = k.sb("ln_mean", [P, T])
    rstd = k.sb("ln_rstd", [P, T])
    summed, centred, squared, scaled = (k.sem(f"{s}_{name}") for s in ("ln_summed", "ln_centred", "ln_squared", "ln_scaled"))
    with nc.Block() as block:
        k.begin()

        @block.tensor
        def _(pe):
            for c in range(KC):
                mm = pe.matmul(k.bank[0][:, 0:T], k.ones[:, :], y[:, c, :], start=(c == 0), stop=(c == KC - 1))
            mm.then_inc(summed, 1)
            for c in range(KC):
                pe.wait_ge(squared, c + 1)
                mm = pe.matmul(k.bank[1][:, 0:T], k.ones[:, :], square[:, c, :], start=(c == 0), stop=(c == KC - 1))
            mm.then_inc(summed, 1)

        @block.vector
        def _(dve):
            S = k.dve
            dve.wait_ge(summed, 1)
            S.step(dve.tensor_scalar(mean[:, :], k.bank[0][:, 0:T], 1.0 / D, None, ALU.mult))
            S.settle(dve)
            for c in range(KC):
                dve.tensor_tensor(y[:, c, :], y[:, c, :], mean[:, :], ALU.subtract).then_inc(centred, 1)
            dve.wait_ge(summed, 2)
            S.step(dve.tensor_copy(rstd[:, :], k.bank[1][:, 0:T]))
            S.settle(dve)
            dve.wait_ge(centred, KC)
            k.ask_root(dve, rstd[:, :], 1.0 / D, 1e-5)
            for c in range(KC):
                dve.tensor_tensor(y[:, c, :], y[:, c, :], rstd[:, :], ALU.mult).then_inc(scaled, 1)
            for c in range(0, KC, 2):
                dve.wait_ge(scaled, c + 1)
                S.step(dve.tensor_scalar(x[:, c, :], y[:, c, :], k.col(g[0], g[1] + c), k.col(b[0], b[1] + c), ALU.mult, ALU.add))

        @block.scalar
        def _(act):
            for c in range(KC):
                act.wait_ge(centred, c + 1)
                act.activation(square[:, c, :], y[:, c, :], ACT.Square).then_inc(squared, 1)
            k.root(act, rstd[:, :])
            for c in range(1, KC, 2):
                act.wait_ge(scaled, c + 1)
                k.act.step(act.activation(x[:, c, :], y[:, c, :], ACT.Identity, bias=k.col(b[0], b[1] + c), scale=k.col(g[0], g[1] + c)))

        @block.sync
        def _(sync):
            k.feed(sync, 0)


def products(k, jobs, blocks, store, owners, name):
    nc = k.nc
    with nc.Block() as block_:
        k.begin()
        fills = Fills(k, owners)

        @block_.tensor
        def _(pe):
            at = -1
            for n, (b, kind, arg) in enumerate(jobs):
                while at < b:
                    if at >= 0:
                        k.release()
                    w = k.take(pe)
                    at += 1
                width = blocks[b]
                fills.wait_free(pe, n)
                bank = fills.bank(n)
                if kind == "token":
                    for c in range(KC):
                        mm = pe.matmul(bank[:, 0:width], k.x[:, c, arg * P:arg * P + P], w[:, c * width:c * width + width],
                                       start=(c == 0), stop=(c == KC - 1))
                else:
                    o = 0
                    for j, f in enumerate(arg):
                        for c in range(KC):
                            mm = pe.matmul(bank[0:f, j * T:j * T + T], w[:, c * width + o:c * width + o + f], k.x[:, c, :],
                                           start=(c == 0), stop=(c == KC - 1))
                        o += f
                fills.fill(mm)
            k.release()

        @block_.scalar
        def _(act):
            for n in range(len(jobs)):
                if owners[n] == "act":
                    fills.wait_full(act, n)
                    fills.drain(n, store("act", act, n, fills.bank(n)))

        @block_.vector
        def _(dve):
            for n in range(len(jobs)):
                if owners[n] == "dve":
                    fills.wait_full(dve, n)
                    fills.drain(n, store("dve", dve, n, fills.bank(n)))

        @block_.sync
        def _(sync):
            k.feed(sync, len(blocks))


def copy(kind, eng, dst, src, func=ACT.Copy):
    if kind == "act":
        return eng.activation(dst, src, func)
    return eng.tensor_copy(dst, src)


GLA_BLOCKS = [256, 256, 256, 256, 256, 256, 16]
RWKV_BLOCKS = [256] * 6 + [160]
RW = 2 * G_H * G_K + 2 * G_H * G_V + G_LORA


def recurrent_project(k, b):
    jobs, owners, where = [], [], []
    for i, name in enumerate(("gq", "gk")):
        jobs.append((i, "feature", (P, P)))
        where.append((b[name][:, :, :], (P, 2 * T)))
        owners.append(("act", "dve")[i])
    for blk in range(2, 6):
        for m in range(2):
            jobs.append((blk, "token", m))
            name = "gv" if blk < 4 else "gg"
            where.append((b[name][:, m, (blk % 2) * WB:(blk % 2) * WB + WB], (P, WB)))
            owners.append("act" if blk >= 4 else "dve")
    jobs.append((6, "feature", (G_LORA,)))
    where.append((b["gal"][:, :], (G_LORA, T)))
    owners.append("dve")
    for i in range(6):
        jobs.append((7 + i, "feature", (P, P)))
        where.append((b["raw"][:, 2 * i:2 * i + 2, :], (P, 2 * T)))
        owners.append(("act", "dve")[i % 2])
    jobs.append((13, "feature", (64, 96)))
    where.append(None)
    owners.append("dve")

    def store(kind, eng, n, bank):
        if where[n] is None:
            k.dve.step(eng.tensor_copy(b["wa"][:, :], bank[0:64, 0:T]))
            return eng.tensor_copy(b["gl"][:, :], bank[0:96, T:2 * T])
        dst, (rows, cols) = where[n]
        src = bank[0:rows, 0:cols]
        if len(dst.shape) == 3:
            src = src.rearrange("p (a t) -> p a t", a=2)
        silu = jobs[n][0] in (4, 5)
        return copy(kind, eng, dst, src, ACT.Silu if silu else ACT.Copy)

    products(k, jobs, GLA_BLOCKS + RWKV_BLOCKS, store, owners, "recurrent")


def recurrent_prepare(k, b, const):
    nc = k.nc
    shift, lshift, t1, t2, gz = b["shift"], b["lshift"], b["t1"], b["t2"], b["gz"]
    shifted = k.sem("shifted")
    lora = k.sem("lora_ready")
    low = k.sem("low_rank_done")
    gates = k.sem("gates_ready")
    logs = k.sem("gla_logs")
    scans = k.sem("scans")
    exps = k.sem("exps")
    norm_sq, norm_sum = k.sem("kk_squared"), k.sem("kk_summed")
    raw, gla_z = b["raw"], gz
    A = lambda x: x[:, :, :]

    def shift_in(eng, S, x, d, c0, c1):
        S.step(eng.tensor_tensor(d[:, c0:c1, 1:T], x[:, c0:c1, 0:T - 1], x[:, c0:c1, 1:T], ALU.subtract))
        S.step(eng.tensor_scalar(d[:, c0:c1, 0:1], x[:, c0:c1, 0:1], -1.0, None, ALU.mult))
        S.settle(eng)
        S.step(eng.tensor_tensor(d[:, c0:c1, :], d[:, c0:c1, :], spread(k.col("mu_rkv", c0, c1 - c0), 2, T), ALU.mult))
        S.settle(eng)
        return eng.tensor_tensor(x[:, c0:c1, :], x[:, c0:c1, :], d[:, c0:c1, :], ALU.add)

    with nc.Block() as block:
        k.begin()

        @block.gpsimd
        def _(pool):
            k.pool.step(shift_in(pool, k.pool, raw, shift, 8, 12))

        @block.tensor
        def _(pe):
            pe.wait_ge(shifted, 2)
            pe.wait_ge(lora, 2)
            for f in range(2):
                mm = pe.matmul(k.bank[0][:, f * T:f * T + T], b["gla_w2"][:, f * P:f * P + P], b["gal"][:, :], start=True, stop=True)
            mm.then_inc(low, 1)
            for f in range(4):
                mm = pe.matmul(k.bank[1 + f // 2][:, (f % 2) * T:(f % 2) * T + T], b["wa2"][0:32, f * P:f * P + P], b["wa"][0:32, :],
                               start=True, stop=True)
            mm.then_inc(low, 1)
            for f in range(4):
                mm = pe.matmul(k.bank[3 + f // 2][:, (f % 2) * T:(f % 2) * T + T], b["wa2"][32:64, f * P:f * P + P], b["wa"][32:64, :],
                               start=True, stop=True)
            mm.then_inc(low, 1)
            for m in range(2):
                mm = pe.matmul(k.bank[5 + m][:, :], b["gl"][:, m * P:m * P + P], b["g2"][:, :], start=True, stop=True)
            mm.then_inc(low, 1)
            pe.wait_ge(norm_sq, 1)
            pe.wait_ge(logs, 1)
            for f in range(4):
                bank = k.bank[7 if f < 2 else 0]
                mm = pe.matmul(bank[:, (f % 2) * T:(f % 2) * T + T], b["headones"], t1[:, f, :], start=True, stop=True)
            mm.then_inc(norm_sum, 1)

        @block.scalar
        def _(act):
            act.wait_ge(shifted, 2)
            act.activation(b["wa"][0:32, :], b["wa"][0:32, :], ACT.Tanh).then_inc(lora, 1)
            act.activation(b["gl"][:, :], b["gl"][:, :], ACT.Sigmoid).then_inc(lora, 1)
            act.wait_ge(low, 2)
            for f in range(4):
                act.activation(b["la"][:, f, :], k.bank[1 + f // 2][:, (f % 2) * T:(f % 2) * T + T], ACT.Sigmoid,
                               bias=k.col("w0", f)).then_inc(gates, 1)
            act.wait_ge(low, 3)
            for f in range(4):
                act.activation(b["a"][:, f, :], k.bank[3 + f // 2][:, (f % 2) * T:(f % 2) * T + T], ACT.Sigmoid,
                               bias=k.col("a0", f)).then_inc(gates, 1)
            act.wait_ge(low, 4)
            for m in range(2):
                act.activation(b["g"][:, m, :], k.bank[5 + m][:, :], ACT.Copy).then_inc(gates, 1)
            act.wait_ge(logs, 1)
            k.act.step(act.activation(A(t2), A(t2), ACT.Exp, scale=-1.0))
            k.act.settle(act)
            act.activation(A(t2), A(t2), ACT.Ln, bias=1.0).then_inc(logs, 1)
            act.wait_ge(scans, 1)
            act.activation(A(b["gdec"]), A(b["gla"]), ACT.Exp).then_inc(exps, 1)
            act.activation(A(b["gneg"]), A(b["gla"]), ACT.Exp, scale=-1.0).then_inc(exps, 1)
            act.wait_ge(scans, 2)
            act.activation(A(b["gout"]), A(b["gout"]), ACT.Exp).then_inc(exps, 1)
            act.wait_ge(scans, 3)
            act.activation(A(b["dec"]), A(b["cum"]), ACT.Exp).then_inc(exps, 1)
            act.activation(A(b["neg"]), A(b["cum"]), ACT.Exp, scale=-1.0).then_inc(exps, 1)
            act.wait_ge(scans, 4)
            act.activation(A(b["la"]), A(b["la"]), ACT.Exp).then_inc(exps, 1)
            k.root(act, A(t1))

        @block.vector
        def _(dve):
            S = k.dve
            for x, rows, j in ((b["wa"], 64, 0), (b["gl"], 96, 1)):
                S.step(dve.tensor_tensor(lshift[0:rows, j, 1:T], x[:, 0:T - 1], x[:, 1:T], ALU.subtract))
                S.step(dve.tensor_scalar(lshift[0:rows, j, 0:1], x[:, 0:1], -1.0, None, ALU.mult))
                S.settle(dve)
                dve.scalar_tensor_tensor(out=x[:, :], in0=lshift[0:rows, j, :], scalar=b["mu_lora"][0:rows, j:j + 1], in1=x[:, :],
                                         op0=ALU.mult, op1=ALU.add).then_inc(shifted, 1)
            S.step(shift_in(dve, S, raw, shift, 0, 8))
            S.settle(dve)
            dve.wait_ge(low, 1)
            S.step(dve.tensor_tensor(A(gz), k.bank[0][:, :].rearrange("p (f t) -> p f t", f=2),
                                     spread(k.col("gla_a_b", 0, 2), 2, T), ALU.add))
            S.settle(dve)
            dve.scalar_tensor_tensor(out=A(t2), in0=A(gz), scalar=-1.0, in1=A(gz), op0=ALU.mult, op1=ALU.max).then_inc(logs, 1)
            S.step(dve.tensor_scalar(A(gz), A(gz), 0.0, None, ALU.min))
            S.step(dve.tensor_tensor(A(b["kk"]), raw[:, 4:8, :], spread(k.col("k_k", 0, 4), 2, T), ALU.mult))
            S.settle(dve)
            dve.tensor_tensor(A(t1), A(b["kk"]), A(b["kk"]), ALU.mult).then_inc(norm_sq, 1)
            dve.wait_ge(logs, 2)
            S.step(dve.tensor_tensor(A(b["gla"]), A(gz), A(t2), ALU.subtract))
            S.settle(dve)
            S.step(dve.tensor_scalar(A(b["gla"]), A(b["gla"]), 1.0 / G_TAU, None, ALU.mult))
            S.settle(dve)
            for f in range(2):
                ins = dve.tensor_tensor_scan(b["gla"][:, f, :], const("within"), b["gla"][:, f, :], 0.0, ALU.mult, ALU.add)
                if f == 0:
                    S.step(ins)
                else:
                    ins.then_inc(scans, 1)
            dve.wait_ge(scans, 1)
            for f in range(2):
                x = b["gla"][:, f, :].rearrange("p (c t) -> p c t", t=CH)
                ins = dve.tensor_tensor(b["gout"][:, f, :].rearrange("p (c t) -> p c t", t=CH),
                                        spread(x[:, :, CH - 1], 2, CH), x, ALU.subtract)
                if f == 0:
                    S.step(ins)
                else:
                    ins.then_inc(scans, 1)
            dve.wait_ge(gates, 4)
            S.step(dve.tensor_scalar(A(b["la"]), A(b["la"]), -DOWN, None, ALU.mult))
            S.settle(dve)
            for f in range(4):
                ins = dve.tensor_tensor_scan(b["cum"][:, f, :], const("within"), b["la"][:, f, :], 0.0, ALU.mult, ALU.add)
                if f < 3:
                    S.step(ins)
                else:
                    ins.then_inc(scans, 1)
            S.settle(dve)
            dve.wait_ge(scans, 3)
            dve.tensor_tensor(A(b["la"]), A(b["cum"]), A(b["la"]), ALU.subtract).then_inc(scans, 1)
            dve.wait_ge(norm_sum, 1)
            for f in range(2):
                S.step(dve.tensor_scalar(t1[:, 2 * f:2 * f + 2, :], k.bank[(7, 0)[f]][:, :].rearrange("p (f t) -> p f t", f=2),
                                         1e-24, None, ALU.max))
            S.settle(dve)
            k.ask_root(dve, A(t1), 1.0, 0.0)
            S.step(dve.tensor_tensor(A(b["kk"]), A(b["kk"]), A(t1), ALU.mult))
            dve.wait_ge(gates, 10)
            S.settle(dve)
            S.step(dve.tensor_scalar(A(t1), A(b["a"]), -1.0, None, ALU.add))
            S.settle(dve)
            S.step(dve.tensor_tensor(A(t1), A(t1), spread(k.col("k_a", 0, 4), 2, T), ALU.mult))
            S.settle(dve)
            S.step(dve.scalar_tensor_tensor(out=A(b["k2"]), in0=A(t1), scalar=1.0, in1=raw[:, 4:8, :], op0=ALU.add, op1=ALU.mult))
            S.settle(dve)
            S.step(dve.tensor_tensor(A(b["rk"]), raw[:, 0:4, :], A(b["k2"]), ALU.mult))
            S.settle(dve)
            S.step(dve.tensor_tensor(A(b["rk"]), A(b["rk"]), spread(k.col("r_k", 0, 4), 2, T), ALU.mult))
            dve.wait_ge(exps, 6)
            S.step(dve.scalar_tensor_tensor(out=A(b["at"]), in0=A(b["kk"]), scalar=-1.0, in1=A(b["la"]), op0=ALU.mult, op1=ALU.mult))
            S.step(dve.tensor_tensor(A(b["bt"]), A(b["kk"]), A(b["a"]), ALU.mult))
            S.settle(dve)
            S.step(dve.tensor_tensor(A(b["bt"]), A(b["bt"]), A(b["neg"]), ALU.mult))
            S.step(dve.tensor_tensor(A(b["kt"]), A(b["k2"]), A(b["neg"]), ALU.mult))
            S.step(dve.tensor_tensor(A(b["rt"]), raw[:, 0:4, :], A(b["dec"]), ALU.mult))
            S.step(dve.scalar_tensor_tensor(out=A(b["gqi"]), in0=A(b["gq"]), scalar=G_K ** -0.5, in1=A(b["gdec"]),
                                            op0=ALU.mult, op1=ALU.mult))
            S.step(dve.tensor_tensor(A(b["gki"]), A(b["gk"]), A(b["gneg"]), ALU.mult))
            S.step(dve.tensor_tensor(A(b["gko"]), A(b["gk"]), A(b["gout"]), ALU.mult))

        @block.sync
        def _(sync):
            k.feed(sync, 0)


def unit(m, h, heads):
    return m * heads + (h % 2) * (heads // 2) + h // 2


def chunk_matrices(k, b, mask):
    nc = k.nc
    filled = k.sem("zeros_ready")
    kinds = [("LT", "bt", "at", "before", 8), ("XT", "bt", "at", "joinT1", 8), ("X", "at", "bt", "join1", 8),
             ("MakT", "kt", "at", "before", 8), ("MrbT", "bt", "rt", "upto", 8), ("MrkT", "kt", "rt", "upto", 8),
             ("AT", "gki", "gqi", "upto", 4)]
    jobs = [(kind, m, g) for kind in kinds for m in range(2) for g in range(2)]
    with nc.Block() as block:
        k.begin()
        fills = Fills(k, ["dve"] * len(jobs))

        @block.gpsimd
        def _(pool):
            for name in ("LT", "MakT", "MrbT", "MrkT", "AT"):
                pool.memset(b[name][:, :, :], 0.0).then_inc(filled, 1)
            pool.memset(b["Z"][:, :, :], 0.0).then_inc(filled, 1)
            pool.memset(b["S"][:, :, :], 0.0).then_inc(filled, 1)
            for name in ("X", "XT"):
                pool.tensor_copy(b[name][:, :, :], spread(k.ident[:, :], 1, 16)).then_inc(filled, 1)

        @block.tensor
        def _(pe):
            for n, ((_, left, right, _, heads), m, g) in enumerate(jobs):
                fills.wait_free(pe, n)
                r = slice(64 * g, 64 * g + 64)
                for j in range(heads // 2):
                    mm = pe.matmul(fills.bank(n)[:, j * P:j * P + P], b[left][r, j, m * P:m * P + P],
                                   b[right][r, j, m * P:m * P + P], start=True, stop=True)
                fills.fill(mm)

        @block.vector
        def _(dve):
            dve.wait_ge(filled, 9)
            for n, ((dst, _, _, which, heads), m, g) in enumerate(jobs):
                fills.wait_full(dve, n)
                u, nu = unit(m, g, heads), heads // 2
                fills.drain(n, dve.copy_predicated(b[dst][:, u:u + nu, :], spread(mask(which), 1, nu),
                                                   fills.bank(n)[:, 0:nu * P].rearrange("p (u t) -> p u t", u=nu)))

        @block.sync
        def _(sync):
            k.feed(sync, 0)


def invert(k, b, mask):
    nc = k.nc
    W = k.sb("LX", [P, 16, P])
    levels = [2 ** i for i in range(1, 6)]
    owners = []
    for _ in levels:
        owners += ["act"] * 4 + ["dve"] * 8
    with nc.Block() as block:
        k.begin()
        fills = Fills(k, owners)

        @block.tensor
        def _(pe):
            n = 0
            for i, _ in enumerate(levels):
                for g in range(4):
                    fills.wait_free(pe, n)
                    if i:
                        fills.wait_drained(pe, n - 12 + 4 - g + 2 * g + 1)
                    for u in range(4 * g, 4 * g + 4):
                        mm = pe.matmul(fills.bank(n)[:, (u % 4) * P:(u % 4) * P + P], b["LT"][:, u, :], b["X"][:, u, :], start=True, stop=True)
                    fills.fill(mm)
                    n += 1
                for g in range(4):
                    fills.wait_drained(pe, n - 4 - g)
                    fills.wait_free(pe, n)
                    for u in range(4 * g, 4 * g + 4):
                        mm = pe.matmul(fills.bank(n)[:, (u % 4) * P:(u % 4) * P + P], b["XT"][:, u, :], W[:, u, :], start=True, stop=True)
                    fills.fill(mm)
                    n += 1
                    fills.wait_free(pe, n)
                    for u in range(4 * g, 4 * g + 4):
                        mm = pe.matmul(fills.bank(n)[:, (u % 4) * P:(u % 4) * P + P], W[:, u, :], b["XT"][:, u, :], start=True, stop=True)
                    fills.fill(mm)
                    n += 1

        @block.scalar
        def _(act):
            for i, _ in enumerate(levels):
                for g in range(4):
                    n = 12 * i + g
                    fills.wait_full(act, n)
                    fills.drain(n, act.activation(W[:, 4 * g:4 * g + 4, :], fills.bank(n)[:, :].rearrange("p (u t) -> p u t", u=4), ACT.Copy))

        @block.vector
        def _(dve):
            for i, m in enumerate(levels):
                for g in range(4):
                    n = 12 * i + 4 + 2 * g
                    fills.wait_full(dve, n + 1)
                    for j, (name, which) in enumerate((("X", f"join{m}"), ("XT", f"joinT{m}"))):
                        fills.drain(n + j, dve.copy_predicated(b[name][:, 4 * g:4 * g + 4, :], spread(mask(which), 1, 4),
                                                               fills.bank(n + j)[:, :].rearrange("p (u t) -> p u t", u=4)))

        @block.sync
        def _(sync):
            k.feed(sync, 0)


def recurrences(k, b):
    nc = k.nc
    R = k.sb("delta_rhs", [P, 512])
    U = k.sb("delta_u", [P, 512])
    pre, pre_out = k.sem("pre_products"), k.sem("pre_drained")
    s1, s1_out, s2, s2_out = k.sem("az"), k.sem("rhs_ready"), k.sem("u_product"), k.sem("u_ready")
    s3, s3_out = k.sem("state_products"), k.sem("states_ready")
    outs, outs_out = k.sem("chunk_outputs"), k.sem("chunk_outputs_drained")
    rows = lambda h: slice(64 * (h % 2), 64 * (h % 2) + 64)
    half = lambda even, odd, h: k.bank[odd if h % 2 else even][:, (h // 2) * 64:(h // 2) * 64 + 64]
    parity = lambda x, q, n: x.rearrange("p (j q e) -> p j q e", q=2, e=n)[:, :, q, :]
    by_head = lambda x, n: x.rearrange("p (j e) -> p j e", e=n)
    with nc.Block() as block:
        k.begin()

        @block.tensor
        def _(pe):
            for m in range(2):
                for h in range(8):
                    mm = pe.matmul(k.bank[m][:, h * 64:h * 64 + 64], b["MakT"][:, unit(m, h, 8), :], b["v"][:, m, h * 64:h * 64 + 64],
                                   start=True, stop=True)
            for m in range(2):
                for f in range(4):
                    mm = pe.matmul(k.bank[2][:, 8 * m + 2 * f:8 * m + 2 * f + 2], b["rk"][:, f, m * P:m * P + P], b["headsel"],
                                   start=True, stop=True)
            mm.then_inc(pre, 1)
            pe.wait_ge(pre_out, 3)
            for c in range(T // CH):
                m, r = c // 2, slice(64 * (c % 2), 64 * (c % 2) + 64)
                t = slice(m * P, m * P + P)
                if c:
                    pe.wait_ge(s3_out, 5 * c)
                    pe.wait_ge(outs_out, 4 * c)
                for h in range(8):
                    mm = pe.matmul(half(0, 6, h), b["at"][rows(h), h // 2, t], b["Z"][rows(h), h // 2, :],
                                   start=True, stop=True)
                mm.then_inc(s1, 1)
                for h in range(4):
                    o = k.bank[(4, 7)[h % 2]][:, (h // 2) * P:(h // 2) * P + P]
                    pe.matmul(o, b["gqi"][rows(h), h // 2, t], b["S"][rows(h), h // 2, :],
                              start=True, stop=False)
                    mm = pe.matmul(o, b["AT"][:, unit(m, h, 4), :], b["gv"][:, m, h * P:h * P + P],
                                   start=False, stop=True)
                mm.then_inc(outs, 1)
                for h in range(4):
                    f = h // 2
                    mm = pe.matmul(k.bank[5][:, h * P:h * P + P], b["gkoT"][r, m, f * P:f * P + P], b["gv"][r, m, h * P:h * P + P],
                                   start=True, stop=True)
                mm.then_inc(s3, 1)
                pe.wait_ge(s1_out, 2 * c + 4)
                for h in range(8):
                    mm = pe.matmul(k.bank[1][:, h * 64:h * 64 + 64], b["XT"][r, unit(m, h, 8), :], R[r, h * 64:h * 64 + 64],
                                   start=True, stop=True)
                mm.then_inc(s2, 1)
                pe.wait_ge(s2_out, c + 1)
                for h in range(8):
                    o, e = half(2, 6, h), slice(h * 64, h * 64 + 64)
                    pe.matmul(o, b["rt"][rows(h), h // 2, t], b["Z"][rows(h), h // 2, :], start=True, stop=False)
                    pe.matmul(o, b["MrbT"][:, unit(m, h, 8), :], U[:, e], start=False, stop=False)
                    mm = pe.matmul(o, b["MrkT"][:, unit(m, h, 8), :], b["v"][:, m, e], start=False, stop=True)
                mm.then_inc(outs, 1)
                for h in range(8):
                    o, e, f = k.bank[3][:, h * 64:h * 64 + 64], slice(h * 64, h * 64 + 64), slice((h // 2) * P, (h // 2) * P + P)
                    pe.matmul(o, b["btT"][r, m, f], U[r, e], start=True, stop=False)
                    mm = pe.matmul(o, b["ktT"][r, m, f], b["v"][r, m, e], start=False, stop=True)
                mm.then_inc(s3, 1)

        @block.vector
        def _(dve):
            S = k.dve
            dve.memset(U[:, :], 0.0).then_inc(s1_out, 1)
            dve.memset(R[:, :], 0.0).then_inc(s1_out, 1)
            dve.wait_ge(s1_out, 2)
            dve.wait_ge(pre, 1)
            for m in range(2):
                dve.tensor_copy(b["MV"][:, m, :], k.bank[m][:, :]).then_inc(pre_out, 1)
            dve.tensor_copy(b["bonus"][:, :], k.bank[2][:, 0:16]).then_inc(pre_out, 1)
            dve.wait_ge(pre_out, 3)
            for c in range(T // CH):
                m, r = c // 2, slice(64 * (c % 2), 64 * (c % 2) + 64)
                last = c * CH + CH - 1
                dve.wait_ge(s1, c + 1)
                for q in range(2):
                    dve.tensor_tensor(parity(R[r, :], q, 64), by_head(k.bank[(0, 6)[q]][r, 0:256], 64),
                                      parity(b["MV"][r, m, :], q, 64), ALU.add).then_inc(s1_out, 1)
                dve.wait_ge(outs, 2 * c + 1)
                S.step(dve.tensor_tensor(b["S"][:, :, :], b["S"][:, :, :], spread(b["gdec"][:, :, last], 2, P), ALU.mult))
                S.settle(dve)
                dve.wait_ge(s3, 2 * c + 1)
                for p in range(2):
                    pr = slice(64 * p, 64 * p + 64)
                    dve.tensor_tensor(b["S"][pr, :, :], b["S"][pr, :, :],
                                      k.bank[5][pr, :].rearrange("p (f q e) -> p f q e", f=2, q=2)[:, :, p, :], ALU.add).then_inc(s3_out, 1)
                dve.wait_ge(s3, 2 * c + 2)
                for p in range(2):
                    pr = slice(64 * p, 64 * p + 64)
                    dve.tensor_tensor(b["Z"][pr, :, :], b["Z"][pr, :, :],
                                      k.bank[3][pr, :].rearrange("p (f q e) -> p f q e", f=4, q=2)[:, :, p, :], ALU.add).then_inc(s3_out, 1)
                dve.wait_ge(s3_out, 5 * c + 4)
                dve.tensor_tensor(b["Z"][:, :, :], b["Z"][:, :, :], spread(b["dec"][:, :, last], 2, 64), ALU.mult).then_inc(s3_out, 1)
                dve.wait_ge(s3_out, 5 * c + 5)

        @block.scalar
        def _(act):
            for c in range(T // CH):
                m, r = c // 2, slice(64 * (c % 2), 64 * (c % 2) + 64)
                act.wait_ge(outs, 2 * c + 1)
                for q in range(2):
                    act.activation(parity(b["go"][r, m, :], q, G_V), by_head(k.bank[(4, 7)[q]][r, 0:256], G_V), ACT.Copy).then_inc(outs_out, 1)
                act.wait_ge(s2, c + 1)
                act.wait_ge(s1_out, 2)
                act.activation(U[r, :], k.bank[1][r, :], ACT.Copy).then_inc(s2_out, 1)
                act.wait_ge(outs, 2 * c + 2)
                for q in range(2):
                    act.activation(parity(b["y"][r, m, :], q, 64), by_head(k.bank[(2, 6)[q]][r, 0:256], 64), ACT.Copy).then_inc(outs_out, 1)

        @block.sync
        def _(sync):
            k.feed(sync, 0)


def recurrent_finish(k, b, row, mix):
    nc = k.nc
    t = k.sb("fin_tmp", [P, 2, 512])
    ss = k.sb("fin_ss", [P, 8])
    mean = k.sb("fin_mean", [P, 16])
    var = k.sb("fin_var", [P, 16])
    go, y = b["go"], b["y"]
    flat = lambda x, n: x[:, :, :].rearrange("p m (h e) -> p (m h) e", e=n)
    with nc.Block() as block:
        k.begin()

        @block.scalar
        def _(act):
            k.root(act, ss[:, :])
            k.root(act, var[:, :])

        @block.vector
        def _(dve):
            S = k.dve

            def do(ins):
                S.step(ins)
                S.settle(dve)

            do(dve.tensor_tensor(t[:, :, :], go[:, :, :], go[:, :, :], ALU.mult))
            do(dve.tensor_reduce(ss[:, :], flat(t, G_V), AX_X, ALU.add))
            k.ask_root(dve, ss[:, :], 1.0 / G_V, 1e-5)
            do(dve.tensor_tensor(flat(go, G_V), flat(go, G_V), spread(ss[:, :], 2, G_V), ALU.mult))
            do(dve.tensor_tensor(flat(go, G_V), flat(go, G_V), spread(row("gla_g"), 1, 8), ALU.mult))
            do(dve.tensor_tensor(mix[:, :, 0:512], go[:, :, :], b["gg"][:, :, :], ALU.mult))
            do(dve.tensor_reduce(mean[:, :], flat(y, 64), AX_X, ALU.add))
            do(dve.tensor_scalar(mean[:, :], mean[:, :], 1.0 / 64, None, ALU.mult))
            do(dve.tensor_tensor(flat(y, 64), flat(y, 64), spread(mean[:, :], 2, 64), ALU.subtract))
            do(dve.tensor_tensor(t[:, :, :], y[:, :, :], y[:, :, :], ALU.mult))
            do(dve.tensor_reduce(var[:, :], flat(t, 64), AX_X, ALU.add))
            k.ask_root(dve, var[:, :], 1.0 / 64, 64e-5)
            do(dve.tensor_tensor(flat(y, 64), flat(y, 64), spread(var[:, :], 2, 64), ALU.mult))
            do(dve.tensor_tensor(y[:, :, :], y[:, :, :], spread(row("lnx_g"), 1, 2), ALU.mult))
            do(dve.tensor_tensor(y[:, :, :], y[:, :, :], spread(row("lnx_b"), 1, 2), ALU.add))
            do(dve.tensor_tensor(flat(t, 64), flat(b["v"], 64), spread(b["bonus"][:, :], 2, 64), ALU.mult))
            do(dve.tensor_tensor(y[:, :, :], y[:, :, :], t[:, :, :], ALU.add))
            do(dve.tensor_tensor(mix[:, :, 512:1024], y[:, :, :], b["g"][:, :, :], ALU.mult))

        @block.sync
        def _(sync):
            k.feed(sync, 0)


def to_residual(k, y):
    def update(dve, n, bank):
        return dve.scalar_tensor_tensor(out=y[:, n, :], in0=k.x[:, n, :], scalar=DN_ALPHA, in1=bank[:, 0:T],
                                        op0=ALU.mult, op1=ALU.add)
    return update


def recurrent_layer(k):
    d = k.d
    c = lambda name: d["const"][:, CONST_AT[name][0]:CONST_AT[name][0] + CONST_AT[name][1]]

    def lay(host, names):
        flat, o = host.rearrange("p a b -> p (a b)"), 0
        for name, n in names:
            b[name] = flat[:, o:o + n * T].rearrange("p (a b) -> p a b", a=n)
            o += n * T
        assert o <= flat.shape[1]

    with k.room():
        b = {}
        cpart = k.sb("cpart", [P, P + 2 + T])
        masks_sb = k.sb("masks", [P, MASK.shape[1]], U32)
        mask = lambda name: masks_sb[:, MASK_AT[name][0]:MASK_AT[name][0] + P]
        b["headones"], b["headsel"] = cpart[:, 0:P], cpart[:, P:P + 2]
        const = lambda name: cpart[:, P + 2:P + 2 + T]
        for n, shape in (("gla_w2", [G_LORA, 256]), ("wa2", [64, 512]), ("g2", [96, 512]), ("mu_lora", [96, 2]),
                         ("gv", [P, 2, 512]), ("gg", [P, 2, 512]), ("g", [P, 2, 512]), ("v", [P, 2, 512]),
                         ("bonus", [P, 16])):
            b[n] = k.sb(n, shape)
        mix = k.sb("mix2", [P, 2, D])
        with k.room():
            for n, f in (("gdec", 2), ("dec", 4), ("gqi", 2), ("at", 4), ("rt", 4), ("rk", 4)):
                b[n] = k.sb(n, [P, f, T])
            matrices = k.sb("matrices", [P, 6 * 16, P])
            b["AT"] = k.sb("AT", [P, 8, P])
            b["Z"] = k.sb("Z", [P, 4, 64])
            b["S"] = k.sb("S", [P, 2, P])
            for n, f in (("gkoT", 256), ("btT", 512), ("ktT", 512)):
                b[n] = k.sb(n, [P, 2, f])
            load(k, "second", [(cpart[:, 0:P], c("headones")),
                               (cpart[:, P:P + 2], c("headsel")), (cpart[:, P + 2:P + 2 + T], c("within")),
                               (masks_sb[:, :], d["mask"]), (b["gla_w2"][:, :], d["gla_a_w2_2"]),
                               (b["wa2"][0:32, :], d["rwkv_w2_2"]), (b["wa2"][32:64, :], d["rwkv_a2_2"]), (b["g2"][:, :], d["rwkv_g2_2"]),
                               (b["mu_lora"][0:64, 0:1], d["mu_lora"][0:64, :]), (b["mu_lora"][0:96, 1:2], d["mu_lora"][64:160, :])])
            with k.room():
                for n, f in (("gko", 2), ("gki", 2), ("bt", 4), ("kt", 4), ("raw", 12)):
                    b[n] = k.sb(n, [P, f, T])
                lay(matrices[:, :, :], [("shift", 12), ("lshift", 2), ("gla", 2), ("gneg", 2), ("gout", 2), ("la", 4),
                                        ("a", 4), ("cum", 4), ("neg", 4), ("kk", 4), ("k2", 4)])
                lay(mix[:, :, :], [("t1", 4), ("t2", 2), ("gz", 2)])
                lay(b["btT"][:, :, :], [("gq", 2), ("gk", 2)])
                lay(b["ktT"][:, :, :], [("gal", 1), ("wa", 1), ("gl", 1)])
                for n, rows_ in (("gal", G_LORA), ("wa", 64), ("gl", 96)):
                    b[n] = b[n][0:rows_, 0, :]
                recurrent_project(k, b)
                with k.room():
                    recurrent_prepare(k, b, const)
                for i, n in enumerate(("X", "XT", "LT", "MrbT", "MrkT", "MakT")):
                    b[n] = matrices[:, 16 * i:16 * i + 16, :]
                chunk_matrices(k, b, mask)
                jobs = []
                for m in range(2):
                    t = slice(m * P, m * P + P)
                    jobs += [([b["raw"][:, 8 + f, t] for f in range(4)], b["v"][:, m, :]), ([b["bt"][:, f, t] for f in range(4)], b["btT"][:, m, :]),
                             ([b["kt"][:, f, t] for f in range(4)], b["ktT"][:, m, :]), ([b["gko"][:, f, t] for f in range(2)], b["gkoT"][:, m, :])]
                to_feature_major(k, jobs, "recurrent")
            with k.room():
                invert(k, b, mask)
            for n in ("MV", "go", "y"):
                b[n] = k.sb(n, [P, 2, 512])
            with k.room():
                recurrences(k, b)
            n0, n1 = ROW_AT["gla_g"][0], NROWS
            rows = k.sb("rows2", [P, n1 - n0])
            row = lambda name: rows[:, ROW_AT[name][0] - n0:ROW_AT[name][0] - n0 + ROW_AT[name][1]]
            load(k, "rows2", [(rows[:, :], d["rows"][n0:n1].partition_broadcast(P))])
            with k.room():
                recurrent_finish(k, b, row, mix)
        mixT = k.sb("mixT2", [P, KC, T])
        y = k.sb("y2", [P, KC, T])
        jobs = [([mix[:, m, 512 * g + P * f:512 * g + P * f + P] for f in range(4)], mixT[:, 4 * g:4 * g + 4, m * P:m * P + P])
                for g in range(2) for m in range(2)]
        to_feature_major(k, jobs, "recurrent_mix")
        project_out(k, mixT, T, to_residual(k, y), "recurrent")
        with k.room():
            layer_norm(k, y, ("mix_g", 0), ("mix_b", 0), "mix0")


DSA_BLOCKS = [WB] * 4 + [2 * S_D] + [WB] * 2 + [I_D + I_H]


def sparse_project(k, b):
    jobs = [(blk, "token", m) for blk in range(8) for m in range(2)]
    owners = [("act", "dve")[n % 2] for n in range(16)]

    def store(kind, eng, n, bank):
        blk, m = n // 2, n % 2
        if blk < 4:
            dst = b["q"][:, m, blk * WB:blk * WB + WB]
        elif blk == 4:
            dst = b["kv"][:, m, :]
        elif blk < 7:
            dst = b["qi"][:, m, (blk - 5) * WB:(blk - 5) * WB + WB]
        else:
            dst = b["kw"][:, m, 0:I_D + I_H]
        return copy(kind, eng, dst, bank[:, 0:DSA_BLOCKS[blk]])

    products(k, jobs, DSA_BLOCKS, store, owners, "sparse")


def rotate_halves(eng, S, x, heads, cos, sin, tmp):
    half = cos.shape[1]
    x3 = x.rearrange("p (g e) -> p g e", e=half)
    t3 = tmp[:, 0:heads * 2 * half].rearrange("p (g e) -> p g e", e=half)
    x4 = x.rearrange("p (h s e) -> p h s e", s=2, e=half)
    t4 = tmp[:, 0:heads * 2 * half].rearrange("p (h s e) -> p h s e", s=2, e=half)
    S.step(eng.tensor_tensor(t3, x3, spread(sin, 1, 2 * heads), ALU.mult))
    S.settle(eng)
    S.step(eng.tensor_tensor(x3, x3, spread(cos, 1, 2 * heads), ALU.mult))
    S.settle(eng)
    S.step(eng.tensor_tensor(x4[:, :, 0, :], x4[:, :, 0, :], t4[:, :, 1, :], ALU.subtract))
    S.step(eng.tensor_tensor(x4[:, :, 1, :], x4[:, :, 1, :], t4[:, :, 0, :], ALU.add))
    S.settle(eng)


def sparse_rotate(k, b, const):
    nc = k.nc
    tmp_q, tmp_i = k.sb("rot_q", [P, D]), k.sb("rot_i", [P, 512])
    with nc.Block() as block:
        k.begin()

        @block.vector
        def _(dve):
            for m in range(2):
                rotate_halves(dve, k.dve, b["q"][:, m, :], S_H, const("cosA", m), const("sinA", m), tmp_q)
                k.dve.step(dve.tensor_scalar(b["wi"][:, m, :], b["kw"][:, m, I_D:I_D + I_H], I_H ** -0.5 * I_D ** -0.5, None, ALU.mult))

        @block.gpsimd
        def _(pool):
            for m in range(2):
                rotate_halves(pool, k.pool, b["kv"][:, m, 0:S_D], 1, const("cosA", m), const("sinA", m), tmp_i)
                rotate_halves(pool, k.pool, b["kw"][:, m, 0:I_D], 1, const("cosI", m), const("sinI", m), tmp_i)
                k.pool.step(pool.tensor_copy(b["ki2"][:, m, 0:I_D], b["kw"][:, m, 0:I_D]))
                k.pool.step(pool.tensor_copy(b["ki2"][:, m, I_D:2 * I_D], b["kw"][:, m, 0:I_D]))
                rotate_halves(pool, k.pool, b["qi"][:, m, :], I_H, const("cosI", m), const("sinI", m), tmp_i)

        @block.sync
        def _(sync):
            k.feed(sync, 0)


def select_keys(k, b, const):
    nc = k.nc
    relu = k.sb("relu", [P, 2, 2, T])
    best = k.sb("best8", [P, 2, 8])
    scored, rectified, used = k.sem("index_scored"), k.sem("rectified"), k.sem("relu_used")
    units = [(h, m) for h in range(I_H) for m in range(2)]
    with nc.Block() as block:
        k.begin()

        @block.tensor
        def _(pe):
            for n, (h, m) in enumerate(units):
                r = slice(64 * (h % 2), 64 * (h % 2) + 64)
                if n >= BANKS:
                    pe.wait_ge(rectified, n - BANKS + 1)
                pe.matmul(k.bank[n % BANKS][:, 0:T], b["qiT"][r, h // 2, m * P:m * P + P], b["ki2T"][r, :],
                          start=True, stop=True).then_inc(scored, 1)

        @block.scalar
        def _(act):
            for n, (h, m) in enumerate(units):
                act.wait_ge(scored, n + 1)
                if n >= 4:
                    act.wait_ge(used, n - 3)
                act.activation(relu[:, (n // 2) % 2, m, :], k.bank[n % BANKS][:, 0:T], ACT.Relu).then_inc(rectified, 1)

        @block.vector
        def _(dve):
            S = k.dve
            score, bias = b["score"], b["bias"]
            for n, (h, m) in enumerate(units):
                dve.wait_ge(rectified, n + 1)
                r, w = relu[:, (n // 2) % 2, m, :], b["wi"][:, m, h:h + 1]
                if h == 0:
                    dve.tensor_scalar(score[:, m, :], r, w, None, ALU.mult).then_inc(used, 1)
                else:
                    dve.wait_ge(used, n - 1)
                    dve.scalar_tensor_tensor(out=score[:, m, :], in0=r, scalar=w, in1=score[:, m, :],
                                             op0=ALU.mult, op1=ALU.add).then_inc(used, 1)
            dve.wait_ge(used, len(units))
            S.step(dve.tensor_tensor(score[:, :, :], score[:, :, :], const("causal"), ALU.mult))
            S.settle(dve)
            S.step(dve.tensor_tensor(score[:, :, :], score[:, :, :], const("notcausal"), ALU.add))
            S.settle(dve)
            for _ in range(TOPK // 8):
                for m in range(2):
                    S.step(dve.max(best[:, m, :], score[:, m, :]))
                S.settle(dve)
                for m in range(2):
                    S.step(dve.match_replace(score[:, m, :], best[:, m, :], score[:, m, :], GONE))
                S.settle(dve)
            S.step(dve.tensor_scalar(bias[:, :, :], score[:, :, :], 10 * NEG, None, ALU.is_lt))
            S.settle(dve)
            S.step(dve.tensor_tensor(bias[:, :, :], bias[:, :, :], const("causal"), ALU.mult))
            S.settle(dve)
            S.step(dve.tensor_scalar(bias[:, :, :], bias[:, :, :], -1.0, -NEG, ALU.add, ALU.mult))

        @block.sync
        def _(sync):
            k.feed(sync, 0)


def sparse_layer(k):
    d = k.d
    with k.room():
        b = {}
        y = k.sb("y3", [P, KC, T])
        mixT = k.sb("mixT3", [P, S_H, T])
        with k.room():
            n0 = CONST_AT["cosA"][0]
            n1 = CONST_AT["notcausal"][0] + CONST_AT["notcausal"][1]
            cs = k.sb("consts3", [P, n1 - n0])

            def const(name, m=None):
                o, n = CONST_AT[name]
                if m is None:
                    return cs[:, o - n0:o - n0 + n].rearrange("p (m t) -> p m t", m=2)
                return cs[:, o - n0 + m * (n // 2):o - n0 + (m + 1) * (n // 2)]

            for name, shape in (("q", [P, 2, D]), ("kv", [P, 2, 2 * S_D]), ("qi", [P, 2, 512]), ("kw", [P, 2, I_D + I_H]),
                                ("ki2", [P, 2, 2 * I_D]), ("wi", [P, 2, I_H]), ("qT", [P, S_H, T]), ("kT", [P, T]),
                                ("qiT", [P, 4, T]), ("ki2T", [P, T]), ("score", [P, 2, T]), ("bias", [P, 2, T])):
                b[name] = k.sb("s_" + name, shape)
            load(k, "sparse", [(cs[:, :], d["const"][:, n0:n1])])
            sparse_project(k, b)
            with k.room():
                sparse_rotate(k, b, const)
            jobs = []
            for m in range(2):
                t = slice(m * P, m * P + P)
                jobs += [([b["q"][:, m, 512 * g + P * f:512 * g + P * f + P] for f in range(4)], b["qT"][:, 4 * g:4 * g + 4, t]) for g in range(2)]
                jobs += [([b["qi"][:, m, P * f:P * f + P] for f in range(4)], b["qiT"][:, :, t]), ([b["kv"][:, m, 0:S_D]], b["kT"][:, t]),
                         ([b["ki2"][:, m, :]], b["ki2T"][:, t])]
            to_feature_major(k, jobs, "sparse")
            with k.room():
                select_keys(k, b, const)

            def scores_of(pe, unit, out):
                m, h = unit
                return pe.matmul(out, b["qT"][:, h, m * P:m * P + P], b["kT"][:, :], start=True, stop=True)

            with k.room():
                attention(k, [(m, h) for m in range(2) for h in range(S_H)], T, scores_of,
                          lambda u, c: b["kv"][:, c, S_D:2 * S_D], S_D ** -0.5, lambda u: b["bias"][:, u[0], :],
                          lambda dve, u, bank: dve.tensor_copy(mixT[:, u[1], u[0] * P:u[0] * P + P], bank), "sparse")
        project_out(k, mixT, T, to_residual(k, y), "sparse")
        with k.room():
            layer_norm(k, y, ("mix_g", 8), ("mix_b", 8), "mix1")


def peer_queries(k, qT):
    jobs = [(blk, "feature", (P, P)) for blk in range(4)]

    def store(kind, eng, n, bank):
        return copy(kind, eng, qT[:, 2 * n:2 * n + 2, :], bank[:, :].rearrange("p (h t) -> p h t", h=2))

    products(k, jobs, [WB] * 4, store, ["act", "dve"] * 2, "peer_q")


def peer_select(k, layer, qT, keys, row_of, col_of, gate, iota16):
    nc = k.nc
    s = k.sb("peer_s", [P, 2, 16, P_N])
    v16 = k.sb("peer_v16", [P, 2, 16, 16])
    i16 = k.sb("peer_i16", [P, 2, 16, 16], U32)
    i16f = k.sb("peer_i16f", [P, 2, 16, 16])
    cand = k.sb("peer_cand", [P, 2, P_H, 256])
    best = k.sb("peer_best", [P, 2, P_H, 16])
    pos = k.sb("peer_pos", [P, 2, P_H, 16], U32)
    half = k.sb("peer_half", [P, 2, 2, P_H * 16], U32)
    halff = k.sb("peer_halff", [P, 2, 2, P_H * 16])
    pick = k.sb("peer_pick", [P, P_H * 16, 16])
    sums = k.sb("peer_sums", [P, 2, P_H])
    shifted, exped = k.sem(f"peer_shifted{layer}"), k.sem(f"peer_exped{layer}")
    with nc.Block() as block:
        k.begin()
        fills = Fills(k, ["act"] * 8)

        @block.tensor
        def _(pe):
            for n in range(8):
                m, g, side = n // 4, (n // 2) % 2, n % 2
                r = slice(64 * side, 64 * side + 64)
                fills.wait_free(pe, n)
                for j in range(4):
                    h = 4 * g + j
                    mm = pe.matmul(fills.bank(n)[:, j * P:j * P + P], qT[r, h, m * P:m * P + P], keys[r, h, :], start=True, stop=True)
                fills.fill(mm)

        @block.scalar
        def _(act):
            for n in range(8):
                m, g, side = n // 4, (n // 2) % 2, n % 2
                fills.wait_full(act, n)
                dst = s[:, m, :, :].rearrange("p (h c) n -> p h c n", c=2)[:, 4 * g:4 * g + 4, side, :]
                fills.drain(n, act.activation(dst, fills.bank(n)[:, :].rearrange("p (h n) -> p h n", h=4), ACT.Copy))
            for m in range(2):
                act.wait_ge(shifted, m + 1)
                act.activation(gate[:, m, :, :], gate[:, m, :, :], ACT.Exp).then_inc(exped, 1)

        @block.vector
        def _(dve):
            S = k.dve

            def top16(rows, values, indices):
                for i, x in enumerate(rows):
                    S.step(dve.max(values(i)[:, 0:8], x))
                S.settle(dve)
                for i, x in enumerate(rows):
                    S.step(dve.max_index(indices(i)[:, 0:8], values(i)[:, 0:8], x))
                S.settle(dve)
                for i, x in enumerate(rows):
                    S.step(dve.match_replace(x, values(i)[:, 0:8], x, GONE))
                S.settle(dve)
                for i, x in enumerate(rows):
                    S.step(dve.max(values(i)[:, 8:16], x))
                S.settle(dve)
                for i, x in enumerate(rows):
                    S.step(dve.max_index(indices(i)[:, 8:16], values(i)[:, 8:16], x))

            for m in range(2):
                fills.wait_full(dve, 4 * m + 3)
                fills.wait_drained(dve, 4 * m + 3)
                top16([s[:, m, i, :] for i in range(16)], lambda i: v16[:, m, i, :], lambda i: i16[:, m, i, :])
                S.settle(dve)
                S.step(dve.tensor_copy(i16f[:, m, :, :], i16[:, m, :, :]))
                vv = v16[:, m, :, :].rearrange("p (h c) n -> p h c n", c=2)
                S.step(dve.tensor_tensor(cand[:, m, :, :].rearrange("p h (a b) -> p h a b", a=16),
                                         spread(vv[:, :, 0, :], 3, 16), spread(vv[:, :, 1, :], 2, 16), ALU.add))
                S.settle(dve)
                top16([cand[:, m, h, :] for h in range(P_H)], lambda i: best[:, m, i, :], lambda i: pos[:, m, i, :])
                S.settle(dve)
                dve.tensor_tensor(gate[:, m, :, :], best[:, m, :, :], spread(best[:, m, :, 0], 2, 16), ALU.subtract).then_inc(shifted, 1)
                p = pos[:, m, :, :].rearrange("p h n -> p (h n)")
                S.step(dve.tensor_single_scalar(half[:, m, 0, :], p, 4, ALU.logical_shift_right))
                S.step(dve.tensor_single_scalar(half[:, m, 1, :], p, 15, ALU.bitwise_and))
                S.settle(dve)
                S.step(dve.tensor_copy(halff[:, m, :, :], half[:, m, :, :]))
                S.settle(dve)
                ii = i16f[:, m, :, :].rearrange("p (h c) n -> p h c n", c=2)
                for side, out in ((0, row_of), (1, col_of)):
                    S.step(dve.tensor_tensor(pick[:, :, :], spread(halff[:, m, side, :], 2, 16), spread(iota16, 1, P_H * 16), ALU.is_equal))
                    S.settle(dve)
                    p4 = pick[:, :, :].rearrange("p (h n) a -> p h n a", h=P_H)
                    S.step(dve.tensor_tensor(p4, p4, spread(ii[:, :, side, :], 2, 16), ALU.mult))
                    S.settle(dve)
                    S.step(dve.tensor_reduce(out[:, m, :], pick[:, :, :], AX_X, ALU.add))
                    S.settle(dve)
                dve.wait_ge(exped, m + 1)
                S.step(dve.tensor_reduce(sums[:, m, :], gate[:, m, :, :], AX_X, ALU.add))
                S.settle(dve)
                S.step(dve.reciprocal(sums[:, m, :], sums[:, m, :]))
                S.settle(dve)
                S.step(dve.tensor_tensor(gate[:, m, :, :], gate[:, m, :, :], spread(sums[:, m, :], 2, 16), ALU.mult))

        @block.sync
        def _(sync):
            k.feed(sync, 0)


PAIR = 2
STREAM = P_N // PAIR


def peer_source(k, layer, side, j):
    if side == "u":
        return k.d["peer_uT"][layer, bass.ds(j, PAIR)].rearrange("j p k i -> p j (k i)")
    return k.d["peer_v_2"][layer].rearrange("(i j) d -> i j d", j=P_N)[:, bass.ds(j, PAIR), :]


def feed_stream(k, sync, layer, side):
    first = k.fed
    base = k.free_at[first - SLOTS]
    with sync.Fori(0, STREAM // SLOTS - 1) as i:
        for s in range(SLOTS):
            slot = (first + s) % SLOTS
            sync.wait_ge(k.filled, i * SLOTS + (base + s))
            sync.dma_start(k.ring[slot][:, :].rearrange("p (j n) -> p j n", j=PAIR),
                           peer_source(k, layer, side, i * (PAIR * SLOTS) + PAIR * (SLOTS + s))).then_inc(k.landed[slot], 16)
    k.fed += STREAM - SLOTS
    k.feed(sync, STREAM)


def begin_stream(k):
    k.begin()
    first, base = k.taken, k.nfilled
    k.taken += STREAM
    k.nfilled += STREAM
    k.free_at += [base + s + 1 for s in range(STREAM)]
    return first, base


def peer_up(k, layer, hidden):
    nc = k.nc
    with nc.Block() as block:
        first, base = begin_stream(k)
        dbase = k.ndrained["act"]
        assert dbase >= SLOTS
        k.ndrained["act"] += STREAM

        @block.tensor
        def _(pe):
            with pe.Fori(0, STREAM // SLOTS) as i:
                for s in range(SLOTS):
                    w = k.ring[(first + s) % SLOTS]
                    pe.wait_ge(k.landed[(first + s) % SLOTS], i * 16 + 16 * ((first + s) // SLOTS + 1))
                    pe.wait_ge(k.drained["act"], i * SLOTS + (dbase + s + 1 - SLOTS))
                    for j in range(PAIR):
                        for c in range(KC):
                            o = j * D + c * P
                            mm = pe.matmul(k.bank[s][:, j * T:j * T + T], w[:, o:o + P], k.x[:, c, :], start=(c == 0), stop=(c == KC - 1))
                    mm.then_inc(k.filled, 1)

        @block.scalar
        def _(act):
            with act.Fori(0, STREAM // SLOTS) as i:
                for s in range(SLOTS):
                    act.wait_ge(k.filled, i * SLOTS + (base + s + 1))
                    act.activation(hidden[:, bass.ds(i * (SLOTS * PAIR * T) + s * PAIR * T, PAIR * T)], k.bank[s][:, :],
                                   ACT.Gelu).then_inc(k.drained["act"], 1)

        @block.sync
        def _(sync):
            feed_stream(k, sync, layer, "u")


GROUP = 4


def peer_gates(k, layer, hidden, rowT, colT, gateT, iota):
    nc = k.nc
    left = k.sb("onehot_rows", [P, 2, GROUP, P])
    right = k.sb("onehot_cols", [P, 2, GROUP, P])
    ready = k.sem(f"onehots_ready{layer}")
    dense = k.sem(f"gates_dense{layer}")
    applied = k.sem(f"gates_applied{layer}")
    hjt = hidden.rearrange("p (j t) -> p j t", t=T)
    with nc.Block() as block:
        k.begin()

        @block.tensor
        def _(pe):
            with pe.Fori(0, T // GROUP // 2) as i:
                for g in range(2):
                    pe.wait_ge(ready, i * 2 + (g + 1))
                    for t in range(GROUP):
                        mm = pe.matmul(k.bank[g][:, t * P:t * P + P], left[:, g, t, :], right[:, g, t, :], start=True, stop=True)
                    mm.then_inc(dense, 1)

        @block.vector
        def _(dve):
            with dve.Fori(0, T // GROUP // 2) as i:
                for g in range(2):
                    for t in range(GROUP):
                        at = bass.ds(i * (2 * GROUP) + (g * GROUP + t), 1)
                        dve.tensor_scalar(left[:, g, t, :], iota, rowT[:, at], gateT[:, at], ALU.is_equal, ALU.mult)
                        ins = dve.tensor_scalar(right[:, g, t, :], iota, colT[:, at], None, ALU.is_equal)
                    ins.then_inc(ready, 1)
                for g in range(2):
                    dve.wait_ge(dense, i * 2 + (g + 1))
                    h = hjt[:, :, bass.ds(i * (2 * GROUP) + g * GROUP, GROUP)]
                    dve.tensor_tensor(h, h, k.bank[g][:, :].rearrange("p (t j) -> p j t", t=GROUP), ALU.mult).then_inc(applied, 1)

        @block.sync
        def _(sync):
            k.feed(sync, 0)


def peer_down(k, layer, hidden):
    nc = k.nc
    zero = k.sb("zero", [P, 2 * T])
    cleared = k.sem(f"down_cleared{layer}")
    done = k.sem(f"down_done{layer}")
    with nc.Block() as block:
        first, base = begin_stream(k)

        @block.tensor
        def _(pe):
            pe.wait_ge(cleared, 1)
            for q in range(4):
                pe.matmul(k.bank[q][:, :], zero[:, 0:P], zero[:, :], start=True, stop=False, skip_group_check=True)
            with pe.Fori(0, STREAM // SLOTS) as i:
                for s in range(SLOTS):
                    w = k.ring[(first + s) % SLOTS]
                    pe.wait_ge(k.landed[(first + s) % SLOTS], i * 16 + 16 * ((first + s) // SLOTS + 1))
                    for j in range(PAIR):
                        h = hidden[:, bass.ds(i * (SLOTS * PAIR * T) + (s * PAIR + j) * T, T)]
                        for c in range(KC):
                            mm = pe.matmul(k.bank[c // 2][:, (c % 2) * T:(c % 2) * T + T], w[:, j * D + c * P:j * D + c * P + P], h,
                                           start=False, stop=False, skip_group_check=True)
                    mm.then_inc(k.filled, 1)
            for q in range(4):
                mm = pe.matmul(k.bank[q][:, :], zero[:, 0:P], zero[:, :], start=False, stop=True, skip_group_check=True)
            mm.then_inc(done, 1)

        @block.vector
        def _(dve):
            dve.memset(zero[:, :], 0.0).then_inc(cleared, 1)
            dve.wait_ge(done, 1)
            for q in range(4):
                x = k.x[:, 2 * q:2 * q + 2, :]
                k.dve.step(dve.scalar_tensor_tensor(out=x, in0=x, scalar=DN_ALPHA, in1=k.bank[q][:, :].rearrange("p (c t) -> p c t", c=2),
                                                    op0=ALU.mult, op1=ALU.add))

        @block.sync
        def _(sync):
            feed_stream(k, sync, layer, "v")


def peer_layer(k, layer):
    d = k.d
    c = lambda name: d["const"][:, CONST_AT[name][0]:CONST_AT[name][0] + CONST_AT[name][1]]
    with k.room():
        iota = k.sb("iota", [P, P])
        iota16 = k.sb("iota16", [P, 16])
        rowT, colT, gateT = (k.sb(n, [P, T]) for n in ("rowT", "colT", "gateT"))
        with k.room():
            qT = k.sb("peer_qT", [P, P_H, T])
            keys = k.sb("peer_keys", [P, P_H, P_N])
            load(k, f"peer{layer}", [(iota[:, :], c("iota")), (iota16[:, :], c("iota16")), (keys[:, :, :], d["sub_keysT"][:, layer])])
            peer_queries(k, qT)
            row_of, col_of = (k.sb(n, [P, 2, P_H * P_K]) for n in ("row_of", "col_of"))
            gate = k.sb("gate", [P, 2, P_H, P_K])
            with k.room():
                peer_select(k, layer, qT, keys, row_of, col_of, gate, iota16[:, :])
            jobs = []
            for src, dst in ((row_of[:, :, :], rowT), (col_of[:, :, :], colT), (gate[:, :, :, :].rearrange("p m h n -> p m (h n)"), gateT)):
                jobs.append(([src[:, m, :] for m in range(2)], dst[:, :]))
            to_feature_major(k, jobs, f"picks{layer}")
        with k.room():
            hidden = k.sb("hidden", [P, P_N * T])
            peer_up(k, layer, hidden[:, :])
            with k.room():
                peer_gates(k, layer, hidden[:, :], rowT, colT, gateT, iota[:, :])
            with k.room():
                peer_down(k, layer, hidden[:, :])
        with k.room():
            y = k.sb("peer_y", [P, KC, T])
            with k.room():
                copy_residual(k, y)
                layer_norm(k, y, ("ffn_g", 8 * layer), ("ffn_b", 8 * layer), f"ffn{layer}")


def copy_residual(k, y):
    nc = k.nc
    with nc.Block() as block:
        k.begin()

        @block.vector
        def _(dve):
            k.dve.step(dve.tensor_copy(y[:, :, :], k.x[:, :, :]))

        @block.sync
        def _(sync):
            k.feed(sync, 0)


def plan_peer(k, layer):
    plan_columns(k, k.d["peer_w_q_2"][layer], 0, D)
    for side in ("u", "v"):
        k.plan += [(peer_source(k, layer, side, PAIR * s), SLOT) for s in range(STREAM)]


def plan_second(k):
    d = k.d
    w, o = d["even_w_in_2"], 0
    for n in GLA_BLOCKS + RWKV_BLOCKS:
        plan_columns(k, w, o, o + n)
        o += n
    plan_columns(k, d["even_w_out_2"], 0, D)
    plan_peer(k, 0)
    o = 0
    for n in DSA_BLOCKS:
        plan_columns(k, d["odd_w_in_2"], o, o + n)
        o += n
    plan_columns(k, d["odd_w_out_2"], 0, D)
    plan_peer(k, 1)


def second_block(k, out):
    nc = k.nc
    recurrent_layer(k)
    peer_layer(k, 0)
    sparse_layer(k)
    peer_layer(k, 1)
    stored = k.sem("out_stored")
    with nc.Block() as block:
        @block.sync
        def _(sync):
            sync.dma_start(out.rearrange("(k p) t -> p k t", p=P), k.x[:, :, :]).then_inc(stored, 16)
            sync.wait_ge(stored, 16)


def plan_weights(k):
    d = k.d
    for layer in range(2):
        plan_columns(k, d["ada_w"][layer], 0, 3 * D)
    plan_columns(k, d["even_w_in"], 0, 7 * A_W)
    plan_columns(k, d["even_w_out"], 0, D)
    plan_columns(k, d["odd_w_in"], 0, C_Q)
    plan_columns(k, d["odd_w_in"], C_Q, C_Q + C_KV + C_R)
    plan_columns(k, d["odd_w_in"], C_Q + C_KV + C_R, C_Q + C_KV + C_R + D)
    for g in range(2):
        k.plan.append((d["c_wq_b"].rearrange("(k p) n -> p k n", p=P)[:, :, 768 * g:768 * g + 768], 2 * 768))
    k.plan.append((d["c_wkv_b"], SLOT))
    plan_columns(k, d["odd_w_out"], 0, D)
    plan_second(k)


def program(nc, d, out):
    with ExitStack() as ctx:
        k = Core(nc, ctx, d)
        plan_weights(k)
        k.x = k.sb("x", [P, KC, T])
        with k.room():
            setup(k)
            first_block(k)
        second_block(k, out)


INPUTS = ["ada_w", "even_w_in", "even_w_out", "odd_w_in", "c_wq_b", "c_wkv_b", "odd_w_out", "even_w_in_2",
          "gla_a_w2_2", "rwkv_w2_2", "rwkv_a2_2", "rwkv_g2_2", "even_w_out_2", "odd_w_in_2", "odd_w_out_2",
          "peer_w_q_2", "peer_v_2"]


def columns(v):
    return np.asarray(v).reshape(-1, P).T


def lay_out(inputs):
    a = {n: np.ascontiguousarray(inputs[n]) for n in INPUTS}
    for n in INPUTS:
        if a[n].ndim == 3 and a[n].shape[0] == 1:
            a[n] = a[n][0]
    f = {n: np.asarray(v) for n, v in inputs.items()}
    a["xT"] = np.ascontiguousarray(f["x"][0].T)
    a["ctxT"] = np.ascontiguousarray(f["ctx"][0].T)
    a["a_wsT"] = np.ascontiguousarray(f["a_ws"][0].transpose(2, 0, 1))
    cond = np.stack([columns(f["c"][0]), columns(f["c_ctx"])], -1).reshape(P, 16)
    mu = f["rwkv_mu_2"][0]
    pack = {"norm_w": columns(f["norm_w"]), "ada_b": columns(f["ada_b"]), "final_w": columns(f["final_w"]),
            "mix_g": columns(f["mix_ln_g_2"]), "mix_b": columns(f["mix_ln_b_2"]), "ffn_g": columns(f["ffn_ln_g_2"]),
            "ffn_b": columns(f["ffn_ln_b_2"]), "mu_rkv": columns(mu[:1536]), "w0": columns(f["rwkv_w0_2"]),
            "a0": columns(f["rwkv_a0_2"]), "k_k": columns(f["rwkv_k_k_2"]), "k_a": columns(f["rwkv_k_a_2"]),
            "r_k": columns(f["rwkv_r_k_2"]), "gla_a_b": columns(f["gla_a_b_2"]), "a_bs": f["a_bs"][0].T, "cond": cond}
    a["cols"] = np.ascontiguousarray(np.concatenate([pack[n] for n, _ in COLS], 1))
    a["mu_lora"] = np.ascontiguousarray(mu[1536:].reshape(-1, 1))
    pack = {"a_ln_w": f["a_ln_w"], "a_ln_b": f["a_ln_b"], "subln_w": f["b_subln_w"], "lq1": f["b_lq1"], "lk1": f["b_lk1"],
            "lq2": f["b_lq2"], "lk2": f["b_lk2"], "q_norm": f["c_q_norm_w"], "kv_norm": f["c_kv_norm_w"],
            "gla_g": f["gla_norm_g_2"], "lnx_g": f["rwkv_lnx_g_2"], "lnx_b": f["rwkv_lnx_b_2"]}
    a["rows"] = np.ascontiguousarray(np.concatenate([pack[n].reshape(-1) for n, _ in ROWS]))
    a["sub_keysT"] = np.ascontiguousarray(f["peer_sub_keys_2"].transpose(2, 4, 0, 1, 3).reshape(P, 2, P_H, P_N))
    a["peer_uT"] = np.ascontiguousarray(f["peer_u_2"].reshape(2, P_N, P_N, KC, P).transpose(0, 2, 4, 3, 1))
    a["const"], a["mask"] = CONST, MASK
    return a


def kernel(**inputs):
    import concourse.bacc as bacc
    from concourse.bass_utils import run_bass_kernel_spmd

    nc = bacc.Bacc("TRN2", target_bir_lowering=False, num_devices=1)
    arrays = {f"in_{n}": a for n, a in lay_out(inputs).items()}
    d = {n[3:]: nc.dram_tensor(n, a.shape, mybir.dt.from_np(a.dtype), kind="ExternalInput").ap() for n, a in arrays.items()}
    out = nc.dram_tensor("out_T", (D, T), F32, kind="ExternalOutput").ap()
    program(nc, d, out)
    r = run_bass_kernel_spmd(nc, [arrays], core_ids=[0])
    return np.ascontiguousarray(r.results[0]["out_T"].T).reshape(1, T, D)
```

```python
import math
from contextlib import ExitStack, contextmanager

import numpy as np

import concourse.bass as bass
from concourse import mybir

F32 = mybir.dt.float32
F32R = mybir.dt.float32r
BF16 = mybir.dt.bfloat16
U32 = mybir.dt.uint32
ALU = mybir.AluOpType
ACT = mybir.ActivationFunctionType
AX_X = mybir.AxisListType.X

P = 128
D = 1024
KC = D // P
T = 256
TC = 512
SLOT = 2048
SLOTS = 4
WB = SLOT // KC
PARTS = 4
PART = SLOT // PARTS
BANK = 512
BANKS = 8

A_W, A_G = 512, 8
B_H, B_D, B_V = 4, 64, 128
C_H, C_N, C_R, C_V, C_Q, C_KV = 8, 128, 64, 128, 256, 128
G_H, G_K, G_V, G_LORA, G_TAU = 4, 64, 128, 16, 16.0
R_H, R_N = 8, 64
CH = 64
S_H, S_D, I_H, I_D, TOPK = 8, 128, 8, 64, 64
NEG = -1e30
GONE = -3e38
P_H, P_K, P_N = 8, 16, 128
DN_ALPHA = 4 ** 0.25
DOWN = math.exp(-0.5)


def axial_tables():
    t = np.arange(T)
    half = B_D // 2
    inv = (np.float32(10000.0) ** (-np.arange(0, half, 2, dtype=np.float32) / np.float32(half))).astype(np.float32)
    r = (t // 64)[:, None].astype(np.float32) * inv
    c = (t % 64)[:, None].astype(np.float32) * inv
    ang = np.concatenate([r, r, c, c], -1).astype(np.float32)
    sign = np.tile(np.repeat([-1.0, 1.0], 16), 2)
    return np.cos(ang), np.sin(ang) * sign


def rope_tables(dim):
    inv = (np.float32(10000.0) ** (-np.arange(0, dim, 2, dtype=np.float32) / np.float32(dim))).astype(np.float32)
    ang = np.arange(T, dtype=np.float32)[:, None] * inv
    return np.cos(ang), np.sin(ang)


def constants():
    i = np.arange(P)
    tiles = lambda a: np.concatenate([a[:P], a[P:]], -1)
    parts = {
        "ident": np.eye(P),
        "ones": np.ones((P, P)),
        "headones": (i[:, None] // 64 == i[None, :] // 64) * 1.0,
        "iota": np.tile(i, (P, 1)) * 1.0,
        "iota16": np.tile(np.arange(16), (P, 1)) * 1.0,
        "headsel": (i[:, None] // 64 == np.arange(2)[None, :]) * 1.0,
        "within": np.tile((np.arange(T) % CH != 0) * 1.0, (P, 1)),
    }
    ca, sa = axial_tables()
    parts["axcos"], parts["axsin"] = tiles(ca), tiles(sa)
    c, s = rope_tables(S_D)
    parts["cosA"], parts["sinA"] = tiles(c), tiles(s)
    c, s = rope_tables(I_D)
    parts["cosI"], parts["sinI"] = tiles(c), tiles(s)
    q = np.arange(T)
    causal = (q[None, :] <= q[:, None]) * 1.0
    parts["causal"] = tiles(causal)
    parts["notcausal"] = tiles((1 - causal) * NEG)
    at, off = {}, 0
    for name, a in parts.items():
        at[name] = (off, a.shape[1])
        off += a.shape[1]
    return np.concatenate(list(parts.values()), 1).astype(np.float32), at


def masks():
    i = np.arange(P)
    a, b = i[:, None], i[None, :]
    chunk = a // CH == b // CH
    parts = {"before": chunk & (a < b), "upto": chunk & (a <= b)}
    m = 1
    while m < CH:
        lower = (a // (2 * m) == b // (2 * m)) & ((a // m) % 2 == 1) & ((b // m) % 2 == 0)
        parts[f"join{m}"] = lower
        parts[f"joinT{m}"] = lower.T
        m *= 2
    at, off = {}, 0
    for name, x in parts.items():
        at[name] = (off, x.shape[1])
        off += x.shape[1]
    return np.concatenate(list(parts.values()), 1).astype(np.uint32), at


CONST, CONST_AT = constants()
MASK, MASK_AT = masks()

COLS = [("norm_w", 16), ("ada_b", 48), ("final_w", 8), ("mix_g", 16), ("mix_b", 16), ("ffn_g", 16),
        ("ffn_b", 16), ("mu_rkv", 12), ("w0", 4), ("a0", 4), ("k_k", 4), ("k_a", 4), ("r_k", 4),
        ("gla_a_b", 2), ("a_bs", 8), ("cond", 16)]
COL_AT, _o = {}, 0
for _n, _w in COLS:
    COL_AT[_n] = (_o, _w)
    _o += _w
NCOLS = _o
ROWS = [("a_ln_w", 512), ("a_ln_b", 512), ("subln_w", 128), ("lq1", 64), ("lq2", 64), ("lk1", 64), ("lk2", 64),
        ("q_norm", 256), ("kv_norm", 128), ("gla_g", 128), ("lnx_g", 512), ("lnx_b", 512)]
ROW_AT, _o = {}, 0
for _n, _w in ROWS:
    ROW_AT[_n] = (_o, _w)
    _o += _w
NROWS = _o


class Steps:

    def __init__(self, sem):
        self.sem, self.n = sem, 0

    def step(self, ins):
        ins.then_inc(self.sem, 1)
        self.n += 1
        return self.n

    def settle(self, eng, n=None):
        eng.wait_ge(self.sem, self.n if n is None else n)


def spread(ap, axis, n):
    a = ap.unsqueeze(axis)
    shape = list(a.shape)
    shape[axis] = n
    return a.broadcast_to(shape)


class Core:

    def __init__(self, nc, ctx, dram):
        self.made = {}
        self.nc, self.ctx, self.whole, self.d = nc, ctx, ctx, dram
        self.ident = self.sb("ident", [P, P])
        self.ones = self.sb("ones", [P, P])
        self.cols = self.sb("cols", [P, NCOLS])
        self.ring = [self.sb(f"ring{s}", [P, SLOT]) for s in range(SLOTS)]
        self.bank = [ctx.enter_context(nc.psum_tensor(f"bank{b}", [P, BANK], F32)) for b in range(BANKS)]
        self.landed = [self.sem(f"weights_landed{s}") for s in range(SLOTS)]
        self.filled = self.sem("bank_filled")
        self.drained = {"act": self.sem("act_drained"), "dve": self.sem("dve_drained")}
        self.nfilled = 0
        self.hi = [self.sb(f"w_hi{i}", [P, PART], F32R) for i in range(PARTS)]
        self.lo = [self.sb(f"w_lo{i}", [P, PART], F32R) for i in range(PARTS)]
        self.hi_ready, self.lo_ready, self.consumed = self.sem("w_hi_ready"), self.sem("w_lo_ready"), self.sem("w_consumed")
        self.nparts = 0
        self.ndrained = {"act": 0, "dve": 0}
        self.dve = Steps(self.sem("dve_step"))
        self.act = Steps(self.sem("act_step"))
        self.pool = Steps(self.sem("pool_step"))
        self.radicand, self.rooted = self.sem("radicand_ready"), self.sem("rooted")
        self.asked = self.answered = 0
        self.plan = []
        self.free_at = []
        self.fed = 0
        self.taken = 0

    def sb(self, name, shape, dt=F32):
        self.made[name] = self.made.get(name, 0) + 1
        if self.made[name] > 1:
            name = f"{name}_{self.made[name]}"
        return self.ctx.enter_context(self.nc.sbuf_tensor(name, shape, dt))

    @contextmanager
    def room(self):
        outer = self.ctx
        with ExitStack() as self.ctx:
            yield
        self.ctx = outer

    def sem(self, name):
        return self.whole.enter_context(self.nc.semaphore(name))

    def col(self, name, i=0, n=1):
        o = COL_AT[name][0] + i
        return self.cols[:, o:o + n]

    def feed(self, sync, count):
        end = min(len(self.plan), self.taken_before + count + SLOTS)
        while self.fed < end:
            b = self.fed
            if b >= SLOTS:
                sync.wait_ge(*self.free_at[b - SLOTS])
            src, n = self.plan[b]
            dst = self.ring[b % SLOTS][:, 0:n]
            if len(src.shape) == 3:
                dst = dst.rearrange("p (k n) -> p k n", k=src.shape[1])
            sync.dma_start(dst, src).then_inc(self.landed[b % SLOTS], 16)
            self.fed += 1

    def ask_root(self, dve, x, scale, eps):
        dve.tensor_scalar(x, x, scale, eps, ALU.mult, ALU.add).then_inc(self.radicand, 1)
        self.asked += 1
        dve.wait_ge(self.rooted, self.asked)
        self.dve.step(dve.reciprocal(x, x))
        self.dve.settle(dve)

    def root(self, act, x):
        self.answered += 1
        act.wait_ge(self.radicand, self.answered)
        act.activation(x, x, ACT.Sqrt).then_inc(self.rooted, 1)

    def begin(self):
        self.taken_before = self.taken

    def take(self, pe):
        b = self.taken
        pe.wait_ge(self.landed[b % SLOTS], 16 * (b // SLOTS + 1))
        self.taken += 1
        return self.ring[b % SLOTS]

    def release(self):
        self.free_at.append((self.filled, self.nfilled))


class Fills:

    def __init__(self, k, owners):
        self.k, self.owners = k, owners
        self.base = k.nfilled
        self.dbase = dict(k.ndrained)
        seen = dict(self.dbase)
        self.count = []
        for o in owners:
            seen[o] += 1
            self.count.append((o, seen[o]))
        k.ndrained.update(seen)

    def bank(self, n):
        return self.k.bank[n % BANKS]

    def wait_free(self, pe, n):
        if n >= BANKS:
            owner, count = self.count[n - BANKS]
            pe.wait_ge(self.k.drained[owner], count)

    def wait_drained(self, eng, n):
        owner, count = self.count[n]
        eng.wait_ge(self.k.drained[owner], count)

    def fill(self, ins):
        ins.then_inc(self.k.filled, 1)
        self.k.nfilled += 1

    def wait_full(self, eng, n):
        eng.wait_ge(self.k.filled, self.base + n + 1)

    def drain(self, n, ins):
        ins.then_inc(self.k.drained[self.owners[n]], 1)


class Split:

    def __init__(self, k, widths):
        self.k, self.widths = k, widths
        self.b0, self.h0 = k.taken, k.nparts
        k.taken += len(widths)
        k.nparts += PARTS * len(widths)
        k.free_at += [(k.lo_ready, self.h0 + PARTS * (b + 1)) for b in range(len(widths))]

    def source(self, h):
        b = self.b0 + h // PARTS
        n = self.widths[h // PARTS] * KC // PARTS
        return self.k.ring[b % SLOTS][:, (h % PARTS) * n:(h % PARTS) * n + n], n

    def high(self, act, h):
        k, b, g = self.k, self.b0 + h // PARTS, self.h0 + h
        src, n = self.source(h)
        act.wait_ge(k.landed[b % SLOTS], 16 * (b // SLOTS + 1))
        if g >= PARTS:
            act.wait_ge(k.consumed, g - PARTS + 1)
        act.activation(k.hi[g % PARTS][:, 0:n], src, ACT.Copy).then_inc(k.hi_ready, 1)

    def low(self, eng, h):
        k, g = self.k, self.h0 + h
        src, n = self.source(h)
        eng.wait_ge(k.hi_ready, g + 1)
        eng.tensor_tensor(k.lo[g % PARTS][:, 0:n], src, k.hi[g % PARTS][:, 0:n].bitcast(F32), ALU.subtract).then_inc(k.lo_ready, 1)

    def parts(self, pe, h):
        k, g, w = self.k, self.h0 + h, self.widths[h // PARTS]
        pe.wait_ge(k.hi_ready, g + 1)
        pe.wait_ge(k.lo_ready, g + 1)
        view = lambda x: x[:, 0:w * KC // PARTS].rearrange("p (c n) -> p c n", n=w)
        return view(k.hi[g % PARTS]), view(k.lo[g % PARTS])

    def done(self, mm):
        mm.then_inc(self.k.consumed, 1)

    def wait_done(self, eng, h):
        eng.wait_ge(self.k.consumed, self.h0 + h + 1)


def project(k, x, tokens, widths, outs, store, owner, low_on="pool"):
    nc = k.nc
    n = len(widths)
    with nc.Block() as block:
        k.begin()
        split = Split(k, widths)
        counts, seen = [], dict(k.ndrained)
        for b in range(n):
            for i in range(len(outs(b))):
                seen[owner(b, i)] += 1
            counts.append(dict(seen))
        before = dict(k.ndrained)
        k.ndrained.update(seen)

        @block.tensor
        def _(pe):
            for b in range(n):
                if b >= 2:
                    for name in ("act", "dve"):
                        pe.wait_ge(k.drained[name], counts[b - 2][name])
                for part in range(PARTS):
                    w = split.parts(pe, PARTS * b + part)
                    for i, (kind, arg) in enumerate(outs(b)):
                        bank = k.bank[4 * (b % 2) + i]
                        groups = [(0, widths[b])] if kind == "token" else arg
                        for j, (f0, f1) in enumerate(groups):
                            for c in range(KC // PARTS):
                                cc = KC // PARTS * part + c
                                for q, (wp, xp) in enumerate(((0, 0), (0, 1), (1, 0))):
                                    if kind == "token":
                                        out, lhs, rhs = bank[:, 0:f1], x[xp][:, cc, arg * P:arg * P + P], w[wp][:, c, :]
                                    else:
                                        out, lhs, rhs = bank[0:f1 - f0, j * tokens:(j + 1) * tokens], w[wp][:, c, f0:f1], x[xp][:, cc, 0:tokens]
                                    mm = pe.matmul(out, lhs, rhs, start=(j == 0 and cc == 0 and q == 0),
                                                   stop=(cc == KC - 1 and q == 2), skip_group_check=True)
                    split.done(mm)

        def program(name, eng):
            act, low = name == "act", name == low_on
            if not act and not low and not any(owner(b, i) == name for b in range(n) for i in range(len(outs(b)))):
                return
            for b in range(-1, n):
                for h in range(PARTS * (b + 1), PARTS * (b + 2)):
                    if h < PARTS * n and act:
                        split.high(eng, h)
                    if h < PARTS * n and low:
                        split.low(eng, h)
                if b >= 0 and name != "pool":
                    for i in range(len(outs(b))):
                        if owner(b, i) == name:
                            split.wait_done(eng, PARTS * b + PARTS - 1)
                            store(name, eng, b, i, k.bank[4 * (b % 2) + i]).then_inc(k.drained[name], 1)

        @block.scalar
        def _(act):
            program("act", act)

        @block.vector
        def _(dve):
            program("dve", dve)

        @block.gpsimd
        def _(pool):
            program("pool", pool)

        @block.sync
        def _(sync):
            k.feed(sync, n)


def copy(kind, eng, dst, src, func=ACT.Copy):
    if kind == "act":
        return eng.activation(dst, src, func)
    return eng.tensor_copy(dst, src)


def plan_columns(k, w, c0, c1):
    for c in range(c0, c1, WB):
        n = min(WB, c1 - c)
        k.plan.append((w.rearrange("(k p) n -> p k n", p=P)[:, :, c:c + n], KC * n))


def setup(k):
    nc, d = k.nc, k.d
    k.h = k.sb("residual", [P, KC, TC])
    loaded = k.sem("setup_loaded")
    with nc.Block() as block:
        k.begin()

        @block.sync
        def _(sync):
            sync.dma_start(k.cols[:, :], d["cols"]).then_inc(loaded, 16)
            k.feed(sync, 0)

        @block.scalar
        def _(act):
            o = CONST_AT["ident"][0]
            act.dma_start(k.ident[:, :], d["const"][:, o:o + P]).then_inc(loaded, 16)
            o = CONST_AT["ones"][0]
            act.dma_start(k.ones[:, :], d["const"][:, o:o + P]).then_inc(loaded, 16)
            act.dma_start(k.h[:, :, 0:T], d["xT"].rearrange("(k p) t -> p k t", p=P)).then_inc(loaded, 16)
            act.dma_start(k.h[:, :, T:TC], d["ctxT"].rearrange("(k p) t -> p k t", p=P)).then_inc(loaded, 16)
            act.wait_ge(loaded, 80)


def modulation(k):
    nc = k.nc
    k.mod = k.sb("mod", [P, 2, 24, 2])
    n = 24
    with k.room():
        cond = k.sb("silu_cond", [P, KC, 2])
        parts = k.sb("cond_parts", [P, KC, 4], F32R)
        rowed = k.sb("mod_rows", [4, n, WB])
        ready, turned = k.sem("cond_ready"), k.sem("mod_turned")
        with nc.Block() as block:
            k.begin()
            split = Split(k, [WB] * n)

            @block.scalar
            def _(act):
                k.act.step(act.activation(cond[:, :, :].rearrange("p k c -> p (k c)"), k.col("cond", 0, 16), ACT.Silu))
                k.act.settle(act)
                act.activation(parts[:, :, 0:2], cond[:, :, :], ACT.Copy).then_inc(ready, 1)
                for h in range(PARTS * n):
                    split.high(act, h)

            @block.tensor
            def _(pe):
                pe.wait_ge(ready, 2)
                for b in range(n):
                    if b >= BANKS:
                        pe.wait_ge(k.drained["dve"], k.ndrained["dve"] + b - BANKS + 1)
                    for part in range(PARTS):
                        hi, lo = split.parts(pe, PARTS * b + part)
                        for c in range(KC // PARTS):
                            cc = KC // PARTS * part + c
                            pe.matmul(k.bank[b % BANKS][0:4, 0:WB], parts[:, cc, :], hi[:, c, :], start=(cc == 0), stop=False,
                                      skip_group_check=True)
                            mm = pe.matmul(k.bank[b % BANKS][0:2, 0:WB], parts[:, cc, 0:2], lo[:, c, :], start=False,
                                           stop=(cc == KC - 1), skip_group_check=True)
                        split.done(mm)
                for layer in range(2):
                    pe.wait_ge(k.drained["dve"], k.ndrained["dve"] + 12 * (layer + 1))
                    for f in range(24):
                        mm = pe.transpose(k.bank[layer][:, 4 * f:4 * f + 4], rowed[:, 12 * layer + f // 2, (f % 2) * P:(f % 2) * P + P],
                                          k.ident[0:4, 0:4])
                    mm.then_inc(turned, 1)

            @block.vector
            def _(dve):
                S = k.dve
                dve.wait_ge(ready, 1)
                dve.tensor_tensor(parts[:, :, 2:4], cond[:, :, :], parts[:, :, 0:2].bitcast(F32), ALU.subtract).then_inc(ready, 1)
                for b in range(n + 1):
                    if b < n:
                        for part in range(PARTS):
                            split.low(dve, PARTS * b + part)
                    if b >= 1:
                        split.wait_done(dve, PARTS * b - 1)
                        dve.tensor_copy(rowed[:, b - 1, :], k.bank[(b - 1) % BANKS][0:4, 0:WB]).then_inc(k.drained["dve"], 1)
                for layer in range(2):
                    dve.wait_ge(turned, layer + 1)
                    bank = k.bank[layer][:, 0:96].rearrange("p (f q c) -> p f q c", q=2, c=2)
                    mod = k.mod[:, layer, :, :]
                    S.step(dve.tensor_tensor(mod, bank[:, :, 0, :], spread(k.col("ada_b", 24 * layer, 24), 2, 2), ALU.add))
                    S.settle(dve)
                    S.step(dve.tensor_tensor(mod, mod, bank[:, :, 1, :], ALU.add))
                    S.settle(dve)
                    scale = k.mod[:, layer, 8:16, :]
                    S.step(dve.scalar_tensor_tensor(out=scale, in0=scale, scalar=1.0, in1=spread(k.col("norm_w", 8 * layer, 8), 2, 2),
                                                    op0=ALU.add, op1=ALU.mult))

            @block.sync
            def _(sync):
                k.feed(sync, n)
        k.ndrained["dve"] += n


def rms_modulate(k, layer, tokens, out, work):
    nc = k.nc
    h = k.h
    hi, lo = out
    squared, summed = k.sem(f"squared_{layer}"), k.sem(f"summed_{layer}")
    scaled, rounded = k.sem(f"scaled_{layer}"), k.sem(f"rounded_{layer}")
    rstd = k.sb("rms_rstd", [P, tokens])
    with nc.Block() as block:
        k.begin()

        @block.scalar
        def _(act):
            for c in range(KC):
                act.activation(work[:, c, 0:tokens], h[:, c, 0:tokens], ACT.Square).then_inc(squared, 1)
            k.root(act, rstd[:, :])
            for c in range(KC):
                act.wait_ge(scaled, c + 1)
                x = work[:, c, 0:tokens]
                if layer is None:
                    k.act.step(act.activation(x, x, ACT.Copy, scale=k.col("final_w", c)))
                else:
                    for s in range(tokens // T):
                        o = work[:, c, s * T:s * T + T]
                        k.act.step(act.activation(o, o, ACT.Identity, bias=k.mod[:, layer, c, s:s + 1],
                                                  scale=k.mod[:, layer, 8 + c, s:s + 1]))
                k.act.settle(act)
                act.activation(hi[:, c, 0:tokens], x, ACT.Copy).then_inc(rounded, 1)

        @block.tensor
        def _(pe):
            for c in range(KC):
                pe.wait_ge(squared, c + 1)
                mm = pe.matmul(k.bank[0][:, 0:tokens], k.ones[:, :], work[:, c, 0:tokens], start=(c == 0), stop=(c == KC - 1))
            mm.then_inc(summed, 1)

        @block.vector
        def _(dve):
            dve.wait_ge(summed, 1)
            k.dve.step(dve.tensor_copy(rstd[:, :], k.bank[0][:, 0:tokens]))
            k.dve.settle(dve)
            k.ask_root(dve, rstd[:, :], 1.0 / D, 1e-6)
            for c in range(KC + 2):
                if c < KC:
                    dve.tensor_tensor(work[:, c, 0:tokens], h[:, c, 0:tokens], rstd[:, :], ALU.mult).then_inc(scaled, 1)
                if c >= 2:
                    dve.wait_ge(rounded, c - 1)
                    k.dve.step(dve.tensor_tensor(lo[:, c - 2, 0:tokens], work[:, c - 2, 0:tokens], hi[:, c - 2, 0:tokens].bitcast(F32),
                                                 ALU.subtract))

        @block.sync
        def _(sync):
            k.feed(sync, 0)


def project_out(k, src, tokens, update, name):
    per = 2 if tokens == T else 1
    outs = [("feature", [(0, P), (P, 2 * P)])] if per == 2 else [("feature", [(0, P)]), ("feature", [(P, 2 * P)])]
    project(k, src, tokens, [WB] * (D // WB), lambda b: outs,
            lambda kind, eng, b, i, bank: update(eng, 2 * b + i, bank), lambda b, i: "dve")


def to_feature_major(k, jobs, name):
    nc = k.nc
    pairs = isinstance(jobs[0][1], tuple)
    highs = k.sem(f"turned_high_{name}") if pairs else None
    with nc.Block() as block:
        k.begin()
        fills = Fills(k, ["dve" if pairs else ("act", "dve")[n % 2] for n in range(len(jobs))])

        def views(n):
            dst = jobs[n][1][0] if pairs else jobs[n][1]
            src = fills.bank(n)[0:dst.shape[0], 0:len(jobs[n][0]) * P]
            return src.rearrange("p (a b) -> p a b", a=dst.shape[1]) if len(dst.shape) == 3 else src

        @block.tensor
        def _(pe):
            for n, (sources, _) in enumerate(jobs):
                fills.wait_free(pe, n)
                for j, s in enumerate(sources):
                    w = s.shape[1]
                    mm = pe.transpose(fills.bank(n)[0:w, j * P:j * P + P], s, k.ident[:, :])
                fills.fill(mm)

        @block.scalar
        def _(act):
            for n in range(0, len(jobs), 1 if pairs else 2):
                fills.wait_full(act, n)
                if pairs:
                    act.activation(jobs[n][1][0], views(n), ACT.Copy).then_inc(highs, 1)
                else:
                    fills.drain(n, act.activation(jobs[n][1], views(n), ACT.Copy))

        @block.vector
        def _(dve):
            for n in range(0 if pairs else 1, len(jobs), 1 if pairs else 2):
                fills.wait_full(dve, n)
                if pairs:
                    dve.wait_ge(highs, n + 1)
                    fills.drain(n, dve.tensor_tensor(jobs[n][1][1], views(n), jobs[n][1][0].bitcast(F32), ALU.subtract))
                else:
                    fills.drain(n, dve.tensor_copy(jobs[n][1], views(n)))

        @block.sync
        def _(sync):
            k.feed(sync, 0)


def rope_axial(pool, k, x, cos, sin, heads, tmp):
    xv = x.rearrange("p (h s e d) -> p (h s) e d", h=heads, s=2, e=2)
    tv = tmp.rearrange("p (h s e d) -> p (h s) e d", h=heads, s=2, e=2)
    x4 = x.rearrange("p (h s e d) -> p h s e d", h=heads, s=2, e=2)
    t4 = tmp.rearrange("p (h s e d) -> p h s e d", h=heads, s=2, e=2)
    s4 = sin.rearrange("p (s e d) -> p s e d", s=2, e=2)
    for s in range(2):
        for e in range(2):
            k.pool.step(pool.tensor_tensor(t4[:, :, s, e, :], x4[:, :, s, 1 - e, :], spread(s4[:, s, e, :], 1, heads), ALU.mult))
    k.pool.settle(pool)
    x3, t3 = x.rearrange("p (h d) -> p h d", h=heads), tmp.rearrange("p (h d) -> p h d", h=heads)
    k.pool.step(pool.tensor_tensor(x3, x3, spread(cos, 1, heads), ALU.mult))
    k.pool.settle(pool)
    k.pool.step(pool.tensor_tensor(x3, x3, t3, ALU.add))


def even_project(k, xn, proj):
    kinds = ["gelu"] * 4 + ["silu"] * 2 + ["copy"] * 6 + ["silu"] * 2

    def store(name, eng, b, i, bank):
        func = {"gelu": ACT.Gelu, "silu": ACT.Silu, "copy": ACT.Copy}[kinds[b]]
        return copy(name, eng, proj[:, i, b * WB:b * WB + WB], bank[:, 0:WB], func)

    project(k, xn, TC, [WB] * 14, lambda b: [("token", m) for m in range(TC // P)], store,
            lambda b, i: "dve" if kinds[b] == "copy" else "act")


def spatial_gating(k, proj, wsT, row, const, mix, lam):
    nc = k.nc
    tmp = k.sb("rope_tmp", [P, B_H * 2 * B_D])
    vn = k.sb("vn", [P, 2, A_W])
    stats = k.sb("stats", [P, 4, 6])
    mean = k.sb("mean", [P, 4, 2])
    rstd = k.sb("rstd", [P, 4])
    lsum = k.sb("lsum", [P, 2])
    lprod = k.sb("lprod", [P, 2 * B_D])
    normed = k.sem("v_normed")
    mixed = k.sem("v_mixed")
    gated = k.sem("gated")
    lams = k.sem("lambda_sums")
    tiles = TC // P
    with nc.Block() as block:
        k.begin()

        @block.gpsimd
        def _(pool):
            for m in range(T // P):
                cos, sin = const("axcos")[:, m * B_D:m * B_D + B_D], const("axsin")[:, m * B_D:m * B_D + B_D]
                for c0 in (3 * A_W, 4 * A_W):
                    rope_axial(pool, k, proj[:, m, c0:c0 + 512], cos, sin, 2 * B_H, tmp[:, :])
                    k.pool.settle(pool)

        @block.tensor
        def _(pe):
            for m in range(tiles):
                pe.wait_ge(normed, m + 1)
                if m >= 2:
                    pe.wait_ge(gated, m - 1)
                for g in range(A_G):
                    mm = pe.matmul(k.bank[m % 2][:, g * 64:g * 64 + 64], wsT[:, g, :], vn[:, m % 2, g * 64:g * 64 + 64],
                                   start=True, stop=True)
                mm.then_inc(mixed, 1)

        @block.vector
        def _(dve):
            S = k.dve

            def norm(m):
                v = proj[:, m, A_W:2 * A_W]
                x = vn[:, m % 2, :]
                if m >= 2:
                    dve.wait_ge(mixed, m - 1)
                S.step(dve.tensor_scalar(x, v, mean[:, m, 0:1], rstd[:, m:m + 1], ALU.subtract, ALU.mult))
                S.settle(dve)
                S.step(dve.tensor_tensor(x, x, row("a_ln_w"), ALU.mult))
                S.settle(dve)
                dve.tensor_tensor(x, x, row("a_ln_b"), ALU.add).then_inc(normed, 1)

            def gate(m):
                dve.wait_ge(mixed, m + 1)
                out = mix[:, m, 0:A_W]
                o3 = out.rearrange("p (g d) -> p g d", g=A_G)
                dve.tensor_tensor(o3, k.bank[m % 2][:, :].rearrange("p (g d) -> p g d", g=A_G),
                                  spread(k.col("a_bs", 0, 8), 2, 64), ALU.add).then_inc(gated, 1)
                dve.wait_ge(gated, m + 1)
                S.step(dve.tensor_tensor(out, out, proj[:, m, 0:A_W], ALU.mult))
                S.settle(dve)
                S.step(dve.tensor_tensor(out, out, proj[:, m, 2 * A_W:3 * A_W], ALU.mult))

            S.step(dve.tensor_tensor(lprod[:, :], row("lq1", 128), row("lk1", 128), ALU.mult))
            S.settle(dve)
            dve.tensor_reduce(lsum[:, :], lprod[:, :].rearrange("p (a b) -> p a b", a=2), AX_X, ALU.add).then_inc(lams, 1)
            for m in range(tiles):
                S.step(dve.bn_stats(stats[:, m, :], proj[:, m, A_W:2 * A_W]))
            S.settle(dve)
            for m in range(tiles):
                S.step(dve.bn_aggr(mean[:, m, :], stats[:, m, :]))
            S.settle(dve)
            S.step(dve.tensor_copy(rstd[:, :], mean[:, :, 1]))
            S.settle(dve)
            k.ask_root(dve, rstd[:, :], 1.0, 1e-5)
            norm(0)
            for m in range(tiles):
                if m + 1 < tiles:
                    norm(m + 1)
                gate(m)
            dve.wait_ge(lams, 2)
            S.step(dve.tensor_tensor(lam, lsum[:, 1:2], lsum[:, 0:1], ALU.subtract))
            S.settle(dve)
            S.step(dve.tensor_scalar(lam, lam, -(0.8 - 0.6 * math.exp(0.0)), None, ALU.add))

        @block.scalar
        def _(act):
            act.wait_ge(lams, 1)
            act.activation(lsum[:, :], lsum[:, :], ACT.Exp).then_inc(lams, 1)
            k.root(act, rstd[:, :])

        @block.sync
        def _(sync):
            k.feed(sync, 0)


def diff_attention(k, proj, qT, kT, row, nlam, mix):
    nc = k.nc
    units = [(m, h) for m in range(TC // P) for h in range(B_H)]
    n_units = len(units)
    prob = k.sb("prob", [P, 2, 2, TC])
    pT = k.sb("pT", [P, 2, TC])
    mx = k.sb("mx", [P, 2, 2])
    sums = k.sb("sums", [P, 2, 2])
    ss = k.sb("ss", [P, len(units)])
    junk = k.sb("junk", [P, B_V])
    scored, maxed, exped = k.sem("scored"), k.sem("maxed"), k.sem("exped")
    combined, turned, turned_out = k.sem("combined"), k.sem("turned"), k.sem("turned_out")
    mixed, squared, finished = k.sem("attended"), k.sem("out_squared"), k.sem("finished")
    keys = lambda m: (0, TC) if m < 2 else (T, TC)
    with nc.Block() as block:
        k.begin()

        @block.tensor
        def _(pe):
            def scores(u):
                m, h = units[u]
                a, b = keys(m)
                if u >= 2:
                    pe.wait_ge(exped, 2 * (u - 1))
                for j in range(2):
                    r = slice(64 * j, 64 * j + 64)
                    pe.matmul(k.bank[4 * (u % 2) + j][:, 0:b - a], qT[r, h, m * P:m * P + P], kT[r, h, a:b],
                              start=True, stop=True).then_inc(scored, 1)

            def turn(u):
                m, h = units[u]
                a, b = keys(m)
                pe.wait_ge(combined, u + 1)
                if u >= 2:
                    pe.wait_ge(turned_out, u - 1)
                for c in range((b - a) // P):
                    mm = pe.transpose(k.bank[4 * (u % 2) + 2][:, c * P:c * P + P], prob[:, u % 2, 0, c * P:c * P + P], k.ident[:, :])
                mm.then_inc(turned, 1)

            def attend(u):
                m, h = units[u]
                a, b = keys(m)
                pe.wait_ge(turned_out, u + 1)
                if u >= 2:
                    pe.wait_ge(finished, u - 1)
                for c in range((b - a) // P):
                    v = proj[:, a // P + c, 5 * A_W + h * B_V:5 * A_W + h * B_V + B_V]
                    mm = pe.matmul(k.bank[4 * (u % 2) + 3][:, 0:B_V], pT[:, u % 2, c * P:c * P + P], v,
                                   start=(c == 0), stop=(c == (b - a) // P - 1))
                mm.then_inc(mixed, 1)

            for u in range(n_units + 1):
                if u < n_units:
                    scores(u)
                if u >= 1:
                    turn(u - 1)
                    attend(u - 1)

        @block.scalar
        def _(act):
            for u in range(n_units + 1):
                if u < n_units:
                    a, b = keys(units[u][0])
                    act.wait_ge(maxed, u + 1)
                    if u >= 2:
                        act.wait_ge(turned, u - 1)
                    for j in range(2):
                        act.activation(prob[:, u % 2, j, 0:b - a], k.bank[4 * (u % 2) + j][:, 0:b - a], ACT.Exp,
                                       bias=mx[:, u % 2, j:j + 1], scale=B_D ** -0.5,
                                       accum_out=sums[:, u % 2, j:j + 1]).then_inc(exped, 1)
                if u >= 1:
                    w = u - 1
                    a, b = keys(units[w][0])
                    act.wait_ge(turned, w + 1)
                    if w >= 2:
                        act.wait_ge(mixed, w - 1)
                    act.activation(pT[:, w % 2, 0:b - a], k.bank[4 * (w % 2) + 2][:, 0:b - a], ACT.Copy).then_inc(turned_out, 1)
                    act.wait_ge(mixed, w + 1)
                    if w >= 2:
                        act.wait_ge(finished, w - 1)
                    if w >= 1:
                        act.wait_ge(squared, w)
                    act.activation(junk[:, :], k.bank[4 * (w % 2) + 3][:, 0:B_V], ACT.Square,
                                   accum_out=ss[:, w:w + 1]).then_inc(squared, 1)
            k.root(act, ss[:, :])

        @block.vector
        def _(dve):
            S = k.dve

            def maxes(u):
                a, b = keys(units[u][0])
                if u >= 2:
                    dve.wait_ge(exped, 2 * (u - 1))
                for j in range(2):
                    dve.wait_ge(scored, 2 * u + j + 1)
                    S.step(dve.reduce_max(mx[:, u % 2, j:j + 1], k.bank[4 * (u % 2) + j][:, 0:b - a], AX_X))
                S.settle(dve)
                dve.tensor_scalar(mx[:, u % 2, :], mx[:, u % 2, :], -(B_D ** -0.5), None, ALU.mult).then_inc(maxed, 1)

            def combine(u):
                a, b = keys(units[u][0])
                s, p0, p1 = sums[:, u % 2, :], prob[:, u % 2, 0, 0:b - a], prob[:, u % 2, 1, 0:b - a]
                dve.wait_ge(exped, 2 * u + 2)
                S.step(dve.reciprocal(s, s))
                S.settle(dve)
                S.step(dve.tensor_scalar(s[:, 1:2], s[:, 1:2], nlam, None, ALU.mult))
                S.step(dve.tensor_scalar(p0, p0, s[:, 0:1], None, ALU.mult))
                S.settle(dve)
                dve.scalar_tensor_tensor(out=p0, in0=p1, scalar=s[:, 1:2], in1=p0, op0=ALU.mult, op1=ALU.add).then_inc(combined, 1)

            def finish(u):
                m, h = units[u]
                out = mix[:, m, A_W + h * B_V:A_W + h * B_V + B_V]
                dve.wait_ge(squared, u + 1)
                dve.tensor_tensor(out, k.bank[4 * (u % 2) + 3][:, 0:B_V], row("subln_w"), ALU.mult).then_inc(finished, 1)
                dve.wait_ge(finished, u + 1)
                z = proj[:, m, 6 * A_W + h * B_V:6 * A_W + h * B_V + B_V]
                S.step(dve.scalar_tensor_tensor(out=out, in0=out, scalar=1.0 - (0.8 - 0.6 * math.exp(0.0)), in1=z,
                                                op0=ALU.mult, op1=ALU.mult))

            for u in range(n_units + 2):
                if u < n_units:
                    maxes(u)
                if 1 <= u <= n_units:
                    combine(u - 1)
                if u >= 2:
                    finish(u - 2)
            k.ask_root(dve, ss[:, :], 1.0 / B_V, 1e-5)
            for m in range(TC // P):
                out = mix[:, m, A_W:D].rearrange("p (h v) -> p h v", h=B_H)
                S.step(dve.tensor_tensor(out, out, spread(ss[:, B_H * m:B_H * m + B_H], 2, B_V), ALU.mult))

        @block.sync
        def _(sync):
            k.feed(sync, 0)


def attention(k, units, n_keys, scores_of, value_of, scale, bias_of, store, name):
    nc = k.nc
    N = len(units)
    nchunk = n_keys // P
    prob = k.sb(f"prob_{name}", [P, 2, n_keys])
    pT = k.sb(f"pT_{name}", [P, 2, n_keys])
    mx = k.sb(f"mx_{name}", [P, 2])
    sums = k.sb(f"sums_{name}", [P, 2])
    scored, maxed, exped = k.sem(f"scored_{name}"), k.sem(f"maxed_{name}"), k.sem(f"exped_{name}")
    normed, turned, turned_out = k.sem(f"normed_{name}"), k.sem(f"turned_{name}"), k.sem(f"turned_out_{name}")
    mixed, stored = k.sem(f"attended_{name}"), k.sem(f"stored_{name}")
    with nc.Block() as block:
        k.begin()

        @block.tensor
        def _(pe):
            for u in range(N + 1):
                if u < N:
                    if u >= 2:
                        pe.wait_ge(exped, u - 1)
                    scores_of(pe, units[u], k.bank[u % 2][:, 0:n_keys]).then_inc(scored, 1)
                if u >= 1:
                    w = u - 1
                    pe.wait_ge(normed, w + 1)
                    if w >= 2:
                        pe.wait_ge(turned_out, w - 1)
                    for c in range(nchunk):
                        mm = pe.transpose(k.bank[2 + w % 2][:, c * P:c * P + P], prob[:, w % 2, c * P:c * P + P], k.ident[:, :])
                    mm.then_inc(turned, 1)
                    pe.wait_ge(turned_out, w + 1)
                    if w >= 2:
                        pe.wait_ge(stored, w - 1)
                    for c in range(nchunk):
                        mm = pe.matmul(k.bank[4 + w % 2][:, 0:P], value_of(units[w], c), pT[:, w % 2, c * P:c * P + P],
                                       start=(c == 0), stop=(c == nchunk - 1))
                    mm.then_inc(mixed, 1)

        @block.scalar
        def _(act):
            for u in range(N + 1):
                if u < N:
                    act.wait_ge(maxed, u + 1)
                    if u >= 2:
                        act.wait_ge(turned, u - 1)
                    src = k.bank[u % 2][:, 0:n_keys] if bias_of is None else prob[:, u % 2, :]
                    act.activation(prob[:, u % 2, :], src, ACT.Exp, bias=mx[:, u % 2:u % 2 + 1],
                                   scale=scale if bias_of is None else 1.0,
                                   accum_out=sums[:, u % 2:u % 2 + 1]).then_inc(exped, 1)
                if u >= 1:
                    w = u - 1
                    act.wait_ge(turned, w + 1)
                    if w >= 2:
                        act.wait_ge(mixed, w - 1)
                    act.activation(pT[:, w % 2, :], k.bank[2 + w % 2][:, 0:n_keys], ACT.Copy).then_inc(turned_out, 1)

        @block.vector
        def _(dve):
            S = k.dve
            for u in range(N + 2):
                if u < N:
                    dve.wait_ge(scored, u + 1)
                    src, m = k.bank[u % 2][:, 0:n_keys], mx[:, u % 2:u % 2 + 1]
                    if u >= 2:
                        dve.wait_ge(exped, u - 1)
                    if bias_of is not None:
                        if u >= 2:
                            dve.wait_ge(turned, u - 1)
                        S.step(dve.scalar_tensor_tensor(out=prob[:, u % 2, :], in0=src, scalar=scale, in1=bias_of(units[u]),
                                                        op0=ALU.mult, op1=ALU.add))
                        S.settle(dve)
                        src = prob[:, u % 2, :]
                    S.step(dve.reduce_max(m, src, AX_X))
                    S.settle(dve)
                    dve.tensor_scalar(m, m, -scale if bias_of is None else -1.0, None, ALU.mult).then_inc(maxed, 1)
                if 1 <= u <= N:
                    w = u - 1
                    s = sums[:, w % 2:w % 2 + 1]
                    dve.wait_ge(exped, w + 1)
                    S.step(dve.reciprocal(s, s))
                    S.settle(dve)
                    dve.tensor_scalar(prob[:, w % 2, :], prob[:, w % 2, :], s, None, ALU.mult).then_inc(normed, 1)
                if u >= 2:
                    w = u - 2
                    dve.wait_ge(mixed, w + 1)
                    store(dve, units[w], k.bank[4 + w % 2][:, 0:P]).then_inc(stored, 1)

        @block.sync
        def _(sync):
            k.feed(sync, 0)


def odd_project(k, xn, cq, ckv, zT):
    def outs(b):
        if b < 2:
            return [("token", m) for m in range(2 if b == 0 else 4)]
        return [("feature", [(0, P), (P, 2 * P)])]

    def store(name, eng, b, i, bank):
        if b < 2:
            dst = cq[:, i, :] if b == 0 else ckv[:, i, 0:C_KV + C_R]
            return copy(name, eng, dst, bank[:, 0:dst.shape[1]])
        return copy(name, eng, zT[:, 2 * (b - 2):2 * (b - 2) + 2, :], bank[:, :].rearrange("p (f t) -> p f t", f=2), ACT.Silu)

    project(k, xn, T, [WB, C_KV + C_R] + [WB] * 4, outs, store, lambda b, i: "dve" if b < 2 else "act")


def latent_norms(k, cq, ckv, row, const):
    nc = k.nc
    tmp = k.sb("odd_tmp", [P, C_Q])
    ss = k.sb("odd_ss", [P, 6])
    pooltmp = k.sb("krope_tmp", [P, C_R])
    with nc.Block() as block:
        k.begin()

        @block.gpsimd
        def _(pool):
            for m in range(4):
                kr = ckv[:, m, C_KV:C_KV + C_R]
                if m < 2:
                    rope_axial(pool, k, kr, const("axcos")[:, m * 64:m * 64 + 64], const("axsin")[:, m * 64:m * 64 + 64],
                               1, pooltmp[:, :])
                    k.pool.settle(pool)
                k.pool.step(pool.tensor_copy(ckv[:, m, C_KV + C_R:C_KV + 2 * C_R], kr))

        @block.vector
        def _(dve):
            S = k.dve
            jobs = [(cq[:, m, :], "q_norm") for m in range(2)] + [(ckv[:, m, 0:C_KV], "kv_norm") for m in range(4)]
            for n, (x, w) in enumerate(jobs):
                width = x.shape[1]
                s = ss[:, n:n + 1]
                S.step(dve.tensor_tensor(tmp[:, 0:width], x, x, ALU.mult))
                S.settle(dve)
                S.step(dve.tensor_reduce(s, tmp[:, 0:width], AX_X, ALU.add))
                S.settle(dve)
            k.ask_root(dve, ss[:, 0:2], 1.0 / C_Q, 1e-6)
            k.ask_root(dve, ss[:, 2:6], 1.0 / C_KV, 1e-6)
            for n, (x, w) in enumerate(jobs):
                S.step(dve.scalar_tensor_tensor(out=x, in0=x, scalar=ss[:, n:n + 1], in1=row(w), op0=ALU.mult, op1=ALU.mult))

        @block.scalar
        def _(act):
            k.root(act, ss[:, 0:2])
            k.root(act, ss[:, 2:6])

        @block.sync
        def _(sync):
            k.feed(sync, 0)


def odd_queries(k, cqT, ckvT, qnT, qr, knT, v):
    nc = k.nc
    with nc.Block() as block:
        k.begin()
        jobs = []
        for g in range(2):
            jobs += [("qn", g, i) for i in range(2)] + [("qr", g, i) for i in range(2)]
        jobs += [("kn", 0, h) for h in range(C_H)] + [("v", 0, i) for i in range(8)]
        fills = Fills(k, [("act", "dve")[n % 2] for n in range(len(jobs))])

        def piece(n):
            kind, g, i = jobs[n]
            bank = fills.bank(n)
            if kind == "qn":
                h = 4 * g + 2 * i
                return qnT[:, h:h + 2, :], bank[:, :].rearrange("p (h t) -> p h t", h=2)
            if kind == "qr":
                return (qr[:, i, 256 * g:256 * g + 256], bank[:, 0:256])
            if kind == "kn":
                return knT[:, i, :], bank[:, :]
            m, half = divmod(i, 2)
            return v[:, m, 512 * half:512 * half + 512], bank[:, :]

        @block.tensor
        def _(pe):
            for n, (kind, g, i) in enumerate(jobs):
                bank = fills.bank(n)
                if n in (0, 4, 8):
                    if n:
                        k.release()
                    w = k.take(pe)
                    wq = w[:, 0:2 * 768].rearrange("p (k h d) -> p k h d", k=2, h=4)
                    wkv = w[:, :].rearrange("p (h e) -> p h e", h=C_H)
                fills.wait_free(pe, n)
                if kind == "qn":
                    for j in range(2):
                        for c in range(2):
                            mm = pe.matmul(bank[:, j * T:j * T + T], wq[:, c, 2 * i + j, 0:C_N], cqT[:, c, :],
                                           start=(c == 0), stop=(c == 1))
                elif kind == "qr":
                    for c in range(2):
                        mm = pe.matmul(bank[:, 0:256].rearrange("p (h d) -> p h d", h=4), cqT[:, c, i * P:i * P + P], wq[:, c, :, C_N:C_N + C_R],
                                       start=(c == 0), stop=(c == 1))
                elif kind == "kn":
                    mm = pe.matmul(bank[:, :], wkv[:, i, 0:C_N], ckvT[:, :], start=True, stop=True)
                else:
                    m, half = divmod(i, 2)
                    mm = pe.matmul(bank[:, :].rearrange("p (h d) -> p h d", h=4), ckvT[:, m * P:m * P + P], wkv[:, 4 * half:4 * half + 4, C_N:C_N + C_V],
                                   start=True, stop=True)
                fills.fill(mm)
            k.release()

        @block.scalar
        def _(act):
            for n in range(0, len(jobs), 2):
                dst, src = piece(n)
                fills.wait_full(act, n)
                fills.drain(n, act.activation(dst, src, ACT.Copy))

        @block.vector
        def _(dve):
            for n in range(1, len(jobs), 2):
                dst, src = piece(n)
                fills.wait_full(dve, n)
                fills.drain(n, dve.tensor_copy(dst, src))

        @block.sync
        def _(sync):
            k.feed(sync, 3)


def rotate_queries(k, qr, const):
    nc = k.nc
    tmp = k.sb("qrope_tmp", [P, C_H * C_R])
    with nc.Block() as block:
        k.begin()

        @block.gpsimd
        def _(pool):
            for m in range(2):
                rope_axial(pool, k, qr[:, m, :], const("axcos")[:, m * 64:m * 64 + 64], const("axsin")[:, m * 64:m * 64 + 64],
                           C_H, tmp[:, :])
                k.pool.settle(pool)

        @block.sync
        def _(sync):
            k.feed(sync, 0)


def load(k, name, pairs):
    nc = k.nc
    loaded = k.sem(f"loaded_{name}")
    with nc.Block() as block:
        k.begin()

        @block.sync
        def _(sync):
            k.feed(sync, 0)

        @block.scalar
        def _(act):
            for dst, src in pairs:
                act.dma_start(dst, src).then_inc(loaded, 16)
            act.wait_ge(loaded, 16 * len(pairs))


def first_block(k):
    nc, d = k.nc, k.d
    h = k.h

    def residual(layer):
        def update(dve, n, bank):
            for s in range(2):
                c, o, which = (n, h[:, n, s * T:s * T + T], s) if layer == 0 else (n + s, h[:, n + s, 0:T], 0)
                ins = dve.scalar_tensor_tensor(out=o, in0=bank[:, s * T:s * T + T], scalar=k.mod[:, layer, 16 + c, which:which + 1],
                                               in1=o, op0=ALU.mult, op1=ALU.add)
                if s == 0:
                    k.dve.step(ins)
            return ins
        return update

    with k.room():
        rows = k.sb("rows", [P, NROWS])
        consts = k.sb("consts", [P, 2 * 128])
        wsT = k.sb("wsT", [P, A_G, P])
        row = lambda name, n=None: rows[:, ROW_AT[name][0]:ROW_AT[name][0] + (n or ROW_AT[name][1])]
        const = lambda name: consts[:, 0:128] if name == "axcos" else consts[:, 128:256]
        o = CONST_AT["axcos"][0]
        load(k, "rows1", [(rows[:, :], d["rows"].partition_broadcast(P)), (consts[:, :], d["const"][:, o:o + 256]),
                          (wsT[:, :, :], d["a_wsT"])])
        modulation(k)
        nlam = k.sb("nlam", [P, 1])
        with k.room():
            mix = k.sb("mix", [P, 4, D])
            with k.room():
                proj = k.sb("proj", [P, 4, 7 * A_W])
                with k.room():
                    xn = k.sb("xn_hi", [P, KC, TC], F32R), k.sb("xn_lo", [P, KC, TC], F32R)
                    with k.room():
                        rms_modulate(k, 0, TC, xn, proj.rearrange("p m n -> p (m n)")[:, 0:KC * TC].rearrange("p (c t) -> p c t", c=KC))
                    even_project(k, xn, proj)
                with k.room():
                    spatial_gating(k, proj, wsT, row, const, mix, nlam[:, :])
                qT = k.sb("qT", [P, B_H, TC])
                kT = k.sb("kT", [P, B_H, TC])
                jobs = []
                for c0, dst in ((3 * A_W, qT), (4 * A_W, kT)):
                    for m in range(4):
                        jobs.append(([proj[:, m, c0 + P * f:c0 + P * f + P] for f in range(4)], dst[:, :, m * P:m * P + P]))
                to_feature_major(k, jobs, "even_qk")
                with k.room():
                    diff_attention(k, proj, qT, kT, row, nlam[:, :], mix)
            mixT = k.sb("mixT_hi", [P, KC, TC], F32R), k.sb("mixT_lo", [P, KC, TC], F32R)
            jobs = [([mix[:, m, 512 * g + P * f:512 * g + P * f + P] for f in range(4)],
                     tuple(x[:, 4 * g:4 * g + 4, m * P:m * P + P] for x in mixT)) for g in range(2) for m in range(4)]
            to_feature_major(k, jobs, "even_mix")
            project_out(k, mixT, TC, residual(0), "even")
        with k.room():
            cq = k.sb("cq", [P, 2, C_Q])
            ckv = k.sb("ckv", [P, 4, C_KV + 2 * C_R])
            zT = k.sb("zT", [P, C_H, T])
            with k.room():
                xn = k.sb("xn1_hi", [P, KC, TC], F32R), k.sb("xn1_lo", [P, KC, TC], F32R)
                with k.room():
                    rms_modulate(k, 1, TC, xn, k.sb("square1", [P, KC, TC]))
                odd_project(k, xn, cq, ckv, zT)
            with k.room():
                latent_norms(k, cq, ckv, row, const)
            cqT = k.sb("cqT", [P, 2, T])
            ckvT = k.sb("ckvT", [P, 2, TC])
            jobs = [([cq[:, m, P * f:P * f + P] for f in range(2)], cqT[:, :, m * P:m * P + P]) for m in range(2)]
            jobs += [([ckv[:, m, P * f:P * f + P] for f in range(2)], ckvT[:, :, m * P:m * P + P]) for m in range(4)]
            to_feature_major(k, jobs, "odd_latent")
            qnT = k.sb("qnT", [P, C_H, T])
            qr = k.sb("qr", [P, 2, C_H * C_R])
            qrT = k.sb("qrT", [P, 4, T])
            knT = k.sb("knT", [P, C_H, TC])
            v = k.sb("v_odd", [P, 4, C_H * C_V])
            odd_queries(k, cqT, ckvT[:, 0, :], qnT, qr, knT, v)
            with k.room():
                rotate_queries(k, qr, const)
            to_feature_major(k, [([qr[:, m, P * f:P * f + P] for f in range(4)], qrT[:, :, m * P:m * P + P]) for m in range(2)],
                             "odd_qr")
            mixT = k.sb("mixT1_hi", [P, C_H, T], F32R), k.sb("mixT1_lo", [P, C_H, T], F32R)

            def scores_of(pe, unit, out):
                m, hd = unit
                r = slice(64 * (hd % 2), 64 * (hd % 2) + 64)
                pe.matmul(out, qnT[:, hd, m * P:m * P + P], knT[:, hd, :], start=True, stop=False)
                return pe.matmul(out, qrT[r, hd // 2, m * P:m * P + P], ckvT[r, 1, :], start=False, stop=True)

            def store(dve, unit, bank):
                m, hd = unit
                t = slice(m * P, m * P + P)
                gated = zT[:, hd, t]
                k.dve.step(dve.tensor_tensor(gated, bank, gated, ALU.mult))
                k.dve.settle(dve)
                k.dve.step(dve.tensor_copy(mixT[0][:, hd, t], gated))
                k.dve.settle(dve)
                return dve.tensor_tensor(mixT[1][:, hd, t], gated, mixT[0][:, hd, t].bitcast(F32), ALU.subtract)

            with k.room():
                attention(k, [(m, hd) for m in range(2) for hd in range(C_H)], TC, scores_of,
                          lambda unit, c: v[:, c, unit[1] * C_V:unit[1] * C_V + C_V],
                          (C_N + C_R) ** -0.5, None, store, "odd")
            project_out(k, mixT, T, residual(1), "odd")
        with k.room():
            rms_modulate(k, None, T, (k.xh, k.xl), k.sb("square2", [P, KC, TC]))


def layer_norm(k, y, g, b, name, work=None):
    nc = k.nc
    if work is None:
        work = k.sb("ln_work", [P, KC + 2, T])
    square, mean, rstd = work[:, 0:KC, :], work[:, KC, :], work[:, KC + 1, :]
    summed, centred, squared, scaled, rounded = (k.sem(f"{s}_{name}") for s in ("ln_summed", "ln_centred", "ln_squared", "ln_scaled", "ln_rounded"))
    with nc.Block() as block:
        k.begin()

        @block.tensor
        def _(pe):
            for c in range(KC):
                mm = pe.matmul(k.bank[0][:, 0:T], k.ones[:, :], y[:, c, :], start=(c == 0), stop=(c == KC - 1))
            mm.then_inc(summed, 1)
            for c in range(KC):
                pe.wait_ge(squared, c + 1)
                mm = pe.matmul(k.bank[1][:, 0:T], k.ones[:, :], square[:, c, :], start=(c == 0), stop=(c == KC - 1))
            mm.then_inc(summed, 1)

        @block.vector
        def _(dve):
            S = k.dve
            dve.wait_ge(summed, 1)
            S.step(dve.tensor_scalar(mean, k.bank[0][:, 0:T], 1.0 / D, None, ALU.mult))
            S.settle(dve)
            for c in range(KC):
                dve.tensor_tensor(y[:, c, :], y[:, c, :], mean, ALU.subtract).then_inc(centred, 1)
            dve.wait_ge(summed, 2)
            S.step(dve.tensor_copy(rstd, k.bank[1][:, 0:T]))
            S.settle(dve)
            dve.wait_ge(centred, KC)
            k.ask_root(dve, rstd, 1.0 / D, 1e-5)
            for c in range(KC + 2):
                if c < KC:
                    dve.tensor_tensor(y[:, c, :], y[:, c, :], rstd, ALU.mult).then_inc(scaled, 1)
                if c >= 2:
                    dve.wait_ge(rounded, c - 1)
                    S.step(dve.tensor_tensor(k.xl[:, c - 2, :], y[:, c - 2, :], k.xh[:, c - 2, :].bitcast(F32), ALU.subtract))

        @block.scalar
        def _(act):
            for c in range(KC):
                act.wait_ge(centred, c + 1)
                act.activation(square[:, c, :], y[:, c, :], ACT.Square).then_inc(squared, 1)
            k.root(act, rstd)
            for c in range(KC):
                act.wait_ge(scaled, c + 1)
                k.act.step(act.activation(y[:, c, :], y[:, c, :], ACT.Identity, bias=k.col(b[0], b[1] + c), scale=k.col(g[0], g[1] + c)))
                k.act.settle(act)
                act.activation(k.xh[:, c, :], y[:, c, :], ACT.Copy).then_inc(rounded, 1)

        @block.sync
        def _(sync):
            k.feed(sync, 0)


GLA_BLOCKS = [256, 256, 256, 256, 256, 256, 16]
RWKV_BLOCKS = [256] * 6 + [160]
RW = 2 * G_H * G_K + 2 * G_H * G_V + G_LORA


def recurrent_project(k, b):
    widths = GLA_BLOCKS + RWKV_BLOCKS
    feature = [("feature", [(0, P), (P, 2 * P)])]

    def outs(blk):
        if 2 <= blk < 6:
            return [("token", 0), ("token", 1)]
        if blk == 6:
            return [("feature", [(0, G_LORA)])]
        return [("feature", [(64, 160), (0, 64)])] if blk == 13 else feature

    def owner(blk, i):
        return "act" if blk in (0, 4, 5, 7, 9, 11) else "dve"

    def store(kind, eng, blk, i, bank):
        if blk < 2:
            return copy(kind, eng, b[("gq", "gk")[blk]], bank[:, :].rearrange("p (a t) -> p a t", a=2))
        if blk < 6:
            name = "gv" if blk < 4 else "gg"
            return copy(kind, eng, b[name][:, i, (blk % 2) * WB:(blk % 2) * WB + WB], bank[:, 0:WB], ACT.Silu if blk >= 4 else ACT.Copy)
        if blk == 6:
            return copy(kind, eng, b["gal"][:, :], bank[0:G_LORA, 0:T])
        if blk < 13:
            return copy(kind, eng, b["raw"][:, 2 * (blk - 7):2 * (blk - 7) + 2, :], bank[:, :].rearrange("p (a t) -> p a t", a=2))
        k.dve.step(eng.tensor_copy(b["wa"][:, :], bank[0:64, T:2 * T]))
        return eng.tensor_copy(b["gl"][:, :], bank[0:96, 0:T])

    project(k, (k.xh, k.xl), T, widths, outs, store, owner)


def recurrent_prepare(k, b, const):
    nc = k.nc
    shift, lshift, t1, t2, gz = b["shift"], b["lshift"], b["t1"], b["t2"], b["gz"]
    shifted = k.sem("shifted")
    lora = k.sem("lora_ready")
    low = k.sem("low_rank_done")
    gates = k.sem("gates_ready")
    logs = k.sem("gla_logs")
    scans = k.sem("scans")
    exps = k.sem("exps")
    norm_sq, norm_sum = k.sem("kk_squared"), k.sem("kk_summed")
    raw, gla_z = b["raw"], gz
    A = lambda x: x[:, :, :]

    def shift_in(eng, S, x, d, c0, c1):
        S.step(eng.tensor_tensor(d[:, c0:c1, 1:T], x[:, c0:c1, 0:T - 1], x[:, c0:c1, 1:T], ALU.subtract))
        S.step(eng.tensor_scalar(d[:, c0:c1, 0:1], x[:, c0:c1, 0:1], -1.0, None, ALU.mult))
        S.settle(eng)
        S.step(eng.tensor_tensor(d[:, c0:c1, :], d[:, c0:c1, :], spread(k.col("mu_rkv", c0, c1 - c0), 2, T), ALU.mult))
        S.settle(eng)
        return eng.tensor_tensor(x[:, c0:c1, :], x[:, c0:c1, :], d[:, c0:c1, :], ALU.add)

    with nc.Block() as block:
        k.begin()

        @block.gpsimd
        def _(pool):
            k.pool.step(shift_in(pool, k.pool, raw, shift, 8, 12))

        @block.tensor
        def _(pe):
            pe.wait_ge(shifted, 2)
            pe.wait_ge(lora, 2)
            for f in range(2):
                mm = pe.matmul(k.bank[0][:, f * T:f * T + T], b["gla_w2"][:, f * P:f * P + P], b["gal"][:, :], start=True, stop=True)
            mm.then_inc(low, 1)
            for f in range(4):
                mm = pe.matmul(k.bank[1 + f // 2][:, (f % 2) * T:(f % 2) * T + T], b["wa2"][0:32, f * P:f * P + P], b["wa"][0:32, :],
                               start=True, stop=True)
            mm.then_inc(low, 1)
            for f in range(4):
                mm = pe.matmul(k.bank[3 + f // 2][:, (f % 2) * T:(f % 2) * T + T], b["wa2"][32:64, f * P:f * P + P], b["wa"][32:64, :],
                               start=True, stop=True)
            mm.then_inc(low, 1)
            for m in range(2):
                mm = pe.matmul(k.bank[5 + m][:, :], b["gl"][:, m * P:m * P + P], b["g2"][:, :], start=True, stop=True)
            mm.then_inc(low, 1)
            pe.wait_ge(norm_sq, 1)
            pe.wait_ge(logs, 1)
            for f in range(4):
                bank = k.bank[7 if f < 2 else 0]
                mm = pe.matmul(bank[:, (f % 2) * T:(f % 2) * T + T], b["headones"], t1[:, f, :], start=True, stop=True)
            mm.then_inc(norm_sum, 1)

        @block.scalar
        def _(act):
            act.wait_ge(shifted, 2)
            act.activation(b["wa"][0:32, :], b["wa"][0:32, :], ACT.Tanh).then_inc(lora, 1)
            act.activation(b["gl"][:, :], b["gl"][:, :], ACT.Sigmoid).then_inc(lora, 1)
            act.wait_ge(low, 2)
            for f in range(4):
                act.activation(b["la"][:, f, :], k.bank[1 + f // 2][:, (f % 2) * T:(f % 2) * T + T], ACT.Sigmoid,
                               bias=k.col("w0", f)).then_inc(gates, 1)
            act.wait_ge(low, 3)
            for f in range(4):
                act.activation(b["a"][:, f, :], k.bank[3 + f // 2][:, (f % 2) * T:(f % 2) * T + T], ACT.Sigmoid,
                               bias=k.col("a0", f)).then_inc(gates, 1)
            act.wait_ge(low, 4)
            for m in range(2):
                act.activation(b["g"][:, m, :], k.bank[5 + m][:, :], ACT.Copy).then_inc(gates, 1)
            act.wait_ge(logs, 1)
            k.act.step(act.activation(A(t2), A(t2), ACT.Exp, scale=-1.0))
            k.act.settle(act)
            act.activation(A(t2), A(t2), ACT.Ln, bias=1.0).then_inc(logs, 1)
            act.wait_ge(scans, 1)
            act.activation(A(b["gdec"]), A(b["gla"]), ACT.Exp).then_inc(exps, 1)
            act.activation(A(b["gneg"]), A(b["gla"]), ACT.Exp, scale=-1.0).then_inc(exps, 1)
            act.wait_ge(scans, 2)
            act.activation(A(b["gout"]), A(b["gout"]), ACT.Exp).then_inc(exps, 1)
            act.wait_ge(scans, 3)
            act.activation(A(b["dec"]), A(b["cum"]), ACT.Exp).then_inc(exps, 1)
            act.activation(A(b["neg"]), A(b["cum"]), ACT.Exp, scale=-1.0).then_inc(exps, 1)
            act.wait_ge(scans, 4)
            act.activation(A(b["la"]), A(b["la"]), ACT.Exp).then_inc(exps, 1)
            k.root(act, A(t1))

        @block.vector
        def _(dve):
            S = k.dve
            for x, rows, j in ((b["wa"], 64, 0), (b["gl"], 96, 1)):
                S.step(dve.tensor_tensor(lshift[0:rows, j, 1:T], x[:, 0:T - 1], x[:, 1:T], ALU.subtract))
                S.step(dve.tensor_scalar(lshift[0:rows, j, 0:1], x[:, 0:1], -1.0, None, ALU.mult))
                S.settle(dve)
                dve.scalar_tensor_tensor(out=x[:, :], in0=lshift[0:rows, j, :], scalar=b["mu_lora"][0:rows, j:j + 1], in1=x[:, :],
                                         op0=ALU.mult, op1=ALU.add).then_inc(shifted, 1)
            S.step(shift_in(dve, S, raw, shift, 0, 8))
            S.settle(dve)
            dve.wait_ge(low, 1)
            S.step(dve.tensor_tensor(A(gz), k.bank[0][:, :].rearrange("p (f t) -> p f t", f=2),
                                     spread(k.col("gla_a_b", 0, 2), 2, T), ALU.add))
            S.settle(dve)
            dve.scalar_tensor_tensor(out=A(t2), in0=A(gz), scalar=-1.0, in1=A(gz), op0=ALU.mult, op1=ALU.max).then_inc(logs, 1)
            S.step(dve.tensor_scalar(A(gz), A(gz), 0.0, None, ALU.min))
            S.step(dve.tensor_tensor(A(b["kk"]), raw[:, 4:8, :], spread(k.col("k_k", 0, 4), 2, T), ALU.mult))
            S.settle(dve)
            dve.tensor_tensor(A(t1), A(b["kk"]), A(b["kk"]), ALU.mult).then_inc(norm_sq, 1)
            dve.wait_ge(logs, 2)
            S.step(dve.tensor_tensor(A(b["gla"]), A(gz), A(t2), ALU.subtract))
            S.settle(dve)
            S.step(dve.tensor_scalar(A(b["gla"]), A(b["gla"]), 1.0 / G_TAU, None, ALU.mult))
            S.settle(dve)
            for f in range(2):
                ins = dve.tensor_tensor_scan(b["gla"][:, f, :], const("within"), b["gla"][:, f, :], 0.0, ALU.mult, ALU.add)
                if f == 0:
                    S.step(ins)
                else:
                    ins.then_inc(scans, 1)
            dve.wait_ge(scans, 1)
            for f in range(2):
                x = b["gla"][:, f, :].rearrange("p (c t) -> p c t", t=CH)
                ins = dve.tensor_tensor(b["gout"][:, f, :].rearrange("p (c t) -> p c t", t=CH),
                                        spread(x[:, :, CH - 1], 2, CH), x, ALU.subtract)
                if f == 0:
                    S.step(ins)
                else:
                    ins.then_inc(scans, 1)
            dve.wait_ge(gates, 4)
            S.step(dve.tensor_scalar(A(b["la"]), A(b["la"]), -DOWN, None, ALU.mult))
            S.settle(dve)
            for f in range(4):
                ins = dve.tensor_tensor_scan(b["cum"][:, f, :], const("within"), b["la"][:, f, :], 0.0, ALU.mult, ALU.add)
                if f < 3:
                    S.step(ins)
                else:
                    ins.then_inc(scans, 1)
            S.settle(dve)
            dve.wait_ge(scans, 3)
            dve.tensor_tensor(A(b["la"]), A(b["cum"]), A(b["la"]), ALU.subtract).then_inc(scans, 1)
            dve.wait_ge(norm_sum, 1)
            for f in range(2):
                S.step(dve.tensor_scalar(t1[:, 2 * f:2 * f + 2, :], k.bank[(7, 0)[f]][:, :].rearrange("p (f t) -> p f t", f=2),
                                         1e-24, None, ALU.max))
            S.settle(dve)
            k.ask_root(dve, A(t1), 1.0, 0.0)
            S.step(dve.tensor_tensor(A(b["kk"]), A(b["kk"]), A(t1), ALU.mult))
            dve.wait_ge(gates, 10)
            S.settle(dve)
            S.step(dve.tensor_scalar(A(t1), A(b["a"]), -1.0, None, ALU.add))
            S.settle(dve)
            S.step(dve.tensor_tensor(A(t1), A(t1), spread(k.col("k_a", 0, 4), 2, T), ALU.mult))
            S.settle(dve)
            S.step(dve.scalar_tensor_tensor(out=A(b["k2"]), in0=A(t1), scalar=1.0, in1=raw[:, 4:8, :], op0=ALU.add, op1=ALU.mult))
            S.settle(dve)
            S.step(dve.tensor_tensor(A(b["rk"]), raw[:, 0:4, :], A(b["k2"]), ALU.mult))
            S.settle(dve)
            S.step(dve.tensor_tensor(A(b["rk"]), A(b["rk"]), spread(k.col("r_k", 0, 4), 2, T), ALU.mult))
            dve.wait_ge(exps, 6)
            S.step(dve.scalar_tensor_tensor(out=A(b["at"]), in0=A(b["kk"]), scalar=-1.0, in1=A(b["la"]), op0=ALU.mult, op1=ALU.mult))
            S.step(dve.tensor_tensor(A(b["bt"]), A(b["kk"]), A(b["a"]), ALU.mult))
            S.settle(dve)
            S.step(dve.tensor_tensor(A(b["bt"]), A(b["bt"]), A(b["neg"]), ALU.mult))
            S.step(dve.tensor_tensor(A(b["kt"]), A(b["k2"]), A(b["neg"]), ALU.mult))
            S.step(dve.tensor_tensor(A(b["rt"]), raw[:, 0:4, :], A(b["dec"]), ALU.mult))
            S.step(dve.scalar_tensor_tensor(out=A(b["gqi"]), in0=A(b["gq"]), scalar=G_K ** -0.5, in1=A(b["gdec"]),
                                            op0=ALU.mult, op1=ALU.mult))
            S.step(dve.tensor_tensor(A(b["gki"]), A(b["gk"]), A(b["gneg"]), ALU.mult))
            S.step(dve.tensor_tensor(A(b["gko"]), A(b["gk"]), A(b["gout"]), ALU.mult))

        @block.sync
        def _(sync):
            k.feed(sync, 0)


def unit(m, h, heads):
    return m * heads + (h % 2) * (heads // 2) + h // 2


def chunk_matrices(k, b, mask):
    nc = k.nc
    filled = k.sem("zeros_ready")
    kinds = [("LT", "bt", "at", "before", 8), ("XT", "bt", "at", "joinT1", 8), ("X", "at", "bt", "join1", 8),
             ("MakT", "kt", "at", "before", 8), ("MrbT", "bt", "rt", "upto", 8), ("MrkT", "kt", "rt", "upto", 8),
             ("AT", "gki", "gqi", "upto", 4)]
    jobs = [(kind, m, g) for kind in kinds for m in range(2) for g in range(2)]
    with nc.Block() as block:
        k.begin()
        fills = Fills(k, ["dve"] * len(jobs))

        @block.gpsimd
        def _(pool):
            for name in ("LT", "MakT", "MrbT", "MrkT", "AT"):
                pool.memset(b[name][:, :, :], 0.0).then_inc(filled, 1)
            pool.memset(b["Z"][:, :, :], 0.0).then_inc(filled, 1)
            pool.memset(b["S"][:, :, :], 0.0).then_inc(filled, 1)
            for name in ("X", "XT"):
                pool.tensor_copy(b[name][:, :, :], spread(k.ident[:, :], 1, 16)).then_inc(filled, 1)

        @block.tensor
        def _(pe):
            for n, ((_, left, right, _, heads), m, g) in enumerate(jobs):
                fills.wait_free(pe, n)
                r = slice(64 * g, 64 * g + 64)
                for j in range(heads // 2):
                    mm = pe.matmul(fills.bank(n)[:, j * P:j * P + P], b[left][r, j, m * P:m * P + P],
                                   b[right][r, j, m * P:m * P + P], start=True, stop=True)
                fills.fill(mm)

        @block.vector
        def _(dve):
            dve.wait_ge(filled, 9)
            for n, ((dst, _, _, which, heads), m, g) in enumerate(jobs):
                fills.wait_full(dve, n)
                u, nu = unit(m, g, heads), heads // 2
                fills.drain(n, dve.copy_predicated(b[dst][:, u:u + nu, :], spread(mask(which), 1, nu),
                                                   fills.bank(n)[:, 0:nu * P].rearrange("p (u t) -> p u t", u=nu)))

        @block.sync
        def _(sync):
            k.feed(sync, 0)


def invert(k, b, mask):
    nc = k.nc
    W = k.sb("LX", [P, 16, P])
    levels = [2 ** i for i in range(1, 6)]
    owners = []
    for _ in levels:
        owners += ["act"] * 4 + ["dve"] * 8
    with nc.Block() as block:
        k.begin()
        fills = Fills(k, owners)

        @block.tensor
        def _(pe):
            n = 0
            for i, _ in enumerate(levels):
                for g in range(4):
                    fills.wait_free(pe, n)
                    if i:
                        fills.wait_drained(pe, n - 12 + 4 - g + 2 * g + 1)
                    for u in range(4 * g, 4 * g + 4):
                        mm = pe.matmul(fills.bank(n)[:, (u % 4) * P:(u % 4) * P + P], b["LT"][:, u, :], b["X"][:, u, :], start=True, stop=True)
                    fills.fill(mm)
                    n += 1
                for g in range(4):
                    fills.wait_drained(pe, n - 4 - g)
                    fills.wait_free(pe, n)
                    for u in range(4 * g, 4 * g + 4):
                        mm = pe.matmul(fills.bank(n)[:, (u % 4) * P:(u % 4) * P + P], b["XT"][:, u, :], W[:, u, :], start=True, stop=True)
                    fills.fill(mm)
                    n += 1
                    fills.wait_free(pe, n)
                    for u in range(4 * g, 4 * g + 4):
                        mm = pe.matmul(fills.bank(n)[:, (u % 4) * P:(u % 4) * P + P], W[:, u, :], b["XT"][:, u, :], start=True, stop=True)
                    fills.fill(mm)
                    n += 1

        @block.scalar
        def _(act):
            for i, _ in enumerate(levels):
                for g in range(4):
                    n = 12 * i + g
                    fills.wait_full(act, n)
                    fills.drain(n, act.activation(W[:, 4 * g:4 * g + 4, :], fills.bank(n)[:, :].rearrange("p (u t) -> p u t", u=4), ACT.Copy))

        @block.vector
        def _(dve):
            for i, m in enumerate(levels):
                for g in range(4):
                    n = 12 * i + 4 + 2 * g
                    fills.wait_full(dve, n + 1)
                    for j, (name, which) in enumerate((("X", f"join{m}"), ("XT", f"joinT{m}"))):
                        fills.drain(n + j, dve.copy_predicated(b[name][:, 4 * g:4 * g + 4, :], spread(mask(which), 1, 4),
                                                               fills.bank(n + j)[:, :].rearrange("p (u t) -> p u t", u=4)))

        @block.sync
        def _(sync):
            k.feed(sync, 0)


def recurrences(k, b):
    nc = k.nc
    R = k.sb("delta_rhs", [P, 512])
    U = k.sb("delta_u", [P, 512])
    pre, pre_out = k.sem("pre_products"), k.sem("pre_drained")
    s1, s1_out, s2, s2_out = k.sem("az"), k.sem("rhs_ready"), k.sem("u_product"), k.sem("u_ready")
    s3, s3_out = k.sem("state_products"), k.sem("states_ready")
    outs, outs_out = k.sem("chunk_outputs"), k.sem("chunk_outputs_drained")
    rows = lambda h: slice(64 * (h % 2), 64 * (h % 2) + 64)
    half = lambda even, odd, h: k.bank[odd if h % 2 else even][:, (h // 2) * 64:(h // 2) * 64 + 64]
    parity = lambda x, q, n: x.rearrange("p (j q e) -> p j q e", q=2, e=n)[:, :, q, :]
    by_head = lambda x, n: x.rearrange("p (j e) -> p j e", e=n)
    with nc.Block() as block:
        k.begin()

        @block.tensor
        def _(pe):
            for m in range(2):
                for h in range(8):
                    mm = pe.matmul(k.bank[m][:, h * 64:h * 64 + 64], b["MakT"][:, unit(m, h, 8), :], b["v"][:, m, h * 64:h * 64 + 64],
                                   start=True, stop=True)
            for m in range(2):
                for f in range(4):
                    mm = pe.matmul(k.bank[2][:, 8 * m + 2 * f:8 * m + 2 * f + 2], b["rk"][:, f, m * P:m * P + P], b["headsel"],
                                   start=True, stop=True)
            mm.then_inc(pre, 1)
            pe.wait_ge(pre_out, 3)
            for c in range(T // CH):
                m, r = c // 2, slice(64 * (c % 2), 64 * (c % 2) + 64)
                t = slice(m * P, m * P + P)
                if c:
                    pe.wait_ge(s3_out, 5 * c)
                    pe.wait_ge(outs_out, 4 * c)
                for h in range(8):
                    mm = pe.matmul(half(0, 6, h), b["at"][rows(h), h // 2, t], b["Z"][rows(h), h // 2, :],
                                   start=True, stop=True)
                mm.then_inc(s1, 1)
                for h in range(4):
                    o = k.bank[(4, 7)[h % 2]][:, (h // 2) * P:(h // 2) * P + P]
                    pe.matmul(o, b["gqi"][rows(h), h // 2, t], b["S"][rows(h), h // 2, :],
                              start=True, stop=False)
                    mm = pe.matmul(o, b["AT"][:, unit(m, h, 4), :], b["gv"][:, m, h * P:h * P + P],
                                   start=False, stop=True)
                mm.then_inc(outs, 1)
                for h in range(4):
                    f = h // 2
                    mm = pe.matmul(k.bank[5][:, h * P:h * P + P], b["gkoT"][r, m, f * P:f * P + P], b["gv"][r, m, h * P:h * P + P],
                                   start=True, stop=True)
                mm.then_inc(s3, 1)
                pe.wait_ge(s1_out, 2 * c + 4)
                for h in range(8):
                    mm = pe.matmul(k.bank[1][:, h * 64:h * 64 + 64], b["XT"][r, unit(m, h, 8), :], R[r, h * 64:h * 64 + 64],
                                   start=True, stop=True)
                mm.then_inc(s2, 1)
                pe.wait_ge(s2_out, c + 1)
                for h in range(8):
                    o, e = half(2, 6, h), slice(h * 64, h * 64 + 64)
                    pe.matmul(o, b["rt"][rows(h), h // 2, t], b["Z"][rows(h), h // 2, :], start=True, stop=False)
                    pe.matmul(o, b["MrbT"][:, unit(m, h, 8), :], U[:, e], start=False, stop=False)
                    mm = pe.matmul(o, b["MrkT"][:, unit(m, h, 8), :], b["v"][:, m, e], start=False, stop=True)
                mm.then_inc(outs, 1)
                for h in range(8):
                    o, e, f = k.bank[3][:, h * 64:h * 64 + 64], slice(h * 64, h * 64 + 64), slice((h // 2) * P, (h // 2) * P + P)
                    pe.matmul(o, b["btT"][r, m, f], U[r, e], start=True, stop=False)
                    mm = pe.matmul(o, b["ktT"][r, m, f], b["v"][r, m, e], start=False, stop=True)
                mm.then_inc(s3, 1)

        @block.vector
        def _(dve):
            S = k.dve
            dve.memset(U[:, :], 0.0).then_inc(s1_out, 1)
            dve.memset(R[:, :], 0.0).then_inc(s1_out, 1)
            dve.wait_ge(s1_out, 2)
            dve.wait_ge(pre, 1)
            for m in range(2):
                dve.tensor_copy(b["MV"][:, m, :], k.bank[m][:, :]).then_inc(pre_out, 1)
            dve.tensor_copy(b["bonus"][:, :], k.bank[2][:, 0:16]).then_inc(pre_out, 1)
            dve.wait_ge(pre_out, 3)
            for c in range(T // CH):
                m, r = c // 2, slice(64 * (c % 2), 64 * (c % 2) + 64)
                last = c * CH + CH - 1
                dve.wait_ge(s1, c + 1)
                for q in range(2):
                    dve.tensor_tensor(parity(R[r, :], q, 64), by_head(k.bank[(0, 6)[q]][r, 0:256], 64),
                                      parity(b["MV"][r, m, :], q, 64), ALU.add).then_inc(s1_out, 1)
                dve.wait_ge(outs, 2 * c + 1)
                S.step(dve.tensor_tensor(b["S"][:, :, :], b["S"][:, :, :], spread(b["gdec"][:, :, last], 2, P), ALU.mult))
                S.settle(dve)
                dve.wait_ge(s3, 2 * c + 1)
                for p in range(2):
                    pr = slice(64 * p, 64 * p + 64)
                    dve.tensor_tensor(b["S"][pr, :, :], b["S"][pr, :, :],
                                      k.bank[5][pr, :].rearrange("p (f q e) -> p f q e", f=2, q=2)[:, :, p, :], ALU.add).then_inc(s3_out, 1)
                dve.wait_ge(s3, 2 * c + 2)
                for p in range(2):
                    pr = slice(64 * p, 64 * p + 64)
                    dve.tensor_tensor(b["Z"][pr, :, :], b["Z"][pr, :, :],
                                      k.bank[3][pr, :].rearrange("p (f q e) -> p f q e", f=4, q=2)[:, :, p, :], ALU.add).then_inc(s3_out, 1)
                dve.wait_ge(s3_out, 5 * c + 4)
                dve.tensor_tensor(b["Z"][:, :, :], b["Z"][:, :, :], spread(b["dec"][:, :, last], 2, 64), ALU.mult).then_inc(s3_out, 1)
                dve.wait_ge(s3_out, 5 * c + 5)

        @block.scalar
        def _(act):
            for c in range(T // CH):
                m, r = c // 2, slice(64 * (c % 2), 64 * (c % 2) + 64)
                act.wait_ge(outs, 2 * c + 1)
                for q in range(2):
                    act.activation(parity(b["go"][r, m, :], q, G_V), by_head(k.bank[(4, 7)[q]][r, 0:256], G_V), ACT.Copy).then_inc(outs_out, 1)
                act.wait_ge(s2, c + 1)
                act.wait_ge(s1_out, 2)
                act.activation(U[r, :], k.bank[1][r, :], ACT.Copy).then_inc(s2_out, 1)
                act.wait_ge(outs, 2 * c + 2)
                for q in range(2):
                    act.activation(parity(b["y"][r, m, :], q, 64), by_head(k.bank[(2, 6)[q]][r, 0:256], 64), ACT.Copy).then_inc(outs_out, 1)

        @block.sync
        def _(sync):
            k.feed(sync, 0)


def recurrent_finish(k, b, row, mix):
    nc = k.nc
    t = b["MV"]
    ss = k.sb("fin_ss", [P, 8])
    mean = k.sb("fin_mean", [P, 16])
    var = k.sb("fin_var", [P, 16])
    go, y = b["go"], b["y"]
    flat = lambda x, n: x[:, :, :].rearrange("p m (h e) -> p (m h) e", e=n)
    with nc.Block() as block:
        k.begin()

        @block.scalar
        def _(act):
            k.root(act, ss[:, :])
            k.root(act, var[:, :])

        @block.vector
        def _(dve):
            S = k.dve

            def do(ins):
                S.step(ins)
                S.settle(dve)

            do(dve.tensor_tensor(t[:, :, :], go[:, :, :], go[:, :, :], ALU.mult))
            do(dve.tensor_reduce(ss[:, :], flat(t, G_V), AX_X, ALU.add))
            k.ask_root(dve, ss[:, :], 1.0 / G_V, 1e-5)
            do(dve.tensor_tensor(flat(go, G_V), flat(go, G_V), spread(ss[:, :], 2, G_V), ALU.mult))
            do(dve.tensor_tensor(flat(go, G_V), flat(go, G_V), spread(row("gla_g"), 1, 8), ALU.mult))
            do(dve.tensor_tensor(mix[:, :, 0:512], go[:, :, :], b["gg"][:, :, :], ALU.mult))
            do(dve.tensor_reduce(mean[:, :], flat(y, 64), AX_X, ALU.add))
            do(dve.tensor_scalar(mean[:, :], mean[:, :], 1.0 / 64, None, ALU.mult))
            do(dve.tensor_tensor(flat(y, 64), flat(y, 64), spread(mean[:, :], 2, 64), ALU.subtract))
            do(dve.tensor_tensor(t[:, :, :], y[:, :, :], y[:, :, :], ALU.mult))
            do(dve.tensor_reduce(var[:, :], flat(t, 64), AX_X, ALU.add))
            k.ask_root(dve, var[:, :], 1.0 / 64, 64e-5)
            do(dve.tensor_tensor(flat(y, 64), flat(y, 64), spread(var[:, :], 2, 64), ALU.mult))
            do(dve.tensor_tensor(y[:, :, :], y[:, :, :], spread(row("lnx_g"), 1, 2), ALU.mult))
            do(dve.tensor_tensor(y[:, :, :], y[:, :, :], spread(row("lnx_b"), 1, 2), ALU.add))
            do(dve.tensor_tensor(flat(t, 64), flat(b["v"], 64), spread(b["bonus"][:, :], 2, 64), ALU.mult))
            do(dve.tensor_tensor(y[:, :, :], y[:, :, :], t[:, :, :], ALU.add))
            do(dve.tensor_tensor(mix[:, :, 512:1024], y[:, :, :], b["g"][:, :, :], ALU.mult))

        @block.sync
        def _(sync):
            k.feed(sync, 0)


def to_residual(k, y):
    def update(dve, n, bank):
        out, xh, xl = y[:, n:n + 2, :], k.xh[:, n:n + 2, :].bitcast(F32), k.xl[:, n:n + 2, :].bitcast(F32)
        k.dve.step(dve.tensor_tensor(out, xh, xl, ALU.add))
        k.dve.settle(dve)
        return dve.scalar_tensor_tensor(out=out, in0=out, scalar=DN_ALPHA, in1=bank[:, :].rearrange("p (c t) -> p c t", c=2),
                                        op0=ALU.mult, op1=ALU.add)
    return update


def recurrent_layer(k):
    d = k.d
    c = lambda name: d["const"][:, CONST_AT[name][0]:CONST_AT[name][0] + CONST_AT[name][1]]

    def lay(host, names):
        flat, o = host.rearrange("p a b -> p (a b)"), 0
        for name, n in names:
            b[name] = flat[:, o:o + n * T].rearrange("p (a b) -> p a b", a=n)
            o += n * T
        assert o <= flat.shape[1]

    with k.room():
        b = {}
        cpart = k.sb("cpart", [P, P + 2 + T])
        masks_sb = k.sb("masks", [P, MASK.shape[1]], U32)
        mask = lambda name: masks_sb[:, MASK_AT[name][0]:MASK_AT[name][0] + P]
        b["headones"], b["headsel"] = cpart[:, 0:P], cpart[:, P:P + 2]
        const = lambda name: cpart[:, P + 2:P + 2 + T]
        for n, shape in (("gla_w2", [G_LORA, 256]), ("wa2", [64, 512]), ("g2", [96, 512]), ("mu_lora", [96, 2]),
                         ("gv", [P, 2, 512]), ("gg", [P, 2, 512]), ("g", [P, 2, 512]), ("v", [P, 2, 512]),
                         ("bonus", [P, 16])):
            b[n] = k.sb(n, shape)
        mix = k.sb("mix2", [P, 2, D])
        with k.room():
            for n, f in (("gdec", 2), ("dec", 4), ("gqi", 2), ("at", 4), ("rt", 4), ("rk", 4)):
                b[n] = k.sb(n, [P, f, T])
            matrices = k.sb("matrices", [P, 6 * 16, P])
            b["AT"] = k.sb("AT", [P, 8, P])
            states = k.sb("states", [P, 2, T])
            b["Z"] = states[:, 0, :].rearrange("p (a b) -> p a b", a=4)
            b["S"] = states[:, 1, :].rearrange("p (a b) -> p a b", a=2)
            for n, f in (("gkoT", 256), ("btT", 512), ("ktT", 512)):
                b[n] = k.sb(n, [P, 2, f])
            load(k, "second", [(cpart[:, 0:P], c("headones")),
                               (cpart[:, P:P + 2], c("headsel")), (cpart[:, P + 2:P + 2 + T], c("within")),
                               (masks_sb[:, :], d["mask"]), (b["gla_w2"][:, :], d["gla_a_w2_2"]),
                               (b["wa2"][0:32, :], d["rwkv_w2_2"]), (b["wa2"][32:64, :], d["rwkv_a2_2"]), (b["g2"][:, :], d["rwkv_g2_2"]),
                               (b["mu_lora"][0:64, 0:1], d["mu_lora"][0:64, :]), (b["mu_lora"][0:96, 1:2], d["mu_lora"][64:160, :])])
            with k.room():
                for n, f in (("gko", 2), ("gki", 2), ("bt", 4), ("kt", 4)):
                    b[n] = k.sb(n, [P, f, T])
                lay(matrices[:, :, :], [("raw", 12), ("shift", 12), ("gla", 2), ("gout", 2),
                                        ("a", 4), ("cum", 4), ("neg", 4), ("kk", 4), ("k2", 4)])
                lay(b["AT"][:, :, :], [("la", 4)])
                lay(states[:, :, :], [("gneg", 2)])
                lay(b["gkoT"][:, :, :], [("lshift", 2)])
                lay(mix[:, :, :], [("t1", 4), ("t2", 2), ("gz", 2)])
                lay(b["btT"][:, :, :], [("gq", 2), ("gk", 2)])
                lay(b["ktT"][:, :, :], [("gal", 1), ("wa", 1), ("gl", 1)])
                for n, rows_ in (("gal", G_LORA), ("wa", 64), ("gl", 96)):
                    b[n] = b[n][0:rows_, 0, :]
                recurrent_project(k, b)
                with k.room():
                    recurrent_prepare(k, b, const)
                jobs = []
                for m in range(2):
                    t = slice(m * P, m * P + P)
                    jobs += [([b["raw"][:, 8 + f, t] for f in range(4)], b["v"][:, m, :]), ([b["bt"][:, f, t] for f in range(4)], b["btT"][:, m, :]),
                             ([b["kt"][:, f, t] for f in range(4)], b["ktT"][:, m, :]), ([b["gko"][:, f, t] for f in range(2)], b["gkoT"][:, m, :])]
                to_feature_major(k, jobs, "recurrent")
                for i, n in enumerate(("X", "XT", "LT", "MrbT", "MrkT", "MakT")):
                    b[n] = matrices[:, 16 * i:16 * i + 16, :]
                chunk_matrices(k, b, mask)
            with k.room():
                invert(k, b, mask)
            for n in ("MV", "go", "y"):
                b[n] = k.sb(n, [P, 2, 512])
            with k.room():
                recurrences(k, b)
            n0, n1 = ROW_AT["gla_g"][0], NROWS
            rows = k.sb("rows2", [P, n1 - n0])
            row = lambda name: rows[:, ROW_AT[name][0] - n0:ROW_AT[name][0] - n0 + ROW_AT[name][1]]
            load(k, "rows2", [(rows[:, :], d["rows"][n0:n1].partition_broadcast(P))])
            with k.room():
                recurrent_finish(k, b, row, mix)
        mixT = k.sb("mixT2_hi", [P, KC, T], F32R), k.sb("mixT2_lo", [P, KC, T], F32R)
        y = k.sb("y2", [P, KC, T])
        jobs = [([mix[:, m, 512 * g + P * f:512 * g + P * f + P] for f in range(4)],
                 tuple(x[:, 4 * g:4 * g + 4, m * P:m * P + P] for x in mixT)) for g in range(2) for m in range(2)]
        to_feature_major(k, jobs, "recurrent_mix")
        project_out(k, mixT, T, to_residual(k, y), "recurrent")
        with k.room():
            layer_norm(k, y, ("mix_g", 0), ("mix_b", 0), "mix0")


DSA_BLOCKS = [WB] * 4 + [2 * S_D] + [WB] * 2 + [I_D + I_H]


def sparse_project(k, b):
    def store(name, eng, blk, m, bank):
        if blk < 4:
            dst = b["q"][:, m, blk * WB:blk * WB + WB]
        elif blk == 4:
            dst = b["kv"][:, m, :]
        elif blk < 7:
            dst = b["qi"][:, m, (blk - 5) * WB:(blk - 5) * WB + WB]
        else:
            dst = b["kw"][:, m, 0:I_D + I_H]
        return copy(name, eng, dst, bank[:, 0:DSA_BLOCKS[blk]])

    project(k, (k.xh, k.xl), T, DSA_BLOCKS, lambda blk: [("token", 0), ("token", 1)], store, lambda blk, m: "dve")


def rotate_halves(eng, S, x, heads, cos, sin, tmp):
    half = cos.shape[1]
    x3 = x.rearrange("p (g e) -> p g e", e=half)
    t3 = tmp[:, 0:heads * 2 * half].rearrange("p (g e) -> p g e", e=half)
    x4 = x.rearrange("p (h s e) -> p h s e", s=2, e=half)
    t4 = tmp[:, 0:heads * 2 * half].rearrange("p (h s e) -> p h s e", s=2, e=half)
    S.step(eng.tensor_tensor(t3, x3, spread(sin, 1, 2 * heads), ALU.mult))
    S.settle(eng)
    S.step(eng.tensor_tensor(x3, x3, spread(cos, 1, 2 * heads), ALU.mult))
    S.settle(eng)
    S.step(eng.tensor_tensor(x4[:, :, 0, :], x4[:, :, 0, :], t4[:, :, 1, :], ALU.subtract))
    S.step(eng.tensor_tensor(x4[:, :, 1, :], x4[:, :, 1, :], t4[:, :, 0, :], ALU.add))
    S.settle(eng)


def sparse_rotate(k, b, const):
    nc = k.nc
    tmp_q, tmp_i = k.sb("rot_q", [P, D]), k.sb("rot_i", [P, 512])
    with nc.Block() as block:
        k.begin()

        @block.vector
        def _(dve):
            for m in range(2):
                rotate_halves(dve, k.dve, b["q"][:, m, :], S_H, const("cosA", m), const("sinA", m), tmp_q)
                k.dve.step(dve.tensor_scalar(b["wi"][:, m, :], b["kw"][:, m, I_D:I_D + I_H], I_H ** -0.5 * I_D ** -0.5, None, ALU.mult))

        @block.gpsimd
        def _(pool):
            for m in range(2):
                rotate_halves(pool, k.pool, b["kv"][:, m, 0:S_D], 1, const("cosA", m), const("sinA", m), tmp_i)
                rotate_halves(pool, k.pool, b["kw"][:, m, 0:I_D], 1, const("cosI", m), const("sinI", m), tmp_i)
                k.pool.step(pool.tensor_copy(b["ki2"][:, m, 0:I_D], b["kw"][:, m, 0:I_D]))
                k.pool.step(pool.tensor_copy(b["ki2"][:, m, I_D:2 * I_D], b["kw"][:, m, 0:I_D]))
                rotate_halves(pool, k.pool, b["qi"][:, m, :], I_H, const("cosI", m), const("sinI", m), tmp_i)

        @block.sync
        def _(sync):
            k.feed(sync, 0)


def select_keys(k, b, const):
    nc = k.nc
    relu = k.sb("relu", [P, 2, 2, T])
    best = k.sb("best8", [P, 2, 8])
    scored, rectified, used = k.sem("index_scored"), k.sem("rectified"), k.sem("relu_used")
    units = [(h, m) for h in range(I_H) for m in range(2)]
    with nc.Block() as block:
        k.begin()

        @block.tensor
        def _(pe):
            for n, (h, m) in enumerate(units):
                r = slice(64 * (h % 2), 64 * (h % 2) + 64)
                if n >= BANKS:
                    pe.wait_ge(rectified, n - BANKS + 1)
                pe.matmul(k.bank[n % BANKS][:, 0:T], b["qiT"][r, h // 2, m * P:m * P + P], b["ki2T"][r, :],
                          start=True, stop=True).then_inc(scored, 1)

        @block.scalar
        def _(act):
            for n, (h, m) in enumerate(units):
                act.wait_ge(scored, n + 1)
                if n >= 4:
                    act.wait_ge(used, n - 3)
                act.activation(relu[:, (n // 2) % 2, m, :], k.bank[n % BANKS][:, 0:T], ACT.Relu).then_inc(rectified, 1)

        @block.vector
        def _(dve):
            S = k.dve
            score, bias = b["score"], b["bias"]
            for n, (h, m) in enumerate(units):
                dve.wait_ge(rectified, n + 1)
                r, w = relu[:, (n // 2) % 2, m, :], b["wi"][:, m, h:h + 1]
                if h == 0:
                    dve.tensor_scalar(score[:, m, :], r, w, None, ALU.mult).then_inc(used, 1)
                else:
                    dve.wait_ge(used, n - 1)
                    dve.scalar_tensor_tensor(out=score[:, m, :], in0=r, scalar=w, in1=score[:, m, :],
                                             op0=ALU.mult, op1=ALU.add).then_inc(used, 1)
            dve.wait_ge(used, len(units))
            S.step(dve.tensor_tensor(score[:, :, :], score[:, :, :], const("causal"), ALU.mult))
            S.settle(dve)
            S.step(dve.tensor_tensor(score[:, :, :], score[:, :, :], const("notcausal"), ALU.add))
            S.settle(dve)
            for _ in range(TOPK // 8):
                for m in range(2):
                    S.step(dve.max(best[:, m, :], score[:, m, :]))
                S.settle(dve)
                for m in range(2):
                    S.step(dve.match_replace(score[:, m, :], best[:, m, :], score[:, m, :], GONE))
                S.settle(dve)
            S.step(dve.tensor_scalar(bias[:, :, :], score[:, :, :], 10 * NEG, None, ALU.is_lt))
            S.settle(dve)
            S.step(dve.tensor_tensor(bias[:, :, :], bias[:, :, :], const("causal"), ALU.mult))
            S.settle(dve)
            S.step(dve.tensor_scalar(bias[:, :, :], bias[:, :, :], -1.0, -NEG, ALU.add, ALU.mult))

        @block.sync
        def _(sync):
            k.feed(sync, 0)


def sparse_layer(k):
    d = k.d
    with k.room():
        b = {}
        y = k.sb("y3", [P, KC, T])
        mixT = k.sb("mixT3_hi", [P, S_H, T], F32R), k.sb("mixT3_lo", [P, S_H, T], F32R)
        with k.room():
            n0 = CONST_AT["cosA"][0]
            n1 = CONST_AT["notcausal"][0] + CONST_AT["notcausal"][1]
            cs = k.sb("consts3", [P, n1 - n0])

            def const(name, m=None):
                o, n = CONST_AT[name]
                if m is None:
                    return cs[:, o - n0:o - n0 + n].rearrange("p (m t) -> p m t", m=2)
                return cs[:, o - n0 + m * (n // 2):o - n0 + (m + 1) * (n // 2)]

            for name, shape in (("q", [P, 2, D]), ("kv", [P, 2, 2 * S_D]), ("qi", [P, 2, 512]), ("kw", [P, 2, I_D + I_H]),
                                ("ki2", [P, 2, 2 * I_D]), ("wi", [P, 2, I_H]), ("qT", [P, S_H, T]), ("kT", [P, T]),
                                ("qiT", [P, 4, T]), ("ki2T", [P, T]), ("score", [P, 2, T]), ("bias", [P, 2, T])):
                b[name] = k.sb("s_" + name, shape)
            load(k, "sparse", [(cs[:, :], d["const"][:, n0:n1])])
            sparse_project(k, b)
            with k.room():
                sparse_rotate(k, b, const)
            jobs = []
            for m in range(2):
                t = slice(m * P, m * P + P)
                jobs += [([b["q"][:, m, 512 * g + P * f:512 * g + P * f + P] for f in range(4)], b["qT"][:, 4 * g:4 * g + 4, t]) for g in range(2)]
                jobs += [([b["qi"][:, m, P * f:P * f + P] for f in range(4)], b["qiT"][:, :, t]), ([b["kv"][:, m, 0:S_D]], b["kT"][:, t]),
                         ([b["ki2"][:, m, :]], b["ki2T"][:, t])]
            to_feature_major(k, jobs, "sparse")
            with k.room():
                select_keys(k, b, const)

            def scores_of(pe, unit, out):
                m, h = unit
                return pe.matmul(out, b["qT"][:, h, m * P:m * P + P], b["kT"][:, :], start=True, stop=True)

            def store(dve, u, bank):
                m, h = u
                t = slice(m * P, m * P + P)
                k.dve.step(dve.tensor_copy(mixT[0][:, h, t], bank))
                k.dve.settle(dve)
                return dve.tensor_tensor(mixT[1][:, h, t], bank, mixT[0][:, h, t].bitcast(F32), ALU.subtract)

            with k.room():
                attention(k, [(m, h) for m in range(2) for h in range(S_H)], T, scores_of,
                          lambda u, c: b["kv"][:, c, S_D:2 * S_D], S_D ** -0.5, lambda u: b["bias"][:, u[0], :], store, "sparse")
        project_out(k, mixT, T, to_residual(k, y), "sparse")
        with k.room():
            layer_norm(k, y, ("mix_g", 8), ("mix_b", 8), "mix1")


PAIR = 2
STREAM = P_N // PAIR
ROUND = SLOTS
ROUNDS = STREAM // ROUND // 2
STEPS = ROUND * PAIR
HALF_J = P_N // 2
GROUP = 4
QUART = PART // P


def peer_source(k, layer, side, j):
    if side == "u":
        return k.d["peer_uT"][layer, bass.ds(j, PAIR)].rearrange("j p k i -> p j (k i)")
    return k.d["peer_v_2"][layer].rearrange("(i j) d -> i j d", j=P_N)[:, bass.ds(j, PAIR), :]


def peer_queries(k, qT):
    project(k, (k.xh, k.xl), T, [WB] * 4, lambda b: [("feature", [(0, P), (P, 2 * P)])],
            lambda name, eng, b, i, bank: copy(name, eng, qT[:, 2 * b:2 * b + 2, :], bank[:, :].rearrange("p (h t) -> p h t", h=2)),
            lambda b, i: "dve")


class Peer:

    def __init__(self, k, layer, hidden, qT, keys, iota, iota16):
        self.k, self.layer, self.hidden, self.qT, self.keys, self.iota, self.iota16 = k, layer, hidden, qT, keys, iota, iota16
        self.o = HALF_J * T
        self.s = self.scratch(2 * 16 * P_N).rearrange("p (m i n) -> p m i n", m=2, i=16)
        self.v16 = self.scratch(512).rearrange("p (m i n) -> p m i n", m=2, i=16)
        self.i16 = self.scratch(512).bitcast(U32).rearrange("p (m i n) -> p m i n", m=2, i=16)
        self.i16f = self.scratch(512).rearrange("p (m i n) -> p m i n", m=2, i=16)
        self.cand = self.scratch(2 * P_H * 256).rearrange("p (m i n) -> p m i n", m=2, i=P_H)
        self.best = self.scratch(256).rearrange("p (m i n) -> p m i n", m=2, i=P_H)
        self.pos = self.scratch(256).bitcast(U32).rearrange("p (m i n) -> p m i n", m=2, i=P_H)
        self.half = self.scratch(512).bitcast(U32).rearrange("p (m s n) -> p m s n", m=2, s=2)
        self.halff = self.scratch(512).rearrange("p (m s n) -> p m s n", m=2, s=2)
        self.pick = self.scratch(P * 16).rearrange("p (i n) -> p i n", n=16)
        self.sums = self.scratch(16).rearrange("p (m n) -> p m n", m=2)
        self.row_of, self.col_of = (self.scratch(256).rearrange("p (m n) -> p m n", m=2) for _ in range(2))
        self.gate = self.scratch(256).rearrange("p (m i n) -> p m i n", m=2, i=P_H)
        self.rest = self.scratch(256)
        self.rowT, self.colT = k.sb("rowT", [P, T], BF16), k.sb("colT", [P, T], BF16)
        self.gateT = k.sb("gateT", [P, T, 3], BF16)
        self.left = k.sb("onehot_rows", [P, 2, GROUP, P], BF16)
        self.right = k.sb("gated_cols", [P, 2, GROUP, 3, HALF_J], BF16)
        self.hot = k.sb("onehot_cols", [P, GROUP, HALF_J], BF16)
        self.zero = k.sb("zero", [P, T], BF16)
        self.hh = k.sb("hidden_hi", [P, 2, T], F32R)
        self.hl = k.sb("hidden_lo", [P, 2, T], F32R)
        self.scored, self.copied, self.shifted, self.exped, self.picked, self.turned, self.ready, self.dense, self.applied, \
            self.stored, self.hh_ready, self.hl_ready, self.hot_ready, self.summed = (k.sem(f"peer_{n}{layer}") for n in (
                "scored", "scores_copied", "shifted", "exped", "picked", "picks_turned", "onehots_ready", "gates_dense",
                "gates_applied", "up_stored", "hidden_hi_ready", "hidden_lo_ready", "column_onehots", "down_summed"))

    def scratch(self, n):
        self.o += n
        assert self.o <= P_N * T
        return self.hidden[:, self.o - n:self.o]

    def begin(self):
        k = self.k
        k.begin()
        self.b0, self.h0 = k.taken, k.nparts
        assert k.fed == self.b0 + SLOTS, "the ring is full of the first slots"
        k.taken += 2 * STREAM
        k.nparts += 2 * STREAM * PARTS
        k.free_at += [(k.lo_ready, self.h0 + PARTS * (b + 1)) for b in range(2 * STREAM)]

    def high(self, act, r, s, q):
        k = self.k
        slot = (self.b0 + s) % SLOTS
        if q == 0:
            act.wait_ge(k.landed[slot], r * 16 + 16 * ((self.b0 + s) // SLOTS + 1))
        act.wait_ge(k.consumed, r * (ROUND * PARTS) + (self.h0 + s * PARTS + q - PARTS + 1))
        act.activation(k.hi[q][:, :], k.ring[slot][:, q * PART:q * PART + PART], ACT.Copy).then_inc(k.hi_ready, 1)

    def low(self, eng, r, s, q):
        k = self.k
        slot = (self.b0 + s) % SLOTS
        eng.wait_ge(k.hi_ready, r * (ROUND * PARTS) + (self.h0 + s * PARTS + q + 1))
        eng.tensor_tensor(k.lo[q][:, :], k.ring[slot][:, q * PART:q * PART + PART], k.hi[q][:, :].bitcast(F32),
                          ALU.subtract).then_inc(k.lo_ready, 1)

    def wait_parts(self, pe, r, s, q):
        k = self.k
        pe.wait_ge(k.hi_ready, r * (ROUND * PARTS) + (self.h0 + s * PARTS + q + 1))
        pe.wait_ge(k.lo_ready, r * (ROUND * PARTS) + (self.h0 + s * PARTS + q + 1))

    def scores(self, pe):
        for n in range(8):
            m, g, side = n // 4, (n // 2) % 2, n % 2
            r = slice(64 * side, 64 * side + 64)
            for j in range(4):
                h = 4 * g + j
                mm = pe.matmul(self.k.bank[n][:, j * P:j * P + P], self.qT[r, h, m * P:m * P + P], self.keys[r, h, :], start=True, stop=True)
            mm.then_inc(self.scored, 1)

    def up_column(self, pe, r, s, j):
        k = self.k
        if j == 0:
            pe.wait_ge(self.stored, r * ROUND + (s + 1))
        for q in (2 * j, 2 * j + 1):
            self.wait_parts(pe, r, s, q)
            for c in range(QUART):
                cc = (q % 2) * QUART + c
                w = slice(c * P, c * P + P)
                for n, (a, b) in enumerate(((k.hi, k.xh), (k.hi, k.xl), (k.lo, k.xh))):
                    mm = pe.matmul(k.bank[s][:, j * T:j * T + T], a[q][:, w], b[:, cc, :], start=(cc == 0 and n == 0),
                                   stop=(cc == KC - 1 and n == 2))
            mm.then_inc(k.consumed, 1)

    def down_column(self, pe, r, s, j):
        k = self.k
        count = r * STEPS + (s * PAIR + j + 1 - P_N)
        pe.wait_ge(self.hh_ready, count)
        pe.wait_ge(self.hl_ready, count)
        for q in (2 * j, 2 * j + 1):
            self.wait_parts(pe, r, s, q)
            for c in range(QUART):
                cc = (q % 2) * QUART + c
                w = slice(c * P, c * P + P)
                out = k.bank[cc // 2][:, (cc % 2) * T:(cc % 2) * T + T]
                for a, b in ((k.hi, self.hh), (k.hi, self.hl), (k.lo, self.hh)):
                    mm = pe.matmul(out, a[q][:, w], b[:, j, :], start=False, stop=False, skip_group_check=True)
            mm.then_inc(k.consumed, 1)

    def dense_gates(self, pe, r, n):
        k = self.k
        g = n % 2
        pe.wait_ge(self.ready, r * STEPS + (n + 1 - HALF_J))
        for t in range(GROUP):
            for part in range(3):
                mm = pe.matmul(k.bank[4 + g][:, t * HALF_J:(t + 1) * HALF_J], self.left[:, g, t, :], self.right[:, g, t, part, :],
                               start=(t == 0 and part == 0), stop=(t == GROUP - 1 and part == 2), skip_group_check=True)
        mm.then_inc(self.dense, 1)

    def turn_picks(self, pe):
        k = self.k
        pe.wait_ge(self.picked, 1)
        for i, x in enumerate((self.row_of, self.col_of)):
            for m in range(2):
                pe.transpose(k.bank[6][:, i * T + m * P:i * T + m * P + P], x[:, m, :], k.ident[:, :])
        for m in range(2):
            mm = pe.transpose(k.bank[7][:, m * P:m * P + P], self.gate[:, m, :, :].rearrange("p h n -> p (h n)"), k.ident[:, :])
        mm.then_inc(self.turned, 1)

    def zeros(self, pe, start):
        for q in range(4):
            for c in range(2):
                mm = pe.matmul(self.k.bank[q][:, c * T:c * T + T], self.zero[:, 0:P], self.zero[:, :],
                               start=start and c == 0, stop=not start and c == 1, skip_group_check=True)
        return mm

    def tensor(self, pe):
        self.scores(pe)
        pe.wait_ge(self.copied, 4)
        with pe.Fori(0, ROUNDS - 1) as r:
            for n in range(STEPS):
                self.up_column(pe, r, n // PAIR, n % PAIR)
        for n in range(STEPS):
            self.up_column(pe, ROUNDS - 1, n // PAIR, n % PAIR)
            if n == STEPS - 3:
                self.turn_picks(pe)
        with pe.Fori(0, ROUNDS) as r:
            for n in range(STEPS):
                self.dense_gates(pe, r + ROUNDS, n)
                self.up_column(pe, r + ROUNDS, n // PAIR, n % PAIR)
        pe.wait_ge(self.stored, ROUND + STREAM)
        self.zeros(pe, True)
        with pe.Fori(0, ROUNDS) as r:
            for n in range(STEPS):
                self.dense_gates(pe, r + 2 * ROUNDS, n)
                self.down_column(pe, r + 2 * ROUNDS, n // PAIR, n % PAIR)
        with pe.Fori(0, ROUNDS) as r:
            for n in range(STEPS):
                self.down_column(pe, r + 3 * ROUNDS, n // PAIR, n % PAIR)
        self.zeros(pe, False).then_inc(self.summed, 1)

    def up_slot(self, act, r, s):
        for q in range(PARTS):
            self.high(act, r + (s + 1) // ROUND, (s + 1) % ROUND, q)
        act.wait_ge(self.k.consumed, r * (ROUND * PARTS) + (self.h0 + PARTS * (s + 1)))
        act.activation(self.hidden[:, bass.ds(r * (STEPS * T) + s * PAIR * T, PAIR * T)], self.k.bank[s][:, :],
                       ACT.Gelu).then_inc(self.stored, 1)

    def hidden_high(self, act, r, n):
        act.wait_ge(self.k.consumed, r * (ROUND * PARTS) + (self.h0 + (n - 1) * 2))
        act.activation(self.hh[:, n % 2, :], self.hidden[:, bass.ds(r * (STEPS * T) + (n * T - P_N * T), T)],
                       ACT.Copy).then_inc(self.hh_ready, 1)

    def down_slot(self, act, r, s, gates, last=False):
        for j in range(PAIR):
            n = s * PAIR + j
            if gates:
                act.wait_ge(self.applied, r * STEPS + (n + 1 - HALF_J))
            if not (last and j == PAIR - 1):
                self.hidden_high(act, r, n + 1)
            if not last:
                for q in (2 * j, 2 * j + 1):
                    self.high(act, r + (s + 1) // ROUND, (s + 1) % ROUND, q)

    def scalar(self, act):
        k = self.k
        for q in range(PARTS):
            self.high(act, 0, 0, q)
        for n in range(8):
            m, g, side = n // 4, (n // 2) % 2, n % 2
            act.wait_ge(self.scored, n + 1)
            dst = self.s[:, m, :, :].rearrange("p (h c) n -> p h c n", c=2)[:, 4 * g:4 * g + 4, side, :]
            act.activation(dst, k.bank[n][:, :].rearrange("p (h n) -> p h n", h=4), ACT.Copy).then_inc(self.copied if n < 4 else self.stored, 1)
        with act.Fori(0, ROUNDS - 1) as r:
            for s in range(ROUND):
                self.up_slot(act, r, s)
        act.wait_ge(self.shifted, 2)
        act.activation(self.gate, self.gate, ACT.Exp).then_inc(self.exped, 1)
        for s in range(ROUND):
            self.up_slot(act, ROUNDS - 1, s)
        with act.Fori(0, ROUNDS) as r:
            for s in range(ROUND):
                self.up_slot(act, r + ROUNDS, s)
        act.wait_ge(self.applied, HALF_J)
        self.hidden_high(act, 2 * ROUNDS, 0)
        with act.Fori(0, ROUNDS) as r:
            for s in range(ROUND):
                self.down_slot(act, r + 2 * ROUNDS, s, True)
        with act.Fori(0, ROUNDS - 1) as r:
            for s in range(ROUND):
                self.down_slot(act, r + 3 * ROUNDS, s, False)
        for s in range(ROUND):
            self.down_slot(act, 4 * ROUNDS - 1, s, False, s == ROUND - 1)

    def select(self, dve):
        k, S = self.k, self.k.dve
        s, v16, i16, i16f, cand, best, pos, half, halff, pick, gate = (
            self.s, self.v16, self.i16, self.i16f, self.cand, self.best, self.pos, self.half, self.halff, self.pick, self.gate)

        def top16(rows, values, indices):
            for i, x in enumerate(rows):
                S.step(dve.max(values(i)[:, 0:8], x))
            S.settle(dve)
            for i, x in enumerate(rows):
                S.step(dve.max_index(indices(i)[:, 0:8], values(i)[:, 0:8], x))
            S.settle(dve)
            for i, x in enumerate(rows):
                S.step(dve.match_replace(x, values(i)[:, 0:8], x, GONE))
            S.settle(dve)
            for i, x in enumerate(rows):
                S.step(dve.max(values(i)[:, 8:16], x))
            S.settle(dve)
            for i, x in enumerate(rows):
                S.step(dve.max_index(indices(i)[:, 8:16], values(i)[:, 8:16], x))

        for m in range(2):
            dve.wait_ge(self.stored if m else self.copied, 4)
            top16([s[:, m, i, :] for i in range(16)], lambda i: v16[:, m, i, :], lambda i: i16[:, m, i, :])
            S.settle(dve)
            S.step(dve.tensor_copy(i16f[:, m, :, :], i16[:, m, :, :]))
            vv = v16[:, m, :, :].rearrange("p (h c) n -> p h c n", c=2)
            S.step(dve.tensor_tensor(cand[:, m, :, :].rearrange("p h (a b) -> p h a b", a=16),
                                     spread(vv[:, :, 0, :], 3, 16), spread(vv[:, :, 1, :], 2, 16), ALU.add))
            S.settle(dve)
            top16([cand[:, m, h, :] for h in range(P_H)], lambda i: best[:, m, i, :], lambda i: pos[:, m, i, :])
            S.settle(dve)
            dve.tensor_tensor(gate[:, m, :, :], best[:, m, :, :], spread(best[:, m, :, 0], 2, 16), ALU.subtract).then_inc(self.shifted, 1)
            p = pos[:, m, :, :].rearrange("p h n -> p (h n)")
            S.step(dve.tensor_single_scalar(half[:, m, 0, :], p, 4, ALU.logical_shift_right))
            S.step(dve.tensor_single_scalar(half[:, m, 1, :], p, 15, ALU.bitwise_and))
            S.settle(dve)
            S.step(dve.tensor_copy(halff[:, m, :, :], half[:, m, :, :]))
            S.settle(dve)
            ii = i16f[:, m, :, :].rearrange("p (h c) n -> p h c n", c=2)
            for side, out in ((0, self.row_of), (1, self.col_of)):
                S.step(dve.tensor_tensor(pick, spread(halff[:, m, side, :], 2, 16), spread(self.iota16, 1, P_H * 16), ALU.is_equal))
                S.settle(dve)
                p4 = pick.rearrange("p (h n) a -> p h n a", h=P_H)
                S.step(dve.tensor_tensor(p4, p4, spread(ii[:, :, side, :], 2, 16), ALU.mult))
                S.settle(dve)
                S.step(dve.tensor_reduce(out[:, m, :], pick, AX_X, ALU.add))
                S.settle(dve)
        dve.wait_ge(self.exped, 1)
        S.step(dve.tensor_reduce(self.sums, gate, AX_X, ALU.add))
        S.settle(dve)
        S.step(dve.reciprocal(self.sums, self.sums))
        S.settle(dve)
        dve.tensor_tensor(gate, gate, spread(self.sums, 3, 16), ALU.mult).then_inc(self.picked, 1)

    def split_gates(self, dve):
        k, S = self.k, self.k.dve
        dve.wait_ge(self.turned, 1)
        S.step(dve.tensor_copy(self.rowT[:, :], k.bank[6][:, 0:T]))
        S.step(dve.tensor_copy(self.colT[:, :], k.bank[6][:, T:2 * T]))
        S.step(dve.tensor_copy(self.gateT[:, :, 0], k.bank[7][:, 0:T]))
        S.settle(dve)
        S.step(dve.tensor_tensor(self.rest, k.bank[7][:, 0:T], self.gateT[:, :, 0], ALU.subtract))
        S.settle(dve)
        S.step(dve.tensor_copy(self.gateT[:, :, 1], self.rest))
        S.settle(dve)
        S.step(dve.tensor_tensor(self.gateT[:, :, 2], self.rest, self.gateT[:, :, 1], ALU.subtract))
        S.settle(dve)

    def onehots(self, dve, phase, r, n):
        g = n % 2
        at = bass.ds(r * (STEPS * GROUP) + n * GROUP, GROUP)
        j = self.iota[:, phase * HALF_J:(phase + 1) * HALF_J]
        dve.tensor_tensor(self.hot[:, :, :], spread(j, 1, GROUP), spread(self.colT[:, at], 2, HALF_J), ALU.is_equal).then_inc(self.hot_ready, 1)
        dve.tensor_tensor(self.left[:, g, :, :], spread(self.iota, 1, GROUP), spread(self.rowT[:, at], 2, P), ALU.is_equal)
        dve.wait_ge(self.hot_ready, r * STEPS + (phase * HALF_J + n + 1))
        dve.tensor_tensor(self.right[:, g, :, :, :], spread(self.hot[:, :, :], 2, 3), spread(self.gateT[:, at, :], 3, HALF_J),
                          ALU.mult).then_inc(self.ready, 1)

    def apply(self, dve, phase, r, n):
        dve.wait_ge(self.dense, r * STEPS + (phase * HALF_J + n + 1))
        h = self.hidden.rearrange("p (j t) -> p j t", t=T)[:, phase * HALF_J:(phase + 1) * HALF_J, bass.ds(r * (STEPS * GROUP) + n * GROUP, GROUP)]
        gates = self.k.bank[4 + n % 2][:, 0:GROUP * HALF_J].rearrange("p (t j) -> p j t", t=GROUP)
        dve.tensor_tensor(h, h, gates, ALU.mult).then_inc(self.applied, 1)

    def hidden_low(self, dve, r, n):
        dve.wait_ge(self.hh_ready, r * STEPS + (n + 1))
        dve.tensor_tensor(self.hl[:, n % 2, :], self.hidden[:, bass.ds(r * (STEPS * T) + n * T, T)], self.hh[:, n % 2, :].bitcast(F32),
                          ALU.subtract).then_inc(self.hl_ready, 1)

    def vector(self, dve, y):
        k = self.k
        k.dve.step(dve.memset(self.zero[:, :], 0.0))
        self.select(dve)
        self.split_gates(dve)
        self.onehots(dve, 0, 0, 0)
        dve.wait_ge(self.stored, ROUND + STREAM // 2)
        with dve.Fori(0, ROUNDS - 1) as r:
            for n in range(STEPS):
                self.apply(dve, 0, r, n)
                self.onehots(dve, 0, r, n + 1)
        for n in range(STEPS):
            self.apply(dve, 0, ROUNDS - 1, n)
            if n < STEPS - 1:
                self.onehots(dve, 0, ROUNDS - 1, n + 1)
        self.onehots(dve, 1, 0, 0)
        self.hidden_low(dve, 0, 0)
        with dve.Fori(0, ROUNDS - 1) as r:
            for n in range(STEPS):
                self.apply(dve, 1, r, n)
                self.onehots(dve, 1, r, n + 1)
                self.hidden_low(dve, r, n + 1)
        for n in range(STEPS):
            self.apply(dve, 1, ROUNDS - 1, n)
            if n < STEPS - 1:
                self.onehots(dve, 1, ROUNDS - 1, n + 1)
            self.hidden_low(dve, ROUNDS - 1, n + 1)
        with dve.Fori(0, ROUNDS - 1) as r:
            for n in range(STEPS):
                self.hidden_low(dve, r + ROUNDS, n + 1)
        for n in range(STEPS - 1):
            self.hidden_low(dve, 2 * ROUNDS - 1, n + 1)
        for q in range(KC // 2):
            at = slice(2 * q, 2 * q + 2)
            k.dve.step(dve.tensor_tensor(y[:, at, :], k.xh[:, at, :].bitcast(F32), k.xl[:, at, :].bitcast(F32), ALU.add))
        k.dve.settle(dve)
        dve.wait_ge(self.summed, 1)
        for q in range(KC // 2):
            at = slice(2 * q, 2 * q + 2)
            k.dve.step(dve.scalar_tensor_tensor(out=y[:, at, :], in0=y[:, at, :], scalar=DN_ALPHA,
                                                in1=k.bank[q][:, :].rearrange("p (c t) -> p c t", c=2), op0=ALU.mult, op1=ALU.add))

    def gpsimd(self, pool):
        with pool.Fori(0, 4 * ROUNDS) as r:
            for s in range(ROUND):
                for q in range(PARTS):
                    self.low(pool, r, s, q)

    def load_slot(self, sync, side, r, s, j):
        k = self.k
        slot = (self.b0 + s) % SLOTS
        sync.wait_ge(k.lo_ready, r * (ROUND * PARTS) + (self.h0 + PARTS * (s + 1) - ROUND * PARTS))
        sync.dma_start(k.ring[slot][:, :].rearrange("p (j n) -> p j n", j=PAIR), peer_source(k, self.layer, side, j)).then_inc(k.landed[slot], 16)

    def sync(self, sync):
        with sync.Fori(0, 2 * ROUNDS - 1) as r:
            for s in range(ROUND):
                self.load_slot(sync, "u", r + 1, s, r * STEPS + (STEPS + PAIR * s))
        with sync.Fori(0, 2 * ROUNDS) as r:
            for s in range(ROUND):
                self.load_slot(sync, "v", r + 2 * ROUNDS, s, r * STEPS + PAIR * s)
        self.k.fed += 2 * STREAM - SLOTS
        self.k.feed(sync, 2 * STREAM)


def peer_layer(k, layer):
    nc, d = k.nc, k.d
    c = lambda name: d["const"][:, CONST_AT[name][0]:CONST_AT[name][0] + CONST_AT[name][1]]
    with k.room():
        iota = k.sb("iota", [P, P])
        iota16 = k.sb("iota16", [P, 16])
        hidden = k.sb("hidden", [P, P_N * T])
        view = lambda o, n, t=T: hidden[:, o * t:(o + n) * t].rearrange("p (a b) -> p a b", a=n)
        qT, keys = view(0, P_H), view(2 * P_H, P_H, P_N)
        load(k, f"peer{layer}", [(iota[:, :], c("iota")), (iota16[:, :], c("iota16")), (keys, d["sub_keysT"][:, layer])])
        peer_queries(k, qT)
        y, work = view(0, KC), view(KC, KC + 2)
        peer = Peer(k, layer, hidden, qT, keys, iota[:, :], iota16[:, :])
        with nc.Block() as block:
            peer.begin()

            @block.tensor
            def _(pe):
                peer.tensor(pe)

            @block.scalar
            def _(act):
                peer.scalar(act)

            @block.vector
            def _(dve):
                peer.vector(dve, y)

            @block.gpsimd
            def _(pool):
                peer.gpsimd(pool)

            @block.sync
            def _(sync):
                peer.sync(sync)
        layer_norm(k, y, ("ffn_g", 8 * layer), ("ffn_b", 8 * layer), f"ffn{layer}", work)


def plan_peer(k, layer):
    plan_columns(k, k.d["peer_w_q_2"][layer], 0, D)
    for side in ("u", "v"):
        k.plan += [(peer_source(k, layer, side, PAIR * s), SLOT) for s in range(STREAM)]


def plan_second(k):
    d = k.d
    w, o = d["even_w_in_2"], 0
    for n in GLA_BLOCKS + RWKV_BLOCKS:
        plan_columns(k, w, o, o + n)
        o += n
    plan_columns(k, d["even_w_out_2"], 0, D)
    plan_peer(k, 0)
    o = 0
    for n in DSA_BLOCKS:
        plan_columns(k, d["odd_w_in_2"], o, o + n)
        o += n
    plan_columns(k, d["odd_w_out_2"], 0, D)
    plan_peer(k, 1)


def second_block(k, out):
    nc = k.nc
    recurrent_layer(k)
    peer_layer(k, 0)
    sparse_layer(k)
    peer_layer(k, 1)
    x = k.sb("result", [P, KC, T])
    summed, stored = k.sem("result_summed"), k.sem("out_stored")
    with nc.Block() as block:
        @block.vector
        def _(dve):
            for c in range(0, KC, 2):
                at = slice(c, c + 2)
                dve.tensor_tensor(x[:, at, :], k.xh[:, at, :].bitcast(F32), k.xl[:, at, :].bitcast(F32), ALU.add).then_inc(summed, 1)

        @block.sync
        def _(sync):
            for c in range(0, KC, 2):
                sync.wait_ge(summed, c // 2 + 1)
                sync.dma_start(out.rearrange("(k p) t -> p k t", p=P)[:, c:c + 2, :], x[:, c:c + 2, :]).then_inc(stored, 16)
            sync.wait_ge(stored, 16 * (KC // 2))




def plan_weights(k):
    d = k.d
    for layer in range(2):
        plan_columns(k, d["ada_w"][layer], 0, 3 * D)
    plan_columns(k, d["even_w_in"], 0, 7 * A_W)
    plan_columns(k, d["even_w_out"], 0, D)
    plan_columns(k, d["odd_w_in"], 0, C_Q)
    plan_columns(k, d["odd_w_in"], C_Q, C_Q + C_KV + C_R)
    plan_columns(k, d["odd_w_in"], C_Q + C_KV + C_R, C_Q + C_KV + C_R + D)
    for g in range(2):
        k.plan.append((d["c_wq_b"].rearrange("(k p) n -> p k n", p=P)[:, :, 768 * g:768 * g + 768], 2 * 768))
    k.plan.append((d["c_wkv_b"], SLOT))
    plan_columns(k, d["odd_w_out"], 0, D)
    plan_second(k)


def program(nc, d, out):
    with ExitStack() as ctx:
        k = Core(nc, ctx, d)
        plan_weights(k)
        k.xh, k.xl = k.sb("x_hi", [P, KC, T], F32R), k.sb("x_lo", [P, KC, T], F32R)
        with k.room():
            setup(k)
            first_block(k)
        second_block(k, out)


INPUTS = ["ada_w", "even_w_in", "even_w_out", "odd_w_in", "c_wq_b", "c_wkv_b", "odd_w_out", "even_w_in_2",
          "gla_a_w2_2", "rwkv_w2_2", "rwkv_a2_2", "rwkv_g2_2", "even_w_out_2", "odd_w_in_2", "odd_w_out_2",
          "peer_w_q_2", "peer_v_2"]


def columns(v):
    return np.asarray(v).reshape(-1, P).T


def lay_out(inputs):
    a = {n: np.ascontiguousarray(inputs[n]) for n in INPUTS}
    for n in INPUTS:
        if a[n].ndim == 3 and a[n].shape[0] == 1:
            a[n] = a[n][0]
    f = {n: np.asarray(v) for n, v in inputs.items()}
    a["xT"] = np.ascontiguousarray(f["x"][0].T)
    a["ctxT"] = np.ascontiguousarray(f["ctx"][0].T)
    a["a_wsT"] = np.ascontiguousarray(f["a_ws"][0].transpose(2, 0, 1))
    cond = np.stack([columns(f["c"][0]), columns(f["c_ctx"])], -1).reshape(P, 16)
    mu = f["rwkv_mu_2"][0]
    pack = {"norm_w": columns(f["norm_w"]), "ada_b": columns(f["ada_b"]), "final_w": columns(f["final_w"]),
            "mix_g": columns(f["mix_ln_g_2"]), "mix_b": columns(f["mix_ln_b_2"]), "ffn_g": columns(f["ffn_ln_g_2"]),
            "ffn_b": columns(f["ffn_ln_b_2"]), "mu_rkv": columns(mu[:1536]), "w0": columns(f["rwkv_w0_2"]),
            "a0": columns(f["rwkv_a0_2"]), "k_k": columns(f["rwkv_k_k_2"]), "k_a": columns(f["rwkv_k_a_2"]),
            "r_k": columns(f["rwkv_r_k_2"]), "gla_a_b": columns(f["gla_a_b_2"]), "a_bs": f["a_bs"][0].T, "cond": cond}
    a["cols"] = np.ascontiguousarray(np.concatenate([pack[n] for n, _ in COLS], 1))
    a["mu_lora"] = np.ascontiguousarray(mu[1536:].reshape(-1, 1))
    pack = {"a_ln_w": f["a_ln_w"], "a_ln_b": f["a_ln_b"], "subln_w": f["b_subln_w"], "lq1": f["b_lq1"], "lk1": f["b_lk1"],
            "lq2": f["b_lq2"], "lk2": f["b_lk2"], "q_norm": f["c_q_norm_w"], "kv_norm": f["c_kv_norm_w"],
            "gla_g": f["gla_norm_g_2"], "lnx_g": f["rwkv_lnx_g_2"], "lnx_b": f["rwkv_lnx_b_2"]}
    a["rows"] = np.ascontiguousarray(np.concatenate([pack[n].reshape(-1) for n, _ in ROWS]))
    a["sub_keysT"] = np.ascontiguousarray(f["peer_sub_keys_2"].transpose(2, 4, 0, 1, 3).reshape(P, 2, P_H, P_N))
    a["peer_uT"] = np.ascontiguousarray(f["peer_u_2"].reshape(2, P_N, P_N, KC, P).transpose(0, 2, 4, 3, 1))
    a["const"], a["mask"] = CONST, MASK
    return a


def kernel(**inputs):
    import concourse.bacc as bacc
    from concourse.bass_utils import run_bass_kernel_spmd

    nc = bacc.Bacc("TRN2", target_bir_lowering=False, num_devices=1)
    arrays = {f"in_{n}": a for n, a in lay_out(inputs).items()}
    d = {n[3:]: nc.dram_tensor(n, a.shape, mybir.dt.from_np(a.dtype), kind="ExternalInput").ap() for n, a in arrays.items()}
    out = nc.dram_tensor("out_T", (D, T), F32, kind="ExternalOutput").ap()
    program(nc, d, out)
    r = run_bass_kernel_spmd(nc, [arrays], core_ids=[0])
    return np.ascontiguousarray(r.results[0]["out_T"].T).reshape(1, T, D)
```

```python
import math
from contextlib import ExitStack, contextmanager

import numpy as np

import concourse.bass as bass
from concourse import mybir

F32 = mybir.dt.float32
F32R = mybir.dt.float32r
BF16 = mybir.dt.bfloat16
U32 = mybir.dt.uint32
ALU = mybir.AluOpType
ACT = mybir.ActivationFunctionType
AX_X = mybir.AxisListType.X

P = 128
D = 1024
KC = D // P
T = 256
TC = 512
SLOT = 2048
SLOTS = 4
WB = SLOT // KC
PARTS = 4
PART = SLOT // PARTS
BANK = 512
BANKS = 8

A_W, A_G = 512, 8
B_H, B_D, B_V = 4, 64, 128
C_H, C_N, C_R, C_V, C_Q, C_KV = 8, 128, 64, 128, 256, 128
G_H, G_K, G_V, G_LORA, G_TAU = 4, 64, 128, 16, 16.0
R_H, R_N = 8, 64
CH = 64
S_H, S_D, I_H, I_D, TOPK = 8, 128, 8, 64, 64
NEG = -1e30
GONE = -3e38
P_H, P_K, P_N = 8, 16, 128
DN_ALPHA = 4 ** 0.25
DOWN = math.exp(-0.5)


def axial_tables():
    t = np.arange(T)
    half = B_D // 2
    inv = (np.float32(10000.0) ** (-np.arange(0, half, 2, dtype=np.float32) / np.float32(half))).astype(np.float32)
    r = (t // 64)[:, None].astype(np.float32) * inv
    c = (t % 64)[:, None].astype(np.float32) * inv
    ang = np.concatenate([r, r, c, c], -1).astype(np.float32)
    sign = np.tile(np.repeat([-1.0, 1.0], 16), 2)
    return np.cos(ang), np.sin(ang) * sign


def rope_tables(dim):
    inv = (np.float32(10000.0) ** (-np.arange(0, dim, 2, dtype=np.float32) / np.float32(dim))).astype(np.float32)
    ang = np.arange(T, dtype=np.float32)[:, None] * inv
    return np.cos(ang), np.sin(ang)


def constants():
    i = np.arange(P)
    tiles = lambda a: np.concatenate([a[:P], a[P:]], -1)
    parts = {
        "ident": np.eye(P),
        "ones": np.ones((P, P)),
        "headones": (i[:, None] // 64 == i[None, :] // 64) * 1.0,
        "iota": np.tile(i, (P, 1)) * 1.0,
        "iota16": np.tile(np.arange(16), (P, 1)) * 1.0,
        "headsel": (i[:, None] // 64 == np.arange(2)[None, :]) * 1.0,
        "within": np.tile((np.arange(T) % CH != 0) * 1.0, (P, 1)),
    }
    ca, sa = axial_tables()
    parts["axcos"], parts["axsin"] = tiles(ca), tiles(sa)
    c, s = rope_tables(S_D)
    parts["cosA"], parts["sinA"] = tiles(c), tiles(s)
    c, s = rope_tables(I_D)
    parts["cosI"], parts["sinI"] = tiles(c), tiles(s)
    q = np.arange(T)
    causal = (q[None, :] <= q[:, None]) * 1.0
    parts["causal"] = tiles(causal)
    parts["notcausal"] = tiles((1 - causal) * NEG)
    at, off = {}, 0
    for name, a in parts.items():
        at[name] = (off, a.shape[1])
        off += a.shape[1]
    return np.concatenate(list(parts.values()), 1).astype(np.float32), at


def masks():
    i = np.arange(P)
    a, b = i[:, None], i[None, :]
    chunk = a // CH == b // CH
    parts = {"before": chunk & (a < b), "upto": chunk & (a <= b)}
    m = 1
    while m < CH:
        lower = (a // (2 * m) == b // (2 * m)) & ((a // m) % 2 == 1) & ((b // m) % 2 == 0)
        parts[f"join{m}"] = lower
        parts[f"joinT{m}"] = lower.T
        m *= 2
    at, off = {}, 0
    for name, x in parts.items():
        at[name] = (off, x.shape[1])
        off += x.shape[1]
    return np.concatenate(list(parts.values()), 1).astype(np.uint32), at


CONST, CONST_AT = constants()
MASK, MASK_AT = masks()

COLS = [("norm_w", 16), ("ada_b", 48), ("final_w", 8), ("mix_g", 16), ("mix_b", 16), ("ffn_g", 16),
        ("ffn_b", 16), ("mu_rkv", 12), ("w0", 4), ("a0", 4), ("k_k", 4), ("k_a", 4), ("r_k", 4),
        ("gla_a_b", 2), ("a_bs", 8), ("cond", 16)]
COL_AT, _o = {}, 0
for _n, _w in COLS:
    COL_AT[_n] = (_o, _w)
    _o += _w
NCOLS = _o
ROWS = [("a_ln_w", 512), ("a_ln_b", 512), ("subln_w", 128), ("lq1", 64), ("lq2", 64), ("lk1", 64), ("lk2", 64),
        ("q_norm", 256), ("kv_norm", 128), ("gla_g", 128), ("lnx_g", 512), ("lnx_b", 512)]
ROW_AT, _o = {}, 0
for _n, _w in ROWS:
    ROW_AT[_n] = (_o, _w)
    _o += _w
NROWS = _o


class Steps:

    def __init__(self, sem):
        self.sem, self.n = sem, 0

    def step(self, ins):
        ins.then_inc(self.sem, 1)
        self.n += 1
        return self.n

    def settle(self, eng, n=None):
        eng.wait_ge(self.sem, self.n if n is None else n)


def spread(ap, axis, n):
    a = ap.unsqueeze(axis)
    shape = list(a.shape)
    shape[axis] = n
    return a.broadcast_to(shape)


class Core:

    def __init__(self, nc, ctx, dram):
        self.made = {}
        self.nc, self.ctx, self.whole, self.d = nc, ctx, ctx, dram
        self.ident = self.sb("ident", [P, P])
        self.ones = self.sb("ones", [P, P])
        self.cols = self.sb("cols", [P, NCOLS])
        self.ring = [self.sb(f"ring{s}", [P, SLOT]) for s in range(SLOTS)]
        self.bank = [ctx.enter_context(nc.psum_tensor(f"bank{b}", [P, BANK], F32)) for b in range(BANKS)]
        self.landed = [self.sem(f"weights_landed{s}") for s in range(SLOTS)]
        self.filled = self.sem("bank_filled")
        self.drained = {"act": self.sem("act_drained"), "dve": self.sem("dve_drained")}
        self.nfilled = 0
        self.hi = [self.sb(f"w_hi{i}", [P, PART], F32R) for i in range(PARTS)]
        self.lo = [self.sb(f"w_lo{i}", [P, PART], F32R) for i in range(PARTS)]
        self.hi_ready, self.lo_ready, self.consumed = self.sem("w_hi_ready"), self.sem("w_lo_ready"), self.sem("w_consumed")
        self.nparts = 0
        self.split_ahead = 0
        self.ndrained = {"act": 0, "dve": 0}
        self.dve = Steps(self.sem("dve_step"))
        self.act = Steps(self.sem("act_step"))
        self.pool = Steps(self.sem("pool_step"))
        self.radicand, self.rooted = self.sem("radicand_ready"), self.sem("rooted")
        self.asked = self.answered = 0
        self.plan = []
        self.free_at = []
        self.fed = 0
        self.taken = 0

    def sb(self, name, shape, dt=F32):
        self.made[name] = self.made.get(name, 0) + 1
        if self.made[name] > 1:
            name = f"{name}_{self.made[name]}"
        return self.ctx.enter_context(self.nc.sbuf_tensor(name, shape, dt))

    @contextmanager
    def room(self):
        outer = self.ctx
        with ExitStack() as self.ctx:
            yield
        self.ctx = outer

    def sem(self, name):
        return self.whole.enter_context(self.nc.semaphore(name))

    def col(self, name, i=0, n=1):
        o = COL_AT[name][0] + i
        return self.cols[:, o:o + n]

    def feed(self, sync, count):
        end = min(len(self.plan), self.taken_before + count + SLOTS)
        while self.fed < end:
            b = self.fed
            if b >= SLOTS:
                sync.wait_ge(*self.free_at[b - SLOTS])
            src, n = self.plan[b]
            dst = self.ring[b % SLOTS][:, 0:n]
            if len(src.shape) == 3:
                dst = dst.rearrange("p (k n) -> p k n", k=src.shape[1])
            sync.dma_start(dst, src).then_inc(self.landed[b % SLOTS], 16)
            self.fed += 1

    def ask_root(self, dve, x, scale, eps):
        dve.tensor_scalar(x, x, scale, eps, ALU.mult, ALU.add).then_inc(self.radicand, 1)
        self.asked += 1
        dve.wait_ge(self.rooted, self.asked)
        self.dve.step(dve.reciprocal(x, x))
        self.dve.settle(dve)

    def root(self, act, x):
        self.answered += 1
        act.wait_ge(self.radicand, self.answered)
        act.activation(x, x, ACT.Sqrt).then_inc(self.rooted, 1)

    def begin(self):
        self.taken_before = self.taken

    def take(self, pe):
        b = self.taken
        pe.wait_ge(self.landed[b % SLOTS], 16 * (b // SLOTS + 1))
        self.taken += 1
        return self.ring[b % SLOTS]

    def release(self):
        self.free_at.append((self.filled, self.nfilled))


class Fills:

    def __init__(self, k, owners):
        self.k, self.owners = k, owners
        self.base = k.nfilled
        self.dbase = dict(k.ndrained)
        seen = dict(self.dbase)
        self.count = []
        for o in owners:
            seen[o] += 1
            self.count.append((o, seen[o]))
        k.ndrained.update(seen)

    def bank(self, n):
        return self.k.bank[n % BANKS]

    def wait_free(self, pe, n):
        if n >= BANKS:
            owner, count = self.count[n - BANKS]
            pe.wait_ge(self.k.drained[owner], count)

    def wait_drained(self, eng, n):
        owner, count = self.count[n]
        eng.wait_ge(self.k.drained[owner], count)

    def fill(self, ins):
        ins.then_inc(self.k.filled, 1)
        self.k.nfilled += 1

    def wait_full(self, eng, n):
        eng.wait_ge(self.k.filled, self.base + n + 1)

    def drain(self, n, ins):
        ins.then_inc(self.k.drained[self.owners[n]], 1)


class Split:

    def __init__(self, k, widths, ahead=False):
        self.k, self.widths = k, widths
        self.b0, self.h0 = k.taken, k.nparts
        self.done_before = 0
        if ahead:
            return
        k.taken += len(widths)
        k.nparts += PARTS * len(widths)
        k.free_at += [(k.lo_ready, self.h0 + PARTS * (b + 1)) for b in range(len(widths))]

        self.done_before = k.split_ahead
        k.split_ahead = 0

    def source(self, h):
        b = self.b0 + h // PARTS
        n = self.widths[h // PARTS] * KC // PARTS
        return self.k.ring[b % SLOTS][:, (h % PARTS) * n:(h % PARTS) * n + n], n

    def high(self, act, h):
        k, b, g = self.k, self.b0 + h // PARTS, self.h0 + h
        if h < self.done_before:
            return
        src, n = self.source(h)
        act.wait_ge(k.landed[b % SLOTS], 16 * (b // SLOTS + 1))
        if g >= PARTS:
            act.wait_ge(k.consumed, g - PARTS + 1)
        act.activation(k.hi[g % PARTS][:, 0:n], src, ACT.Copy).then_inc(k.hi_ready, 1)

    def low(self, eng, h):
        k, g = self.k, self.h0 + h
        if h < self.done_before:
            return
        src, n = self.source(h)
        eng.wait_ge(k.hi_ready, g + 1)
        eng.tensor_tensor(k.lo[g % PARTS][:, 0:n], src, k.hi[g % PARTS][:, 0:n].bitcast(F32), ALU.subtract).then_inc(k.lo_ready, 1)

    def parts(self, pe, h):
        k, g, w = self.k, self.h0 + h, self.widths[h // PARTS]
        pe.wait_ge(k.hi_ready, g + 1)
        pe.wait_ge(k.lo_ready, g + 1)
        view = lambda x: x[:, 0:w * KC // PARTS].rearrange("p (c n) -> p c n", n=w)
        return view(k.hi[g % PARTS]), view(k.lo[g % PARTS])

    def done(self, mm):
        mm.then_inc(self.k.consumed, 1)

    def wait_done(self, eng, h):
        eng.wait_ge(self.k.consumed, self.h0 + h + 1)


class Ahead:

    def __init__(self, k):
        self.split = Split(k, [k.plan[k.taken][1] // KC], ahead=True)
        k.split_ahead = PARTS

    def high(self, act):
        for h in range(PARTS):
            self.split.high(act, h)

    def low(self, pool):
        for h in range(PARTS):
            self.split.low(pool, h)


def project(k, x, tokens, widths, outs, store, owner, low_on="pool", norm=None, loads=()):
    nc = k.nc
    n = len(widths)
    loaded = k.sem(f"loaded{k.taken}") if loads else None
    with nc.Block() as block:
        k.begin()
        split = Split(k, widths)
        counts, seen = [], dict(k.ndrained)
        for b in range(n):
            for i in range(len(outs(b))):
                seen[owner(b, i)] += 1
            counts.append(dict(seen))
        before = dict(k.ndrained)
        k.ndrained.update(seen)

        @block.tensor
        def _(pe):
            if norm:
                norm.tensor(pe)
            for b in range(n):
                if b >= 2:
                    for name in ("act", "dve"):
                        pe.wait_ge(k.drained[name], counts[b - 2][name])
                for part in range(PARTS):
                    w = split.parts(pe, PARTS * b + part)
                    if norm and b == 0:
                        norm.wait_chunk(pe, KC // PARTS * (part + 1) - 1)
                    for i, (kind, arg) in enumerate(outs(b)):
                        bank = k.bank[4 * (b % 2) + i]
                        groups = [(0, widths[b])] if kind == "token" else arg
                        for j, (f0, f1) in enumerate(groups):
                            for c in range(KC // PARTS):
                                cc = KC // PARTS * part + c
                                for q, (wp, xp) in enumerate(((0, 0), (0, 1), (1, 0))):
                                    if kind == "token":
                                        out, lhs, rhs = bank[:, 0:f1], x[xp][:, cc, arg * P:arg * P + P], w[wp][:, c, :]
                                    else:
                                        out, lhs, rhs = bank[0:f1 - f0, j * tokens:(j + 1) * tokens], w[wp][:, c, f0:f1], x[xp][:, cc, 0:tokens]
                                    mm = pe.matmul(out, lhs, rhs, start=(j == 0 and cc == 0 and q == 0),
                                                   stop=(cc == KC - 1 and q == 2), skip_group_check=True)
                    split.done(mm)

        def program(name, eng):
            act, low = name == "act", name == low_on
            if norm and act:
                norm.squares(eng)
            for b in range(-1, n):
                for h in range(PARTS * (b + 1), PARTS * (b + 2)):
                    if h < PARTS * n and act:
                        split.high(eng, h)
                    if h < PARTS * n and low:
                        split.low(eng, h)
                if norm and b == -1 and name != "pool":
                    (norm.scalar if act else norm.vector)(eng)
                if b >= 0 and name != "pool":
                    for i in range(len(outs(b))):
                        if owner(b, i) == name:
                            split.wait_done(eng, PARTS * b + PARTS - 1)
                            store(name, eng, b, i, k.bank[4 * (b % 2) + i]).then_inc(k.drained[name], 1)

        @block.scalar
        def _(act):
            program("act", act)

        @block.vector
        def _(dve):
            program("dve", dve)

        @block.gpsimd
        def _(pool):
            program("pool", pool)

        @block.sync
        def _(sync):
            for dst, src in loads:
                sync.dma_start(dst, src).then_inc(loaded, 16)
            k.feed(sync, n)
            if loads:
                sync.wait_ge(loaded, 16 * len(loads))


def copy(kind, eng, dst, src, func=ACT.Copy):
    if kind == "act":
        return eng.activation(dst, src, func)
    return eng.tensor_copy(dst, src)


def plan_columns(k, w, c0, c1):
    for c in range(c0, c1, WB):
        n = min(WB, c1 - c)
        k.plan.append((w.rearrange("(k p) n -> p k n", p=P)[:, :, c:c + n], KC * n))


def setup(k):
    nc, d = k.nc, k.d
    k.h = k.sb("residual", [P, KC, TC])
    loaded = k.sem("setup_loaded")
    with nc.Block() as block:
        k.begin()

        @block.sync
        def _(sync):
            sync.dma_start(k.cols[:, :], d["cols"]).then_inc(loaded, 16)
            k.feed(sync, 0)

        @block.scalar
        def _(act):
            o = CONST_AT["ident"][0]
            act.dma_start(k.ident[:, :], d["const"][:, o:o + P]).then_inc(loaded, 16)
            o = CONST_AT["ones"][0]
            act.dma_start(k.ones[:, :], d["const"][:, o:o + P]).then_inc(loaded, 16)
            act.dma_start(k.h[:, :, 0:T], d["xT"].rearrange("(k p) t -> p k t", p=P)).then_inc(loaded, 16)
            act.dma_start(k.h[:, :, T:TC], d["ctxT"].rearrange("(k p) t -> p k t", p=P)).then_inc(loaded, 16)
            act.wait_ge(loaded, 80)


def modulation(k):
    nc = k.nc
    k.mod = k.sb("mod", [P, 2, 24, 2])
    n = 24
    with k.room():
        cond = k.sb("silu_cond", [P, KC, 2])
        parts = k.sb("cond_parts", [P, KC, 4], F32R)
        rowed = k.sb("mod_rows", [4, n, WB])
        ready, turned = k.sem("cond_ready"), k.sem("mod_turned")
        with nc.Block() as block:
            k.begin()
            split = Split(k, [WB] * n)

            @block.scalar
            def _(act):
                k.act.step(act.activation(cond[:, :, :].rearrange("p k c -> p (k c)"), k.col("cond", 0, 16), ACT.Silu))
                k.act.settle(act)
                act.activation(parts[:, :, 0:2], cond[:, :, :], ACT.Copy).then_inc(ready, 1)
                for h in range(PARTS * n):
                    split.high(act, h)

            @block.tensor
            def _(pe):
                pe.wait_ge(ready, 2)
                for b in range(n):
                    if b >= BANKS:
                        pe.wait_ge(k.drained["dve"], k.ndrained["dve"] + b - BANKS + 1)
                    for part in range(PARTS):
                        hi, lo = split.parts(pe, PARTS * b + part)
                        for c in range(KC // PARTS):
                            cc = KC // PARTS * part + c
                            pe.matmul(k.bank[b % BANKS][0:4, 0:WB], parts[:, cc, :], hi[:, c, :], start=(cc == 0), stop=False,
                                      skip_group_check=True)
                            mm = pe.matmul(k.bank[b % BANKS][0:2, 0:WB], parts[:, cc, 0:2], lo[:, c, :], start=False,
                                           stop=(cc == KC - 1), skip_group_check=True)
                        split.done(mm)
                for layer in range(2):
                    pe.wait_ge(k.drained["dve"], k.ndrained["dve"] + 12 * (layer + 1))
                    for f in range(24):
                        mm = pe.transpose(k.bank[layer][:, 4 * f:4 * f + 4], rowed[:, 12 * layer + f // 2, (f % 2) * P:(f % 2) * P + P],
                                          k.ident[0:4, 0:4])
                    mm.then_inc(turned, 1)

            @block.vector
            def _(dve):
                S = k.dve
                dve.wait_ge(ready, 1)
                dve.tensor_tensor(parts[:, :, 2:4], cond[:, :, :], parts[:, :, 0:2].bitcast(F32), ALU.subtract).then_inc(ready, 1)
                for b in range(n + 1):
                    if b < n:
                        for part in range(PARTS):
                            split.low(dve, PARTS * b + part)
                    if b >= 1:
                        split.wait_done(dve, PARTS * b - 1)
                        dve.tensor_copy(rowed[:, b - 1, :], k.bank[(b - 1) % BANKS][0:4, 0:WB]).then_inc(k.drained["dve"], 1)
                for layer in range(2):
                    dve.wait_ge(turned, layer + 1)
                    bank = k.bank[layer][:, 0:96].rearrange("p (f q c) -> p f q c", q=2, c=2)
                    mod = k.mod[:, layer, :, :]
                    S.step(dve.tensor_tensor(mod, bank[:, :, 0, :], spread(k.col("ada_b", 24 * layer, 24), 2, 2), ALU.add))
                    S.settle(dve)
                    S.step(dve.tensor_tensor(mod, mod, bank[:, :, 1, :], ALU.add))
                    S.settle(dve)
                    scale = k.mod[:, layer, 8:16, :]
                    S.step(dve.scalar_tensor_tensor(out=scale, in0=scale, scalar=1.0, in1=spread(k.col("norm_w", 8 * layer, 8), 2, 2),
                                                    op0=ALU.add, op1=ALU.mult))

            @block.sync
            def _(sync):
                k.feed(sync, n)
        k.ndrained["dve"] += n


class RmsNorm:

    def __init__(self, k, layer, tokens, out, work):
        self.k, self.layer, self.tokens, self.out, self.work = k, layer, tokens, out, work
        self.squared, self.summed, self.scaled, self.rounded, self.ready = (
            k.sem(f"{s}_{layer}") for s in ("squared", "summed", "scaled", "rounded", "normed"))
        self.rstd = k.sb("rms_rstd", [P, tokens])

    def squares(self, act):
        for c in range(KC):
            act.activation(self.work[:, c, 0:self.tokens], self.k.h[:, c, 0:self.tokens], ACT.Square).then_inc(self.squared, 1)

    def tensor(self, pe):
        k = self.k
        for c in range(KC):
            pe.wait_ge(self.squared, c + 1)
            mm = pe.matmul(k.bank[7][:, 0:self.tokens], k.ones[:, :], self.work[:, c, 0:self.tokens], start=(c == 0), stop=(c == KC - 1))
        mm.then_inc(self.summed, 1)

    def scalar(self, act):
        k = self.k
        k.root(act, self.rstd[:, :])
        for c in range(KC):
            act.wait_ge(self.scaled, c + 1)
            x = self.work[:, c, 0:self.tokens]
            if self.layer is None:
                k.act.step(act.activation(x, x, ACT.Copy, scale=k.col("final_w", c)))
            else:
                for s in range(self.tokens // T):
                    o = self.work[:, c, s * T:s * T + T]
                    k.act.step(act.activation(o, o, ACT.Identity, bias=k.mod[:, self.layer, c, s:s + 1],
                                              scale=k.mod[:, self.layer, 8 + c, s:s + 1]))
            k.act.settle(act)
            act.activation(self.out[0][:, c, 0:self.tokens], x, ACT.Copy).then_inc(self.rounded, 1)

    def vector(self, dve):
        k, n = self.k, self.tokens
        hi, lo = self.out
        dve.wait_ge(self.summed, 1)
        k.dve.step(dve.tensor_copy(self.rstd[:, :], k.bank[7][:, 0:n]))
        k.dve.settle(dve)
        k.ask_root(dve, self.rstd[:, :], 1.0 / D, 1e-6)
        for c in range(KC + 2):
            if c < KC:
                dve.tensor_tensor(self.work[:, c, 0:n], k.h[:, c, 0:n], self.rstd[:, :], ALU.mult).then_inc(self.scaled, 1)
            if c >= 2:
                dve.wait_ge(self.rounded, c - 1)
                dve.tensor_tensor(lo[:, c - 2, 0:n], self.work[:, c - 2, 0:n], hi[:, c - 2, 0:n].bitcast(F32), ALU.subtract).then_inc(self.ready, 1)

    def wait_chunk(self, pe, c):
        pe.wait_ge(self.ready, c + 1)


def alone(k, norm):
    with k.nc.Block() as block:
        k.begin()
        ahead = Ahead(k)

        @block.tensor
        def _(pe):
            norm.tensor(pe)

        @block.gpsimd
        def _(pool):
            ahead.low(pool)

        @block.scalar
        def _(act):
            norm.squares(act)
            ahead.high(act)
            norm.scalar(act)

        @block.vector
        def _(dve):
            norm.vector(dve)

        @block.sync
        def _(sync):
            k.feed(sync, 0)


def project_out(k, src, tokens, update, name):
    per = 2 if tokens == T else 1
    outs = [("feature", [(0, P), (P, 2 * P)])] if per == 2 else [("feature", [(0, P)]), ("feature", [(P, 2 * P)])]
    project(k, src, tokens, [WB] * (D // WB), lambda b: outs,
            lambda kind, eng, b, i, bank: update(eng, 2 * b + i, bank), lambda b, i: "dve")


def to_feature_major(k, jobs, name, project_next=False):
    nc = k.nc
    pairs = isinstance(jobs[0][1], tuple)
    highs = k.sem(f"turned_high_{name}") if pairs else None
    with nc.Block() as block:
        k.begin()
        ahead = Ahead(k) if project_next else None
        fills = Fills(k, ["dve" if pairs else ("act", "dve")[n % 2] for n in range(len(jobs))])

        def views(n):
            dst = jobs[n][1][0] if pairs else jobs[n][1]
            src = fills.bank(n)[0:dst.shape[0], 0:len(jobs[n][0]) * P]
            return src.rearrange("p (a b) -> p a b", a=dst.shape[1]) if len(dst.shape) == 3 else src

        @block.tensor
        def _(pe):
            for n, (sources, _) in enumerate(jobs):
                fills.wait_free(pe, n)
                for j, s in enumerate(sources):
                    w = s.shape[1]
                    mm = pe.transpose(fills.bank(n)[0:w, j * P:j * P + P], s, k.ident[:, :])
                fills.fill(mm)

        @block.scalar
        def _(act):
            if ahead:
                ahead.high(act)
            for n in range(0, len(jobs), 1 if pairs else 2):
                fills.wait_full(act, n)
                if pairs:
                    act.activation(jobs[n][1][0], views(n), ACT.Copy).then_inc(highs, 1)
                else:
                    fills.drain(n, act.activation(jobs[n][1], views(n), ACT.Copy))

        @block.vector
        def _(dve):
            for n in range(0 if pairs else 1, len(jobs), 1 if pairs else 2):
                fills.wait_full(dve, n)
                if pairs:
                    dve.wait_ge(highs, n + 1)
                    fills.drain(n, dve.tensor_tensor(jobs[n][1][1], views(n), jobs[n][1][0].bitcast(F32), ALU.subtract))
                else:
                    fills.drain(n, dve.tensor_copy(jobs[n][1], views(n)))

        @block.gpsimd
        def _(pool):
            if ahead:
                ahead.low(pool)

        @block.sync
        def _(sync):
            k.feed(sync, 0)


def rope_axial(eng, k, x, cos, sin, heads, tmp, S=None):
    S = S or k.pool
    xv = x.rearrange("p (h s e d) -> p (h s) e d", h=heads, s=2, e=2)
    tv = tmp.rearrange("p (h s e d) -> p (h s) e d", h=heads, s=2, e=2)
    x4 = x.rearrange("p (h s e d) -> p h s e d", h=heads, s=2, e=2)
    t4 = tmp.rearrange("p (h s e d) -> p h s e d", h=heads, s=2, e=2)
    s4 = sin.rearrange("p (s e d) -> p s e d", s=2, e=2)
    for s in range(2):
        for e in range(2):
            S.step(eng.tensor_tensor(t4[:, :, s, e, :], x4[:, :, s, 1 - e, :], spread(s4[:, s, e, :], 1, heads), ALU.mult))
    S.settle(eng)
    x3, t3 = x.rearrange("p (h d) -> p h d", h=heads), tmp.rearrange("p (h d) -> p h d", h=heads)
    S.step(eng.tensor_tensor(x3, x3, spread(cos, 1, heads), ALU.mult))
    S.settle(eng)
    S.step(eng.tensor_tensor(x3, x3, t3, ALU.add))


def even_project(k, xn, proj, norm):
    kinds = ["gelu"] * 4 + ["silu"] * 2 + ["copy"] * 6 + ["silu"] * 2

    def store(name, eng, b, i, bank):
        func = {"gelu": ACT.Gelu, "silu": ACT.Silu, "copy": ACT.Copy}[kinds[b]]
        return copy(name, eng, proj[:, i, b * WB:b * WB + WB], bank[:, 0:WB], func)

    project(k, xn, TC, [WB] * 14, lambda b: [("token", m) for m in range(TC // P)], store,
            lambda b, i: "dve" if kinds[b] == "copy" else "act", norm=norm)


def spatial_gating(k, proj, wsT, row, const, mix, lam):
    nc = k.nc
    tmp = k.sb("rope_tmp", [P, B_H * 2 * B_D])
    vn = k.sb("vn", [P, 2, A_W])
    stats = k.sb("stats", [P, 4, 6])
    mean = k.sb("mean", [P, 4, 2])
    rstd = k.sb("rstd", [P, 4])
    lsum = k.sb("lsum", [P, 2])
    lprod = k.sb("lprod", [P, 2 * B_D])
    normed = k.sem("v_normed")
    mixed = k.sem("v_mixed")
    gated = k.sem("gated")
    lams = k.sem("lambda_sums")
    tiles = TC // P
    with nc.Block() as block:
        k.begin()

        @block.gpsimd
        def _(pool):
            for m in range(T // P):
                cos, sin = const("axcos")[:, m * B_D:m * B_D + B_D], const("axsin")[:, m * B_D:m * B_D + B_D]
                for c0 in (3 * A_W, 4 * A_W):
                    rope_axial(pool, k, proj[:, m, c0:c0 + 512], cos, sin, 2 * B_H, tmp[:, :])
                    k.pool.settle(pool)

        @block.tensor
        def _(pe):
            for m in range(tiles):
                pe.wait_ge(normed, m + 1)
                if m >= 2:
                    pe.wait_ge(gated, m - 1)
                for g in range(A_G):
                    mm = pe.matmul(k.bank[m % 2][:, g * 64:g * 64 + 64], wsT[:, g, :], vn[:, m % 2, g * 64:g * 64 + 64],
                                   start=True, stop=True)
                mm.then_inc(mixed, 1)

        @block.vector
        def _(dve):
            S = k.dve

            def norm(m):
                v = proj[:, m, A_W:2 * A_W]
                x = vn[:, m % 2, :]
                if m >= 2:
                    dve.wait_ge(mixed, m - 1)
                S.step(dve.tensor_scalar(x, v, mean[:, m, 0:1], rstd[:, m:m + 1], ALU.subtract, ALU.mult))
                S.settle(dve)
                S.step(dve.tensor_tensor(x, x, row("a_ln_w"), ALU.mult))
                S.settle(dve)
                dve.tensor_tensor(x, x, row("a_ln_b"), ALU.add).then_inc(normed, 1)

            def gate(m):
                dve.wait_ge(mixed, m + 1)
                out = mix[:, m, 0:A_W]
                o3 = out.rearrange("p (g d) -> p g d", g=A_G)
                dve.tensor_tensor(o3, k.bank[m % 2][:, :].rearrange("p (g d) -> p g d", g=A_G),
                                  spread(k.col("a_bs", 0, 8), 2, 64), ALU.add).then_inc(gated, 1)
                dve.wait_ge(gated, m + 1)
                S.step(dve.tensor_tensor(out, out, proj[:, m, 0:A_W], ALU.mult))
                S.settle(dve)
                S.step(dve.tensor_tensor(out, out, proj[:, m, 2 * A_W:3 * A_W], ALU.mult))

            S.step(dve.tensor_tensor(lprod[:, :], row("lq1", 128), row("lk1", 128), ALU.mult))
            S.settle(dve)
            dve.tensor_reduce(lsum[:, :], lprod[:, :].rearrange("p (a b) -> p a b", a=2), AX_X, ALU.add).then_inc(lams, 1)
            for m in range(tiles):
                S.step(dve.bn_stats(stats[:, m, :], proj[:, m, A_W:2 * A_W]))
            S.settle(dve)
            for m in range(tiles):
                S.step(dve.bn_aggr(mean[:, m, :], stats[:, m, :]))
            S.settle(dve)
            S.step(dve.tensor_copy(rstd[:, :], mean[:, :, 1]))
            S.settle(dve)
            k.ask_root(dve, rstd[:, :], 1.0, 1e-5)
            norm(0)
            for m in range(tiles):
                if m + 1 < tiles:
                    norm(m + 1)
                gate(m)
            dve.wait_ge(lams, 2)
            S.step(dve.tensor_tensor(lam, lsum[:, 1:2], lsum[:, 0:1], ALU.subtract))
            S.settle(dve)
            S.step(dve.tensor_scalar(lam, lam, -(0.8 - 0.6 * math.exp(0.0)), None, ALU.add))

        @block.scalar
        def _(act):
            act.wait_ge(lams, 1)
            act.activation(lsum[:, :], lsum[:, :], ACT.Exp).then_inc(lams, 1)
            k.root(act, rstd[:, :])

        @block.sync
        def _(sync):
            k.feed(sync, 0)


def diff_attention(k, proj, qT, kT, row, nlam, mix):
    nc = k.nc
    units = [(m, h) for m in range(TC // P) for h in range(B_H)]
    n_units = len(units)
    prob = k.sb("prob", [P, 3, 2, TC])
    pT = k.sb("pT", [P, 2, TC])
    mx = k.sb("mx", [P, 3, 2])
    sums = k.sb("sums", [P, 3, 2])
    ss = k.sb("ss", [P, len(units)])
    junk = k.sb("junk", [P, B_V])
    scored, maxed, exped = k.sem("scored"), k.sem("maxed"), k.sem("exped")
    combined, turned, turned_out = k.sem("combined"), k.sem("turned"), k.sem("turned_out")
    mixed, squared, finished = k.sem("attended"), k.sem("out_squared"), k.sem("finished")
    keys = lambda m: (0, TC) if m < 2 else (T, TC)
    with nc.Block() as block:
        k.begin()

        @block.tensor
        def _(pe):
            def scores(u):
                m, h = units[u]
                a, b = keys(m)
                if u >= 2:
                    pe.wait_ge(exped, 2 * (u - 1))
                for j in range(2):
                    r = slice(64 * j, 64 * j + 64)
                    pe.matmul(k.bank[4 * (u % 2) + j][:, 0:b - a], qT[r, h, m * P:m * P + P], kT[r, h, a:b],
                              start=True, stop=True).then_inc(scored, 1)

            def turn(u):
                m, h = units[u]
                a, b = keys(m)
                pe.wait_ge(combined, u + 1)
                if u >= 2:
                    pe.wait_ge(turned_out, u - 1)
                for c in range((b - a) // P):
                    mm = pe.transpose(k.bank[4 * (u % 2) + 2][:, c * P:c * P + P], prob[:, u % 3, 0, c * P:c * P + P], k.ident[:, :])
                mm.then_inc(turned, 1)

            def attend(u):
                m, h = units[u]
                a, b = keys(m)
                pe.wait_ge(turned_out, u + 1)
                if u >= 2:
                    pe.wait_ge(finished, u - 1)
                for c in range((b - a) // P):
                    v = proj[:, a // P + c, 5 * A_W + h * B_V:5 * A_W + h * B_V + B_V]
                    mm = pe.matmul(k.bank[4 * (u % 2) + 3][:, 0:B_V], pT[:, u % 2, c * P:c * P + P], v,
                                   start=(c == 0), stop=(c == (b - a) // P - 1))
                mm.then_inc(mixed, 1)

            for u in range(n_units + 3):
                if u < n_units:
                    scores(u)
                if 2 <= u <= n_units + 1:
                    turn(u - 2)
                if u >= 3:
                    attend(u - 3)

        @block.scalar
        def _(act):
            for u in range(n_units + 4):
                if u < n_units:
                    a, b = keys(units[u][0])
                    act.wait_ge(maxed, u + 1)
                    if u >= 3:
                        act.wait_ge(turned, u - 2)
                    for j in range(2):
                        act.activation(prob[:, u % 3, j, 0:b - a], k.bank[4 * (u % 2) + j][:, 0:b - a], ACT.Exp,
                                       bias=mx[:, u % 3, j:j + 1], scale=B_D ** -0.5,
                                       accum_out=sums[:, u % 3, j:j + 1]).then_inc(exped, 1)
                if 2 <= u <= n_units + 1:
                    w = u - 2
                    a, b = keys(units[w][0])
                    act.wait_ge(turned, w + 1)
                    if w >= 2:
                        act.wait_ge(mixed, w - 1)
                    act.activation(pT[:, w % 2, 0:b - a], k.bank[4 * (w % 2) + 2][:, 0:b - a], ACT.Copy).then_inc(turned_out, 1)
                if u >= 4:
                    w = u - 4
                    act.wait_ge(mixed, w + 1)
                    if w >= 2:
                        act.wait_ge(finished, w - 1)
                    if w >= 1:
                        act.wait_ge(squared, w)
                    act.activation(junk[:, :], k.bank[4 * (w % 2) + 3][:, 0:B_V], ACT.Square,
                                   accum_out=ss[:, w:w + 1]).then_inc(squared, 1)
            k.root(act, ss[:, :])

        @block.vector
        def _(dve):
            S = k.dve

            def maxes(u):
                a, b = keys(units[u][0])
                if u >= 3:
                    dve.wait_ge(exped, 2 * (u - 2))
                for j in range(2):
                    dve.wait_ge(scored, 2 * u + j + 1)
                    S.step(dve.reduce_max(mx[:, u % 3, j:j + 1], k.bank[4 * (u % 2) + j][:, 0:b - a], AX_X))
                S.settle(dve)
                dve.tensor_scalar(mx[:, u % 3, :], mx[:, u % 3, :], -(B_D ** -0.5), None, ALU.mult).then_inc(maxed, 1)

            def combine(u):
                a, b = keys(units[u][0])
                s, p0, p1 = sums[:, u % 3, :], prob[:, u % 3, 0, 0:b - a], prob[:, u % 3, 1, 0:b - a]
                dve.wait_ge(exped, 2 * u + 2)
                S.step(dve.reciprocal(s, s))
                S.settle(dve)
                S.step(dve.tensor_scalar(s[:, 1:2], s[:, 1:2], nlam, None, ALU.mult))
                S.step(dve.tensor_scalar(p0, p0, s[:, 0:1], None, ALU.mult))
                S.settle(dve)
                dve.scalar_tensor_tensor(out=p0, in0=p1, scalar=s[:, 1:2], in1=p0, op0=ALU.mult, op1=ALU.add).then_inc(combined, 1)

            def finish(u):
                m, h = units[u]
                out = mix[:, m, A_W + h * B_V:A_W + h * B_V + B_V]
                dve.wait_ge(squared, u + 1)
                dve.tensor_tensor(out, k.bank[4 * (u % 2) + 3][:, 0:B_V], row("subln_w"), ALU.mult).then_inc(finished, 1)
                dve.wait_ge(finished, u + 1)
                z = proj[:, m, 6 * A_W + h * B_V:6 * A_W + h * B_V + B_V]
                S.step(dve.scalar_tensor_tensor(out=out, in0=out, scalar=1.0 - (0.8 - 0.6 * math.exp(0.0)), in1=z,
                                                op0=ALU.mult, op1=ALU.mult))

            for u in range(n_units + 4):
                if u < n_units:
                    maxes(u)
                if u >= 4:
                    finish(u - 4)
                if 1 <= u <= n_units:
                    combine(u - 1)
            k.ask_root(dve, ss[:, :], 1.0 / B_V, 1e-5)
            for m in range(TC // P):
                out = mix[:, m, A_W:D].rearrange("p (h v) -> p h v", h=B_H)
                S.step(dve.tensor_tensor(out, out, spread(ss[:, B_H * m:B_H * m + B_H], 2, B_V), ALU.mult))

        @block.sync
        def _(sync):
            k.feed(sync, 0)


def attention(k, units, n_keys, scores_of, value_of, scale, bias_of, store, name):
    nc = k.nc
    N = len(units)
    nchunk = n_keys // P
    prob = k.sb(f"prob_{name}", [P, 2, n_keys])
    pT = k.sb(f"pT_{name}", [P, 2, n_keys])
    mx = k.sb(f"mx_{name}", [P, 2])
    sums = k.sb(f"sums_{name}", [P, 2])
    scored, maxed, exped = k.sem(f"scored_{name}"), k.sem(f"maxed_{name}"), k.sem(f"exped_{name}")
    normed, turned, turned_out = k.sem(f"normed_{name}"), k.sem(f"turned_{name}"), k.sem(f"turned_out_{name}")
    mixed, stored = k.sem(f"attended_{name}"), k.sem(f"stored_{name}")
    with nc.Block() as block:
        k.begin()
        ahead = Ahead(k)

        @block.tensor
        def _(pe):
            for u in range(N + 2):
                if u < N:
                    if u >= 2:
                        pe.wait_ge(exped, u - 1)
                    scores_of(pe, units[u], k.bank[u % 2][:, 0:n_keys]).then_inc(scored, 1)
                if 1 <= u <= N:
                    w = u - 1
                    pe.wait_ge(normed, w + 1)
                    if w >= 2:
                        pe.wait_ge(turned_out, w - 1)
                    for c in range(nchunk):
                        mm = pe.transpose(k.bank[2 + w % 2][:, c * P:c * P + P], prob[:, w % 2, c * P:c * P + P], k.ident[:, :])
                    mm.then_inc(turned, 1)
                if u >= 2:
                    w = u - 2
                    pe.wait_ge(turned_out, w + 1)
                    if w >= 2:
                        pe.wait_ge(stored, w - 1)
                    for c in range(nchunk):
                        mm = pe.matmul(k.bank[4 + w % 2][:, 0:P], value_of(units[w], c), pT[:, w % 2, c * P:c * P + P],
                                       start=(c == 0), stop=(c == nchunk - 1))
                    mm.then_inc(mixed, 1)

        @block.scalar
        def _(act):
            ahead.high(act)
            for u in range(N + 1):
                if u < N:
                    act.wait_ge(maxed, u + 1)
                    if u >= 2:
                        act.wait_ge(turned, u - 1)
                    src = k.bank[u % 2][:, 0:n_keys] if bias_of is None else prob[:, u % 2, :]
                    act.activation(prob[:, u % 2, :], src, ACT.Exp, bias=mx[:, u % 2:u % 2 + 1],
                                   scale=scale if bias_of is None else 1.0,
                                   accum_out=sums[:, u % 2:u % 2 + 1]).then_inc(exped, 1)
                if u >= 1:
                    w = u - 1
                    act.wait_ge(turned, w + 1)
                    if w >= 2:
                        act.wait_ge(mixed, w - 1)
                    act.activation(pT[:, w % 2, :], k.bank[2 + w % 2][:, 0:n_keys], ACT.Copy).then_inc(turned_out, 1)

        @block.vector
        def _(dve):
            S = k.dve
            for u in range(N + 3):
                if u < N:
                    dve.wait_ge(scored, u + 1)
                    src, m = k.bank[u % 2][:, 0:n_keys], mx[:, u % 2:u % 2 + 1]
                    if u >= 2:
                        dve.wait_ge(exped, u - 1)
                    if bias_of is not None:
                        if u >= 2:
                            dve.wait_ge(turned, u - 1)
                        S.step(dve.scalar_tensor_tensor(out=prob[:, u % 2, :], in0=src, scalar=scale, in1=bias_of(units[u]),
                                                        op0=ALU.mult, op1=ALU.add))
                        S.settle(dve)
                        src = prob[:, u % 2, :]
                    S.step(dve.reduce_max(m, src, AX_X))
                    S.settle(dve)
                    dve.tensor_scalar(m, m, -scale if bias_of is None else -1.0, None, ALU.mult).then_inc(maxed, 1)
                if u >= 3:
                    w = u - 3
                    dve.wait_ge(mixed, w + 1)
                    store(dve, units[w], k.bank[4 + w % 2][:, 0:P]).then_inc(stored, 1)
                if u < N:
                    s = sums[:, u % 2:u % 2 + 1]
                    dve.wait_ge(exped, u + 1)
                    S.step(dve.reciprocal(s, s))
                    S.settle(dve)
                    dve.tensor_scalar(prob[:, u % 2, :], prob[:, u % 2, :], s, None, ALU.mult).then_inc(normed, 1)

        @block.gpsimd
        def _(pool):
            ahead.low(pool)

        @block.sync
        def _(sync):
            k.feed(sync, 0)


def odd_project(k, xn, cq, ckv, zT, norm):
    def outs(b):
        if b < 2:
            return [("token", m) for m in range(2 if b == 0 else 4)]
        return [("feature", [(0, P), (P, 2 * P)])]

    def store(name, eng, b, i, bank):
        if b < 2:
            dst = cq[:, i, :] if b == 0 else ckv[:, i, 0:C_KV + C_R]
            return copy(name, eng, dst, bank[:, 0:dst.shape[1]])
        return copy(name, eng, zT[:, 2 * (b - 2):2 * (b - 2) + 2, :], bank[:, :].rearrange("p (f t) -> p f t", f=2), ACT.Silu)

    project(k, xn, T, [WB, C_KV + C_R] + [WB] * 4, outs, store, lambda b, i: "dve" if b < 2 else "act", norm=norm)


def latent_norms(k, cq, ckv, row, const):
    nc = k.nc
    tmp = k.sb("odd_tmp", [P, C_Q])
    ss = k.sb("odd_ss", [P, 6])
    pooltmp = k.sb("krope_tmp", [P, C_R])
    with nc.Block() as block:
        k.begin()

        @block.gpsimd
        def _(pool):
            for m in range(4):
                kr = ckv[:, m, C_KV:C_KV + C_R]
                if m < 2:
                    rope_axial(pool, k, kr, const("axcos")[:, m * 64:m * 64 + 64], const("axsin")[:, m * 64:m * 64 + 64],
                               1, pooltmp[:, :])
                    k.pool.settle(pool)
                k.pool.step(pool.tensor_copy(ckv[:, m, C_KV + C_R:C_KV + 2 * C_R], kr))

        @block.vector
        def _(dve):
            S = k.dve
            jobs = [(cq[:, m, :], "q_norm") for m in range(2)] + [(ckv[:, m, 0:C_KV], "kv_norm") for m in range(4)]
            for n, (x, w) in enumerate(jobs):
                width = x.shape[1]
                s = ss[:, n:n + 1]
                S.step(dve.tensor_tensor(tmp[:, 0:width], x, x, ALU.mult))
                S.settle(dve)
                S.step(dve.tensor_reduce(s, tmp[:, 0:width], AX_X, ALU.add))
                S.settle(dve)
            k.ask_root(dve, ss[:, 0:2], 1.0 / C_Q, 1e-6)
            k.ask_root(dve, ss[:, 2:6], 1.0 / C_KV, 1e-6)
            for n, (x, w) in enumerate(jobs):
                S.step(dve.scalar_tensor_tensor(out=x, in0=x, scalar=ss[:, n:n + 1], in1=row(w), op0=ALU.mult, op1=ALU.mult))

        @block.scalar
        def _(act):
            k.root(act, ss[:, 0:2])
            k.root(act, ss[:, 2:6])

        @block.sync
        def _(sync):
            k.feed(sync, 0)


def odd_queries(k, cqT, ckvT, qnT, qr, knT, v):
    nc = k.nc
    with nc.Block() as block:
        k.begin()
        jobs = []
        for g in range(2):
            jobs += [("qn", g, i) for i in range(2)] + [("qr", g, i) for i in range(2)]
        jobs += [("kn", 0, h) for h in range(C_H)] + [("v", 0, i) for i in range(8)]
        fills = Fills(k, [("act", "dve")[n % 2] for n in range(len(jobs))])

        def piece(n):
            kind, g, i = jobs[n]
            bank = fills.bank(n)
            if kind == "qn":
                h = 4 * g + 2 * i
                return qnT[:, h:h + 2, :], bank[:, :].rearrange("p (h t) -> p h t", h=2)
            if kind == "qr":
                return (qr[:, i, 256 * g:256 * g + 256], bank[:, 0:256])
            if kind == "kn":
                return knT[:, i, :], bank[:, :]
            m, half = divmod(i, 2)
            return v[:, m, 512 * half:512 * half + 512], bank[:, :]

        @block.tensor
        def _(pe):
            for n, (kind, g, i) in enumerate(jobs):
                bank = fills.bank(n)
                if n in (0, 4, 8):
                    if n:
                        k.release()
                    w = k.take(pe)
                    wq = w[:, 0:2 * 768].rearrange("p (k h d) -> p k h d", k=2, h=4)
                    wkv = w[:, :].rearrange("p (h e) -> p h e", h=C_H)
                fills.wait_free(pe, n)
                if kind == "qn":
                    for j in range(2):
                        for c in range(2):
                            mm = pe.matmul(bank[:, j * T:j * T + T], wq[:, c, 2 * i + j, 0:C_N], cqT[:, c, :],
                                           start=(c == 0), stop=(c == 1))
                elif kind == "qr":
                    for c in range(2):
                        mm = pe.matmul(bank[:, 0:256].rearrange("p (h d) -> p h d", h=4), cqT[:, c, i * P:i * P + P], wq[:, c, :, C_N:C_N + C_R],
                                       start=(c == 0), stop=(c == 1))
                elif kind == "kn":
                    mm = pe.matmul(bank[:, :], wkv[:, i, 0:C_N], ckvT[:, :], start=True, stop=True)
                else:
                    m, half = divmod(i, 2)
                    mm = pe.matmul(bank[:, :].rearrange("p (h d) -> p h d", h=4), ckvT[:, m * P:m * P + P], wkv[:, 4 * half:4 * half + 4, C_N:C_N + C_V],
                                   start=True, stop=True)
                fills.fill(mm)
            k.release()

        @block.scalar
        def _(act):
            for n in range(0, len(jobs), 2):
                dst, src = piece(n)
                fills.wait_full(act, n)
                fills.drain(n, act.activation(dst, src, ACT.Copy))

        @block.vector
        def _(dve):
            for n in range(1, len(jobs), 2):
                dst, src = piece(n)
                fills.wait_full(dve, n)
                fills.drain(n, dve.tensor_copy(dst, src))

        @block.sync
        def _(sync):
            k.feed(sync, 3)


def rotate_queries(k, qr, const):
    nc = k.nc
    tmp = k.sb("qrope_tmp", [P, 2, C_H * C_R])
    with nc.Block() as block:
        k.begin()

        def rotate(eng, S, m):
            rope_axial(eng, k, qr[:, m, :], const("axcos")[:, m * 64:m * 64 + 64], const("axsin")[:, m * 64:m * 64 + 64],
                       C_H, tmp[:, m, :], S)

        @block.gpsimd
        def _(pool):
            rotate(pool, k.pool, 0)

        @block.vector
        def _(dve):
            rotate(dve, k.dve, 1)

        @block.sync
        def _(sync):
            k.feed(sync, 0)


def load(k, name, pairs):
    nc = k.nc
    loaded = k.sem(f"loaded_{name}")
    with nc.Block() as block:
        k.begin()

        @block.sync
        def _(sync):
            k.feed(sync, 0)

        @block.scalar
        def _(act):
            for dst, src in pairs:
                act.dma_start(dst, src).then_inc(loaded, 16)
            act.wait_ge(loaded, 16 * len(pairs))


def first_block(k):
    nc, d = k.nc, k.d
    h = k.h

    def residual(layer):
        def update(dve, n, bank):
            for s in range(2):
                c, o, which = (n, h[:, n, s * T:s * T + T], s) if layer == 0 else (n + s, h[:, n + s, 0:T], 0)
                ins = dve.scalar_tensor_tensor(out=o, in0=bank[:, s * T:s * T + T], scalar=k.mod[:, layer, 16 + c, which:which + 1],
                                               in1=o, op0=ALU.mult, op1=ALU.add)
                if s == 0:
                    k.dve.step(ins)
            return ins
        return update

    with k.room():
        rows = k.sb("rows", [P, NROWS])
        consts = k.sb("consts", [P, 2 * 128])
        wsT = k.sb("wsT", [P, A_G, P])
        row = lambda name, n=None: rows[:, ROW_AT[name][0]:ROW_AT[name][0] + (n or ROW_AT[name][1])]
        const = lambda name: consts[:, 0:128] if name == "axcos" else consts[:, 128:256]
        o = CONST_AT["axcos"][0]
        load(k, "rows1", [(rows[:, :], d["rows"].partition_broadcast(P)), (consts[:, :], d["const"][:, o:o + 256]),
                          (wsT[:, :, :], d["a_wsT"])])
        modulation(k)
        nlam = k.sb("nlam", [P, 1])
        with k.room():
            mix = k.sb("mix", [P, 4, D])
            with k.room():
                proj = k.sb("proj", [P, 4, 7 * A_W])
                with k.room():
                    xn = k.sb("xn_hi", [P, KC, TC], F32R), k.sb("xn_lo", [P, KC, TC], F32R)
                    work = mix.rearrange("p m n -> p (m n)").rearrange("p (c t) -> p c t", c=KC)
                    even_project(k, xn, proj, RmsNorm(k, 0, TC, xn, work))
                with k.room():
                    spatial_gating(k, proj, wsT, row, const, mix, nlam[:, :])
                qT = k.sb("qT", [P, B_H, TC])
                kT = k.sb("kT", [P, B_H, TC])
                jobs = []
                for c0, dst in ((3 * A_W, qT), (4 * A_W, kT)):
                    for m in range(4):
                        jobs.append(([proj[:, m, c0 + P * f:c0 + P * f + P] for f in range(4)], dst[:, :, m * P:m * P + P]))
                to_feature_major(k, jobs, "even_qk")
                with k.room():
                    diff_attention(k, proj, qT, kT, row, nlam[:, :], mix)
            mixT = k.sb("mixT_hi", [P, KC, TC], F32R), k.sb("mixT_lo", [P, KC, TC], F32R)
            jobs = [([mix[:, m, 512 * g + P * f:512 * g + P * f + P] for f in range(4)],
                     tuple(x[:, 4 * g:4 * g + 4, m * P:m * P + P] for x in mixT)) for g in range(2) for m in range(4)]
            to_feature_major(k, jobs, "even_mix", True)
            project_out(k, mixT, TC, residual(0), "even")
        with k.room():
            cq = k.sb("cq", [P, 2, C_Q])
            ckv = k.sb("ckv", [P, 4, C_KV + 2 * C_R])
            zT = k.sb("zT", [P, C_H, T])
            with k.room():
                xn = k.sb("xn1_hi", [P, KC, TC], F32R), k.sb("xn1_lo", [P, KC, TC], F32R)
                odd_project(k, xn, cq, ckv, zT, RmsNorm(k, 1, TC, xn, k.sb("square1", [P, KC, TC])))
            with k.room():
                latent_norms(k, cq, ckv, row, const)
            cqT = k.sb("cqT", [P, 2, T])
            ckvT = k.sb("ckvT", [P, 2, TC])
            jobs = [([cq[:, m, P * f:P * f + P] for f in range(2)], cqT[:, :, m * P:m * P + P]) for m in range(2)]
            jobs += [([ckv[:, m, P * f:P * f + P] for f in range(2)], ckvT[:, :, m * P:m * P + P]) for m in range(4)]
            to_feature_major(k, jobs, "odd_latent")
            qnT = k.sb("qnT", [P, C_H, T])
            qr = k.sb("qr", [P, 2, C_H * C_R])
            qrT = k.sb("qrT", [P, 4, T])
            knT = k.sb("knT", [P, C_H, TC])
            v = k.sb("v_odd", [P, 4, C_H * C_V])
            odd_queries(k, cqT, ckvT[:, 0, :], qnT, qr, knT, v)
            with k.room():
                rotate_queries(k, qr, const)
            to_feature_major(k, [([qr[:, m, P * f:P * f + P] for f in range(4)], qrT[:, :, m * P:m * P + P]) for m in range(2)],
                             "odd_qr")
            mixT = k.sb("mixT1_hi", [P, C_H, T], F32R), k.sb("mixT1_lo", [P, C_H, T], F32R)

            def scores_of(pe, unit, out):
                m, hd = unit
                r = slice(64 * (hd % 2), 64 * (hd % 2) + 64)
                pe.matmul(out, qnT[:, hd, m * P:m * P + P], knT[:, hd, :], start=True, stop=False)
                return pe.matmul(out, qrT[r, hd // 2, m * P:m * P + P], ckvT[r, 1, :], start=False, stop=True)

            def store(dve, unit, bank):
                m, hd = unit
                t = slice(m * P, m * P + P)
                gated = zT[:, hd, t]
                k.dve.step(dve.tensor_tensor(gated, bank, gated, ALU.mult))
                k.dve.settle(dve)
                k.dve.step(dve.tensor_copy(mixT[0][:, hd, t], gated))
                k.dve.settle(dve)
                return dve.tensor_tensor(mixT[1][:, hd, t], gated, mixT[0][:, hd, t].bitcast(F32), ALU.subtract)

            with k.room():
                attention(k, [(m, hd) for m in range(2) for hd in range(C_H)], TC, scores_of,
                          lambda unit, c: v[:, c, unit[1] * C_V:unit[1] * C_V + C_V],
                          (C_N + C_R) ** -0.5, None, store, "odd")
            project_out(k, mixT, T, residual(1), "odd")
        with k.room():
            alone(k, RmsNorm(k, None, T, (k.xh, k.xl), k.sb("square2", [P, KC, TC])))


class LayerNorm:

    def __init__(self, k, g, b, name, work):
        self.k, self.g, self.b = k, g, b
        self.y = k.y
        self.work, self.mean, self.rstd = work[:, 0:KC, :], work[:, KC, :], work[:, KC + 1, :]
        self.summed, self.centred, self.squared, self.scaled, self.rounded, self.ready = (
            k.sem(f"{s}_{name}") for s in ("ln_summed", "ln_centred", "ln_squared", "ln_scaled", "ln_rounded", "ln_ready"))

    def tensor(self, pe):
        k = self.k
        for c in range(KC):
            mm = pe.matmul(k.bank[6][:, 0:T], k.ones[:, :], self.y[:, c, :], start=(c == 0), stop=(c == KC - 1))
        mm.then_inc(self.summed, 1)
        for c in range(KC):
            pe.wait_ge(self.squared, c + 1)
            mm = pe.matmul(k.bank[7][:, 0:T], k.ones[:, :], self.work[:, c, :], start=(c == 0), stop=(c == KC - 1))
        mm.then_inc(self.summed, 1)

    def squares(self, act):
        for c in range(KC):
            act.wait_ge(self.centred, c + 1)
            act.activation(self.work[:, c, :], self.y[:, c, :], ACT.Square).then_inc(self.squared, 1)

    def scalar(self, act):
        k = self.k
        k.root(act, self.rstd)
        for c in range(KC):
            act.wait_ge(self.scaled, c + 1)
            x = self.work[:, c, :]
            k.act.step(act.activation(x, x, ACT.Identity, bias=k.col(self.b[0], self.b[1] + c), scale=k.col(self.g[0], self.g[1] + c)))
            k.act.settle(act)
            act.activation(k.xh[:, c, :], x, ACT.Copy).then_inc(self.rounded, 1)

    def final(self, act):
        k = self.k
        k.root(act, self.rstd)
        for c in range(KC):
            act.wait_ge(self.scaled, c + 1)
            x = self.work[:, c, :]
            act.activation(x, x, ACT.Identity, bias=k.col(self.b[0], self.b[1] + c), scale=k.col(self.g[0], self.g[1] + c)).then_inc(self.rounded, 1)

    def vector(self, dve, final=False):
        k, S = self.k, self.k.dve
        dve.wait_ge(self.summed, 1)
        S.step(dve.tensor_scalar(self.mean, k.bank[6][:, 0:T], 1.0 / D, None, ALU.mult))
        S.settle(dve)
        for c in range(KC):
            dve.tensor_tensor(self.y[:, c, :], self.y[:, c, :], self.mean, ALU.subtract).then_inc(self.centred, 1)
        dve.wait_ge(self.summed, 2)
        S.step(dve.tensor_copy(self.rstd, k.bank[7][:, 0:T]))
        S.settle(dve)
        dve.wait_ge(self.centred, KC)
        k.ask_root(dve, self.rstd, 1.0 / D, 1e-5)
        for c in range(KC + 2):
            if c < KC:
                dve.tensor_tensor(self.work[:, c, :], self.y[:, c, :], self.rstd, ALU.mult).then_inc(self.scaled, 1)
            if c >= 2 and not final:
                dve.wait_ge(self.rounded, c - 1)
                dve.tensor_tensor(k.xl[:, c - 2, :], self.work[:, c - 2, :], k.xh[:, c - 2, :].bitcast(F32), ALU.subtract).then_inc(self.ready, 1)

    def wait_chunk(self, pe, c):
        pe.wait_ge(self.ready, c + 1)


GLA_BLOCKS = [256, 256, 256, 256, 256, 256, 16]
RWKV_BLOCKS = [256] * 6 + [160]
RW = 2 * G_H * G_K + 2 * G_H * G_V + G_LORA


def recurrent_project(k, b, loads):
    widths = GLA_BLOCKS + RWKV_BLOCKS
    feature = [("feature", [(0, P), (P, 2 * P)])]

    def outs(blk):
        if 2 <= blk < 6:
            return [("token", 0), ("token", 1)]
        if blk == 6:
            return [("feature", [(0, G_LORA)])]
        return [("feature", [(64, 160), (0, 64)])] if blk == 13 else feature

    def owner(blk, i):
        return "act" if blk in (0, 4, 5, 7, 9, 11) else "dve"

    def store(kind, eng, blk, i, bank):
        if blk < 2:
            return copy(kind, eng, b[("gq", "gk")[blk]], bank[:, :].rearrange("p (a t) -> p a t", a=2))
        if blk < 6:
            name = "gv" if blk < 4 else "gg"
            return copy(kind, eng, b[name][:, i, (blk % 2) * WB:(blk % 2) * WB + WB], bank[:, 0:WB], ACT.Silu if blk >= 4 else ACT.Copy)
        if blk == 6:
            return copy(kind, eng, b["gal"][:, :], bank[0:G_LORA, 0:T])
        if blk < 13:
            return copy(kind, eng, b["raw"][:, 2 * (blk - 7):2 * (blk - 7) + 2, :], bank[:, :].rearrange("p (a t) -> p a t", a=2))
        k.dve.step(eng.tensor_copy(b["wa"][:, :], bank[0:64, T:2 * T]))
        return eng.tensor_copy(b["gl"][:, :], bank[0:96, 0:T])

    project(k, (k.xh, k.xl), T, widths, outs, store, owner, loads=loads)


def recurrent_prepare(k, b, const):
    nc = k.nc
    shift, lshift, t1, t2, gz = b["shift"], b["lshift"], b["t1"], b["t2"], b["gz"]
    shifted = k.sem("shifted")
    lora = k.sem("lora_ready")
    low = k.sem("low_rank_done")
    gates = k.sem("gates_ready")
    logs = k.sem("gla_logs")
    scans = k.sem("scans")
    exps = k.sem("exps")
    norm_sq, norm_sum = k.sem("kk_squared"), k.sem("kk_summed")
    raw, gla_z = b["raw"], gz
    A = lambda x: x[:, :, :]

    def shift_in(eng, S, x, d, c0, c1):
        S.step(eng.tensor_tensor(d[:, c0:c1, 1:T], x[:, c0:c1, 0:T - 1], x[:, c0:c1, 1:T], ALU.subtract))
        S.step(eng.tensor_scalar(d[:, c0:c1, 0:1], x[:, c0:c1, 0:1], -1.0, None, ALU.mult))
        S.settle(eng)
        S.step(eng.tensor_tensor(d[:, c0:c1, :], d[:, c0:c1, :], spread(k.col("mu_rkv", c0, c1 - c0), 2, T), ALU.mult))
        S.settle(eng)
        return eng.tensor_tensor(x[:, c0:c1, :], x[:, c0:c1, :], d[:, c0:c1, :], ALU.add)

    with nc.Block() as block:
        k.begin()

        @block.gpsimd
        def _(pool):
            k.pool.step(shift_in(pool, k.pool, raw, shift, 8, 12))
            pool.wait_ge(exps, 3)
            k.pool.step(pool.tensor_tensor(A(b["gki"]), A(b["gk"]), A(b["gneg"]), ALU.mult))
            k.pool.step(pool.tensor_tensor(A(b["gko"]), A(b["gk"]), A(b["gout"]), ALU.mult))
            pool.wait_ge(exps, 4)
            k.pool.step(pool.tensor_tensor(A(b["rt"]), raw[:, 0:4, :], A(b["dec"]), ALU.mult))

        @block.tensor
        def _(pe):
            pe.wait_ge(shifted, 2)
            pe.wait_ge(lora, 2)
            for f in range(2):
                mm = pe.matmul(k.bank[0][:, f * T:f * T + T], b["gla_w2"][:, f * P:f * P + P], b["gal"][:, :], start=True, stop=True)
            mm.then_inc(low, 1)
            for f in range(4):
                mm = pe.matmul(k.bank[1 + f // 2][:, (f % 2) * T:(f % 2) * T + T], b["wa2"][0:32, f * P:f * P + P], b["wa"][0:32, :],
                               start=True, stop=True)
            mm.then_inc(low, 1)
            for f in range(4):
                mm = pe.matmul(k.bank[3 + f // 2][:, (f % 2) * T:(f % 2) * T + T], b["wa2"][32:64, f * P:f * P + P], b["wa"][32:64, :],
                               start=True, stop=True)
            mm.then_inc(low, 1)
            for m in range(2):
                mm = pe.matmul(k.bank[5 + m][:, :], b["gl"][:, m * P:m * P + P], b["g2"][:, :], start=True, stop=True)
            mm.then_inc(low, 1)
            pe.wait_ge(norm_sq, 1)
            pe.wait_ge(logs, 1)
            for f in range(4):
                bank = k.bank[7 if f < 2 else 0]
                mm = pe.matmul(bank[:, (f % 2) * T:(f % 2) * T + T], b["headones"], t1[:, f, :], start=True, stop=True)
            mm.then_inc(norm_sum, 1)

        @block.scalar
        def _(act):
            act.wait_ge(shifted, 2)
            act.activation(b["wa"][0:32, :], b["wa"][0:32, :], ACT.Tanh).then_inc(lora, 1)
            act.activation(b["gl"][:, :], b["gl"][:, :], ACT.Sigmoid).then_inc(lora, 1)
            act.wait_ge(low, 2)
            for f in range(4):
                act.activation(b["la"][:, f, :], k.bank[1 + f // 2][:, (f % 2) * T:(f % 2) * T + T], ACT.Sigmoid,
                               bias=k.col("w0", f)).then_inc(gates, 1)
            act.wait_ge(low, 3)
            for f in range(4):
                act.activation(b["a"][:, f, :], k.bank[3 + f // 2][:, (f % 2) * T:(f % 2) * T + T], ACT.Sigmoid,
                               bias=k.col("a0", f)).then_inc(gates, 1)
            act.wait_ge(low, 4)
            for m in range(2):
                act.activation(b["g"][:, m, :], k.bank[5 + m][:, :], ACT.Copy).then_inc(gates, 1)
            act.wait_ge(logs, 1)
            k.act.step(act.activation(A(t2), A(t2), ACT.Exp, scale=-1.0))
            k.act.settle(act)
            act.activation(A(t2), A(t2), ACT.Ln, bias=1.0).then_inc(logs, 1)
            act.wait_ge(scans, 1)
            act.activation(A(b["gdec"]), A(b["gla"]), ACT.Exp).then_inc(exps, 1)
            act.activation(A(b["gneg"]), A(b["gla"]), ACT.Exp, scale=-1.0).then_inc(exps, 1)
            act.wait_ge(scans, 2)
            act.activation(A(b["gout"]), A(b["gout"]), ACT.Exp).then_inc(exps, 1)
            act.wait_ge(scans, 3)
            act.activation(A(b["dec"]), A(b["cum"]), ACT.Exp).then_inc(exps, 1)
            act.activation(A(b["neg"]), A(b["cum"]), ACT.Exp, scale=-1.0).then_inc(exps, 1)
            act.wait_ge(scans, 4)
            act.activation(A(b["la"]), A(b["la"]), ACT.Exp).then_inc(exps, 1)
            k.root(act, A(t1))

        @block.vector
        def _(dve):
            S = k.dve
            for x, rows, j in ((b["wa"], 64, 0), (b["gl"], 96, 1)):
                S.step(dve.tensor_tensor(lshift[0:rows, j, 1:T], x[:, 0:T - 1], x[:, 1:T], ALU.subtract))
                S.step(dve.tensor_scalar(lshift[0:rows, j, 0:1], x[:, 0:1], -1.0, None, ALU.mult))
                S.settle(dve)
                dve.scalar_tensor_tensor(out=x[:, :], in0=lshift[0:rows, j, :], scalar=b["mu_lora"][0:rows, j:j + 1], in1=x[:, :],
                                         op0=ALU.mult, op1=ALU.add).then_inc(shifted, 1)
            S.step(shift_in(dve, S, raw, shift, 0, 8))
            S.settle(dve)
            dve.wait_ge(low, 1)
            S.step(dve.tensor_tensor(A(gz), k.bank[0][:, :].rearrange("p (f t) -> p f t", f=2),
                                     spread(k.col("gla_a_b", 0, 2), 2, T), ALU.add))
            S.settle(dve)
            dve.scalar_tensor_tensor(out=A(t2), in0=A(gz), scalar=-1.0, in1=A(gz), op0=ALU.mult, op1=ALU.max).then_inc(logs, 1)
            S.step(dve.tensor_scalar(A(gz), A(gz), 0.0, None, ALU.min))
            S.step(dve.tensor_tensor(A(b["kk"]), raw[:, 4:8, :], spread(k.col("k_k", 0, 4), 2, T), ALU.mult))
            S.settle(dve)
            dve.tensor_tensor(A(t1), A(b["kk"]), A(b["kk"]), ALU.mult).then_inc(norm_sq, 1)
            dve.wait_ge(logs, 2)
            S.step(dve.tensor_tensor(A(b["gla"]), A(gz), A(t2), ALU.subtract))
            S.settle(dve)
            S.step(dve.tensor_scalar(A(b["gla"]), A(b["gla"]), 1.0 / G_TAU, None, ALU.mult))
            S.settle(dve)
            for f in range(2):
                ins = dve.tensor_tensor_scan(b["gla"][:, f, :], const("within"), b["gla"][:, f, :], 0.0, ALU.mult, ALU.add)
                if f == 0:
                    S.step(ins)
                else:
                    ins.then_inc(scans, 1)
            dve.wait_ge(scans, 1)
            for f in range(2):
                x = b["gla"][:, f, :].rearrange("p (c t) -> p c t", t=CH)
                ins = dve.tensor_tensor(b["gout"][:, f, :].rearrange("p (c t) -> p c t", t=CH),
                                        spread(x[:, :, CH - 1], 2, CH), x, ALU.subtract)
                if f == 0:
                    S.step(ins)
                else:
                    ins.then_inc(scans, 1)
            dve.wait_ge(gates, 4)
            S.step(dve.tensor_scalar(A(b["la"]), A(b["la"]), -DOWN, None, ALU.mult))
            S.settle(dve)
            for f in range(4):
                ins = dve.tensor_tensor_scan(b["cum"][:, f, :], const("within"), b["la"][:, f, :], 0.0, ALU.mult, ALU.add)
                if f < 3:
                    S.step(ins)
                else:
                    ins.then_inc(scans, 1)
            S.settle(dve)
            dve.wait_ge(scans, 3)
            dve.tensor_tensor(A(b["la"]), A(b["cum"]), A(b["la"]), ALU.subtract).then_inc(scans, 1)
            dve.wait_ge(norm_sum, 1)
            for f in range(2):
                S.step(dve.tensor_scalar(t1[:, 2 * f:2 * f + 2, :], k.bank[(7, 0)[f]][:, :].rearrange("p (f t) -> p f t", f=2),
                                         1e-24, None, ALU.max))
            S.settle(dve)
            k.ask_root(dve, A(t1), 1.0, 0.0)
            S.step(dve.tensor_tensor(A(b["kk"]), A(b["kk"]), A(t1), ALU.mult))
            dve.wait_ge(gates, 10)
            S.settle(dve)
            S.step(dve.tensor_scalar(A(t1), A(b["a"]), -1.0, None, ALU.add))
            S.settle(dve)
            S.step(dve.tensor_tensor(A(t1), A(t1), spread(k.col("k_a", 0, 4), 2, T), ALU.mult))
            S.settle(dve)
            S.step(dve.scalar_tensor_tensor(out=A(b["k2"]), in0=A(t1), scalar=1.0, in1=raw[:, 4:8, :], op0=ALU.add, op1=ALU.mult))
            S.settle(dve)
            S.step(dve.tensor_tensor(A(b["rk"]), raw[:, 0:4, :], A(b["k2"]), ALU.mult))
            S.settle(dve)
            S.step(dve.tensor_tensor(A(b["rk"]), A(b["rk"]), spread(k.col("r_k", 0, 4), 2, T), ALU.mult))
            dve.wait_ge(exps, 6)
            S.step(dve.scalar_tensor_tensor(out=A(b["at"]), in0=A(b["kk"]), scalar=-1.0, in1=A(b["la"]), op0=ALU.mult, op1=ALU.mult))
            S.step(dve.tensor_tensor(A(b["bt"]), A(b["kk"]), A(b["a"]), ALU.mult))
            S.settle(dve)
            S.step(dve.tensor_tensor(A(b["bt"]), A(b["bt"]), A(b["neg"]), ALU.mult))
            S.step(dve.tensor_tensor(A(b["kt"]), A(b["k2"]), A(b["neg"]), ALU.mult))
            S.step(dve.scalar_tensor_tensor(out=A(b["gqi"]), in0=A(b["gq"]), scalar=G_K ** -0.5, in1=A(b["gdec"]),
                                            op0=ALU.mult, op1=ALU.mult))

        @block.sync
        def _(sync):
            k.feed(sync, 0)


def unit(m, h, heads):
    return m * heads + (h % 2) * (heads // 2) + h // 2


def chunk_matrices(k, b, mask):
    nc = k.nc
    filled, copied = k.sem("zeros_ready"), k.sem("first_copied")
    first = {"LT": (2, 0), "XT": (0, 1), "X": (0, 2), "MakT": (3, 0), "MrbT": (0, 3), "MrkT": (4, 0), "AT": (5, 0)}
    kinds = [("XT", "bt", "at", "joinT1", 8), ("LT", "bt", "at", "before", 8), ("X", "at", "bt", "join1", 8),
             ("MakT", "kt", "at", "before", 8), ("MrbT", "bt", "rt", "upto", 8), ("MrkT", "kt", "rt", "upto", 8),
             ("AT", "gki", "gqi", "upto", 4)]
    jobs = [(kind, m, g) for kind in kinds for m in range(2) for g in range(2)]
    with nc.Block() as block:
        k.begin()
        fills = Fills(k, ["dve"] * len(jobs))

        @block.gpsimd
        def _(pool):
            pool.memset(b["Z"][:, :, :], 0.0).then_inc(filled, 1)
            for name in ("LT", "MakT", "MrkT", "AT", "S"):
                pool.memset(b[name][:, :, :], 0.0).then_inc(filled, 1)

        @block.scalar
        def _(act):
            for name in ("XT", "X"):
                act.activation(b[name][:, :, :], spread(k.ident[:, :], 1, 16), ACT.Copy).then_inc(copied, 1)
            act.wait_ge(filled, 1)
            zeros = b["Z"].rearrange("p a b -> p (a b)")[:, 0:P]
            act.activation(b["MrbT"][:, :, :], spread(zeros, 1, 16), ACT.Copy).then_inc(copied, 1)

        @block.tensor
        def _(pe):
            for n, ((_, left, right, _, heads), m, g) in enumerate(jobs):
                fills.wait_free(pe, n)
                r = slice(64 * g, 64 * g + 64)
                for j in range(heads // 2):
                    mm = pe.matmul(fills.bank(n)[:, j * P:j * P + P], b[left][r, j, m * P:m * P + P],
                                   b[right][r, j, m * P:m * P + P], start=True, stop=True)
                fills.fill(mm)

        @block.vector
        def _(dve):
            for n, ((dst, _, _, which, heads), m, g) in enumerate(jobs):
                fills.wait_full(dve, n)
                for sem, count in zip((filled, copied), first[dst]):
                    if count:
                        dve.wait_ge(sem, count)
                u, nu = unit(m, g, heads), heads // 2
                fills.drain(n, dve.copy_predicated(b[dst][:, u:u + nu, :], spread(mask(which), 1, nu),
                                                   fills.bank(n)[:, 0:nu * P].rearrange("p (u t) -> p u t", u=nu)))

        @block.sync
        def _(sync):
            k.feed(sync, 0)


def invert(k, b, mask):
    nc = k.nc
    W = k.sb("LX", [P, 16, P])
    levels = [2 ** i for i in range(1, 6)]
    owners = []
    for _ in levels:
        owners += ["act"] * 4 + ["dve"] * 8
    with nc.Block() as block:
        k.begin()
        fills = Fills(k, owners)

        @block.tensor
        def _(pe):
            n = 0
            for i, _ in enumerate(levels):
                for g in range(4):
                    fills.wait_free(pe, n)
                    if i:
                        fills.wait_drained(pe, n - 12 + 4 - g + 2 * g + 1)
                    for u in range(4 * g, 4 * g + 4):
                        mm = pe.matmul(fills.bank(n)[:, (u % 4) * P:(u % 4) * P + P], b["LT"][:, u, :], b["X"][:, u, :], start=True, stop=True)
                    fills.fill(mm)
                    n += 1
                for g in range(4):
                    fills.wait_drained(pe, n - 4 - g)
                    fills.wait_free(pe, n)
                    for u in range(4 * g, 4 * g + 4):
                        mm = pe.matmul(fills.bank(n)[:, (u % 4) * P:(u % 4) * P + P], b["XT"][:, u, :], W[:, u, :], start=True, stop=True)
                    fills.fill(mm)
                    n += 1
                    fills.wait_free(pe, n)
                    for u in range(4 * g, 4 * g + 4):
                        mm = pe.matmul(fills.bank(n)[:, (u % 4) * P:(u % 4) * P + P], W[:, u, :], b["XT"][:, u, :], start=True, stop=True)
                    fills.fill(mm)
                    n += 1

        @block.scalar
        def _(act):
            for i, _ in enumerate(levels):
                for g in range(4):
                    n = 12 * i + g
                    fills.wait_full(act, n)
                    fills.drain(n, act.activation(W[:, 4 * g:4 * g + 4, :], fills.bank(n)[:, :].rearrange("p (u t) -> p u t", u=4), ACT.Copy))

        @block.vector
        def _(dve):
            for i, m in enumerate(levels):
                for g in range(4):
                    n = 12 * i + 4 + 2 * g
                    fills.wait_full(dve, n + 1)
                    for j, (name, which) in enumerate((("X", f"join{m}"), ("XT", f"joinT{m}"))):
                        fills.drain(n + j, dve.copy_predicated(b[name][:, 4 * g:4 * g + 4, :], spread(mask(which), 1, 4),
                                                               fills.bank(n + j)[:, :].rearrange("p (u t) -> p u t", u=4)))

        @block.sync
        def _(sync):
            k.feed(sync, 0)


def recurrences(k, b):
    nc = k.nc
    R, U = k.small_f32[:, 0:512], k.small_f32[:, 512:1024]
    pre, pre_out = k.sem("pre_products"), k.sem("pre_drained")
    s1, s1_out, s2, s2_out = k.sem("az"), k.sem("rhs_ready"), k.sem("u_product"), k.sem("u_ready")
    s3, s3_out = k.sem("state_products"), k.sem("states_ready")
    outs, outs_out = k.sem("chunk_outputs"), k.sem("chunk_outputs_drained")
    rows = lambda h: slice(64 * (h % 2), 64 * (h % 2) + 64)
    half = lambda even, odd, h: k.bank[odd if h % 2 else even][:, (h // 2) * 64:(h // 2) * 64 + 64]
    parity = lambda x, q, n: x.rearrange("p (j q e) -> p j q e", q=2, e=n)[:, :, q, :]
    by_head = lambda x, n: x.rearrange("p (j e) -> p j e", e=n)
    with nc.Block() as block:
        k.begin()

        @block.tensor
        def _(pe):
            for m in range(2):
                for h in range(8):
                    mm = pe.matmul(k.bank[m][:, h * 64:h * 64 + 64], b["MakT"][:, unit(m, h, 8), :], b["v"][:, m, h * 64:h * 64 + 64],
                                   start=True, stop=True)
            for m in range(2):
                for f in range(4):
                    mm = pe.matmul(k.bank[2][:, 8 * m + 2 * f:8 * m + 2 * f + 2], b["rk"][:, f, m * P:m * P + P], b["headsel"],
                                   start=True, stop=True)
            mm.then_inc(pre, 1)
            pe.wait_ge(pre_out, 3)
            for c in range(T // CH):
                m, r = c // 2, slice(64 * (c % 2), 64 * (c % 2) + 64)
                t = slice(c * CH, c * CH + CH)
                if c:
                    pe.wait_ge(s3_out, 3 * c)
                for h in range(8):
                    mm = pe.matmul(half(0, 1, h)[r, :], b["at"][rows(h), h // 2, t], b["Z"][rows(h), h // 2, :],
                                   start=True, stop=True)
                mm.then_inc(s1, 1)
                if c:
                    pe.wait_ge(outs_out, 4 * c - 2)
                for h in range(4):
                    o = k.bank[(4, 7)[h % 2]][r, (h // 2) * P:(h // 2) * P + P]
                    pe.matmul(o, b["gqi"][rows(h), h // 2, t], b["S"][rows(h), h // 2, :],
                              start=True, stop=False)
                    mm = pe.matmul(o, b["AT"][:, unit(m, h, 4), r], b["gv"][:, m, h * P:h * P + P],
                                   start=False, stop=True)
                mm.then_inc(outs, 1)
                for h in range(4):
                    mm = pe.matmul(k.bank[5][rows(h), (h // 2) * P:(h // 2) * P + P], b["gkoT"][r, m, h * 64:h * 64 + 64], b["gv"][r, m, h * P:h * P + P],
                                   start=True, stop=True)
                mm.then_inc(s3, 1)
                for h in range(8):
                    e = slice(h * 64, h * 64 + 64)
                    pe.matmul(half(3, 3, h)[rows(h), :], b["ktT"][r, m, e], b["v"][r, m, e],
                              start=(h < 2), stop=False, skip_group_check=True)
                pe.wait_ge(s1_out, 2 * c + 4)
                for h in range(8):
                    mm = pe.matmul(k.bank[1][r, h * 64:h * 64 + 64], b["XT"][r, unit(m, h, 8), r], R[r, h * 64:h * 64 + 64],
                                   start=True, stop=True)
                mm.then_inc(s2, 1)
                if c:
                    pe.wait_ge(outs_out, 4 * c)
                for h in range(8):
                    o = half(2, 6, h)[r, :]
                    pe.matmul(o, b["rt"][rows(h), h // 2, t], b["Z"][rows(h), h // 2, :], start=(h < 2), stop=False, skip_group_check=True)
                    pe.matmul(o, b["MrkT"][:, unit(m, h, 8), r], b["v"][:, m, h * 64:h * 64 + 64], start=False, stop=False,
                              skip_group_check=True)
                pe.wait_ge(s2_out, c + 1)
                for h in range(8):
                    e = slice(h * 64, h * 64 + 64)
                    mm = pe.matmul(half(3, 3, h)[rows(h), :], b["btT"][r, m, e], U[r, e], start=False, stop=(h >= 6), skip_group_check=True)
                mm.then_inc(s3, 1)
                for h in range(8):
                    mm = pe.matmul(half(2, 6, h)[r, :], b["MrbT"][:, unit(m, h, 8), r], U[:, h * 64:h * 64 + 64], start=False,
                                   stop=(h >= 6), skip_group_check=True)
                mm.then_inc(outs, 1)

        @block.vector
        def _(dve):
            S = k.dve
            dve.memset(U[:, :], 0.0).then_inc(s1_out, 1)
            dve.memset(R[:, :], 0.0).then_inc(s1_out, 1)
            dve.wait_ge(s1_out, 2)
            dve.wait_ge(pre, 1)
            for m in range(2):
                dve.tensor_copy(b["MV"][:, m, :], k.bank[m][:, :]).then_inc(pre_out, 1)
            dve.tensor_copy(b["bonus"][:, :], k.bank[2][:, 0:16]).then_inc(pre_out, 1)
            dve.wait_ge(pre_out, 3)
            for c in range(T // CH):
                m, r = c // 2, slice(64 * (c % 2), 64 * (c % 2) + 64)
                last = c * CH + CH - 1
                dve.wait_ge(s1, c + 1)
                for q in range(2):
                    dve.tensor_tensor(parity(R[r, :], q, 64), by_head(k.bank[q][r, 0:256], 64),
                                      parity(b["MV"][r, m, :], q, 64), ALU.add).then_inc(s1_out, 1)
                dve.wait_ge(outs, 2 * c + 1)
                S.step(dve.tensor_tensor(b["S"][:, :, :], b["S"][:, :, :], spread(b["gdec"][:, :, last], 2, P), ALU.mult))
                S.settle(dve)
                dve.wait_ge(s3, 2 * c + 1)
                dve.tensor_tensor(b["S"][:, :, :], b["S"][:, :, :], k.bank[5][:, 0:2 * P].rearrange("p (f e) -> p f e", f=2),
                                  ALU.add).then_inc(s3_out, 1)
                dve.wait_ge(s3, 2 * c + 2)
                dve.tensor_tensor(b["Z"][:, :, :], b["Z"][:, :, :], k.bank[3][:, 0:256].rearrange("p (f e) -> p f e", f=4),
                                  ALU.add).then_inc(s3_out, 1)
                dve.wait_ge(s3_out, 3 * c + 2)
                dve.tensor_tensor(b["Z"][:, :, :], b["Z"][:, :, :], spread(b["dec"][:, :, last], 2, 64), ALU.mult).then_inc(s3_out, 1)
                dve.wait_ge(s3_out, 3 * c + 3)

        @block.scalar
        def _(act):
            for c in range(T // CH):
                m, r = c // 2, slice(64 * (c % 2), 64 * (c % 2) + 64)
                act.wait_ge(outs, 2 * c + 1)
                for q in range(2):
                    act.activation(parity(b["go"][r, m, :], q, G_V), by_head(k.bank[(4, 7)[q]][r, 0:256], G_V), ACT.Copy).then_inc(outs_out, 1)
                act.wait_ge(s2, c + 1)
                act.wait_ge(s1_out, 2)
                act.activation(U[r, :], k.bank[1][r, :], ACT.Copy).then_inc(s2_out, 1)
                act.wait_ge(outs, 2 * c + 2)
                for q in range(2):
                    act.activation(parity(b["y"][r, m, :], q, 64), by_head(k.bank[(2, 6)[q]][r, 0:256], 64), ACT.Copy).then_inc(outs_out, 1)

        @block.sync
        def _(sync):
            k.feed(sync, 0)


def recurrent_finish(k, b, row, mix):
    nc = k.nc
    t = b["MV"]
    ss, mean, var = k.small_f32[:, 0:8], k.small_f32[:, 8:24], k.small_f32[:, 24:40]
    go, y = b["go"], b["y"]
    flat = lambda x, n: x[:, :, :].rearrange("p m (h e) -> p (m h) e", e=n)
    gla_rms = k.sem("gla_rms")
    with nc.Block() as block:
        k.begin()

        @block.scalar
        def _(act):
            k.root(act, ss[:, :])
            k.root(act, var[:, :])

        @block.vector
        def _(dve):
            S = k.dve

            def do(ins):
                S.step(ins)
                S.settle(dve)

            do(dve.tensor_tensor(t[:, :, :], go[:, :, :], go[:, :, :], ALU.mult))
            do(dve.tensor_reduce(ss[:, :], flat(t, G_V), AX_X, ALU.add))
            k.ask_root(dve, ss[:, :], 1.0 / G_V, 1e-5)
            dve.tensor_copy(k.small_f32[:, 40:48], ss[:, :]).then_inc(gla_rms, 1)
            do(dve.tensor_reduce(mean[:, :], flat(y, 64), AX_X, ALU.add))
            do(dve.tensor_scalar(mean[:, :], mean[:, :], 1.0 / 64, None, ALU.mult))
            do(dve.tensor_tensor(flat(y, 64), flat(y, 64), spread(mean[:, :], 2, 64), ALU.subtract))
            do(dve.tensor_tensor(t[:, :, :], y[:, :, :], y[:, :, :], ALU.mult))
            do(dve.tensor_reduce(var[:, :], flat(t, 64), AX_X, ALU.add))
            k.ask_root(dve, var[:, :], 1.0 / 64, 64e-5)
            do(dve.tensor_tensor(flat(y, 64), flat(y, 64), spread(var[:, :], 2, 64), ALU.mult))
            do(dve.tensor_tensor(y[:, :, :], y[:, :, :], spread(row("lnx_g"), 1, 2), ALU.mult))
            do(dve.tensor_tensor(y[:, :, :], y[:, :, :], spread(row("lnx_b"), 1, 2), ALU.add))
            do(dve.tensor_tensor(flat(t, 64), flat(b["v"], 64), spread(b["bonus"][:, :], 2, 64), ALU.mult))
            do(dve.tensor_tensor(y[:, :, :], y[:, :, :], t[:, :, :], ALU.add))
            do(dve.tensor_tensor(mix[:, :, 512:1024], y[:, :, :], b["g"][:, :, :], ALU.mult))

        @block.gpsimd
        def _(pool):
            S = k.pool
            S.step(pool.tensor_tensor(b["gg"].rearrange("p m (h e) -> p (m h) e", e=G_V), b["gg"].rearrange("p m (h e) -> p (m h) e", e=G_V),
                                      spread(row("gla_g"), 1, 8), ALU.mult))
            pool.wait_ge(gla_rms, 1)
            S.step(pool.tensor_tensor(flat(go, G_V), flat(go, G_V), spread(k.small_f32[:, 40:48], 2, G_V), ALU.mult))
            S.settle(pool)
            S.step(pool.tensor_tensor(mix[:, :, 0:512], go[:, :, :], b["gg"][:, :, :], ALU.mult))

        @block.sync
        def _(sync):
            k.feed(sync, 0)


def to_residual(k):
    def update(dve, n, bank):
        y, xh, xl = k.y[:, n:n + 2, :], k.xh[:, n:n + 2, :].bitcast(F32), k.xl[:, n:n + 2, :].bitcast(F32)
        k.dve.step(dve.tensor_tensor(y, xh, xl, ALU.add))
        k.dve.settle(dve)
        return dve.scalar_tensor_tensor(out=y, in0=y, scalar=DN_ALPHA, in1=bank[:, :].rearrange("p (c t) -> p c t", c=2),
                                        op0=ALU.mult, op1=ALU.add)
    return update


def recurrent_layer(k):
    d = k.d
    c = lambda name: d["const"][:, CONST_AT[name][0]:CONST_AT[name][0] + CONST_AT[name][1]]

    def lay(host, names):
        flat, o = host.rearrange("p a b -> p (a b)"), 0
        for name, n in names:
            b[name] = flat[:, o:o + n * T].rearrange("p (a b) -> p a b", a=n)
            o += n * T
        assert o <= flat.shape[1]

    with k.room():
        b = {}
        cpart = k.sb("cpart", [P, P + 2 + T])
        masks_sb = k.sb("masks", [P, MASK.shape[1]], U32)
        mask = lambda name: masks_sb[:, MASK_AT[name][0]:MASK_AT[name][0] + P]
        b["headones"], b["headsel"] = cpart[:, 0:P], cpart[:, P:P + 2]
        const = lambda name: cpart[:, P + 2:P + 2 + T]
        for n, shape in (("gla_w2", [G_LORA, 256]), ("wa2", [64, 512]), ("g2", [96, 512]), ("mu_lora", [96, 2]),
                         ("gv", [P, 2, 512]), ("gg", [P, 2, 512]), ("g", [P, 2, 512]), ("v", [P, 2, 512]),
                         ("bonus", [P, 16])):
            b[n] = k.sb(n, shape)
        mix = k.sb("mix2", [P, 2, D])
        with k.room():
            for n, f in (("gdec", 2), ("dec", 4), ("gqi", 2), ("at", 4), ("rt", 4), ("rk", 4)):
                b[n] = k.sb(n, [P, f, T])
            matrices = k.sb("matrices", [P, 6 * 16, P])
            b["AT"] = k.sb("AT", [P, 8, P])
            states = k.sb("states", [P, 2, T])
            b["Z"] = states[:, 0, :].rearrange("p (a b) -> p a b", a=4)
            b["S"] = states[:, 1, :].rearrange("p (a b) -> p a b", a=2)
            for n, f in (("gkoT", 256), ("btT", 512), ("ktT", 512)):
                b[n] = k.sb(n, [P, 2, f])
            with k.room():
                for n, f in (("gko", 2), ("gki", 2), ("bt", 4)):
                    b[n] = k.sb(n, [P, f, T])
                b["kt"] = k.small_f32[:, 0:4 * T].rearrange("p (f t) -> p f t", f=4)
                lay(matrices[:, :, :], [("raw", 12), ("shift", 12), ("gla", 2), ("gout", 2),
                                        ("a", 4), ("cum", 4), ("neg", 4), ("kk", 4), ("k2", 4)])
                lay(b["AT"][:, :, :], [("la", 4)])
                lay(states[:, :, :], [("gneg", 2)])
                lay(b["gkoT"][:, :, :], [("lshift", 2)])
                lay(mix[:, :, :], [("t1", 4), ("t2", 2), ("gz", 2)])
                lay(b["btT"][:, :, :], [("gq", 2), ("gk", 2)])
                lay(b["ktT"][:, :, :], [("gal", 1), ("wa", 1), ("gl", 1)])
                for n, rows_ in (("gal", G_LORA), ("wa", 64), ("gl", 96)):
                    b[n] = b[n][0:rows_, 0, :]
                recurrent_project(k, b, [(cpart[:, 0:P], c("headones")),
                                          (cpart[:, P:P + 2], c("headsel")), (cpart[:, P + 2:P + 2 + T], c("within")),
                                          (masks_sb[:, :], d["mask"]), (b["gla_w2"][:, :], d["gla_a_w2_2"]),
                                          (b["wa2"][0:32, :], d["rwkv_w2_2"]), (b["wa2"][32:64, :], d["rwkv_a2_2"]), (b["g2"][:, :], d["rwkv_g2_2"]),
                                          (b["mu_lora"][0:64, 0:1], d["mu_lora"][0:64, :]), (b["mu_lora"][0:96, 1:2], d["mu_lora"][64:160, :])])
                with k.room():
                    recurrent_prepare(k, b, const)
                jobs = []
                for m in range(2):
                    t = slice(m * P, m * P + P)
                    jobs += [([b["raw"][:, 8 + f, t] for f in range(4)], b["v"][:, m, :]), ([b["bt"][:, f, t] for f in range(4)], b["btT"][:, m, :]),
                             ([b["kt"][:, f, t] for f in range(4)], b["ktT"][:, m, :]), ([b["gko"][:, f, t] for f in range(2)], b["gkoT"][:, m, :])]
                to_feature_major(k, jobs, "recurrent")
                for i, n in enumerate(("X", "XT", "LT", "MrbT", "MrkT", "MakT")):
                    b[n] = matrices[:, 16 * i:16 * i + 16, :]
                chunk_matrices(k, b, mask)
            with k.room():
                invert(k, b, mask)
            lay(b["LT"], [("MV", 4), ("y", 4)])
            lay(b["X"], [("go", 4)])
            for n in ("MV", "go", "y"):
                b[n] = b[n].rearrange("p (m a) t -> p m (a t)", m=2)
            with k.room():
                recurrences(k, b)
            n0, n1 = ROW_AT["gla_g"][0], NROWS
            rows = k.small_f32[:, 1024:1024 + n1 - n0]
            row = lambda name: rows[:, ROW_AT[name][0] - n0:ROW_AT[name][0] - n0 + ROW_AT[name][1]]
            load(k, "rows2", [(rows, d["rows"][n0:n1].partition_broadcast(P))])
            with k.room():
                recurrent_finish(k, b, row, mix)
        mixT = k.sb("mixT2_hi", [P, KC, T], F32R), k.sb("mixT2_lo", [P, KC, T], F32R)
        jobs = [([mix[:, m, 512 * g + P * f:512 * g + P * f + P] for f in range(4)],
                 tuple(x[:, 4 * g:4 * g + 4, m * P:m * P + P] for x in mixT)) for g in range(2) for m in range(2)]
        to_feature_major(k, jobs, "recurrent_mix", True)
        project_out(k, mixT, T, to_residual(k), "recurrent")


DSA_BLOCKS = [WB] * 4 + [2 * S_D] + [WB] * 2 + [I_D + I_H]


def sparse_project(k, b, norm, loads):
    def store(name, eng, blk, m, bank):
        if blk < 4:
            dst = b["q"][:, m, blk * WB:blk * WB + WB]
        elif blk == 4:
            dst = b["kv"][:, m, :]
        elif blk < 7:
            dst = b["qi"][:, m, (blk - 5) * WB:(blk - 5) * WB + WB]
        else:
            dst = b["kw"][:, m, 0:I_D + I_H]
        return copy(name, eng, dst, bank[:, 0:DSA_BLOCKS[blk]])

    project(k, (k.xh, k.xl), T, DSA_BLOCKS, lambda blk: [("token", 0), ("token", 1)], store, lambda blk, m: "dve",
            norm=norm, loads=loads)


def rotate_halves(eng, S, x, heads, cos, sin, tmp):
    half = cos.shape[1]
    x3 = x.rearrange("p (g e) -> p g e", e=half)
    t3 = tmp[:, 0:heads * 2 * half].rearrange("p (g e) -> p g e", e=half)
    x4 = x.rearrange("p (h s e) -> p h s e", s=2, e=half)
    t4 = tmp[:, 0:heads * 2 * half].rearrange("p (h s e) -> p h s e", s=2, e=half)
    S.step(eng.tensor_tensor(t3, x3, spread(sin, 1, 2 * heads), ALU.mult))
    S.settle(eng)
    S.step(eng.tensor_tensor(x3, x3, spread(cos, 1, 2 * heads), ALU.mult))
    S.settle(eng)
    S.step(eng.tensor_tensor(x4[:, :, 0, :], x4[:, :, 0, :], t4[:, :, 1, :], ALU.subtract))
    S.step(eng.tensor_tensor(x4[:, :, 1, :], x4[:, :, 1, :], t4[:, :, 0, :], ALU.add))
    S.settle(eng)


def sparse_rotate(k, b, const):
    nc = k.nc
    tmp_q, tmp_i = k.sb("rot_q", [P, D]), k.sb("rot_i", [P, 512])
    with nc.Block() as block:
        k.begin()

        @block.vector
        def _(dve):
            for m in range(2):
                rotate_halves(dve, k.dve, b["kw"][:, m, 0:I_D], 1, const("cosI", m), const("sinI", m), tmp_q)
                k.dve.step(dve.tensor_copy(b["ki2"][:, m, 0:I_D], b["kw"][:, m, 0:I_D]))
                k.dve.step(dve.tensor_copy(b["ki2"][:, m, I_D:2 * I_D], b["kw"][:, m, 0:I_D]))
                rotate_halves(dve, k.dve, b["q"][:, m, :], S_H, const("cosA", m), const("sinA", m), tmp_q)
                k.dve.step(dve.tensor_scalar(b["wi"][:, m, :], b["kw"][:, m, I_D:I_D + I_H], I_H ** -0.5 * I_D ** -0.5, None, ALU.mult))

        @block.gpsimd
        def _(pool):
            for m in range(2):
                rotate_halves(pool, k.pool, b["kv"][:, m, 0:S_D], 1, const("cosA", m), const("sinA", m), tmp_i)
                rotate_halves(pool, k.pool, b["qi"][:, m, :], I_H, const("cosI", m), const("sinI", m), tmp_i)

        @block.sync
        def _(sync):
            k.feed(sync, 0)


def select_keys(k, b, const):
    nc = k.nc
    relu = k.sb("relu", [P, 2, 2, T])
    best = k.sb("best8", [P, 2, 8])
    scored, rectified, used = k.sem("index_scored"), k.sem("rectified"), k.sem("relu_used")
    units = [(h, m) for h in range(I_H) for m in range(2)]
    with nc.Block() as block:
        k.begin()

        @block.tensor
        def _(pe):
            for n, (h, m) in enumerate(units):
                r = slice(64 * (h % 2), 64 * (h % 2) + 64)
                if n >= BANKS:
                    pe.wait_ge(rectified, n - BANKS + 1)
                pe.matmul(k.bank[n % BANKS][:, 0:T], b["qiT"][r, h // 2, m * P:m * P + P], b["ki2T"][r, :],
                          start=True, stop=True).then_inc(scored, 1)

        @block.scalar
        def _(act):
            for n, (h, m) in enumerate(units):
                act.wait_ge(scored, n + 1)
                if n >= 4:
                    act.wait_ge(used, n - 3)
                act.activation(relu[:, (n // 2) % 2, m, :], k.bank[n % BANKS][:, 0:T], ACT.Relu).then_inc(rectified, 1)

        @block.vector
        def _(dve):
            S = k.dve
            score, bias = b["score"], b["bias"]
            for n, (h, m) in enumerate(units):
                dve.wait_ge(rectified, n + 1)
                r, w = relu[:, (n // 2) % 2, m, :], b["wi"][:, m, h:h + 1]
                if h == 0:
                    dve.tensor_scalar(score[:, m, :], r, w, None, ALU.mult).then_inc(used, 1)
                else:
                    dve.wait_ge(used, n - 1)
                    dve.scalar_tensor_tensor(out=score[:, m, :], in0=r, scalar=w, in1=score[:, m, :],
                                             op0=ALU.mult, op1=ALU.add).then_inc(used, 1)
            dve.wait_ge(used, len(units))
            S.step(dve.tensor_tensor(score[:, :, :], score[:, :, :], const("causal"), ALU.mult))
            S.settle(dve)
            S.step(dve.tensor_tensor(score[:, :, :], score[:, :, :], const("notcausal"), ALU.add))
            S.settle(dve)
            for _ in range(TOPK // 8):
                for m in range(2):
                    S.step(dve.max(best[:, m, :], score[:, m, :]))
                S.settle(dve)
                for m in range(2):
                    S.step(dve.match_replace(score[:, m, :], best[:, m, :], score[:, m, :], GONE))
                S.settle(dve)
            S.step(dve.tensor_scalar(bias[:, :, :], score[:, :, :], 10 * NEG, None, ALU.is_lt))
            S.settle(dve)
            S.step(dve.tensor_tensor(bias[:, :, :], bias[:, :, :], const("causal"), ALU.mult))
            S.settle(dve)
            S.step(dve.tensor_scalar(bias[:, :, :], bias[:, :, :], -1.0, -NEG, ALU.add, ALU.mult))

        @block.sync
        def _(sync):
            k.feed(sync, 0)


def sparse_layer(k):
    d = k.d
    with k.room():
        b = {}
        mixT = k.sb("mixT3_hi", [P, S_H, T], F32R), k.sb("mixT3_lo", [P, S_H, T], F32R)
        with k.room():
            n0 = CONST_AT["cosA"][0]
            n1 = CONST_AT["notcausal"][0] + CONST_AT["notcausal"][1]
            cs = k.sb("consts3", [P, n1 - n0])

            def const(name, m=None):
                o, n = CONST_AT[name]
                if m is None:
                    return cs[:, o - n0:o - n0 + n].rearrange("p (m t) -> p m t", m=2)
                return cs[:, o - n0 + m * (n // 2):o - n0 + (m + 1) * (n // 2)]

            for name, shape in (("q", [P, 2, D]), ("kv", [P, 2, 2 * S_D]), ("qi", [P, 2, 512]), ("kw", [P, 2, I_D + I_H]),
                                ("ki2", [P, 2, 2 * I_D]), ("wi", [P, 2, I_H]), ("qT", [P, S_H, T]), ("kT", [P, T]),
                                ("qiT", [P, 4, T]), ("ki2T", [P, T]), ("score", [P, 2, T]), ("bias", [P, 2, T])):
                b[name] = k.sb("s_" + name, shape)
            with k.room():
                norm = LayerNorm(k, ("ffn_g", 0), ("ffn_b", 0), "ffn0", k.sb("ln_work", [P, KC + 2, T]))
                sparse_project(k, b, norm, [(cs[:, :], d["const"][:, n0:n1])])
            with k.room():
                sparse_rotate(k, b, const)
            jobs = []
            for m in range(2):
                t = slice(m * P, m * P + P)
                jobs += [([b["q"][:, m, 512 * g + P * f:512 * g + P * f + P] for f in range(4)], b["qT"][:, 4 * g:4 * g + 4, t]) for g in range(2)]
                jobs += [([b["qi"][:, m, P * f:P * f + P] for f in range(4)], b["qiT"][:, :, t]), ([b["kv"][:, m, 0:S_D]], b["kT"][:, t]),
                         ([b["ki2"][:, m, :]], b["ki2T"][:, t])]
            to_feature_major(k, jobs, "sparse")
            with k.room():
                select_keys(k, b, const)

            def scores_of(pe, unit, out):
                m, h = unit
                return pe.matmul(out, b["qT"][:, h, m * P:m * P + P], b["kT"][:, :], start=True, stop=True)

            def store(dve, u, bank):
                m, h = u
                t = slice(m * P, m * P + P)
                k.dve.step(dve.tensor_copy(mixT[0][:, h, t], bank))
                k.dve.settle(dve)
                return dve.tensor_tensor(mixT[1][:, h, t], bank, mixT[0][:, h, t].bitcast(F32), ALU.subtract)

            with k.room():
                attention(k, [(m, h) for m in range(2) for h in range(S_H)], T, scores_of,
                          lambda u, c: b["kv"][:, c, S_D:2 * S_D], S_D ** -0.5, lambda u: b["bias"][:, u[0], :], store, "sparse")
        project_out(k, mixT, T, to_residual(k), "sparse")


PAIR = 2
STREAM = P_N // PAIR
ROUND = SLOTS
ROUNDS = STREAM // ROUND // 2
STEPS = ROUND * PAIR
HALF_J = P_N // 2
GROUP = 4
SMALL = 17 * T
QUART = PART // P


def peer_source(k, layer, side, j):
    if side == "u":
        return k.d["peer_uT"][layer, bass.ds(j, PAIR)].rearrange("j p k i -> p j (k i)")
    return k.d["peer_v_2"][layer].rearrange("(i j) d -> i j d", j=P_N)[:, bass.ds(j, PAIR), :]


def peer_queries(k, qT, norm, loads):
    project(k, (k.xh, k.xl), T, [WB] * 4, lambda b: [("feature", [(0, P), (P, 2 * P)])],
            lambda name, eng, b, i, bank: copy(name, eng, qT[:, 2 * b:2 * b + 2, :], bank[:, :].rearrange("p (h t) -> p h t", h=2)),
            lambda b, i: "dve", norm=norm, loads=loads)


class Peer:

    def __init__(self, k, layer, hidden, qT, keys, iota, iota16):
        self.k, self.layer, self.hidden, self.qT, self.keys, self.iota, self.iota16 = k, layer, hidden, qT, keys, iota, iota16
        self.o = HALF_J * T
        self.s = self.scratch(2 * 16 * P_N).rearrange("p (m i n) -> p m i n", m=2, i=16)
        self.v16 = self.scratch(512).rearrange("p (m i n) -> p m i n", m=2, i=16)
        self.i16 = self.scratch(512).bitcast(U32).rearrange("p (m i n) -> p m i n", m=2, i=16)
        self.i16f = self.scratch(512).rearrange("p (m i n) -> p m i n", m=2, i=16)
        self.cand = self.scratch(2 * P_H * 256).rearrange("p (m i n) -> p m i n", m=2, i=P_H)
        self.best = self.scratch(256).rearrange("p (m i n) -> p m i n", m=2, i=P_H)
        self.pos = self.scratch(256).bitcast(U32).rearrange("p (m i n) -> p m i n", m=2, i=P_H)
        self.half = self.scratch(512).bitcast(U32).rearrange("p (m s n) -> p m s n", m=2, s=2)
        self.halff = self.scratch(512).rearrange("p (m s n) -> p m s n", m=2, s=2)
        self.pick = self.scratch(P * 16).rearrange("p (i n) -> p i n", n=16)
        self.sums = self.scratch(16).rearrange("p (m n) -> p m n", m=2)
        self.row_of, self.col_of = (self.scratch(256).rearrange("p (m n) -> p m n", m=2) for _ in range(2))
        self.gate = self.scratch(256).rearrange("p (m i n) -> p m i n", m=2, i=P_H)
        self.rest = self.scratch(256)
        at = 0

        def small(*shape):
            nonlocal at
            n = int(np.prod(shape))
            at += n
            return k.small[:, at - n:at]

        fold = lambda view, names, **sizes: view.rearrange("p (" + names + ") -> p " + names, **sizes)
        self.left = fold(small(2, GROUP, P), "g t i", g=2, t=GROUP)
        self.right = fold(small(2, GROUP, 3, HALF_J), "g t q j", g=2, t=GROUP, q=3)
        self.hot = fold(small(GROUP, HALF_J), "t j", t=GROUP)
        self.rowT, self.colT = small(T), small(T)
        self.gateT = fold(small(T, 3), "t q", q=3)
        self.zero = small(T)
        self.hh = k.sb("hidden_hi", [P, 2, T], F32R)
        self.hl = k.sb("hidden_lo", [P, 2, T], F32R)
        self.scored, self.copied, self.shifted, self.exped, self.picked, self.turned, self.ready, self.dense, self.applied, \
            self.stored, self.hh_ready, self.hl_ready, self.hot_ready, self.summed = (k.sem(f"peer_{n}{layer}") for n in (
                "scored", "scores_copied", "shifted", "exped", "picked", "picks_turned", "onehots_ready", "gates_dense",
                "gates_applied", "up_stored", "hidden_hi_ready", "hidden_lo_ready", "column_onehots", "down_summed"))

    def scratch(self, n):
        self.o += n
        assert self.o <= P_N * T
        return self.hidden[:, self.o - n:self.o]

    def begin(self):
        k = self.k
        k.begin()
        self.b0, self.h0 = k.taken, k.nparts
        assert k.fed == self.b0 + SLOTS, "the ring is full of the first slots"
        k.taken += 2 * STREAM
        k.nparts += 2 * STREAM * PARTS
        k.free_at += [(k.lo_ready, self.h0 + PARTS * (b + 1)) for b in range(2 * STREAM)]

    def high(self, act, r, s, q):
        k = self.k
        slot = (self.b0 + s) % SLOTS
        if q == 0:
            act.wait_ge(k.landed[slot], r * 16 + 16 * ((self.b0 + s) // SLOTS + 1))
        act.wait_ge(k.consumed, r * (ROUND * PARTS) + (self.h0 + s * PARTS + q - PARTS + 1))
        act.activation(k.hi[q][:, :], k.ring[slot][:, q * PART:q * PART + PART], ACT.Copy).then_inc(k.hi_ready, 1)

    def low(self, eng, r, s, q):
        k = self.k
        slot = (self.b0 + s) % SLOTS
        eng.wait_ge(k.hi_ready, r * (ROUND * PARTS) + (self.h0 + s * PARTS + q + 1))
        eng.tensor_tensor(k.lo[q][:, :], k.ring[slot][:, q * PART:q * PART + PART], k.hi[q][:, :].bitcast(F32),
                          ALU.subtract).then_inc(k.lo_ready, 1)

    def wait_parts(self, pe, r, s, q):
        k = self.k
        pe.wait_ge(k.hi_ready, r * (ROUND * PARTS) + (self.h0 + s * PARTS + q + 1))
        pe.wait_ge(k.lo_ready, r * (ROUND * PARTS) + (self.h0 + s * PARTS + q + 1))

    def scores(self, pe):
        for n in range(8):
            m, g, side = n // 4, (n // 2) % 2, n % 2
            r = slice(64 * side, 64 * side + 64)
            for j in range(4):
                h = 4 * g + j
                mm = pe.matmul(self.k.bank[n][:, j * P:j * P + P], self.qT[r, h, m * P:m * P + P], self.keys[r, h, :], start=True, stop=True)
            mm.then_inc(self.scored, 1)

    def up_column(self, pe, r, s, j):
        k = self.k
        if j == 0:
            pe.wait_ge(self.stored, r * ROUND + (s + 1))
        for q in (2 * j, 2 * j + 1):
            self.wait_parts(pe, r, s, q)
            for c in range(QUART):
                cc = (q % 2) * QUART + c
                w = slice(c * P, c * P + P)
                for n, (a, b) in enumerate(((k.hi, k.xh), (k.hi, k.xl), (k.lo, k.xh))):
                    mm = pe.matmul(k.bank[s][:, j * T:j * T + T], a[q][:, w], b[:, cc, :], start=(cc == 0 and n == 0),
                                   stop=(cc == KC - 1 and n == 2))
            mm.then_inc(k.consumed, 1)

    def down_column(self, pe, r, s, j):
        k = self.k
        count = r * STEPS + (s * PAIR + j + 1 - P_N)
        pe.wait_ge(self.hh_ready, count)
        pe.wait_ge(self.hl_ready, count)
        for q in (2 * j, 2 * j + 1):
            self.wait_parts(pe, r, s, q)
            for c in range(QUART):
                cc = (q % 2) * QUART + c
                w = slice(c * P, c * P + P)
                out = k.bank[cc // 2][:, (cc % 2) * T:(cc % 2) * T + T]
                for a, b in ((k.hi, self.hh), (k.hi, self.hl), (k.lo, self.hh)):
                    mm = pe.matmul(out, a[q][:, w], b[:, j, :], start=False, stop=False, skip_group_check=True)
            mm.then_inc(k.consumed, 1)

    def dense_gates(self, pe, r, n):
        k = self.k
        g = n % 2
        pe.wait_ge(self.ready, r * STEPS + (n + 1 - HALF_J))
        for t in range(GROUP):
            for part in range(3):
                mm = pe.matmul(k.bank[4 + g][:, t * HALF_J:(t + 1) * HALF_J], self.left[:, g, t, :], self.right[:, g, t, part, :],
                               start=(t == 0 and part == 0), stop=(t == GROUP - 1 and part == 2), skip_group_check=True)
        mm.then_inc(self.dense, 1)

    def turn_picks(self, pe):
        k = self.k
        pe.wait_ge(self.picked, 1)
        for i, x in enumerate((self.row_of, self.col_of)):
            for m in range(2):
                pe.transpose(k.bank[6][:, i * T + m * P:i * T + m * P + P], x[:, m, :], k.ident[:, :])
        for m in range(2):
            mm = pe.transpose(k.bank[7][:, m * P:m * P + P], self.gate[:, m, :, :].rearrange("p h n -> p (h n)"), k.ident[:, :])
        mm.then_inc(self.turned, 1)

    def zeros(self, pe, start):
        for q in range(4):
            for c in range(2):
                mm = pe.matmul(self.k.bank[q][:, c * T:c * T + T], self.zero[:, 0:P], self.zero[:, :],
                               start=start and c == 0, stop=not start and c == 1, skip_group_check=True)
        return mm

    def tensor(self, pe):
        self.scores(pe)
        pe.wait_ge(self.copied, 4)
        with pe.Fori(0, ROUNDS - 1) as r:
            for n in range(STEPS):
                self.up_column(pe, r, n // PAIR, n % PAIR)
        for n in range(STEPS):
            self.up_column(pe, ROUNDS - 1, n // PAIR, n % PAIR)
            if n == STEPS - 3:
                self.turn_picks(pe)
        with pe.Fori(0, ROUNDS) as r:
            for n in range(STEPS):
                self.dense_gates(pe, r + ROUNDS, n)
                self.up_column(pe, r + ROUNDS, n // PAIR, n % PAIR)
        pe.wait_ge(self.stored, ROUND + STREAM)
        self.zeros(pe, True)
        with pe.Fori(0, ROUNDS) as r:
            for n in range(STEPS):
                self.dense_gates(pe, r + 2 * ROUNDS, n)
                self.down_column(pe, r + 2 * ROUNDS, n // PAIR, n % PAIR)
        with pe.Fori(0, ROUNDS) as r:
            for n in range(STEPS):
                self.down_column(pe, r + 3 * ROUNDS, n // PAIR, n % PAIR)
        self.zeros(pe, False).then_inc(self.summed, 1)

    def up_slot(self, act, r, s):
        for q in range(PARTS):
            self.high(act, r + (s + 1) // ROUND, (s + 1) % ROUND, q)
        act.wait_ge(self.k.consumed, r * (ROUND * PARTS) + (self.h0 + PARTS * (s + 1)))
        act.activation(self.hidden[:, bass.ds(r * (STEPS * T) + s * PAIR * T, PAIR * T)], self.k.bank[s][:, :],
                       ACT.Gelu).then_inc(self.stored, 1)

    def hidden_high(self, act, r, n):
        act.wait_ge(self.k.consumed, r * (ROUND * PARTS) + (self.h0 + (n - 1) * 2))
        act.activation(self.hh[:, n % 2, :], self.hidden[:, bass.ds(r * (STEPS * T) + (n * T - P_N * T), T)],
                       ACT.Copy).then_inc(self.hh_ready, 1)

    def down_slot(self, act, r, s, gates, last=False):
        for j in range(PAIR):
            n = s * PAIR + j
            if gates:
                act.wait_ge(self.applied, r * STEPS + (n + 1 - HALF_J))
            if not (last and j == PAIR - 1):
                self.hidden_high(act, r, n + 1)
            if not last:
                for q in (2 * j, 2 * j + 1):
                    self.high(act, r + (s + 1) // ROUND, (s + 1) % ROUND, q)

    def scalar(self, act):
        k = self.k
        for q in range(PARTS):
            self.high(act, 0, 0, q)
        for n in range(8):
            m, g, side = n // 4, (n // 2) % 2, n % 2
            act.wait_ge(self.scored, n + 1)
            dst = self.s[:, m, :, :].rearrange("p (h c) n -> p h c n", c=2)[:, 4 * g:4 * g + 4, side, :]
            act.activation(dst, k.bank[n][:, :].rearrange("p (h n) -> p h n", h=4), ACT.Copy).then_inc(self.copied if n < 4 else self.stored, 1)
        with act.Fori(0, ROUNDS - 1) as r:
            for s in range(ROUND):
                self.up_slot(act, r, s)
        act.wait_ge(self.shifted, 2)
        act.activation(self.gate, self.gate, ACT.Exp).then_inc(self.exped, 1)
        for s in range(ROUND):
            self.up_slot(act, ROUNDS - 1, s)
        with act.Fori(0, ROUNDS) as r:
            for s in range(ROUND):
                self.up_slot(act, r + ROUNDS, s)
        act.wait_ge(self.applied, HALF_J)
        self.hidden_high(act, 2 * ROUNDS, 0)
        with act.Fori(0, ROUNDS) as r:
            for s in range(ROUND):
                self.down_slot(act, r + 2 * ROUNDS, s, True)
        with act.Fori(0, ROUNDS - 1) as r:
            for s in range(ROUND):
                self.down_slot(act, r + 3 * ROUNDS, s, False)
        for s in range(ROUND):
            self.down_slot(act, 4 * ROUNDS - 1, s, False, s == ROUND - 1)

    def select(self, dve):
        k, S = self.k, self.k.dve
        s, v16, i16, i16f, cand, best, pos, half, halff, pick, gate = (
            self.s, self.v16, self.i16, self.i16f, self.cand, self.best, self.pos, self.half, self.halff, self.pick, self.gate)

        def top16(rows, values, indices):
            for i, x in enumerate(rows):
                S.step(dve.max(values(i)[:, 0:8], x))
            S.settle(dve)
            for i, x in enumerate(rows):
                S.step(dve.max_index(indices(i)[:, 0:8], values(i)[:, 0:8], x))
            S.settle(dve)
            for i, x in enumerate(rows):
                S.step(dve.match_replace(x, values(i)[:, 0:8], x, GONE))
            S.settle(dve)
            for i, x in enumerate(rows):
                S.step(dve.max(values(i)[:, 8:16], x))
            S.settle(dve)
            for i, x in enumerate(rows):
                S.step(dve.max_index(indices(i)[:, 8:16], values(i)[:, 8:16], x))

        for m in range(2):
            dve.wait_ge(self.stored if m else self.copied, 4)
            top16([s[:, m, i, :] for i in range(16)], lambda i: v16[:, m, i, :], lambda i: i16[:, m, i, :])
            S.settle(dve)
            S.step(dve.tensor_copy(i16f[:, m, :, :], i16[:, m, :, :]))
            vv = v16[:, m, :, :].rearrange("p (h c) n -> p h c n", c=2)
            S.step(dve.tensor_tensor(cand[:, m, :, :].rearrange("p h (a b) -> p h a b", a=16),
                                     spread(vv[:, :, 0, :], 3, 16), spread(vv[:, :, 1, :], 2, 16), ALU.add))
            S.settle(dve)
            top16([cand[:, m, h, :] for h in range(P_H)], lambda i: best[:, m, i, :], lambda i: pos[:, m, i, :])
            S.settle(dve)
            dve.tensor_tensor(gate[:, m, :, :], best[:, m, :, :], spread(best[:, m, :, 0], 2, 16), ALU.subtract).then_inc(self.shifted, 1)
            p = pos[:, m, :, :].rearrange("p h n -> p (h n)")
            S.step(dve.tensor_single_scalar(half[:, m, 0, :], p, 4, ALU.logical_shift_right))
            S.step(dve.tensor_single_scalar(half[:, m, 1, :], p, 15, ALU.bitwise_and))
            S.settle(dve)
            S.step(dve.tensor_copy(halff[:, m, :, :], half[:, m, :, :]))
            S.settle(dve)
            ii = i16f[:, m, :, :].rearrange("p (h c) n -> p h c n", c=2)
            for side, out in ((0, self.row_of), (1, self.col_of)):
                S.step(dve.tensor_tensor(pick, spread(halff[:, m, side, :], 2, 16), spread(self.iota16, 1, P_H * 16), ALU.is_equal))
                S.settle(dve)
                p4 = pick.rearrange("p (h n) a -> p h n a", h=P_H)
                S.step(dve.tensor_tensor(p4, p4, spread(ii[:, :, side, :], 2, 16), ALU.mult))
                S.settle(dve)
                S.step(dve.tensor_reduce(out[:, m, :], pick, AX_X, ALU.add))
                S.settle(dve)
        dve.wait_ge(self.exped, 1)
        S.step(dve.tensor_reduce(self.sums, gate, AX_X, ALU.add))
        S.settle(dve)
        S.step(dve.reciprocal(self.sums, self.sums))
        S.settle(dve)
        dve.tensor_tensor(gate, gate, spread(self.sums, 3, 16), ALU.mult).then_inc(self.picked, 1)

    def split_gates(self, dve):
        k, S = self.k, self.k.dve
        dve.wait_ge(self.turned, 1)
        S.step(dve.tensor_copy(self.rowT[:, :], k.bank[6][:, 0:T]))
        S.step(dve.tensor_copy(self.colT[:, :], k.bank[6][:, T:2 * T]))
        S.step(dve.tensor_copy(self.gateT[:, :, 0], k.bank[7][:, 0:T]))
        S.settle(dve)
        S.step(dve.tensor_tensor(self.rest, k.bank[7][:, 0:T], self.gateT[:, :, 0], ALU.subtract))
        S.settle(dve)
        S.step(dve.tensor_copy(self.gateT[:, :, 1], self.rest))
        S.settle(dve)
        S.step(dve.tensor_tensor(self.gateT[:, :, 2], self.rest, self.gateT[:, :, 1], ALU.subtract))
        S.settle(dve)

    def onehots(self, dve, phase, r, n):
        g = n % 2
        at = bass.ds(r * (STEPS * GROUP) + n * GROUP, GROUP)
        j = self.iota[:, phase * HALF_J:(phase + 1) * HALF_J]
        dve.tensor_tensor(self.hot[:, :, :], spread(j, 1, GROUP), spread(self.colT[:, at], 2, HALF_J), ALU.is_equal).then_inc(self.hot_ready, 1)
        dve.tensor_tensor(self.left[:, g, :, :], spread(self.iota, 1, GROUP), spread(self.rowT[:, at], 2, P), ALU.is_equal)
        dve.wait_ge(self.hot_ready, r * STEPS + (phase * HALF_J + n + 1))
        dve.tensor_tensor(self.right[:, g, :, :, :], spread(self.hot[:, :, :], 2, 3), spread(self.gateT[:, at, :], 3, HALF_J),
                          ALU.mult).then_inc(self.ready, 1)

    def apply(self, dve, phase, r, n):
        dve.wait_ge(self.dense, r * STEPS + (phase * HALF_J + n + 1))
        h = self.hidden.rearrange("p (j t) -> p j t", t=T)[:, phase * HALF_J:(phase + 1) * HALF_J, bass.ds(r * (STEPS * GROUP) + n * GROUP, GROUP)]
        gates = self.k.bank[4 + n % 2][:, 0:GROUP * HALF_J].rearrange("p (t j) -> p j t", t=GROUP)
        dve.tensor_tensor(h, h, gates, ALU.mult).then_inc(self.applied, 1)

    def hidden_low(self, dve, r, n):
        dve.wait_ge(self.hh_ready, r * STEPS + (n + 1))
        dve.tensor_tensor(self.hl[:, n % 2, :], self.hidden[:, bass.ds(r * (STEPS * T) + n * T, T)], self.hh[:, n % 2, :].bitcast(F32),
                          ALU.subtract).then_inc(self.hl_ready, 1)

    def vector(self, dve):
        k = self.k
        k.dve.step(dve.memset(self.zero[:, :], 0.0))
        self.select(dve)
        self.split_gates(dve)
        self.onehots(dve, 0, 0, 0)
        dve.wait_ge(self.stored, ROUND + STREAM // 2)
        with dve.Fori(0, ROUNDS - 1) as r:
            for n in range(STEPS):
                self.apply(dve, 0, r, n)
                self.onehots(dve, 0, r, n + 1)
        for n in range(STEPS):
            self.apply(dve, 0, ROUNDS - 1, n)
            if n < STEPS - 1:
                self.onehots(dve, 0, ROUNDS - 1, n + 1)
        self.onehots(dve, 1, 0, 0)
        self.hidden_low(dve, 0, 0)
        with dve.Fori(0, ROUNDS - 1) as r:
            for n in range(STEPS):
                self.apply(dve, 1, r, n)
                self.onehots(dve, 1, r, n + 1)
                self.hidden_low(dve, r, n + 1)
        for n in range(STEPS):
            self.apply(dve, 1, ROUNDS - 1, n)
            if n < STEPS - 1:
                self.onehots(dve, 1, ROUNDS - 1, n + 1)
            self.hidden_low(dve, ROUNDS - 1, n + 1)
        with dve.Fori(0, ROUNDS - 1) as r:
            for n in range(STEPS):
                self.hidden_low(dve, r + ROUNDS, n + 1)
        for n in range(STEPS - 1):
            self.hidden_low(dve, 2 * ROUNDS - 1, n + 1)
        y = k.y
        for q in range(KC // 2):
            at = slice(2 * q, 2 * q + 2)
            k.dve.step(dve.tensor_tensor(y[:, at, :], k.xh[:, at, :].bitcast(F32), k.xl[:, at, :].bitcast(F32), ALU.add))
        k.dve.settle(dve)
        dve.wait_ge(self.summed, 1)
        for q in range(KC // 2):
            at = slice(2 * q, 2 * q + 2)
            k.dve.step(dve.scalar_tensor_tensor(out=y[:, at, :], in0=y[:, at, :], scalar=DN_ALPHA,
                                                in1=k.bank[q][:, :].rearrange("p (c t) -> p c t", c=2), op0=ALU.mult, op1=ALU.add))

    def gpsimd(self, pool):
        with pool.Fori(0, 4 * ROUNDS) as r:
            for s in range(ROUND):
                for q in range(PARTS):
                    self.low(pool, r, s, q)

    def load_slot(self, sync, side, r, s, j):
        k = self.k
        slot = (self.b0 + s) % SLOTS
        sync.wait_ge(k.lo_ready, r * (ROUND * PARTS) + (self.h0 + PARTS * (s + 1) - ROUND * PARTS))
        sync.dma_start(k.ring[slot][:, :].rearrange("p (j n) -> p j n", j=PAIR), peer_source(k, self.layer, side, j)).then_inc(k.landed[slot], 16)

    def sync(self, sync):
        with sync.Fori(0, 2 * ROUNDS - 1) as r:
            for s in range(ROUND):
                self.load_slot(sync, "u", r + 1, s, r * STEPS + (STEPS + PAIR * s))
        with sync.Fori(0, 2 * ROUNDS) as r:
            for s in range(ROUND):
                self.load_slot(sync, "v", r + 2 * ROUNDS, s, r * STEPS + PAIR * s)
        self.k.fed += 2 * STREAM - SLOTS
        self.k.feed(sync, 2 * STREAM)


def peer_layer(k, layer):
    nc, d = k.nc, k.d
    c = lambda name: d["const"][:, CONST_AT[name][0]:CONST_AT[name][0] + CONST_AT[name][1]]
    with k.room():
        iota = k.sb("iota", [P, P])
        iota16 = k.sb("iota16", [P, 16])
        hidden = k.sb("hidden", [P, P_N * T])
        view = lambda o, n, t=T: hidden[:, o * t:(o + n) * t].rearrange("p (a b) -> p a b", a=n)
        qT, keys = view(0, P_H), view(2 * P_H, P_H, P_N)
        norm = LayerNorm(k, ("mix_g", 8 * layer), ("mix_b", 8 * layer), f"mix{layer}", view(HALF_J, KC + 2))
        peer_queries(k, qT, norm, [(iota[:, :], c("iota")), (iota16[:, :], c("iota16")), (keys, d["sub_keysT"][:, layer])])
        peer = Peer(k, layer, hidden, qT, keys, iota[:, :], iota16[:, :])
        with nc.Block() as block:
            peer.begin()

            @block.tensor
            def _(pe):
                peer.tensor(pe)

            @block.scalar
            def _(act):
                peer.scalar(act)

            @block.vector
            def _(dve):
                peer.vector(dve)

            @block.gpsimd
            def _(pool):
                peer.gpsimd(pool)

            @block.sync
            def _(sync):
                peer.sync(sync)


def plan_peer(k, layer):
    plan_columns(k, k.d["peer_w_q_2"][layer], 0, D)
    for side in ("u", "v"):
        k.plan += [(peer_source(k, layer, side, PAIR * s), SLOT) for s in range(STREAM)]


def plan_second(k):
    d = k.d
    w, o = d["even_w_in_2"], 0
    for n in GLA_BLOCKS + RWKV_BLOCKS:
        plan_columns(k, w, o, o + n)
        o += n
    plan_columns(k, d["even_w_out_2"], 0, D)
    plan_peer(k, 0)
    o = 0
    for n in DSA_BLOCKS:
        plan_columns(k, d["odd_w_in_2"], o, o + n)
        o += n
    plan_columns(k, d["odd_w_out_2"], 0, D)
    plan_peer(k, 1)


def second_block(k, out):
    nc = k.nc
    k.small = k.sb("small", [P, SMALL], BF16)
    k.small_f32 = k.small.bitcast(F32)
    k.y = k.small_f32[:, 0:KC * T].rearrange("p (c t) -> p c t", c=KC)
    recurrent_layer(k)
    peer_layer(k, 0)
    sparse_layer(k)
    peer_layer(k, 1)
    norm = LayerNorm(k, ("ffn_g", 8), ("ffn_b", 8), "ffn1", k.sb("ln_work", [P, KC + 2, T]))
    stored = k.sem("out_stored")
    with nc.Block() as block:
        k.begin()

        @block.tensor
        def _(pe):
            norm.tensor(pe)

        @block.scalar
        def _(act):
            norm.squares(act)
            norm.final(act)

        @block.vector
        def _(dve):
            norm.vector(dve, final=True)

        @block.sync
        def _(sync):
            for c in range(0, KC, 2):
                sync.wait_ge(norm.rounded, c + 2)
                sync.dma_start(out.rearrange("(k p) t -> p k t", p=P)[:, c:c + 2, :], norm.work[:, c:c + 2, :]).then_inc(stored, 16)
            sync.wait_ge(stored, 16 * (KC // 2))




def plan_weights(k):
    d = k.d
    for layer in range(2):
        plan_columns(k, d["ada_w"][layer], 0, 3 * D)
    plan_columns(k, d["even_w_in"], 0, 7 * A_W)
    plan_columns(k, d["even_w_out"], 0, D)
    plan_columns(k, d["odd_w_in"], 0, C_Q)
    plan_columns(k, d["odd_w_in"], C_Q, C_Q + C_KV + C_R)
    plan_columns(k, d["odd_w_in"], C_Q + C_KV + C_R, C_Q + C_KV + C_R + D)
    for g in range(2):
        k.plan.append((d["c_wq_b"].rearrange("(k p) n -> p k n", p=P)[:, :, 768 * g:768 * g + 768], 2 * 768))
    k.plan.append((d["c_wkv_b"], SLOT))
    plan_columns(k, d["odd_w_out"], 0, D)
    plan_second(k)


def program(nc, d, out):
    with ExitStack() as ctx:
        k = Core(nc, ctx, d)
        plan_weights(k)
        k.xh, k.xl = k.sb("x_hi", [P, KC, T], F32R), k.sb("x_lo", [P, KC, T], F32R)
        with k.room():
            setup(k)
            first_block(k)
        second_block(k, out)


INPUTS = ["ada_w", "even_w_in", "even_w_out", "odd_w_in", "c_wq_b", "c_wkv_b", "odd_w_out", "even_w_in_2",
          "gla_a_w2_2", "rwkv_w2_2", "rwkv_a2_2", "rwkv_g2_2", "even_w_out_2", "odd_w_in_2", "odd_w_out_2",
          "peer_w_q_2", "peer_v_2"]


def columns(v):
    return np.asarray(v).reshape(-1, P).T


def lay_out(inputs):
    a = {n: np.ascontiguousarray(inputs[n]) for n in INPUTS}
    for n in INPUTS:
        if a[n].ndim == 3 and a[n].shape[0] == 1:
            a[n] = a[n][0]
    f = {n: np.asarray(v) for n, v in inputs.items()}
    a["xT"] = np.ascontiguousarray(f["x"][0].T)
    a["ctxT"] = np.ascontiguousarray(f["ctx"][0].T)
    a["a_wsT"] = np.ascontiguousarray(f["a_ws"][0].transpose(2, 0, 1))
    cond = np.stack([columns(f["c"][0]), columns(f["c_ctx"])], -1).reshape(P, 16)
    mu = f["rwkv_mu_2"][0]
    pack = {"norm_w": columns(f["norm_w"]), "ada_b": columns(f["ada_b"]), "final_w": columns(f["final_w"]),
            "mix_g": columns(f["mix_ln_g_2"]), "mix_b": columns(f["mix_ln_b_2"]), "ffn_g": columns(f["ffn_ln_g_2"]),
            "ffn_b": columns(f["ffn_ln_b_2"]), "mu_rkv": columns(mu[:1536]), "w0": columns(f["rwkv_w0_2"]),
            "a0": columns(f["rwkv_a0_2"]), "k_k": columns(f["rwkv_k_k_2"]), "k_a": columns(f["rwkv_k_a_2"]),
            "r_k": columns(f["rwkv_r_k_2"]), "gla_a_b": columns(f["gla_a_b_2"]), "a_bs": f["a_bs"][0].T, "cond": cond}
    a["cols"] = np.ascontiguousarray(np.concatenate([pack[n] for n, _ in COLS], 1))
    a["mu_lora"] = np.ascontiguousarray(mu[1536:].reshape(-1, 1))
    pack = {"a_ln_w": f["a_ln_w"], "a_ln_b": f["a_ln_b"], "subln_w": f["b_subln_w"], "lq1": f["b_lq1"], "lk1": f["b_lk1"],
            "lq2": f["b_lq2"], "lk2": f["b_lk2"], "q_norm": f["c_q_norm_w"], "kv_norm": f["c_kv_norm_w"],
            "gla_g": f["gla_norm_g_2"], "lnx_g": f["rwkv_lnx_g_2"], "lnx_b": f["rwkv_lnx_b_2"]}
    a["rows"] = np.ascontiguousarray(np.concatenate([pack[n].reshape(-1) for n, _ in ROWS]))
    a["sub_keysT"] = np.ascontiguousarray(f["peer_sub_keys_2"].transpose(2, 4, 0, 1, 3).reshape(P, 2, P_H, P_N))
    a["peer_uT"] = np.ascontiguousarray(f["peer_u_2"].reshape(2, P_N, P_N, KC, P).transpose(0, 2, 4, 3, 1))
    a["const"], a["mask"] = CONST, MASK
    return a


def kernel(**inputs):
    import concourse.bacc as bacc
    from concourse.bass_utils import run_bass_kernel_spmd

    nc = bacc.Bacc("TRN2", target_bir_lowering=False, num_devices=1)
    arrays = {f"in_{n}": a for n, a in lay_out(inputs).items()}
    d = {n[3:]: nc.dram_tensor(n, a.shape, mybir.dt.from_np(a.dtype), kind="ExternalInput").ap() for n, a in arrays.items()}
    out = nc.dram_tensor("out_T", (D, T), F32, kind="ExternalOutput").ap()
    program(nc, d, out)
    r = run_bass_kernel_spmd(nc, [arrays], core_ids=[0])
    return np.ascontiguousarray(r.results[0]["out_T"].T).reshape(1, T, D)
```
